# Optimizing a Trainium2 kernel written in Bass

```python
import jax, jax.numpy as jnp
from jax import lax
import numpy as np

D_MODEL = 1024
BATCH = 1
SEQ = 1024
DEPTH = 1
DEC_BATCH = 8
DEC_SEQ = 8
PAST_LEN = 1024
PAGE_SIZE = 128

HEAD_DIM = 64
H_A = 6
A_PATTERNS = ((128, 1), (512, 4), (2048, 16))
A_WINDOW = 2048
H_B = 4
DK_B = 64
DV_B = 64
B_CHUNK = 16
H_C = 6
G_C = 2
R_C = H_C // G_C
CMP_BLK = 32
CMP_STRIDE = 16
SLC_BLK = 64
SLC_TOPK = 16
C_WINDOW = 512
N_GROUPS = 4
EXPERTS_PER_GROUP = 4
N_EXPERTS = N_GROUPS * EXPERTS_PER_GROUP
D_EXPERT = 256
TOPK_INNER = 2

BLOCK_Q = 128
EPS = 1e-6
NEG = -1e30
TINY = 1e-30
FORCE_SCORE = 1e4
SCALE = HEAD_DIM ** -0.5
A_W = H_A * HEAD_DIM
B_KW = H_B * DK_B
B_VW = H_B * DV_B
C_QW = H_C * HEAD_DIM
C_KW = G_C * HEAD_DIM
IN_WIDTHS = (A_W, A_W, A_W, B_KW, B_KW, B_VW, B_VW, C_QW, C_KW, C_KW, C_KW, C_KW, C_KW, C_KW, 3 * H_C)
D_IN = sum(IN_WIDTHS)
SPLIT_IDX = tuple(int(v) for v in np.cumsum(IN_WIDTHS)[:-1])
D_MIX = A_W + B_VW + C_QW

kernel_name = 'hybrid_dilated_hgrn2_nsa_hmoe_step'

def rms_norm(x, g):
    x32 = x.astype(jnp.float32)
    y = x32 * lax.rsqrt(jnp.mean(x32 * x32, axis=-1, keepdims=True) + EPS)
    return (y * g.astype(jnp.float32)).astype(x.dtype)

def masked_softmax(s, mask):
    s = jnp.where(mask, s.astype(jnp.float32), NEG)
    m = jnp.max(s, axis=-1, keepdims=True)
    e = jnp.where(mask, jnp.exp(s - m), 0.0)
    l = jnp.sum(e, axis=-1, keepdims=True)
    l_safe = jnp.maximum(l, TINY)
    p = e / l_safe
    return p, (m + jnp.log(l_safe))[..., 0]

def banded_attention(q, k, v, window):
    B, L, G, R, Dh = q.shape
    blk = BLOCK_Q
    nb = -(-L // blk)
    nback = -(-window // blk)
    Lp = nb * blk
    qb = jnp.pad(q, ((0, 0), (0, Lp - L), (0, 0), (0, 0), (0, 0))).reshape(B, nb, blk, G, R, Dh)
    kv_pad = ((0, 0), (nback * blk, Lp - L), (0, 0), (0, 0))
    kb = jnp.pad(k, kv_pad).reshape(B, nb + nback, blk, G, Dh)
    vb = jnp.pad(v, kv_pad).reshape(B, nb + nback, blk, G, Dh)
    keys = jnp.concatenate([kb[:, j:j + nb] for j in range(nback + 1)], axis=2)
    vals = jnp.concatenate([vb[:, j:j + nb] for j in range(nback + 1)], axis=2)
    s = jnp.einsum('bnqgrd,bnkgd->bngrqk', qb, keys) * SCALE
    qpos = jnp.arange(nb)[:, None] * blk + jnp.arange(blk)[None, :]
    kpos = (jnp.arange(nb)[:, None] - nback) * blk + jnp.arange((nback + 1) * blk)[None, :]
    dist = qpos[:, :, None] - kpos[:, None, :]
    mask = (dist >= 0) & (dist <= window) & (kpos[:, None, :] >= 0)
    p, lse = masked_softmax(s, mask[None, :, None, None])
    o = jnp.einsum('bngrqk,bnkgd->bnqgrd', p.astype(vals.dtype), vals).reshape(B, Lp, G, R, Dh)[:, :L]
    lse = lse.transpose(0, 1, 4, 2, 3).reshape(B, Lp, G, R)[:, :L]
    return o, lse

def combine_by_denominators(outs, lses):
    w = jax.nn.softmax(jnp.stack(lses, 0), axis=0)
    return sum(w[i][..., None] * outs[i].astype(jnp.float32) for i in range(len(outs)))

def dilated_attention_prompt(q, k, v):
    B, S, H, Dh = q.shape
    outs, lses = [], []
    for window, dil in A_PATTERNS:
        L = S // dil
        def sub(t):
            return t.reshape(B, L, dil, H, Dh).transpose(0, 2, 1, 3, 4).reshape(B * dil, L, H, Dh)
        o, lse = banded_attention(sub(q)[:, :, :, None], sub(k), sub(v), window // dil)
        outs.append(o[:, :, :, 0].reshape(B, dil, L, H, Dh).transpose(0, 2, 1, 3, 4).reshape(B, S, H, Dh))
        lses.append(lse[..., 0].reshape(B, dil, L, H).transpose(0, 2, 1, 3).reshape(B, S, H))
    return combine_by_denominators(outs, lses)

def dilated_attention_sample(q, k_all, v_all, n_buf):
    Ls = q.shape[1]
    outs, lses = [], []
    for window, dil in A_PATTERNS:
        n = window // dil
        idx = n_buf + jnp.arange(Ls)[:, None] - dil * jnp.arange(n + 1)[None, :]
        valid = idx >= 0
        idx = jnp.maximum(idx, 0)
        kg, vg = k_all[:, idx], v_all[:, idx]
        s = jnp.einsum('bqhd,bqjhd->bhqj', q, kg) * SCALE
        p, lse = masked_softmax(s, valid[None, None])
        outs.append(jnp.einsum('bhqj,bqjhd->bqhd', p.astype(vg.dtype), vg))
        lses.append(lse.transpose(0, 2, 1))
    return combine_by_denominators(outs, lses)

def hgrn2_chunked(q, log_f, k, v, s0):
    B, L = q.shape[:2]
    C = B_CHUNK
    Lp = -(-L // C) * C
    N = Lp // C
    pad = ((0, 0), (0, Lp - L), (0, 0), (0, 0))
    q, log_f, k, v = [jnp.pad(t.astype(jnp.float32), pad).reshape(B, N, C, H_B, t.shape[-1]) for t in (q, log_f, k, v)]
    b = jnp.cumsum(log_f, axis=2)
    tri = jnp.tril(jnp.ones((C, C), bool))[None, None, :, :, None, None]
    diff = b[:, :, :, None] - b[:, :, None, :]
    decay = jnp.where(tri, jnp.exp(jnp.where(tri, diff, 0.0)), 0.0)
    attn = jnp.einsum('bnthc,bntshc,bnshc->bnhts', q, decay, k)
    o = jnp.einsum('bnhts,bnshv->bnthv', attn, v)
    b_last = b[:, :, -1]
    q_dec = q * jnp.exp(b)
    k_dec = k * jnp.exp(b_last[:, :, None] - b)

    def step(S, inp):
        qd, kd, vv, bl = inp
        o_int = jnp.einsum('bthc,bhcv->bthv', qd, S)
        S = jnp.exp(bl)[..., None] * S + jnp.einsum('bshc,bshv->bhcv', kd, vv)
        return S, o_int

    s_fin, o_int = lax.scan(step, s0.astype(jnp.float32),
                            (q_dec.swapaxes(0, 1), k_dec.swapaxes(0, 1), v.swapaxes(0, 1), b_last.swapaxes(0, 1)))
    o = o + o_int.swapaxes(0, 1)
    return o.reshape(B, Lp, H_B, DV_B)[:, :L], s_fin

def compress_blocks(k_raw, v_raw, cmp_w, cmp_pe, kn_cmp):
    T = k_raw.shape[1]
    nc = (T - CMP_BLK) // CMP_STRIDE + 1
    idx = jnp.arange(nc)[:, None] * CMP_STRIDE + jnp.arange(CMP_BLK)[None, :]

    def comp(x, w, pe):
        blocks = x[:, idx] + pe[:, None, :]
        return jnp.einsum('bnlgd,lde->bnge', blocks, w.reshape(CMP_BLK, HEAD_DIM, HEAD_DIM))

    kc = rms_norm(comp(k_raw, cmp_w[0], cmp_pe[0]), kn_cmp)
    vc = comp(v_raw, cmp_w[1], cmp_pe[1])
    return kc, vc, jnp.arange(nc) * CMP_STRIDE + CMP_BLK - 1

def to_select_blocks(x):
    B, T = x.shape[:2]
    ns = -(-T // SLC_BLK)
    x = jnp.pad(x, ((0, 0), (0, ns * SLC_BLK - T), (0, 0), (0, 0)))
    return x.reshape(B, ns, SLC_BLK, G_C, HEAD_DIM).transpose(0, 3, 1, 2, 4).reshape(B, G_C, ns, SLC_BLK * HEAD_DIM)

def cmp_to_slc_weights(nc, ns):
    cs = jnp.arange(nc) * CMP_STRIDE
    ss = jnp.arange(ns) * SLC_BLK
    shared = jnp.minimum(cs[:, None] + CMP_BLK - 1, ss[None, :] + SLC_BLK - 1) - jnp.maximum(cs[:, None], ss[None, :]) + 1
    return jnp.maximum(shared, 0).astype(jnp.float32) / CMP_BLK

def nsa_query_block(q, qpos, kc, vc, cend, m, ks_bg, vs_bg):
    B, Q = q.shape[:2]
    s = jnp.einsum('bqgrd,bngd->bgrqn', q, kc) * SCALE
    p_cmp, _ = masked_softmax(s, (cend[None, :] <= qpos[:, None])[None, None, None])
    o_cmp = jnp.einsum('bgrqn,bngd->bqgrd', p_cmp.astype(vc.dtype), vc)
    imp = jnp.einsum('bgrqn,nm->bgqm', p_cmp, m)
    ns = m.shape[1]
    blk = jnp.arange(ns)[None, :]
    cur = (qpos // SLC_BLK)[:, None]
    forced = (blk == 0) | (blk == cur) | (blk == cur - 1)
    score = jnp.where(forced, FORCE_SCORE, jnp.where(blk <= cur, imp, NEG))
    n_sel = min(SLC_TOPK, ns)
    top_v, top_i = lax.top_k(score, n_sel)
    sel_ok = top_v > 0.5 * NEG
    bi = jnp.arange(B)[:, None, None, None]
    gi = jnp.arange(G_C)[None, :, None, None]
    kb = ks_bg[bi, gi, top_i].reshape(B, G_C, Q, n_sel * SLC_BLK, HEAD_DIM)
    vb = vs_bg[bi, gi, top_i].reshape(B, G_C, Q, n_sel * SLC_BLK, HEAD_DIM)
    s2 = jnp.einsum('bqgrd,bgqkd->bgrqk', q, kb) * SCALE
    tok = top_i[..., None] * SLC_BLK + jnp.arange(SLC_BLK)
    mask2 = (tok <= qpos[None, None, :, None, None]) & sel_ok[..., None]
    p2, _ = masked_softmax(s2, mask2.reshape(B, G_C, 1, Q, n_sel * SLC_BLK))
    o_slc = jnp.einsum('bgrqk,bgqkd->bqgrd', p2.astype(vb.dtype), vb)
    return o_cmp, o_slc

def nsa_compressed_selected(q, qpos, kc_raw, vc_raw, ks, vs, kn_cmp, cmp_w, cmp_pe, q_block):
    kc, vc, cend = compress_blocks(kc_raw, vc_raw, cmp_w, cmp_pe, kn_cmp)
    ks_bg, vs_bg = to_select_blocks(ks), to_select_blocks(vs)
    m = cmp_to_slc_weights(kc.shape[1], ks_bg.shape[2])
    B, Lq = q.shape[:2]
    nqb = Lq // q_block
    qb = q.reshape(B, nqb, q_block, G_C, R_C, HEAD_DIM).swapaxes(0, 1)
    pb = qpos.reshape(nqb, q_block)
    o_cmp, o_slc = lax.map(lambda a: nsa_query_block(a[0], a[1], kc, vc, cend, m, ks_bg, vs_bg), (qb, pb))
    unblock = lambda o: o.swapaxes(0, 1).reshape(B, Lq, G_C, R_C, HEAD_DIM)
    return unblock(o_cmp), unblock(o_slc)

def window_attention_sample(q, k_all, v_all, n_buf):
    Ls, Tk = q.shape[1], k_all.shape[1]
    s = jnp.einsum('bqgrd,bkgd->bgrqk', q, k_all) * SCALE
    dist = n_buf + jnp.arange(Ls)[:, None] - jnp.arange(Tk)[None, :]
    p, _ = masked_softmax(s, (dist >= 0) & (dist <= C_WINDOW))
    return jnp.einsum('bgrqk,bkgd->bqgrd', p.astype(v_all.dtype), v_all)

def project(h, lb, w_in_l, a_qn, a_kn, c_qn, c_kn):
    lead = h.shape[:-1]
    pt = jnp.split(h @ w_in_l, SPLIT_IDX, axis=-1)
    hd = lambda t, n: t.reshape(*lead, n, HEAD_DIM)
    a_q, a_k, a_v = rms_norm(hd(pt[0], H_A), a_qn), rms_norm(hd(pt[1], H_A), a_kn), hd(pt[2], H_A)
    b_q = pt[3].reshape(*lead, H_B, DK_B)
    zf = pt[4].reshape(*lead, H_B, DK_B).astype(jnp.float32)
    lb = lb.reshape(H_B, DK_B)
    f = lb + (1.0 - lb) * jax.nn.sigmoid(zf)
    b_logf = jnp.log(jnp.maximum(f, TINY))
    b_k = (1.0 - lb) * jax.nn.sigmoid(-zf)
    b_v = pt[5].reshape(*lead, H_B, DV_B)
    b_g = pt[6].reshape(*lead, H_B, DV_B)
    c_q = rms_norm(pt[7].reshape(*lead, G_C, R_C, HEAD_DIM), c_qn)
    c_kc, c_vc = hd(pt[8], G_C), hd(pt[9], G_C)
    c_ks, c_vs = rms_norm(hd(pt[10], G_C), c_kn[1]), hd(pt[11], G_C)
    c_kw, c_vw = rms_norm(hd(pt[12], G_C), c_kn[2]), hd(pt[13], G_C)
    c_gate = jax.nn.sigmoid(pt[14].astype(jnp.float32)).reshape(*lead, G_C, R_C, 3)
    return a_q, a_k, a_v, b_q, b_logf, b_k, b_v, b_g, c_q, c_kc, c_vc, c_ks, c_vs, c_kw, c_vw, c_gate

def mix_out(o_a, o_b, b_g, b_on, o_cmp, o_slc, o_win, c_gate, w_o_l, dt):
    lead = o_a.shape[:-2]
    ob = rms_norm(o_b.astype(dt), b_on) * jax.nn.silu(b_g)
    oc = c_gate[..., 0:1] * o_cmp + c_gate[..., 1:2] * o_slc + c_gate[..., 2:3] * o_win
    cat = jnp.concatenate([o_a.reshape(*lead, A_W).astype(dt), ob.reshape(*lead, B_VW),
                           oc.reshape(*lead, C_QW).astype(dt)], axis=-1)
    return cat @ w_o_l

def mixer_prompt(h, lb, w_in_l, a_qn, a_kn, b_on, c_qn, c_kn, cmp_w, cmp_pe, w_o_l):
    B, S = h.shape[:2]
    (a_q, a_k, a_v, b_q, b_logf, b_k, b_v, b_g, c_q, c_kc, c_vc, c_ks, c_vs, c_kw, c_vw,
     c_gate) = project(h, lb, w_in_l, a_qn, a_kn, c_qn, c_kn)
    o_a = dilated_attention_prompt(a_q, a_k, a_v)
    o_b, s_b = hgrn2_chunked(b_q, b_logf, b_k, b_v, jnp.zeros((B, H_B, DK_B, DV_B), jnp.float32))
    o_cmp, o_slc = nsa_compressed_selected(c_q, jnp.arange(S), c_kc, c_vc, c_ks, c_vs, c_kn[0], cmp_w, cmp_pe, BLOCK_Q)
    o_win, _ = banded_attention(c_q, c_kw, c_vw, C_WINDOW)
    y = mix_out(o_a, o_b, b_g, b_on, o_cmp, o_slc, o_win, c_gate, w_o_l, h.dtype)
    new_a = jnp.stack([a_k, a_v], axis=2)[:, -A_WINDOW:]
    new_c = jnp.stack([c_kc, c_vc, c_ks, c_vs], axis=2)
    new_w = jnp.stack([c_kw, c_vw], axis=2)[:, -C_WINDOW:]
    return y, new_a, s_b.astype(h.dtype), new_c, new_w

def mixer_sample(h, a_buf, b_state, c_past, c_wbuf, lb, w_in_l, a_qn, a_kn, b_on, c_qn, c_kn, cmp_w, cmp_pe, w_o_l):
    Ls = h.shape[1]
    past = c_past.shape[1]
    (a_q, a_k, a_v, b_q, b_logf, b_k, b_v, b_g, c_q, c_kc, c_vc, c_ks, c_vs, c_kw, c_vw,
     c_gate) = project(h, lb, w_in_l, a_qn, a_kn, c_qn, c_kn)
    n_a = a_buf.shape[1]
    a_all = jnp.concatenate([a_buf, jnp.stack([a_k, a_v], axis=2)], axis=1)
    o_a = dilated_attention_sample(a_q, a_all[:, :, 0], a_all[:, :, 1], n_a)
    o_b, s_b = hgrn2_chunked(b_q, b_logf, b_k, b_v, b_state)
    new_c = jnp.stack([c_kc, c_vc, c_ks, c_vs], axis=2)
    c_all = jnp.concatenate([c_past, new_c], axis=1)
    o_cmp, o_slc = nsa_compressed_selected(c_q, past + jnp.arange(Ls), c_all[:, :, 0], c_all[:, :, 1],
                                           c_all[:, :, 2], c_all[:, :, 3], c_kn[0], cmp_w, cmp_pe, Ls)
    n_w = c_wbuf.shape[1]
    w_all = jnp.concatenate([c_wbuf, jnp.stack([c_kw, c_vw], axis=2)], axis=1)
    o_win = window_attention_sample(c_q, w_all[:, :, 0], w_all[:, :, 1], n_w)
    y = mix_out(o_a, o_b, b_g, b_on, o_cmp, o_slc, o_win, c_gate, w_o_l, h.dtype)
    return y, a_all[:, -n_a:], s_b.astype(h.dtype), new_c, w_all[:, -n_w:]

def hier_moe(h, wg, bg, we, be, w1, w3, w2):
    lead = h.shape[:-1]
    t = h.reshape(-1, D_MODEL)
    g_logit = (t @ wg + bg).astype(jnp.float32)
    g_prob = jax.nn.softmax(g_logit, axis=-1)
    g_idx = jnp.argmax(g_logit, axis=-1)
    g_w = jnp.take_along_axis(g_prob, g_idx[:, None], axis=1)
    e_logit = (t @ we + be).astype(jnp.float32).reshape(-1, N_GROUPS, EXPERTS_PER_GROUP)
    e_logit = jnp.take_along_axis(e_logit, g_idx[:, None, None], axis=1)[:, 0]
    top_v, top_i = lax.top_k(e_logit, TOPK_INNER)
    w = g_w * jax.nn.softmax(top_v, axis=-1)
    eid = g_idx[:, None] * EXPERTS_PER_GROUP + top_i
    comb = jnp.sum(jax.nn.one_hot(eid, N_EXPERTS, dtype=jnp.float32) * w[..., None], axis=1)
    hid = jax.nn.silu(jnp.einsum('td,edf->tef', t, w1)) * jnp.einsum('td,edf->tef', t, w3)
    hid = hid * comb[..., None].astype(hid.dtype)
    return jnp.einsum('tef,efd->td', hid, w2).reshape(*lead, D_MODEL)

def setup_inputs(seed: int = 0) -> dict:
    key = jax.random.key(seed)
    keys = list(jax.random.split(key, 40))

    def nrm(shape, scale=1.0):
        return scale * jax.random.normal(keys.pop(), shape, jnp.float32)

    def gain(shape):
        return 1.0 + nrm(shape, 0.05)

    n_pages = PAST_LEN // PAGE_SIZE
    n_used = DEC_BATCH * n_pages
    n_phys = n_used + n_used // 4
    win_a = min(A_WINDOW, PAST_LEN)
    win_c = min(C_WINDOW, PAST_LEN)
    page_table = jax.random.permutation(keys.pop(), n_phys)[:n_used].reshape(DEC_BATCH, n_pages).astype(jnp.int32)
    return {
        'x_prompt': nrm((BATCH, SEQ, D_MODEL)),
        'x_sample': nrm((DEC_BATCH, DEC_SEQ, D_MODEL)),
        'cache_a_kv': nrm((DEPTH, DEC_BATCH, win_a, 2, H_A, HEAD_DIM)),
        'state_b': nrm((DEPTH, DEC_BATCH, H_B, DK_B, DV_B), 0.5),
        'cache_c_kv': nrm((DEPTH, n_phys, PAGE_SIZE, 4, G_C, HEAD_DIM)),
        'cache_c_win': nrm((DEPTH, DEC_BATCH, win_c, 2, G_C, HEAD_DIM)),
        'page_table': page_table,
        'attn_norm': gain((DEPTH, D_MODEL)),
        'w_in': nrm((DEPTH, D_MODEL, D_IN), D_MODEL ** -0.5),
        'a_qnorm': gain((DEPTH, HEAD_DIM)),
        'a_knorm': gain((DEPTH, HEAD_DIM)),
        'b_lower': nrm((DEPTH, B_KW)),
        'b_onorm': gain((DEPTH, DV_B)),
        'c_qnorm': gain((DEPTH, HEAD_DIM)),
        'c_knorm': gain((DEPTH, 3, HEAD_DIM)),
        'c_cmp_w': nrm((DEPTH, 2, CMP_BLK * HEAD_DIM, HEAD_DIM), (CMP_BLK * HEAD_DIM) ** -0.5),
        'c_cmp_pe': nrm((DEPTH, 2, CMP_BLK, HEAD_DIM), 0.1),
        'w_o': nrm((DEPTH, D_MIX, D_MODEL), D_MIX ** -0.5),
        'ffn_norm': gain((DEPTH, D_MODEL)),
        'moe_wg': nrm((DEPTH, D_MODEL, N_GROUPS), D_MODEL ** -0.5),
        'moe_bg': nrm((DEPTH, N_GROUPS), 0.01),
        'moe_we': nrm((DEPTH, D_MODEL, N_EXPERTS), D_MODEL ** -0.5),
        'moe_be': nrm((DEPTH, N_EXPERTS), 0.01),
        'moe_w1': nrm((DEPTH, N_EXPERTS, D_MODEL, D_EXPERT), D_MODEL ** -0.5),
        'moe_w3': nrm((DEPTH, N_EXPERTS, D_MODEL, D_EXPERT), D_MODEL ** -0.5),
        'moe_w2': nrm((DEPTH, N_EXPERTS, D_EXPERT, D_MODEL), D_EXPERT ** -0.5),
    }

def reference(x_prompt, x_sample, cache_a_kv, state_b, cache_c_kv, cache_c_win, page_table,
              attn_norm, w_in, a_qnorm, a_knorm, b_lower, b_onorm, c_qnorm, c_knorm, c_cmp_w, c_cmp_pe,
              w_o, ffn_norm, moe_wg, moe_bg, moe_we, moe_be, moe_w1, moe_w3, moe_w2):
    sm = jax.nn.softmax(b_lower.astype(jnp.float32), axis=0)
    lower_bounds = jnp.cumsum(sm, axis=0) - sm[0]
    n_seq, n_pages = page_table.shape
    xp, xs = x_prompt, x_sample
    a_p, a_s, b_p, b_s, c_p, c_s, w_p, w_s = [], [], [], [], [], [], [], []
    for l in range(DEPTH):
        params = (w_in[l], a_qnorm[l], a_knorm[l], b_onorm[l], c_qnorm[l], c_knorm[l], c_cmp_w[l], c_cmp_pe[l], w_o[l])
        yp, pa, pb, pc, pw = mixer_prompt(rms_norm(xp, attn_norm[l]), lower_bounds[l], *params)
        c_past = cache_c_kv[l][page_table].reshape(n_seq, n_pages * PAGE_SIZE, 4, G_C, HEAD_DIM)
        ys, sa, sb, sc, sw = mixer_sample(rms_norm(xs, attn_norm[l]), cache_a_kv[l], state_b[l], c_past,
                                          cache_c_win[l], lower_bounds[l], *params)
        xp = xp + yp.astype(xp.dtype)
        xs = xs + ys.astype(xs.dtype)
        moe_params = (moe_wg[l], moe_bg[l], moe_we[l], moe_be[l], moe_w1[l], moe_w3[l], moe_w2[l])
        xp = xp + hier_moe(rms_norm(xp, ffn_norm[l]), *moe_params).astype(xp.dtype)
        xs = xs + hier_moe(rms_norm(xs, ffn_norm[l]), *moe_params).astype(xs.dtype)
        a_p.append(pa); a_s.append(sa); b_p.append(pb); b_s.append(sb)
        c_p.append(pc); c_s.append(sc); w_p.append(pw); w_s.append(sw)
    a_kv_prompt, a_kv_sample = jnp.stack(a_p), jnp.stack(a_s)
    b_state_prompt, b_state_sample = jnp.stack(b_p), jnp.stack(b_s)
    c_kv_prompt, c_kv_sample = jnp.stack(c_p), jnp.stack(c_s)
    c_win_prompt, c_win_sample = jnp.stack(w_p), jnp.stack(w_s)
    return (xp, xs, a_kv_prompt, a_kv_sample, b_state_prompt, b_state_sample,
            c_kv_prompt, c_kv_sample, c_win_prompt, c_win_sample)


_drawn_inputs = setup_inputs


def setup_inputs(seed=0):
    import zlib

    import numpy as np

    out = dict(_drawn_inputs(seed))
    spreads = {}
    factors = {'a_qnorm': 4.549, 'c_qnorm': 6.159, 'moe_bg': 5.581, 'moe_be': 5.807, 'b_onorm': 3.13}
    for name, (base, spread) in spreads.items():
        noise = np.random.default_rng([zlib.crc32(name.encode()), seed]).standard_normal(out[name].shape)
        drawn = base * np.exp(spread * noise) if base else spread * noise
        out[name] = __import__('jax').numpy.asarray(drawn.astype(out[name].dtype))
    for name, factor in factors.items():
        out[name] = (out[name] * factor).astype(out[name].dtype)
    return out
```

```python
from contextlib import ExitStack, contextmanager

import numpy as np
import concourse.bass as bass
from concourse import mybir

F32 = mybir.dt.float32
I32 = mybir.dt.int32
U32 = mybir.dt.uint32
ALU = mybir.AluOpType
ACT = mybir.ActivationFunctionType
AX = mybir.AxisListType

P = 128
D = 1024
KD = D // P
SEQ = 1024
DEC_B, DEC_S = 8, 8
N_DEC = DEC_B * DEC_S
N_TOK = SEQ + N_DEC
PT = SEQ // P
TILES = PT + 1
HD = 64
HA, HB, HC, GC, RC = 6, 4, 6, 2, 3
PAST = 1024
CWIN = 512
NCMP = 63
EPS = 1e-6
NEG = -1e30
TINY = 1e-30
SCALE = HD ** -0.5
NE, DE = 16, 256

AQ, AK, AV, BQ, BF, BV, BG, CQ, CKC, CVC, CKS, CVS, CKW, CVW, CG, D_IN = (
    0, 384, 768, 1152, 1408, 1664, 1920, 2176, 2560, 2688, 2816, 2944, 3072, 3200, 3328, 3346)
Z_AQ, Z_B, Z_CQ, Z_G, Z_W = 0, 384, 1408, 1792, 1810


@contextmanager
def semaphores(nc, stage):
    held = []

    def new(name):
        held.append(nc.alloc_semaphore(stage + name))
        return held[-1]

    yield new
    nc.clear_and_free_semaphores(held)
    nc.all_engine_barrier()


class Count:

    def __init__(self, sem, per=1):
        self.sem, self.per = sem, per

    def open(self, eng):
        eng.sem_inc(self.sem, self.per)

    def at(self, i, n=0):
        return (i + 1) * self.per + n

    def wait(self, eng, i, n=0):
        eng.wait_ge(self.sem, self.at(i, n))


def waits(eng, seen, *pairs):
    for sem, v in pairs:
        eng.wait_ge(sem, v)
        eng.sem_inc(seen, 1)


CHUNKS = [
    (AQ, 384, [(0, 6, 0)]), (AK, 384, [(0, 6, 1)]), (AV, 384, []), (BQ, 512, []), (BV, 512, []),
    (CQ, 384, [(0, 6, 2)]), (CKC, 512, [(256, 2, 3)]), (CKW, 274, [(0, 2, 4)]),
]


def project(nc, t):
    NCH = len(CHUNKS)
    NORMED = [c for c, (_, _, n) in enumerate(CHUNKS) if n]
    with ExitStack() as ctx:
        sb = lambda name, shape, dt=F32: ctx.enter_context(nc.sbuf_tensor("p_" + name, shape, dt))
        ps = lambda name, shape: ctx.enter_context(nc.psum_tensor("p_" + name, shape, F32))
        sem = ctx.enter_context(semaphores(nc, "p_"))
        w = sb("w", [P, KD, D_IN])
        gx = sb("gx", [P, KD])
        gains = sb("gains", [P, 5, HD])
        ident = sb("ident", [P, P])
        x = sb("x", [P, D])
        xn = sb("xn", [P, D])
        sqx = sb("sqx", [P, D])
        hT = sb("hT", [P, KD, P])
        z = sb("z", [P, D_IN])
        sq = sb("sq", [P, 384])
        ssx = sb("ssx", [P, 3])
        ss = sb("ss", [P, 3, 6])
        tp = ps("tp", [P, KD, P])
        acc = [ps(f"acc{n}", [P, 512]) for n in range(4)]
        const_in, seen = sem("const_in"), sem("seen")
        w_in = [sem(f"w_in{c}") for c in range(NCH)]
        x_in, x_sq, x_ms, x_rt, x_rs, xn_ready, xn_read = map(sem, (
            "x_in", "x_sq", "x_ms", "x_rt", "x_rs", "xn_ready", "xn_read"))
        ht_ready, z_ps, z_sq, z_ms, z_rt, z_rs, z_nrm, z_cp, z_dve = map(sem, (
            "ht_ready", "z_ps", "z_sq", "z_ms", "z_rt", "z_rs", "z_nrm", "z_cp", "z_dve"))
        z_out = [sem(f"z_out{c}") for c in range(NCH)]
        shifted = sem("shifted")
        copies = []
        for c0, cw, norms in CHUNKS:
            lo, pieces = 0, []
            for o, h, _ in norms:
                if o > lo:
                    pieces.append((lo, o))
                lo = o + h * HD
            if lo < cw:
                pieces.append((lo, cw))
            copies.append(pieces)
        n_cp = [sum(len(p) for p in copies[:c + 1]) for c in range(NCH)]
        n_nm = [sum(c2 <= c for c2 in NORMED) for c in range(NCH)]
        NCP, NNM = n_cp[-1], n_nm[-1]
        xin, xnr, xnd = Count(x_in, 16), Count(xn_ready), Count(xn_read)
        xsq, xms, xrt, xrs = Count(x_sq), Count(x_ms), Count(x_rt), Count(x_rs)
        htr, zps, cp, nm = Count(ht_ready, 2), Count(z_ps, NCH), Count(z_cp, NCP), Count(z_nrm, NNM)
        zsq, zms, zrt, zdv = Count(z_sq, NNM), Count(z_ms, NNM), Count(z_rt, NNM), Count(z_dve, 3 * NNM)
        out = [Count(z_out[c], 32 if c == NCH - 1 else 16) for c in range(NCH)]
        with nc.Block() as block:

            @block.sync
            def _(sp):
                for c in (xin, *out):
                    c.open(sp)
                sp.dma_start(ident[:, :], t["ident"][:, :]).then_inc(const_in, 16)
                sp.dma_start(gx[:, :], t["attn_norm"][0, :].rearrange("(k p) -> p k", p=P),
                             allow_slow_non_contiguous=True).then_inc(const_in, 16)
                for n, g in enumerate((t["a_qnorm"][0], t["a_knorm"][0], t["c_qnorm"][0],
                                       t["c_knorm"][0, 1], t["c_knorm"][0, 2])):
                    sp.dma_start(gains[:, n, :], g.partition_broadcast(P)).then_inc(const_in, 16)
                sp.dma_start(x[:, :], t["x"][0:P, :]).then_inc(x_in, 16)
                for c, (c0, cw, _) in enumerate(CHUNKS):
                    sp.dma_start(w[:, :, c0:c0 + cw],
                                 t["w_in"][0, :, c0:c0 + cw].rearrange("(k p) n -> p k n", p=P)
                                 ).then_inc(w_in[c], 16)
                with sp.Fori(0, TILES) as i:
                    waits(sp, seen, (xn_ready, xnr.at(i, 1)))
                    sp.dma_start(x[:, :], t["x"][bass.ds((i + 1) * P, P), :]).then_inc(x_in, 16)
                    rows = bass.ds(i * P, P)
                    for c, (c0, cw, norms) in enumerate(CHUNKS):
                        waits(sp, seen, *([(z_cp, cp.at(i, n_cp[c]))] if copies[c] else []),
                              *([(z_nrm, nm.at(i, n_nm[c]))] if norms else []))
                        src = z[:, c0:c0 + cw]
                        if c in (0,):
                            dst = t["zr"][rows, Z_AQ:Z_AQ + 384]
                        elif c in (1, 2):
                            dst = t["a_kv"][rows, c0 - AK:c0 - AK + cw]
                        elif c in (3, 4):
                            dst = t["zr"][rows, Z_B + c0 - BQ:Z_B + c0 - BQ + cw]
                        elif c == 5:
                            dst = t["zr"][rows, Z_CQ:Z_CQ + 384]
                        elif c == 6:
                            dst = t["c_kv"][rows, :]
                        else:
                            sp.dma_start(t["c_win"][rows, :], z[:, CKW:CG]).then_inc(z_out[c], 16)
                            src, dst = z[:, CG:D_IN], t["zr"][rows, Z_G:Z_W]
                        sp.dma_start(dst, src).then_inc(z_out[c], 16)
                xin.wait(sp, TILES + 1)
                for c in out:
                    c.wait(sp, TILES)

            @block.gpsimd
            def _(pool):
                for b in range(DEC_B):
                    pool.dma_start(t["a_s"][b, 0:PAST - DEC_S, :],
                                   t["cache_a"][b, DEC_S:PAST, :]).then_inc(shifted, 16)
                    pool.dma_start(t["w_s"][b, 0:CWIN - DEC_S, :],
                                   t["cache_w"][b, DEC_S:CWIN, :]).then_inc(shifted, 16)
                pool.wait_ge(shifted, 32 * DEC_B)

            @block.tensor
            def _(pe):
                zps.open(pe)
                xnd.open(pe)
                pe.wait_ge(const_in, 16 * 7)
                with pe.Fori(0, TILES) as i:
                    xnr.wait(pe, i, 1)
                    for k in range(KD):
                        last = pe.transpose(tp[:, k, :], xn[:, k * P:(k + 1) * P], ident[:, :])
                    last.then_inc(xn_read, 1)
                    htr.wait(pe, i, 2)
                    for c, (c0, cw, norms) in enumerate(CHUNKS):
                        if c == 0:
                            cp.wait(pe, i)
                            nm.wait(pe, i)
                        if c >= 4:
                            if copies[c - 4]:
                                cp.wait(pe, i, n_cp[c - 4])
                            if CHUNKS[c - 4][2]:
                                nm.wait(pe, i, n_nm[c - 4])
                        pe.wait_ge(w_in[c], 16)
                        for k in range(KD):
                            last = pe.matmul(acc[c % 4][:, 0:cw], hT[:, k, :], w[:, k, c0:c0 + cw],
                                             start=k == 0, stop=k == KD - 1)
                        last.then_inc(z_ps, 1)

            @block.scalar
            def _(act):
                for c in (xsq, xrt, cp, zsq, zrt):
                    c.open(act)

                def norm_x(n):
                    xin.wait(act, n, 16)
                    act.activation(sqx[:, :], x[:, :], ACT.Square, accum_out=ssx[:, 0:1]).then_inc(x_sq, 1)
                    xms.wait(act, n, 1)
                    act.activation(ssx[:, 2:3], ssx[:, 1:2], ACT.Sqrt).then_inc(x_rt, 1)

                norm_x(0)
                with act.Fori(0, TILES) as i:
                    for c, (c0, cw, norms) in enumerate(CHUNKS):
                        zps.wait(act, i, c + 1)
                        out[c].wait(act, i)
                        if norms:
                            (o, h, _), = norms
                            zms.wait(act, i, n_nm[c] - 1)
                            act.activation(sq[:, 0:h * HD], acc[c % 4][:, o:o + h * HD],
                                           ACT.Square).then_inc(z_sq, 1)
                        for lo, hi in copies[c]:
                            act.activation(z[:, c0 + lo:c0 + hi], acc[c % 4][:, lo:hi],
                                           ACT.Copy).then_inc(z_cp, 1)
                        if norms:
                            zms.wait(act, i, n_nm[c])
                            act.activation(ss[:, 2, 0:h], ss[:, 1, 0:h], ACT.Sqrt).then_inc(z_rt, 1)
                        if c == 3:
                            norm_x(i + 1)

            @block.vector
            def _(dve):
                for c in (xms, xrs, xnr, htr, zms, nm, zdv):
                    c.open(dve)

                def norm_x(n):
                    xsq.wait(dve, n, 1)
                    dve.tensor_scalar(ssx[:, 1:2], ssx[:, 0:1], 1.0 / D, EPS, ALU.mult, ALU.add
                                      ).then_inc(x_ms, 1)
                    xrt.wait(dve, n, 1)
                    dve.reciprocal(ssx[:, 2:3], ssx[:, 2:3]).then_inc(x_rs, 1)
                    xrs.wait(dve, n, 1)
                    xnd.wait(dve, n)
                    dve.tensor_scalar(xn[:, :], x[:, :], ssx[:, 2:3], None, ALU.mult
                                      ).then_inc(xn_ready, 1)

                dve.wait_ge(const_in, 16 * 7)
                norm_x(0)
                with dve.Fori(0, TILES) as i:
                    xnd.wait(dve, i, 1)
                    zps.wait(dve, i)
                    for b in range(2):
                        ks = slice(4 * b, 4 * b + 4)
                        dve.tensor_tensor(hT[:, ks, :], tp[:, ks, :],
                                          gx[:, ks].unsqueeze(2).to_broadcast([P, 4, P]),
                                          ALU.mult).then_inc(ht_ready, 1)
                    for c, (c0, cw, norms) in enumerate(CHUNKS):
                        if norms:
                            (o, h, g), = norms
                            m = n_nm[c]
                            zsq.wait(dve, i, m)
                            dve.tensor_reduce(ss[:, 0, 0:h],
                                              sq[:, 0:h * HD].rearrange("p (h d) -> p h d", d=HD),
                                              AX.X, ALU.add).then_inc(z_dve, 1)
                            zdv.wait(dve, i, 3 * m - 2)
                            zrt.wait(dve, i, m - 1)
                            dve.tensor_scalar(ss[:, 1, 0:h], ss[:, 0, 0:h], 1.0 / HD, EPS,
                                              ALU.mult, ALU.add).then_inc(z_ms, 1)
                            zrt.wait(dve, i, m)
                            dve.reciprocal(ss[:, 0, 0:h], ss[:, 2, 0:h]).then_inc(z_dve, 1)
                            zdv.wait(dve, i, 3 * m - 1)
                            out[c].wait(dve, i)
                            src = acc[c % 4][:, o:o + h * HD]
                            dst = z[:, c0 + o:c0 + o + h * HD]
                            if c0 == CQ:
                                src = src.rearrange("p (g r d) -> p g r d", g=GC, r=RC)
                                dst = dst.rearrange("p (r g d) -> p g r d", g=GC, r=RC)
                                rs = ss[:, 0, 0:h].rearrange("p (g r) -> p g r", g=GC).unsqueeze(3
                                    ).to_broadcast([P, GC, RC, HD])
                            else:
                                src = src.rearrange("p (h d) -> p h d", d=HD)
                                dst = dst.rearrange("p (h d) -> p h d", d=HD)
                                rs = ss[:, 0, 0:h].unsqueeze(2).to_broadcast([P, h, HD])
                            dve.tensor_tensor(dst, src, rs, ALU.mult).then_inc(z_dve, 1)
                            zdv.wait(dve, i, 3 * m)
                            dst = z[:, c0 + o:c0 + o + h * HD].rearrange("p (h d) -> p h d", d=HD)
                            gain = gains[:, g, :].unsqueeze(1).to_broadcast([P, h, HD])
                            dve.tensor_tensor(dst, dst, gain, ALU.mult).then_inc(z_nrm, 1)
                        if c == 3:
                            norm_x(i + 1)


class Steps(Count):

    def __init__(self, sem, names):
        self.names = names.split()
        super().__init__(sem, len(self.names))
        self.next = 0

    def did(self, ins, name):
        assert self.names[self.next % self.per] == name, (name, self.names[self.next % self.per])
        self.next += 1
        ins.then_inc(self.sem, 1)

    def after(self, eng, i, name):
        eng.wait_ge(self.sem, self.at(i, self.names.index(name) + 1))


LN_TINY = float(np.log(np.float32(TINY)))


def hgrn(nc, t):
    LV = 7
    with ExitStack() as ctx:
        sb = lambda name, shape, dt=F32: ctx.enter_context(nc.sbuf_tensor("b_" + name, shape, dt))
        ps = lambda name, shape: ctx.enter_context(nc.psum_tensor("b_" + name, shape, F32))
        sem = ctx.enter_context(semaphores(nc, "b_"))
        ident = sb("ident", [P, P])
        sums_m = sb("sums_m", [P, (LV + 1) * P])
        suf_m = sb("suf_m", [P, P])
        pair_m = sb("pair_m", [P, (LV + 1) * P])
        sums_s = sb("sums_s", [N_DEC, 4 * N_DEC])
        suf_s = sb("suf_s", [N_DEC, N_DEC])
        pair_s = sb("pair_s", [N_DEC, 4 * N_DEC])
        rows_s = sb("rows_s", [N_DEC, DEC_B])
        cols_s = sb("cols_s", [P, DEC_B, N_DEC])
        gain = sb("gain", [P, HD])
        zb = sb("zb", [P, 1024])
        z_q, z_f, z_v, z_g = (zb[:, n * 256:(n + 1) * 256] for n in range(4))
        az, tt, ln1, r1, km, kk, lf = (sb(n, [P, 256]) for n in ("az", "tt", "ln1", "r1", "km", "kk", "lf"))
        qkT = sb("qkT", [P, 4, P])
        e = [sb(f"e{p}", [P, (LV + 1) * P]) for p in range(2)]
        x = [sb(f"x{p}", [P, (LV + 1) * P]) for p in range(2)]
        esuf, kdec = sb("esuf", [P, 256]), sb("kdec", [P, 256])
        w = sb("w", [P, (LV + 1) * P])
        at = sb("at", [P, HB, P])
        state = sb("state", [P, HB, HD])
        eg, g1, sil = sb("eg", [P, 256]), sb("g1", [P, 256]), sb("sil", [P, 256])
        oc, sq, ob = sb("oc", [P, 256]), sb("sq", [P, 256]), sb("ob", [P, 256])
        st = sb("st", [P, 4, HB])
        half = sb("half", [P, HB])
        s0 = sb("s0", [P, HB, DEC_B, HD])
        s1 = sb("s1", [P, 2, DEC_B, HD])
        qm = sb("qm", [P, 2, DEC_B, N_DEC])
        vm = sb("vm", [N_DEC, HB, DEC_B, HD])
        tq, sfo = ps("tq", [P, 512]), ps("sfo", [P, 512])
        sm = ps("sm", [P, 1024])
        sc = [ps(f"sc{n}", [P, 1024]) for n in range(2)]
        const_in, seen, zeroed, s_stored = map(sem, ("const_in", "seen", "zeroed", "s_stored"))
        z_in, ob_out = Count(sem("z_in"), 16), Count(sem("ob_out"), 16)
        by_act = Steps(sem("by_act"), "abs exp ln qkT suf sums0 sums1 gate")
        by_pe = Steps(sem("by_pe"), "qT kT suf sums0 sums1 sc0 sc1 sc2 sc3 out state")
        by_dve = Steps(sem("by_dve"), "one rec pick k min lf kdec x0 x1 w0 at0 w1 at1 w2 at2 w3 at3 "
                       "g1 g2 g3 g4 state oc sq ss ms on ob")
        by_pool = Steps(sem("by_pool"), "rsqrt")
        ALL = (z_in, ob_out, by_act, by_pe, by_dve, by_pool)
        fin = {n: sem("fin_" + n) for n in ("qm", "vm", "dec", "s1")}

        with nc.Block() as block:

            @block.sync
            def _(sp):
                z_in.open(sp)
                ob_out.open(sp)
                for a, b in ((ident, "ident"), (sums_m, "b_sums"), (suf_m, "b_suf"), (pair_m, "b_pair"),
                             (sums_s, "bs_sums"), (suf_s, "bs_suf"), (pair_s, "bs_pair"), (rows_s, "bs_rows")):
                    sp.dma_start(a[:, :], t[b][:, :]).then_inc(const_in, 16)
                sp.dma_start(cols_s[:, :, :], t["bs_cols"][:, :, :]).then_inc(const_in, 16)
                sp.dma_start(gain[:, :], t["b_onorm"][0].partition_broadcast(P)).then_inc(const_in, 16)
                sp.wait_ge(zeroed, 3)
                for h in range(HB):
                    r = slice(HD * (h % 2), HD * (h % 2) + HD)
                    sp.dma_start(s0[r, h, :, :], t["state_b"][:, h, :, :].rearrange("b c v -> c b v")
                                 ).then_inc(const_in, 16)
                sp.dma_start(zb[:, :], t["zr"][0:P, Z_B:Z_B + 1024]).then_inc(z_in.sem, 16)
                with sp.Fori(0, PT) as i:
                    waits(sp, seen, (by_dve.sem, by_dve.at(i, by_dve.per)))
                    sp.dma_start(t["cat"][bass.ds(i * P, P), 384:640], ob[:, :]).then_inc(ob_out.sem, 16)
                    waits(sp, seen, (by_pe.sem, by_pe.at(i, by_pe.per)))
                    sp.dma_start(zb[:, :], t["zr"][bass.ds(i * P + P, P), Z_B:Z_B + 1024]
                                 ).then_inc(z_in.sem, 16)
                for h in range(HB):
                    sp.dma_start(t["s_p"][h, :, :], state[HD * (h % 2):HD * (h % 2) + HD, h, :]
                                 ).then_inc(s_stored, 16)
                by_dve.after(sp, PT, "ob")
                sp.dma_start(t["cat"][SEQ:N_TOK, 384:640], ob[0:N_DEC, :]).then_inc(ob_out.sem, 16)
                sp.wait_ge(fin["s1"], 6)
                for p in range(2):
                    sp.dma_start(t["s_s"][:, 2 * p:2 * p + 2, :, :].rearrange("b j c v -> (j c) b v"),
                                 s1[:, p, :, :]).then_inc(s_stored, 16)
                sp.wait_ge(s_stored, 16 * 6)
                ob_out.wait(sp, PT + 1)

            def rows(sample):
                return (N_DEC, 3) if sample else (P, LV)

            @block.tensor
            def _(pe):
                by_pe.open(pe)
                pe.wait_ge(const_in, 16 * 14)

                def tile(i, sample=False):
                    T, L = rows(sample)
                    TP = T * (L + 1)
                    z_in.wait(pe, i, 16)
                    by_act.after(pe, i - 1, "qkT")
                    for p in range(2):
                        last = pe.transpose(tq[:, p * T:(p + 1) * T], z_q[0:T, p * P:(p + 1) * P], ident[0:T, 0:T])
                    by_pe.did(last, "qT")
                    by_dve.after(pe, i, "k")
                    for p in range(2):
                        last = pe.transpose(tq[:, (2 + p) * T:(3 + p) * T], kk[0:T, p * P:(p + 1) * P],
                                            ident[0:T, 0:T])
                    by_pe.did(last, "kT")
                    by_dve.after(pe, i, "lf")
                    by_dve.after(pe, i - 1, "oc")
                    by_pe.did(pe.matmul(sfo[0:T, 0:256], (suf_s if sample else suf_m)[:, :], lf[0:T, :],
                                        start=True, stop=True), "suf")
                    for p in range(2):
                        by_act.after(pe, i if p else i - 1, "sums0" if p else "sums1")
                        for lo in range(0, TP, 512):
                            hi = min(lo + 512, TP)
                            last = pe.matmul(sm[:, lo:hi], lf[0:T, p * P:(p + 1) * P],
                                             (sums_s if sample else sums_m)[:, lo:hi], start=True, stop=True)
                        by_pe.did(last, f"sums{p}")
                    by_act.after(pe, i, "qkT")
                    for h in range(HB):
                        p, r = h // 2, slice(HD * (h % 2), HD * (h % 2) + HD)
                        by_dve.after(pe, i, f"x{p}")
                        by_dve.after(pe, i if h >= 2 else i - 1, f"w{(h - 2) % 4}")
                        for n in range(L):
                            c = slice(n * T, n * T + T)
                            pe.matmul(sc[h % 2][0:T, c], x[p][r, c], x[p][r, c], start=True, stop=True)
                        by_pe.did(pe.matmul(sc[h % 2][0:T, L * T:TP], qkT[r, 2 + p, 0:T], qkT[r, p, 0:T],
                                            start=True, stop=True), f"sc{h}")
                    by_act.after(pe, i, "suf")
                    if sample:
                        pe.wait_ge(fin["qm"], 2)
                    else:
                        by_dve.after(pe, i - 1, "state")
                        pe.wait_ge(zeroed, 3)
                    for h in range(HB):
                        p, r = h // 2, slice(HD * (h % 2), HD * (h % 2) + HD)
                        by_dve.after(pe, i, f"at{h}")
                        dst = sfo[0:T, h * HD:(h + 1) * HD]
                        last = pe.matmul(dst, at[0:T, h, 0:T], z_v[0:T, h * HD:(h + 1) * HD], start=True, stop=False)
                        if sample:
                            for b in range(DEC_B):
                                last = pe.matmul(dst, qm[:, p, b, :], s0[:, h, b, :], start=False,
                                                 stop=b == DEC_B - 1)
                        else:
                            last = pe.matmul(dst, x[p][:, L * T:TP], state[:, h, :], start=False, stop=True)
                    by_pe.did(last, "out")
                    by_dve.after(pe, i, "kdec")
                    if sample:
                        pe.wait_ge(fin["vm"], 4)
                        for h in range(HB):
                            p, r = h // 2, slice(HD * (h % 2), HD * (h % 2) + HD)
                            last = pe.matmul(sm[r, p * 512:(p + 1) * 512], kdec[0:T, h * HD:(h + 1) * HD],
                                             vm[:, h, :, :].rearrange("s b v -> s (b v)"), start=True, stop=True)
                    else:
                        for h in range(HB):
                            p, r = h // 2, slice(HD * (h % 2), HD * (h % 2) + HD)
                            last = pe.matmul(tq[r, p * HD:(p + 1) * HD], kdec[:, h * HD:(h + 1) * HD],
                                             z_v[:, h * HD:(h + 1) * HD], start=True, stop=True)
                    by_pe.did(last, "state")

                with pe.Fori(0, PT) as i:
                    tile(i)
                tile(PT, sample=True)

            @block.scalar
            def _(act):
                by_act.open(act)

                def tile(i, sample=False):
                    T, L = rows(sample)
                    z_in.wait(act, i, 16)
                    by_act.did(act.activation(az[0:T, :], z_f[0:T, :], ACT.Abs), "abs")
                    by_act.after(act, i, "abs")
                    by_act.did(act.activation(tt[0:T, :], az[0:T, :], ACT.Exp, scale=-1.0), "exp")
                    by_act.after(act, i, "exp")
                    by_act.did(act.activation(ln1[0:T, :], tt[0:T, :], ACT.Ln, bias=1.0), "ln")
                    by_pe.after(act, i, "kT")
                    by_pe.after(act, i - 1, "sc3")
                    by_act.did(act.activation(qkT[:, :, 0:T], tq[:, 0:4 * T].rearrange("p (n t) -> p n t", t=T),
                                              ACT.Copy), "qkT")
                    by_pe.after(act, i, "suf")
                    by_act.did(act.activation(esuf[0:T, :], sfo[0:T, 0:256], ACT.Exp), "suf")
                    for p in range(2):
                        by_pe.after(act, i, f"sums{p}")
                        by_act.did(act.activation(e[p][:, 0:T * (L + 1)], sm[:, 0:T * (L + 1)], ACT.Exp), f"sums{p}")
                    by_act.did(act.activation(eg[0:T, :], z_g[0:T, :], ACT.Exp, scale=-1.0), "gate")

                with act.Fori(0, PT) as i:
                    tile(i)
                tile(PT, sample=True)

            @block.gpsimd
            def _(pool):
                by_pool.open(pool)
                pool.memset(state[:, :, :], 0.0).then_inc(zeroed, 1)
                pool.memset(half[:, :], -0.5).then_inc(zeroed, 1)
                pool.memset(s0[:, :, :, :], 0.0).then_inc(zeroed, 1)
                pool.wait_ge(zeroed, 3)

                def tile(i, T):
                    by_dve.after(pool, i, "ms")
                    by_pool.did(pool.tensor_tensor(st[0:T, 2, :], st[0:T, 1, :], half[0:T, :], ALU.pow), "rsqrt")

                with pool.Fori(0, PT) as i:
                    tile(i, P)
                tile(PT, N_DEC)

            @block.vector
            def _(dve):
                by_dve.open(dve)
                dve.wait_ge(const_in, 16 * 14)
                dve.wait_ge(zeroed, 3)

                def tile(i, sample=False):
                    T, L = rows(sample)
                    TP = T * (L + 1)
                    tr = slice(0, T)
                    step = lambda name, ins: (by_dve.did(ins, name), by_dve.after(dve, i, name))
                    by_act.after(dve, i, "exp")
                    step("one", dve.tensor_scalar(r1[tr, :], tt[tr, :], 1.0, None, ALU.add))
                    step("rec", dve.reciprocal(r1[tr, :], r1[tr, :]))
                    step("pick", dve.scalar_tensor_tensor(out=km[tr, :], in0=z_f[tr, :], scalar=0.0,
                                                          in1=tt[tr, :], op0=ALU.is_lt, op1=ALU.max))
                    step("k", dve.tensor_tensor(kk[tr, :], km[tr, :], r1[tr, :], ALU.mult))
                    by_act.after(dve, i, "ln")
                    step("min", dve.scalar_tensor_tensor(out=lf[tr, :], in0=z_f[tr, :], scalar=0.0,
                                                         in1=ln1[tr, :], op0=ALU.min, op1=ALU.subtract))
                    step("lf", dve.tensor_scalar(lf[tr, :], lf[tr, :], LN_TINY, None, ALU.max))
                    by_act.after(dve, i, "suf")
                    by_pe.after(dve, i - 1, "state")
                    step("kdec", dve.tensor_tensor(kdec[tr, :], kk[tr, :], esuf[tr, :], ALU.mult))
                    by_act.after(dve, i, "qkT")
                    for p in range(2):
                        by_act.after(dve, i, f"sums{p}")
                        for n in range(L):
                            m = 1 << (L - 1 - n)
                            v = lambda a: a.rearrange("p (b s m) -> p b s m", s=2, m=m)
                            xv, ev = v(x[p][:, n * T:n * T + T]), v(e[p][:, n * T:n * T + T])
                            for s, src in ((0, qkT[:, 2 + p, tr]), (1, qkT[:, p, tr])):
                                dve.tensor_tensor(xv[:, :, s, :], ev[:, :, s, :], v(src)[:, :, s, :], ALU.mult)
                        last = dve.tensor_tensor(x[p][:, L * T:TP], e[p][:, L * T:TP], qkT[:, p, tr], ALU.mult)
                        step(f"x{p}", last)
                        if sample:
                            dve.tensor_tensor(qm[:, p, :, :], x[p][:, L * T:TP].unsqueeze(1).to_broadcast(
                                [P, DEC_B, N_DEC]), cols_s[:, :, :], ALU.mult).then_inc(fin["qm"], 1)
                    if sample:
                        for h in range(HB):
                            dve.tensor_tensor(vm[:, h, :, :],
                                              z_v[tr, h * HD:(h + 1) * HD].unsqueeze(1).to_broadcast([T, DEC_B, HD]),
                                              rows_s[:, :].unsqueeze(2).to_broadcast([T, DEC_B, HD]),
                                              ALU.mult).then_inc(fin["vm"], 1)
                    for h in range(HB):
                        by_pe.after(dve, i, f"sc{h}")
                        step(f"w{h}", dve.tensor_tensor(w[tr, 0:TP], sc[h % 2][tr, 0:TP],
                                                        (pair_s if sample else pair_m)[:, 0:TP], ALU.mult))
                        step(f"at{h}", dve.tensor_reduce(at[tr, h, 0:T], w[tr, 0:TP].rearrange(
                            "p (n t) -> p t n", t=T), AX.X, ALU.add))
                    by_act.after(dve, i, "gate")
                    step("g1", dve.tensor_scalar(g1[tr, :], eg[tr, :], 1.0, None, ALU.add))
                    step("g2", dve.reciprocal(g1[tr, :], g1[tr, :]))
                    step("g3", dve.tensor_tensor(sil[tr, :], z_g[tr, :], g1[tr, :], ALU.mult))
                    hv = lambda a: a[tr, :].rearrange("p (h d) -> p h d", d=HD)
                    step("g4", dve.tensor_tensor(hv(sil), hv(sil), gain[tr, :].unsqueeze(1).to_broadcast(
                        [T, HB, HD]), ALU.mult))
                    by_pe.after(dve, i, "state")
                    if sample:
                        for h in range(HB):
                            p, r = h // 2, slice(HD * (h % 2), HD * (h % 2) + HD)
                            last_e = e[p][r, L * T:TP].rearrange("p (b q) -> p b q", q=DEC_S)[:, :, DEC_S - 1:DEC_S]
                            dve.tensor_tensor(s1[r, p, :, :], s0[r, h, :, :],
                                              last_e.to_broadcast([HD, DEC_B, HD]), ALU.mult).then_inc(fin["s1"], 1)
                        dve.wait_ge(fin["s1"], 4)
                        for p in range(2):
                            last = dve.tensor_tensor(s1[:, p, :, :], s1[:, p, :, :],
                                                     sm[:, p * 512:(p + 1) * 512].rearrange(
                                                         "p (b v) -> p b v", v=HD), ALU.add)
                            last.then_inc(fin["s1"], 1)
                    else:
                        for h in range(HB):
                            p, r = h // 2, slice(HD * (h % 2), HD * (h % 2) + HD)
                            last = dve.scalar_tensor_tensor(
                                out=state[r, h, :], in0=state[r, h, :], scalar=e[p][r, TP - 1:TP],
                                in1=tq[r, p * HD:(p + 1) * HD], op0=ALU.mult, op1=ALU.add)
                        step("state", last)
                    if sample:
                        by_dve.did(dve.memset(st[tr, 3, :], 0.0), "state")
                    step("oc", dve.tensor_copy(oc[tr, :], sfo[tr, 0:256]))
                    step("sq", dve.tensor_tensor(sq[tr, :], oc[tr, :], oc[tr, :], ALU.mult))
                    step("ss", dve.tensor_reduce(st[tr, 0, :], hv(sq), AX.X, ALU.add))
                    step("ms", dve.tensor_scalar(st[tr, 1, :], st[tr, 0, :], 1.0 / HD, EPS, ALU.mult, ALU.add))
                    by_pool.after(dve, i, "rsqrt")
                    step("on", dve.tensor_tensor(hv(oc), hv(oc), st[tr, 2, :].unsqueeze(2).to_broadcast(
                        [T, HB, HD]), ALU.mult))
                    ob_out.wait(dve, i)
                    step("ob", dve.tensor_tensor(ob[tr, :], oc[tr, :], sil[tr, :], ALU.mult))

                with dve.Fori(0, PT) as i:
                    tile(i)
                tile(PT, sample=True)


def prompt_attention(nc, t, pre, q_src, k_src, v_src, mask_src, dst, units, chunks):
    NU, NC, W = len(units), len(chunks), sum(chunks)
    KP, VW = k_src.shape[1] // P, v_src.shape[1]
    G = -(-NC // 4)
    U = 2 * NU
    FILLS = 2 + U * G
    assert FILLS % 2 == 0 and PT % 2 == 0
    off = [sum(chunks[:c]) for c in range(NC)]
    with ExitStack() as ctx:
        sb = lambda name, shape, dt=F32: ctx.enter_context(nc.sbuf_tensor(pre + name, shape, dt))
        ps = lambda name, shape: ctx.enter_context(nc.psum_tensor(pre + name, shape, F32))
        sem = ctx.enter_context(semaphores(nc, pre))
        ident = sb("ident", [P, P])
        k = sb("k", [P, NC, KP * P])
        v = sb("v", [P, NC, VW])
        kT = sb("kT", [P, KP, W])
        q = [sb(f"q{s}", [P, 384]) for s in range(2)]
        qT = [sb(f"qT{s}", [P, 3, P]) for s in range(2)]
        mask = [sb(f"mask{s}", [P, W]) for s in range(2)]
        p = [sb(f"p{s}", [P, W]) for s in range(2)]
        pT = [sb(f"pT{s}", [P, NC, P]) for s in range(2)]
        mx = sb("mx", [P, U])
        nb = sb("nb", [P, U])
        l = sb("l", [P, U])
        rl = sb("rl", [P, 3, U])
        o = [sb(f"o{s}", [P, NU, HD]) for s in range(2)]
        sc = [ps(f"sc{s}", [P, 1024]) for s in range(2)]
        tp = [ps(f"tp{s}", [P, 4, P]) for s in range(2)]
        op = [ps(f"op{s}", [P, 512]) for s in range(2)]
        kv_in, seen, settled, k_tp, k_ev = map(sem, ("kv_in", "seen", "settled", "k_tp", "k_ev"))
        q_in = [Count(sem(f"q_in{s}"), 16) for s in range(2)]
        mask_in = [Count(sem(f"mask_in{s}"), 16) for s in range(2)]
        o_out = [Count(sem(f"o_out{s}"), 16) for s in range(2)]
        scored = Count(sem("scored"), U)
        masked = Count(sem("masked"), U)
        bias = Count(sem("bias"), U)
        exped = Count(sem("exped"), U)
        filled = Count(sem("filled"), FILLS)
        ev_a = Count(sem("ev_a"), 2 + U)
        ev_d = Count(sem("ev_d"), U * (G - 1) or 1)
        summed = Count(sem("summed"), U)
        rec = Count(sem("rec"), 6)
        done = Count(sem("done"), 2)

        def fill_at(s=None, u=None, g=0):
            if u is None:
                return 0 if s == 0 else 1 + (NU - 1) * G + 0
            return (1 if u < NU - 1 else 2) + u * G + g

        def taken(eng, i, f):
            f -= 2
            if f < 0:
                i, f = i - 1, f + FILLS
            order = {fill_at(s=0): ("a", 1)}
            na, nd = 1, 0
            for u in range(U):
                if u == NU - 1:
                    na += 1
                    order[fill_at(s=1)] = ("a", na)
                for g in range(G):
                    if g == 0:
                        na += 1
                        order[fill_at(u=u)] = ("a", na)
                    else:
                        nd += 1
                        order[fill_at(u=u, g=g)] = ("d", nd)
            who, n = order[f]
            (ev_a if who == "a" else ev_d).wait(eng, i, n)

        def a_no(s=None, u=None):
            if u is None:
                return 1 if s == 0 else NU + 1
            return u + 2 if u < NU - 1 else u + 3

        with nc.Block() as block:

            @block.sync
            def _(sp):
                for c in (*q_in, *mask_in, *o_out):
                    c.open(sp)
                sp.dma_start(ident[:, :], t["ident"][:, :]).then_inc(kv_in, 16)
                if chunks[0] == P:
                    kv = [(x, y.rearrange("(c p) n -> p c n", p=P)) for x, y in ((k, k_src), (v, v_src))]
                else:
                    kv = [(x[0:W, 0], y) for x, y in ((k, k_src), (v, v_src))]
                for x, y in kv:
                    sp.dma_start(x[:, :, :] if chunks[0] == P else x, y).then_inc(kv_in, 16)
                for s in range(2):
                    sp.dma_start(q[s][:, :], q_src(s)).then_inc(q_in[s].sem, 16)
                    sp.dma_start(mask[s][:, :], mask_src(s)).then_inc(mask_in[s].sem, 16)
                with sp.Fori(0, PT // 2) as i:
                    for s in range(2):
                        waits(sp, seen, (done.sem, done.at(i, s + 1)))
                        sp.dma_start(dst(2 * i + s), o[s][:, :, :].rearrange("p h d -> p (h d)")
                                     ).then_inc(o_out[s].sem, 16)
                        waits(sp, seen, (ev_a.sem, ev_a.at(i, a_no(s=s))), (masked.sem, masked.at(i, NU * (s + 1))))
                        sp.dma_start(q[s][:, :], q_src((2 * i + (s + 2)) % PT)).then_inc(q_in[s].sem, 16)
                        sp.dma_start(mask[s][:, :], mask_src((2 * i + (s + 2)) % PT)).then_inc(mask_in[s].sem, 16)
                for s in range(2):
                    q_in[s].wait(sp, PT // 2, 16)
                    mask_in[s].wait(sp, PT // 2, 16)
                    o_out[s].wait(sp, PT // 2)

            @block.tensor
            def _(pe):
                for c in (scored, filled, summed):
                    c.open(pe)
                pe.wait_ge(kv_in, 48)
                n = 0
                for kp in range(KP):
                    for c in range(NC):
                        if n >= 2:
                            pe.wait_ge(k_ev, n - 1)
                        pe.transpose(tp[n % 2][:, 0, 0:chunks[c]], k[0:chunks[c], c, kp * P:(kp + 1) * P],
                                     ident[0:chunks[c], 0:chunks[c]]).then_inc(k_tp, 1)
                        n += 1
                pe.wait_ge(k_ev, KP * NC)

                def queries(i, s):
                    q_in[s].wait(pe, i, 16)
                    f = fill_at(s=s)
                    taken(pe, i, f)
                    for pr in range(3):
                        last = pe.transpose(tp[f % 2][:, pr, :], q[s][:, pr * P:(pr + 1) * P], ident[:, :])
                    last.then_inc(filled.sem, 1)

                def scores(i, u):
                    s = u // NU
                    pr, j, kp, _, _ = units[u % NU]
                    if u % NU == 0:
                        ev_a.wait(pe, i, a_no(s=s))
                    masked.wait(pe, i, u - 1) if u else masked.wait(pe, i - 1, U - 1)
                    r = slice(HD * j, HD * j + HD)
                    for lo in range(0, W, 512):
                        hi = min(lo + 512, W)
                        last = pe.matmul(sc[u % 2][:, lo:hi], qT[s][r, pr, :], kT[r, kp, lo:hi],
                                         start=True, stop=True)
                    last.then_inc(scored.sem, 1)

                def transposes(i, u):
                    exped.wait(pe, i, u + 1)
                    for g in range(G):
                        f = fill_at(u=u, g=g)
                        taken(pe, i, f)
                        if W < P:
                            pe.sem_inc(settled, 1)
                        for c in range(4 * g, min(4 * g + 4, NC)):
                            last = pe.transpose(tp[f % 2][0:chunks[c], c % 4, :],
                                                p[u % 2][:, off[c]:off[c] + chunks[c]], ident[:, :])
                        last.then_inc(filled.sem, 1)

                def values(i, u):
                    _, _, _, vc, h = units[u % NU]
                    if u % NU == 0:
                        done.wait(pe, i, u // NU - 1) if u // NU else done.wait(pe, i - 1, 1)
                    ev_a.wait(pe, i, a_no(u=u))
                    if G > 1:
                        ev_d.wait(pe, i, (u + 1) * (G - 1))
                    for c in range(NC):
                        last = pe.matmul(op[u // NU][:, h * HD:h * HD + HD], pT[u % 2][0:chunks[c], c, :],
                                         v[0:chunks[c], c, vc * HD:vc * HD + HD], start=c == 0, stop=c == NC - 1)
                    last.then_inc(summed.sem, 1)

                with pe.Fori(0, PT // 2) as i:
                    queries(i, 0)
                    for u in range(U + 2):
                        if u < U:
                            if u == NU:
                                queries(i, 1)
                            scores(i, u)
                        if 0 < u <= U:
                            transposes(i, u - 1)
                        if u >= 2:
                            values(i, u - 2)

            @block.scalar
            def _(act):
                for c in (exped, ev_a):
                    c.open(act)
                n = 0
                for kp in range(KP):
                    for c in range(NC):
                        act.wait_ge(k_tp, n + 1)
                        act.activation(kT[:, kp, off[c]:off[c] + chunks[c]], tp[n % 2][:, 0, 0:chunks[c]],
                                       ACT.Copy).then_inc(k_ev, 1)
                        n += 1

                def queries(i, s):
                    f = fill_at(s=s)
                    filled.wait(act, i, f + 1)
                    scored.wait(act, i, NU * s) if s else scored.wait(act, i - 1, NU)
                    act.activation(qT[s][:, :, :], tp[f % 2][:, 0:3, :], ACT.Copy).then_inc(ev_a.sem, 1)

                with act.Fori(0, PT // 2) as i:
                    queries(i, 0)
                    for u in range(U + 1):
                        if u == NU:
                            queries(i, 1)
                        if u > 0:
                            w = u - 1
                            f = fill_at(u=w)
                            filled.wait(act, i, f + 1)
                            summed.wait(act, i, w - 1) if w else summed.wait(act, i - 1, U - 1)
                            nn = min(4, NC)
                            act.activation(pT[w % 2][0:chunks[0], 0:nn, :], tp[f % 2][0:chunks[0], 0:nn, :],
                                           ACT.Copy).then_inc(ev_a.sem, 1)
                        if u < U:
                            bias.wait(act, i, u + 1)
                            act.activation(p[u % 2][:, :], p[u % 2][:, :], ACT.Exp, bias=nb[:, u:u + 1],
                                           scale=SCALE, accum_out=l[:, u:u + 1]).then_inc(exped.sem, 1)

            @block.vector
            def _(dve):
                for c in (masked, bias, ev_d, rec, done):
                    c.open(dve)

                def tile_out(i, s):
                    us = slice(NU * s, NU * s + NU)
                    summed.wait(dve, i, NU * s + NU)
                    dve.tensor_scalar(rl[:, 0, us], l[:, us], TINY, None, ALU.max).then_inc(rec.sem, 1)
                    rec.wait(dve, i, 3 * s + 1)
                    dve.reciprocal(rl[:, 1, us], rl[:, 0, us]).then_inc(rec.sem, 1)
                    rec.wait(dve, i, 3 * s + 2)
                    dve.scalar_tensor_tensor(out=rl[:, 2, us], in0=nb[:, us], scalar=-0.5 * NEG * SCALE,
                                             in1=rl[:, 1, us], op0=ALU.is_lt, op1=ALU.mult
                                             ).then_inc(rec.sem, 1)
                    rec.wait(dve, i, 3 * s + 3)
                    o_out[s].wait(dve, i)
                    hs = [u[4] for u in units]
                    for n in range(NU):
                        ins = dve.tensor_scalar(o[s][:, hs[n], :], op[s][:, hs[n] * HD:hs[n] * HD + HD],
                                                rl[:, 2, NU * s + n:NU * s + n + 1], None, ALU.mult)
                    ins.then_inc(done.sem, 1)

                with dve.Fori(0, PT // 2) as i:
                    for u in range(U + 2):
                        if u < U:
                            s = u // NU
                            if u % NU == 0:
                                mask_in[s].wait(dve, i, 16)
                            scored.wait(dve, i, u + 1)
                            if u >= 2:
                                filled.wait(dve, i, fill_at(u=u - 2, g=G - 1) + 1)
                            else:
                                filled.wait(dve, i - 1, fill_at(u=U + u - 2, g=G - 1) + 1)
                            dve.sem_inc(settled, 1)
                            dve.tensor_tensor_reduce(p[u % 2][:, :], sc[u % 2][:, 0:W], mask[s][:, :], 1.0,
                                                     -3e38, ALU.add, ALU.max, mx[:, u:u + 1]).then_inc(masked.sem, 1)
                            masked.wait(dve, i, u + 1)
                            dve.tensor_scalar(nb[:, u:u + 1], mx[:, u:u + 1], -SCALE, None, ALU.mult
                                              ).then_inc(bias.sem, 1)
                        if 0 < u <= U and G > 1:
                            w = u - 1
                            summed.wait(dve, i, w - 1) if w else summed.wait(dve, i - 1, U - 1)
                            for g in range(1, G):
                                f = fill_at(u=w, g=g)
                                filled.wait(dve, i, f + 1)
                                nn = min(4, NC - 4 * g)
                                dve.tensor_copy(pT[w % 2][:, 4 * g:4 * g + nn, :], tp[f % 2][:, 0:nn, :]
                                                ).then_inc(ev_d.sem, 1)
                        if u == NU + 1 or u == U + 1:
                            tile_out(i, 0 if u == NU + 1 else 1)


def sample_a(nc, t):
    NR, NC, NK, B2 = HA * DEC_S, PAST // P, PAST + DEC_S, 2
    FILLS = 16
    with ExitStack() as ctx:
        sb = lambda name, shape, dt=F32: ctx.enter_context(nc.sbuf_tensor("sa_" + name, shape, dt))
        ps = lambda name, shape: ctx.enter_context(nc.psum_tensor("sa_" + name, shape, F32))
        sem = ctx.enter_context(semaphores(nc, "sa_"))
        ident = sb("ident", [P, P])
        mask = sb("mask", [NR, NK])
        q = sb("q", [N_DEC, 384])
        qz = sb("qz", [P, DEC_B, 3, NR])
        kv = [sb(f"kv{s}", [P, NC, 768]) for s in range(B2)]
        new = [sb(f"new{s}", [DEC_S, 768]) for s in range(B2)]
        qs = [sb(f"qs{s}", [P, 3, NR]) for s in range(B2)]
        kT = sb("kT", [P, 3, NK])
        p = [sb(f"p{s}", [NR, NK]) for s in range(B2)]
        pT = [sb(f"pT{s}", [P, NC + 1, NR]) for s in range(B2)]
        st = sb("st", [NR, B2, 4])
        o = [sb(f"o{s}", [DEC_S, 384]) for s in range(B2)]
        sc = ps("sc", [P, 3 * 512])
        tp = [ps(f"tp{s}", [P, 512]) for s in range(2)]
        op = [ps(f"op{s}", [P, 512]) for s in range(2)]
        const_in, seen, settled, q_tp, q_zero, q_ev = map(sem, ("const_in", "seen", "settled", "q_tp", "q_zero", "q_ev"))
        kv_in = [Count(sem(f"kv_in{s}"), 32) for s in range(B2)]
        o_out = [Count(sem(f"o_out{s}"), 16) for s in range(B2)]
        filled = Count(sem("filled"), FILLS)
        ev_a, ev_d = Count(sem("ev_a"), 8), Count(sem("ev_d"), 8)
        q_here = Count(sem("q_here"), B2)
        scored, masked, biased = (Count(sem(n), B2) for n in ("scored", "masked", "biased"))
        exped, recip, normed = (Count(sem(n), B2) for n in ("exped", "recip", "normed"))
        summed, done = Count(sem("summed"), B2), Count(sem("done"), B2)

        def take_keys(i, s, parity, eng, copy, ev):
            for n in range(7):
                f = 7 * s + n
                if f % 2 != parity:
                    continue
                filled.wait(eng, i, f + 1)
                if n < 6:
                    ins = copy(kT[:, n // 2, 512 * (n % 2):512 * (n % 2) + 512], tp[f % 2][:, :])
                else:
                    ins = copy(kT[:, :, PAST:NK],
                               tp[f % 2][:, 0:3 * DEC_S].rearrange("p (c k) -> p c k", c=3))
                ins.then_inc(ev.sem, 1)

        def take_exps(i, s, eng, copy, ev):
            f = 14 + s
            filled.wait(eng, i, f + 1)
            summed.wait(eng, i - 1, s + 1)
            copy(pT[s][:, 0:NC, :], tp[f % 2][:, 0:NC * NR].rearrange("p (c r) -> p c r", r=NR))
            copy(pT[s][0:DEC_S, NC, :], tp[f % 2][0:DEC_S, NC * NR:(NC + 1) * NR]).then_inc(ev.sem, 1)

        with nc.Block() as block:

            @block.sync
            def _(sp):
                for c in (*kv_in, *o_out):
                    c.open(sp)
                sp.dma_start(ident[:, :], t["ident"][:, :]).then_inc(const_in, 16)
                sp.dma_start(mask[:, :], t["mask_sa"][:, :]).then_inc(const_in, 16)
                sp.dma_start(q[:, :], t["zr"][SEQ:N_TOK, Z_AQ:Z_AQ + 384]).then_inc(const_in, 16)

                def load(s, b):
                    sp.dma_start(kv[s][:, :, :], t["cache_a"][bass.ds(b, 1), :, :].rearrange(
                        "o (c p) n -> p (o c) n", p=P)).then_inc(kv_in[s].sem, 16)
                    sp.dma_start(new[s][:, :], t["a_kv"][bass.ds(b * DEC_S + SEQ, DEC_S), :]
                                 ).then_inc(kv_in[s].sem, 16)

                for s in range(B2):
                    load(s, s)
                with sp.Fori(0, DEC_B // B2) as i:
                    for s in range(B2):
                        waits(sp, seen, (done.sem, done.at(i, s + 1)))
                        sp.dma_start(t["cat"][bass.ds((i * B2 + s) * DEC_S + SEQ, DEC_S), 0:384],
                                     o[s][:, :]).then_inc(o_out[s].sem, 16)
                        waits(sp, seen, (summed.sem, summed.at(i, s + 1)))
                        load(s, (i * B2 + (B2 + s)) % DEC_B)
                for s in range(B2):
                    kv_in[s].wait(sp, DEC_B // B2, 32)
                    o_out[s].wait(sp, DEC_B // B2)

            @block.gpsimd
            def _(pool):
                pool.memset(qz[:, :, :, :], 0.0).then_inc(q_zero, 1)

            @block.tensor
            def _(pe):
                for c in (filled, scored, summed):
                    c.open(pe)
                pe.wait_ge(const_in, 48)
                for pr in range(3):
                    last = pe.transpose(tp[0][:, pr * N_DEC:(pr + 1) * N_DEC], q[:, pr * P:(pr + 1) * P],
                                        ident[0:N_DEC, 0:N_DEC])
                last.then_inc(q_tp, 1)
                pe.wait_ge(q_ev, 6)

                def taken(i, f):
                    f -= 2
                    if f < 0:
                        i, f = i - 1, f + FILLS
                    (ev_d if f % 2 else ev_a).wait(pe, i, f // 2 + 1)

                def keys(i, s):
                    kv_in[s].wait(pe, i, 32)
                    for n in range(6):
                        f = 7 * s + n
                        taken(i, f)
                        for c in range(4):
                            last = pe.transpose(tp[f % 2][:, c * P:(c + 1) * P],
                                                kv[s][:, 4 * (n % 2) + c, (n // 2) * P:(n // 2 + 1) * P], ident[:, :])
                        last.then_inc(filled.sem, 1)
                    f = 7 * s + 6
                    taken(i, f)
                    pe.sem_inc(settled, 1)
                    for pr in range(3):
                        last = pe.transpose(tp[f % 2][:, pr * DEC_S:(pr + 1) * DEC_S],
                                            new[s][:, pr * P:(pr + 1) * P], ident[0:DEC_S, 0:DEC_S])
                    last.then_inc(filled.sem, 1)

                def scores(i, s):
                    q_here.wait(pe, i, s + 1)
                    ev_a.wait(pe, i, 4 + 3 * s)
                    ev_d.wait(pe, i, 3 + 4 * s)
                    masked.wait(pe, i, s)
                    for lo, hi in ((0, 512), (512, 1024), (1024, NK)):
                        for pr in range(3):
                            last = pe.matmul(sc[0:NR, lo:hi], qs[s][:, pr, :], kT[:, pr, lo:hi],
                                             start=pr == 0, stop=pr == 2)
                    last.then_inc(scored.sem, 1)

                def values(i, s):
                    normed.wait(pe, i, s + 1)
                    f = 14 + s
                    taken(i, f)
                    pe.sem_inc(settled, 1)
                    for c in range(NC + 1):
                        kn = P if c < NC else DEC_S
                        last = pe.transpose(tp[f % 2][0:kn, c * NR:(c + 1) * NR],
                                            p[s][:, c * P:c * P + kn], ident[0:NR, 0:NR])
                    last.then_inc(filled.sem, 1)
                    (ev_d if s else ev_a).wait(pe, i, 8)
                    done.wait(pe, i - 1, s + 1)
                    for h in range(HA):
                        vs = slice(384 + h * HD, 384 + h * HD + HD)
                        for c in range(NC + 1):
                            kn = P if c < NC else DEC_S
                            last = pe.matmul(op[s][0:DEC_S, h * HD:(h + 1) * HD],
                                             pT[s][0:kn, c, h * DEC_S:(h + 1) * DEC_S],
                                             kv[s][:, c, vs] if c < NC else new[s][:, vs],
                                             start=c == 0, stop=c == NC)
                    last.then_inc(summed.sem, 1)

                with pe.Fori(0, DEC_B // B2) as i:
                    keys(i, 0)
                    scores(i, 0)
                    keys(i, 1)
                    scores(i, 1)
                    values(i, 0)
                    values(i, 1)

            @block.scalar
            def _(act):
                for c in (ev_a, q_here, exped):
                    c.open(act)
                act.wait_ge(q_zero, 1)
                act.wait_ge(q_tp, 1)
                for h in range(HA):
                    r = slice(HD * (h % 2), HD * (h % 2) + HD)
                    act.activation(qz[r, :, h // 2, h * DEC_S:(h + 1) * DEC_S],
                                   tp[0][r, (h // 2) * N_DEC:(h // 2 + 1) * N_DEC].rearrange(
                                       "p (b q) -> p b q", b=DEC_B), ACT.Copy).then_inc(q_ev, 1)
                act.wait_ge(q_ev, 6)

                copy = lambda out, in_: act.activation(out, in_, ACT.Copy)

                def keys(i, s):
                    scored.wait(act, i, s)
                    act.activation(qs[s][:, :, :], qz[:, bass.ds(i * B2 + s, 1), :, :].rearrange(
                        "p o c r -> p (o c) r"), ACT.Copy).then_inc(q_here.sem, 1)
                    take_keys(i, s, 0, act, copy, ev_a)

                def exps(i, s):
                    biased.wait(act, i, s + 1)
                    act.activation(p[s][:, :], p[s][:, :], ACT.Exp, bias=st[:, s, 1:2], scale=SCALE,
                                   accum_out=st[:, s, 2:3]).then_inc(exped.sem, 1)

                with act.Fori(0, DEC_B // B2) as i:
                    keys(i, 0)
                    exps(i, 0)
                    keys(i, 1)
                    take_exps(i, 0, act, copy, ev_a)
                    exps(i, 1)

            @block.vector
            def _(dve):
                for c in (ev_d, masked, biased, recip, normed, done):
                    c.open(dve)
                dve.wait_ge(const_in, 48)

                def keys(i, s):
                    scored.wait(dve, i, s)
                    take_keys(i, s, 1, dve, dve.tensor_copy, ev_d)

                def softmax(i, s):
                    scored.wait(dve, i, s + 1)
                    filled.wait(dve, i - 1, 15 + s)
                    dve.sem_inc(settled, 1)
                    dve.tensor_tensor_reduce(p[s][:, :], sc[0:NR, 0:NK], mask[:, :], 1.0, -3e38,
                                             ALU.add, ALU.max, st[:, s, 0:1]).then_inc(masked.sem, 1)
                    masked.wait(dve, i, s + 1)
                    dve.tensor_scalar(st[:, s, 1:2], st[:, s, 0:1], -SCALE, None, ALU.mult
                                      ).then_inc(biased.sem, 1)

                def norm(i, s):
                    exped.wait(dve, i, s + 1)
                    dve.reciprocal(st[:, s, 3:4], st[:, s, 2:3]).then_inc(recip.sem, 1)
                    recip.wait(dve, i, s + 1)
                    dve.tensor_scalar(p[s][:, :], p[s][:, :], st[:, s, 3:4], None, ALU.mult
                                      ).then_inc(normed.sem, 1)

                def out(i, s):
                    summed.wait(dve, i, s + 1)
                    o_out[s].wait(dve, i)
                    dve.tensor_copy(o[s][:, :], op[s][0:DEC_S, 0:384]).then_inc(done.sem, 1)

                with dve.Fori(0, DEC_B // B2) as i:
                    keys(i, 0)
                    softmax(i, 0)
                    norm(i, 0)
                    keys(i, 1)
                    softmax(i, 1)
                    norm(i, 1)
                    take_exps(i, 1, dve, dve.tensor_copy, ev_d)
                    out(i, 0)
                    out(i, 1)


def sample_c(nc, t):
    NR, NKS, NKW = 64, PAST + DEC_S, CWIN + DEC_S
    NB = PAST // HD
    with ExitStack() as ctx:
        sb = lambda name, shape, dt=F32: ctx.enter_context(nc.sbuf_tensor("sc_" + name, shape, dt))
        ps = lambda name, shape: ctx.enter_context(nc.psum_tensor("sc_" + name, shape, F32))
        sem = ctx.enter_context(semaphores(nc, "sc_"))
        ident = sb("ident", [P, P])
        wc = sb("wc", [P, 2, 32, P])
        peT = sb("peT", [P, 2, 32])
        peb = sb("peb", [P, 2])
        gain = sb("gain", [P, 1])
        ones = sb("ones", [P, P])
        share = sb("share", [NCMP, NB + 1])
        rsum = sb("rsum", [NR, NR])
        idx = sb("idx", [NR, NB])
        mnew = sb("mnew", [NR, DEC_S])
        mwin = sb("mwin", [NR, CWIN])
        nhalf = sb("nhalf", [P, NCMP])
        q = sb("q", [N_DEC, 384])
        qz = sb("qz", [P, DEC_B, NR])
        x = [sb(f"x{s}", [P, 4, 1024]) for s in range(2)]
        win = [sb(f"win{s}", [P, 4, 256]) for s in range(2)]
        nkv = [sb(f"nkv{s}", [DEC_S, 512]) for s in range(2)]
        nwin = [sb(f"nwin{s}", [DEC_S, 256]) for s in range(2)]
        qs = sb("qs", [P, NR])
        xT = sb("xT", [P, 4, 512])
        ksT, kwT, knT = sb("ksT", [P, 2, 512]), sb("kwT", [P, CWIN]), sb("knT", [P, 2 * DEC_S])
        kcf, vcf, sqk, msk, rsk, kcT = (sb(n, [P, NCMP]) for n in ("kcf", "vcf", "sqk", "msk", "rsk", "kcT"))
        vc = sb("vc", [NCMP, P])
        kcr = sb("kcr", [NCMP, 2 * P])
        pc, pcT = sb("pc", [NR, NCMP]), sb("pcT", [NCMP, NR])
        imp = sb("imp", [NR, NB + 1])
        sel = sb("sel", [NR, 64])
        drop = sb("drop", [NR, NB])
        pS, pW = sb("pS", [NR, NKS]), sb("pW", [NR, NKW])
        pTs, pTw = sb("pTs", [P, 8, NR]), sb("pTw", [P, 6, NR])
        st = sb("st", [NR, 3, 4])
        o = [sb(f"o{s}", [NR, 3, HD]) for s in range(2)]
        tp = [ps(f"tp{n}", [P, 512]) for n in range(2)]
        cps, ms = ps("cps", [P, 512]), ps("ms", [P, 512])
        sS, sW, sM = ps("sS", [P, 1024]), ps("sW", [P, 512]), ps("sM", [P, 512])
        const_in, seen, settled, zero, qtp, q_ev, pes, peb_in, pr_out = map(sem, (
            "const_in", "seen", "settled", "zero", "qtp", "q_ev", "pes", "peb_in", "pr_out"))
        x_in = [Count(sem(f"x_in{s}"), 16 * 11) for s in range(2)]
        o_out = [Count(sem(f"o_out{s}"), 16 * 6) for s in range(2)]
        two = lambda names: " ".join(f"{n}.{s}" for s in range(2) for n in names.split())
        by_pe = Steps(sem("by_pe"), two("tc0 tc1 tc2 tc3 tk0 tk1 tw tn comp nrm tv scS scC tpc imp1 imp2 tps tpw sum"))
        by_act = Steps(sem("by_act"), two("q tc0 tc1 tc2 tc3 ec es ew tps"))
        by_dve = Steps(sem("by_dve"), two(
            "tk0 tk1 tw tn kcf vcf sqk msk kcT vc mc bc rc pc pcT i1 i2 mn eq mi drop s0 s1 sn mS bS w0 wn mW bW "
            "rS pS rW pW tpw out"))
        by_pool = Steps(sem("by_pool"), two("rsk"))

        with nc.Block() as block:

            @block.sync
            def _(sp):
                for c in (*x_in, *o_out):
                    c.open(sp)
                for a, b in ((ident, "ident"), (ones, "ones2"), (share, "share"), (rsum, "rsum"), (idx, "blk"),
                             (mnew, "mask_new"), (mwin, "mask_sw")):
                    sp.dma_start(a[:, :], t[b][:, :]).then_inc(const_in, 16)
                sp.wait_ge(zero, 3)
                for g in range(2):
                    r = slice(HD * g, HD * g + HD)
                    sp.dma_start(wc[r, :, :, r], t["c_cmp_w"][0].rearrange("k (l r) e -> r k l e", r=HD)
                                 ).then_inc(const_in, 16)
                    sp.dma_start(peT[r, :, :], t["c_cmp_pe"][0].rearrange("k l d -> d k l"),
                                 allow_slow_non_contiguous=True).then_inc(const_in, 16)
                for g in range(2):
                    sp.dma_start(gain[HD * g:HD * g + HD, :], t["c_knorm"][0, 0, :].unsqueeze(1)
                                 ).then_inc(const_in, 16)
                sp.dma_start(q[:, :], t["zr"][SEQ:N_TOK, Z_CQ:Z_CQ + 384]).then_inc(const_in, 16)

                def load(s, b):
                    inc = lambda ins: ins.then_inc(x_in[s].sem, 16)
                    for n in range(8):
                        page = sp.value_load(t["page_table"][bass.ds(b, 1), n:n + 1], min_val=0,
                                             max_val=t["cache_c"].shape[0] - 1)
                        inc(sp.dma_start(x[s][64 * (n % 2):64 * (n % 2) + 64, n // 2, :],
                                         t["cache_c"][bass.ds(page, 1), :, :].rearrange(
                                             "o (a r) n -> (o a) (r n)", r=2)))
                    inc(sp.dma_start(win[s][:, :, :], t["cache_w"][bass.ds(b, 1), :, :].rearrange(
                        "o (c p) n -> p (o c) n", p=P)))
                    inc(sp.dma_start(nkv[s][:, :], t["c_kv"][bass.ds(b * DEC_S + SEQ, DEC_S), :]))
                    inc(sp.dma_start(nwin[s][:, :], t["c_win"][bass.ds(b * DEC_S + SEQ, DEC_S), :]))

                for s in range(2):
                    load(s, s)
                with sp.Fori(0, DEC_B // 2) as i:
                    for s in range(2):
                        waits(sp, seen, (by_dve.sem, by_dve.at(i, by_dve.names.index(f"out.{s}") + 1)))
                        for g in range(2):
                            for r in range(RC):
                                sp.dma_start(t["oc"][bass.ds((i * 2 + s) * DEC_S + SEQ, DEC_S), :, g * RC + r, :],
                                             o[s][32 * g + 8 * r:32 * g + 8 * r + 8, :, :]
                                             ).then_inc(o_out[s].sem, 16)
                        waits(sp, seen, (by_pe.sem, by_pe.at(i, by_pe.names.index(f"sum.{s}") + 1)))
                        load(s, (i * 2 + (2 + s)) % DEC_B)
                for s in range(2):
                    x_in[s].wait(sp, DEC_B // 2, 16 * 11)
                sp.dma_start(x[0][:, :, :], t["c_kv"][0:SEQ, :].rearrange("(c a r) n -> a c (r n)", a=P, r=2)
                             ).then_inc(x_in[0].sem, 16)
                sp.wait_ge(q_ev, 10)
                sp.dma_start(t["pc"][0:NCMP, :], kcr[:, :]).then_inc(pr_out, 16)
                sp.wait_ge(pr_out, 16)
                for s in range(2):
                    o_out[s].wait(sp, DEC_B // 2)

            @block.gpsimd
            def _(pool):
                by_pool.open(pool)
                pool.memset(qz[:, :, :], 0.0).then_inc(zero, 1)
                pool.memset(nhalf[:, :], -0.5).then_inc(zero, 1)
                pool.memset(wc[:, :, :, :], 0.0).then_inc(zero, 1)
                pool.wait_ge(zero, 3)

                def tile(i, s):
                    by_dve.after(pool, i, f"msk.{s}")
                    by_pool.did(pool.tensor_tensor(rsk[:, :], msk[:, :], nhalf[:, :], ALU.pow), f"rsk.{s}")

                with pool.Fori(0, DEC_B // 2) as i:
                    tile(i, 0)
                    tile(i, 1)
                tile(DEC_B // 2, 0)

            @block.tensor
            def _(pe):
                by_pe.open(pe)
                pe.wait_ge(const_in, 16 * 14)
                for r in range(RC):
                    last = pe.transpose(ms[:, r * N_DEC:(r + 1) * N_DEC], q[:, r * P:(r + 1) * P],
                                        ident[0:N_DEC, 0:N_DEC])
                last.then_inc(qtp, 1)
                for k in range(2):
                    for n in range(32):
                        last = pe.matmul(cps[:, k:k + 1], wc[:, k, n, :], peT[:, k, n:n + 1],
                                         start=n == 0, stop=n == 31)
                last.then_inc(pes, 1)
                pe.wait_ge(q_ev, 6)
                pe.wait_ge(peb_in, 1)

                def row_of(s):
                    return lambda c, r, kind: x[s][:, c, 512 * r + P * kind:512 * r + P * kind + P]

                def compress(i, s):
                    prev, row = (i, 0) if s else (i - 1, 1), row_of(s)
                    by_act.after(pe, prev[0], f"tps.{prev[1]}")
                    by_dve.after(pe, prev[0], f"tpw.{prev[1]}")
                    for n in range(4):
                        if n >= 2:
                            by_act.after(pe, i, f"tc{n - 2}.{s}")
                        pe.sem_inc(settled, 1)
                        for c in range(4):
                            last = pe.transpose(tp[n % 2][:, c * P:(c + 1) * P],
                                                row(c, n % 2, n // 2), ident[:, :])
                        by_pe.did(last, f"tc{n}.{s}")

                def products(i, s):
                    prev = (i, 0) if s else (i - 1, 1)
                    by_dve.after(pe, prev[0], f"out.{prev[1]}")
                    by_act.after(pe, i, f"tc3.{s}")
                    for k in range(2):
                        for n in range(32):
                            last = pe.matmul(cps[:, k * 64:k * 64 + NCMP], wc[:, k, n, :],
                                             xT[:, 2 * k + n % 2, n // 2:n // 2 + 8 * (NCMP - 1) + 1:8],
                                             start=n == 0, stop=n == 31)
                    by_pe.did(last, f"comp.{s}")
                    by_dve.after(pe, i, f"sqk.{s}")
                    by_pe.did(pe.matmul(ms[:, 0:NCMP], ones[:, :], sqk[:, :], start=True, stop=True), f"nrm.{s}")
                    by_dve.after(pe, i, f"msk.{s}")
                    by_dve.after(pe, i, f"vcf.{s}")
                    pe.sem_inc(settled, 1)
                    by_pe.did(pe.transpose(ms[0:NCMP, 64:64 + P], vcf[:, :], ident[:, :]), f"tv.{s}")

                def front(i, s):
                    row = row_of(s)
                    compress(i, s)
                    for r in range(2):
                        by_act.after(pe, i, f"tc{2 + r}.{s}")
                        for c in range(4):
                            last = pe.transpose(tp[r][:, c * P:(c + 1) * P], row(c, r, 2), ident[:, :])
                        by_pe.did(last, f"tk{r}.{s}")
                    by_dve.after(pe, i, f"tk0.{s}")
                    for c in range(4):
                        last = pe.transpose(tp[0][:, c * P:(c + 1) * P], win[s][:, c, 0:P], ident[:, :])
                    by_pe.did(last, f"tw.{s}")
                    by_dve.after(pe, i, f"tk1.{s}")
                    pe.sem_inc(settled, 1)
                    pe.transpose(tp[1][:, 0:DEC_S], nkv[s][:, 256:384], ident[0:DEC_S, 0:DEC_S])
                    by_pe.did(pe.transpose(tp[1][:, DEC_S:2 * DEC_S], nwin[s][:, 0:P], ident[0:DEC_S, 0:DEC_S]),
                              f"tn.{s}")
                    products(i, s)

                def tile(i, s):
                    row = row_of(s)
                    x_in[s].wait(pe, i, 16 * 11)
                    front(i, s)
                    by_act.after(pe, i, f"q.{s}")
                    by_dve.after(pe, i, f"tn.{s}")
                    for r in range(2):
                        pe.matmul(sS[0:NR, 512 * r:512 * r + 512], qs[:, :], ksT[:, r, :], start=True, stop=True)
                    pe.matmul(sW[0:NR, :], qs[:, :], kwT[:, :], start=True, stop=True)
                    by_pe.did(pe.matmul(sM[0:NR, 64:64 + 2 * DEC_S], qs[:, :], knT[:, :], start=True, stop=True),
                              f"scS.{s}")
                    by_dve.after(pe, i, f"kcT.{s}")
                    by_pe.did(pe.matmul(sM[0:NR, 0:NCMP], qs[:, :], kcT[:, :], start=True, stop=True), f"scC.{s}")
                    by_dve.after(pe, i, f"pc.{s}")
                    by_dve.after(pe, i, f"vc.{s}")
                    pe.sem_inc(settled, 1)
                    by_pe.did(pe.transpose(ms[0:NCMP, 192:192 + NR], pc[:, :], ident[0:NR, 0:NR]), f"tpc.{s}")
                    by_dve.after(pe, i, f"pcT.{s}")
                    pe.sem_inc(settled, 1)
                    by_pe.did(pe.matmul(ms[0:NR, 256:256 + NB + 1], pcT[:, :], share[:, :], start=True, stop=True),
                              f"imp1.{s}")
                    by_dve.after(pe, i, f"i1.{s}")
                    pe.sem_inc(settled, 1)
                    by_pe.did(pe.matmul(ms[0:NR, 288:288 + NB + 1], rsum[:, :], imp[:, :], start=True, stop=True),
                              f"imp2.{s}")
                    by_dve.after(pe, i, f"pS.{s}")
                    pe.sem_inc(settled, 1)
                    for c in range(8):
                        last = pe.transpose(tp[0][:, c * NR:(c + 1) * NR], pS[:, c * P:(c + 1) * P], ident[0:NR, 0:NR])
                    by_pe.did(last, f"tps.{s}")
                    by_dve.after(pe, i, f"pW.{s}")
                    pe.sem_inc(settled, 1)
                    for c in range(4):
                        pe.transpose(tp[1][:, c * NR:(c + 1) * NR], pW[:, c * P:(c + 1) * P], ident[0:NR, 0:NR])
                    pe.transpose(tp[1][0:DEC_S, 256:256 + NR], pW[:, CWIN:NKW], ident[0:NR, 0:NR])
                    by_pe.did(pe.transpose(tp[1][0:DEC_S, 320:320 + NR], pS[:, PAST:NKS], ident[0:NR, 0:NR]),
                              f"tpw.{s}")
                    by_act.after(pe, i, f"tps.{s}")
                    by_dve.after(pe, i, f"tpw.{s}")
                    pe.sem_inc(settled, 1)
                    out = lambda n: cps[0:NR, P + n * P:2 * P + n * P]
                    pe.matmul(out(0), pcT[:, :], vc[:, :], start=True, stop=True)
                    for c in range(8):
                        pe.matmul(out(1), pTs[:, c, :], row(c % 4, c // 4, 3), start=c == 0, stop=False)
                    pe.matmul(out(1), pTw[0:DEC_S, 5, :], nkv[s][:, 384:512], start=False, stop=True)
                    for c in range(4):
                        pe.matmul(out(2), pTw[:, c, :], win[s][:, c, P:2 * P], start=c == 0, stop=False)
                    by_pe.did(pe.matmul(out(2), pTw[0:DEC_S, 4, :], nwin[s][:, P:2 * P], start=False, stop=True),
                              f"sum.{s}")

                with pe.Fori(0, DEC_B // 2) as i:
                    tile(i, 0)
                    tile(i, 1)
                n = DEC_B // 2
                x_in[0].wait(pe, n + 1, 16)
                front(n, 0)
                by_dve.after(pe, n, "vc.0")
                pe.transpose(ms[0:NCMP, 192:192 + P], kcT[:, :], ident[:, :]).then_inc(qtp, 1)

            @block.scalar
            def _(act):
                by_act.open(act)
                act.wait_ge(zero, 3)
                act.wait_ge(qtp, 1)
                for g in range(2):
                    for r in range(RC):
                        rs = slice(HD * g, HD * g + HD)
                        act.activation(qz[rs, :, 32 * g + 8 * r:32 * g + 8 * r + 8],
                                       ms[rs, r * N_DEC:(r + 1) * N_DEC].rearrange("p (b q) -> p b q", b=DEC_B),
                                       ACT.Copy).then_inc(q_ev, 1)
                act.wait_ge(q_ev, 6)

                def take(i, s):
                    for n in range(4):
                        by_pe.after(act, i, f"tc{n}.{s}")
                        by_act.did(act.activation(xT[:, n, :], tp[n % 2][:, :], ACT.Copy), f"tc{n}.{s}")

                def queries(i, s, b):
                    by_pe.after(act, *((i, "scC.0") if s else (i - 1, "scC.1")))
                    by_act.did(act.activation(qs[:, :], qz[:, bass.ds(b, 1), :].rearrange(
                        "p o r -> p (o r)"), ACT.Copy), f"q.{s}")

                def tile(i, s):
                    queries(i, s, i * 2 + s)
                    take(i, s)
                    for k, buf, n in (("c", pc, 0), ("s", pS, 1), ("w", pW, 2)):
                        by_dve.after(act, i, {"c": f"bc.{s}", "s": f"bS.{s}", "w": f"bW.{s}"}[k])
                        by_act.did(act.activation(buf[:, :], sM[0:NR, 0:NCMP] if n == 0 else buf[:, :], ACT.Exp,
                                                  bias=st[:, n, 1:2], scale=SCALE, accum_out=st[:, n, 2:3]),
                                   f"e{k}.{s}")
                    by_pe.after(act, i, f"tps.{s}")
                    by_act.did(act.activation(pTs[:, :, :], tp[0][:, :].rearrange("p (c r) -> p c r", r=NR),
                                              ACT.Copy), f"tps.{s}")

                with act.Fori(0, DEC_B // 2) as i:
                    tile(i, 0)
                    tile(i, 1)
                queries(DEC_B // 2, 0, 0)
                take(DEC_B // 2, 0)

            @block.vector
            def _(dve):
                by_dve.open(dve)
                dve.wait_ge(const_in, 16 * 14)
                dve.wait_ge(pes, 1)
                dve.tensor_copy(peb[:, :], cps[:, 0:2]).then_inc(peb_in, 1)
                dve.wait_ge(peb_in, 1)

                def compress(i, s):
                    step = lambda name, ins: (by_dve.did(ins, f"{name}.{s}"), by_dve.after(dve, i, f"{name}.{s}"))
                    by_pe.after(dve, i, f"comp.{s}")
                    step("kcf", dve.tensor_scalar(kcf[:, :], cps[:, 0:NCMP], peb[:, 0:1], None, ALU.add))
                    by_pe.after(dve, *((i, "tv.0") if s else (i - 1, "tv.1")))
                    step("vcf", dve.tensor_scalar(vcf[:, :], cps[:, 64:64 + NCMP], peb[:, 1:2], None, ALU.add))
                    step("sqk", dve.tensor_tensor(sqk[:, :], kcf[:, :], kcf[:, :], ALU.mult))
                    by_pe.after(dve, i, f"nrm.{s}")
                    step("msk", dve.tensor_scalar(msk[:, :], ms[:, 0:NCMP], 1.0 / HD, EPS, ALU.mult, ALU.add))
                    by_pool.after(dve, i, f"rsk.{s}")
                    by_pe.after(dve, *((i, "scC.0") if s else (i - 1, "scC.1")))
                    step("kcT", dve.scalar_tensor_tensor(out=kcT[:, :], in0=kcf[:, :], scalar=gain[:, :],
                                                         in1=rsk[:, :], op0=ALU.mult, op1=ALU.mult))
                    by_pe.after(dve, i, f"tv.{s}")
                    by_pe.after(dve, *((i, "sum.0") if s else (i - 1, "sum.1")))
                    step("vc", dve.tensor_copy(vc[:, :], ms[0:NCMP, 64:64 + P]))

                def front(i, s):
                    step = lambda name, ins: (by_dve.did(ins, f"{name}.{s}"), by_dve.after(dve, i, f"{name}.{s}"))
                    prev = (i, 0) if s else (i - 1, 1)
                    by_pe.after(dve, prev[0], f"scS.{prev[1]}")
                    for r in range(2):
                        by_pe.after(dve, i, f"tk{r}.{s}")
                        step(f"tk{r}", dve.tensor_copy(ksT[:, r, :], tp[r][:, :]))
                    by_pe.after(dve, i, f"tw.{s}")
                    step("tw", dve.tensor_copy(kwT[:, :], tp[0][:, :]))
                    by_pe.after(dve, i, f"tn.{s}")
                    step("tn", dve.tensor_copy(knT[:, :], tp[1][:, 0:2 * DEC_S]))
                    compress(i, s)

                def tile(i, s):
                    step = lambda name, ins: (by_dve.did(ins, f"{name}.{s}"), by_dve.after(dve, i, f"{name}.{s}"))
                    prev = (i, 0) if s else (i - 1, 1)
                    front(i, s)
                    by_pe.after(dve, i, f"scC.{s}")
                    step("mc", dve.tensor_reduce(st[:, 0, 0:1], sM[0:NR, 0:NCMP], AX.X, ALU.max))
                    step("bc", dve.tensor_scalar(st[:, 0, 1:2], st[:, 0, 0:1], -SCALE, None, ALU.mult))
                    by_act.after(dve, i, f"ec.{s}")
                    step("rc", dve.reciprocal(st[:, 0, 3:4], st[:, 0, 2:3]))
                    step("pc", dve.tensor_scalar(pc[:, :], pc[:, :], st[:, 0, 3:4], None, ALU.mult))
                    by_pe.after(dve, i, f"tpc.{s}")
                    step("pcT", dve.tensor_copy(pcT[:, :], ms[0:NCMP, 192:192 + NR]))
                    by_pe.after(dve, i, f"imp1.{s}")
                    step("i1", dve.tensor_copy(imp[:, :], ms[0:NR, 256:256 + NB + 1]))
                    by_pe.after(dve, i, f"imp2.{s}")
                    step("i2", dve.tensor_copy(sel[:, 0:NB + 1], ms[0:NR, 288:288 + NB + 1]))
                    step("mn", dve.tensor_reduce(sel[:, 40:41], sel[:, 1:NB - 1], AX.X, ALU.min))
                    step("eq", dve.scalar_tensor_tensor(out=sel[:, 20:20 + NB - 2], in0=sel[:, 1:NB - 1],
                                                        scalar=sel[:, 40:41], in1=idx[:, 1:NB - 1],
                                                        op0=ALU.is_equal, op1=ALU.mult))
                    step("mi", dve.tensor_reduce(sel[:, 41:42], sel[:, 20:20 + NB - 2], AX.X, ALU.max))
                    step("drop", dve.tensor_scalar(drop[:, :], idx[:, :], sel[:, 41:42], NEG, ALU.is_equal, ALU.mult))
                    by_pe.after(dve, prev[0], f"tpw.{prev[1]}")
                    for r in range(2):
                        step(f"s{r}", dve.tensor_tensor(
                            pS[:, 512 * r:512 * r + 512].rearrange("p (b k) -> p b k", b=NB),
                            sS[0:NR, 512 * r:512 * r + 512].rearrange("p (b k) -> p b k", b=NB),
                            drop[:, :].unsqueeze(2).to_broadcast([NR, NB, 32]), ALU.add))
                    step("sn", dve.tensor_tensor(pS[:, PAST:NKS], sM[0:NR, 64:64 + DEC_S], mnew[:, :], ALU.add))
                    step("mS", dve.tensor_reduce(st[:, 1, 0:1], pS[:, :], AX.X, ALU.max))
                    step("bS", dve.tensor_scalar(st[:, 1, 1:2], st[:, 1, 0:1], -SCALE, None, ALU.mult))
                    step("w0", dve.tensor_tensor(pW[:, 0:CWIN], sW[0:NR, :], mwin[:, :], ALU.add))
                    step("wn", dve.tensor_tensor(pW[:, CWIN:NKW], sM[0:NR, 64 + DEC_S:64 + 2 * DEC_S], mnew[:, :],
                                                 ALU.add))
                    step("mW", dve.tensor_reduce(st[:, 2, 0:1], pW[:, :], AX.X, ALU.max))
                    step("bW", dve.tensor_scalar(st[:, 2, 1:2], st[:, 2, 0:1], -SCALE, None, ALU.mult))
                    for n, k, e, buf in ((1, "S", "es", pS), (2, "W", "ew", pW)):
                        by_act.after(dve, i, f"{e}.{s}")
                        step(f"r{k}", dve.reciprocal(st[:, n, 3:4], st[:, n, 2:3]))
                        step(f"p{k}", dve.tensor_scalar(buf[:, :], buf[:, :], st[:, n, 3:4], None, ALU.mult))
                    by_pe.after(dve, i, f"tpw.{s}")
                    dve.tensor_copy(pTw[:, 0:4, :], tp[1][:, 0:256].rearrange("p (c r) -> p c r", r=NR))
                    step("tpw", dve.tensor_copy(pTw[0:DEC_S, 4:6, :], tp[1][0:DEC_S, 256:384].rearrange(
                        "p (c r) -> p c r", r=NR)))
                    by_pe.after(dve, i, f"sum.{s}")
                    o_out[s].wait(dve, i)
                    for g in range(2):
                        rs = slice(32 * g, 32 * g + 32)
                        last = dve.tensor_copy(o[s][rs, :, :], cps[rs, P:4 * P].rearrange(
                            "p (n c) -> p n c", n=3)[:, :, HD * g:HD * g + HD])
                    step("out", last)

                with dve.Fori(0, DEC_B // 2) as i:
                    tile(i, 0)
                    tile(i, 1)
                n = DEC_B // 2
                front(n, 0)
                dve.tensor_copy(kcr[:, P:2 * P], vc[:, :]).then_inc(q_ev, 2)
                dve.wait_ge(qtp, 2)
                dve.tensor_copy(kcr[:, 0:P], ms[0:NCMP, 192:192 + P]).then_inc(q_ev, 2)


SLOTS = (2 * N_TOK + NE * (P - 1)) // P
SW = SLOTS + 2


def mix_and_experts(nc, t):
    with ExitStack() as ctx:
        sb = lambda name, shape, dt=F32: ctx.enter_context(nc.sbuf_tensor("m_" + name, shape, dt))
        ps = lambda name, shape: ctx.enter_context(nc.psum_tensor("m_" + name, shape, F32))
        sem = ctx.enter_context(semaphores(nc, "m_"))
        ident, tri, ones = sb("ident", [P, P]), sb("tri", [P, P]), sb("ones", [P, P])
        wo = sb("wo", [P, KD, D])
        wr = sb("wr", [P, KD, 20])
        rb = sb("rb", [P, 20])
        gain = sb("gain", [P, D])
        pri = sb("pri", [P, 4])
        thr = sb("thr", [P, TILES])
        before = sb("before", [P, NE, NE])
        sno = sb("sno", [P, SW])
        tid = sb("tid", [P, TILES], U32)
        cat = sb("cat", [P, D])
        oc = sb("oc", [P, 3, 384])
        zg = sb("zg", [P, 18])
        eg = sb("eg", [P, 18])
        x = sb("x", [P, D])
        catT = sb("catT", [P, KD, P])
        x1 = sb("x1", [P, TILES, D])
        sq = sb("sq", [P, D])
        st = sb("st", [P, 3])
        nhalf = sb("nhalf", [P, 1])
        h2 = sb("h2", [P, D])
        h2T = sb("h2T", [P, KD, P])
        tp, acc = ps("tp", [P, KD, P]), ps("acc", [P, D])
        hid = [ps(f"hid{s}", [P, 512]) for s in range(2)]
        hTp = ps("hTp", [P, 512])
        N = TILES
        L = sb("L", [P, N, 20])
        gm, gs, m1, m2, mm, pd, ee = (sb(n, [P, N]) for n in ("gm", "gs", "m1", "m2", "mm", "pd", "ee"))
        g4, og, es, o1, o2, tq4 = (sb(n, [P, N, 4]) for n in ("g4", "og", "es", "o1", "o2", "tq4"))
        t16, A, rank = (sb(n, [P, N, NE]) for n in ("t16", "A", "rank"))
        O = sb("O", [P, 2, N, NE])
        wt = sb("wt", [P, 2, N])
        base = sb("base", [P, N + 1, NE])
        tot = sb("tot", [P, N, NE])
        c9, nsl, first, c16 = sb("c9", [P, NE, N]), sb("nsl", [P, NE]), sb("first", [P, NE]), sb("c16", [P, NE, NE])
        K, S, fl, r = (sb(n, [P, 2, N]) for n in ("K", "S", "fl", "r"))
        c8 = sb("c8", [P, 2 * N, N - 1])
        at, pos = sb("at", [P, 2 * N], U32), sb("pos", [P, 2 * N], U32)
        c32, sx = sb("c32", [P, SW, NE]), sb("sx", [P, SW])
        sxi = sb("sxi", [P, SW], I32)
        zi = sb("zi", [P, SW], U32)
        tok = sb("tok", [P, SW], U32)
        w13 = [sb(f"w13_{s}", [P, KD, 2 * DE]) for s in range(2)]
        w2 = [sb(f"w2_{s}", [P, DE // P, D]) for s in range(2)]
        xg = [sb(f"xg{s}", [P, D]) for s in range(2)]
        ix = [sb(f"ix{s}", [P, 1], U32) for s in range(2)]
        xT = sb("xT", [P, KD, P])
        hs, hh = sb("hs", [P, DE]), sb("hh", [P, DE])
        hT = sb("hT", [P, DE // P, P])
        yo = [sb(f"yo{s}", [P, D]) for s in range(2)]
        gy = [sb(f"gy{s}", [P, D]) for s in range(2)]
        iy = [sb(f"iy{s}", [P, 1], U32) for s in range(2)]
        wy = sb("wy", [P, 2])
        yt = sb("yt", [P, D])
        const_in, seen, settled, cleared, rows_out, tab0, scat, sx_out, tok_in, y_end = map(sem, (
            "const_in", "seen", "settled", "cleared", "rows_out", "tab0", "scat", "sx_out", "tok_in", "y_end"))
        cat_in, x_in = Count(sem("cat_in"), 16 * 3), Count(sem("x_in"), 16)
        h2_out = Count(sem("h2_out"), 16)
        pe_s = Steps(sem("pe_s"), "catT wo")
        pe_r = Steps(sem("pe_r"), "h2T rout")
        act_s = Steps(sem("act_s"), "gate catT sq")
        act_r = Steps(sem("act_r"), "h2T")
        dve_s = Steps(sem("dve_s"), "g1 g2 b0 b1 b2 s1 s2 catT x1 ms h2")
        dve_r = Steps(sem("dve_r"), "h2T rout")
        pool_s = Steps(sem("pool_s"), "rs")
        rt_dve, rt_act, rt_pe, rt_pool = map(sem, ("rt_dve", "rt_act", "rt_pe", "rt_pool"))
        w13_in = [Count(sem(f"w13_in{s}"), 32) for s in range(2)]
        w2_in = [Count(sem(f"w2_in{s}"), 16) for s in range(2)]
        xg_in = [Count(sem(f"xg_in{s}"), 16) for s in range(2)]
        ys_out = [Count(sem(f"ys_out{s}"), 16) for s in range(2)]
        two = lambda names: " ".join(f"{n}.{s}" for s in range(2) for n in names.split())
        e_pe = Steps(sem("e_pe"), two("xT hid hT out"))
        e_act = Steps(sem("e_act"), two("xT exp hT out"))
        e_dve = Steps(sem("e_dve"), two("xT one rec sil hh out"))
        e_pool = Steps(sem("e_pool"), two("ix"))
        y_pool = Steps(sem("y_pool"), "ix")
        y_dve = Steps(sem("y_dve"), "wy a b")
        gy_in, yt_out = Count(sem("gy_in"), 32), Count(sem("yt_out"), 16)
        NS = SLOTS // 2
        assert SLOTS % 2 == 0

        with nc.Block() as block:

            @block.sync
            def _(sp):
                for c in (cat_in, x_in, h2_out, *w13_in, *w2_in, *ys_out, yt_out):
                    c.open(sp)
                for a, b in ((ident, "ident"), (tri, "m_tri"), (ones, "m_ones"), (pri, "m_pri"), (thr, "m_thr"),
                             (before, "m_before"), (sno, "m_sno"), (tid, "m_tid")):
                    sp.dma_start(a[:], t[b][:]).then_inc(const_in, 16)
                sp.dma_start(gain[:, :], t["ffn_norm"][0].partition_broadcast(P)).then_inc(const_in, 16)

                def load(rows, T):
                    sp.dma_start(cat[0:T, 0:640], t["cat"][rows, 0:640]).then_inc(cat_in.sem, 16)
                    sp.dma_start(oc[0:T, :, :], t["oc"][rows, :, :, :].rearrange("p b h d -> p b (h d)")
                                 ).then_inc(cat_in.sem, 16)
                    sp.dma_start(zg[0:T, :], t["zr"][rows, Z_G:Z_W]).then_inc(cat_in.sem, 16)

                load(slice(0, P), P)
                sp.dma_start(x[:, :], t["x"][0:P, :]).then_inc(x_in.sem, 16)
                sp.dma_start(wo[:, :, :], t["w_o"][0].rearrange("(k p) n -> p k n", p=P)).then_inc(const_in, 16)
                for lo, hi, w, b in ((0, 4, "moe_wg", "moe_bg"), (4, 20, "moe_we", "moe_be")):
                    sp.dma_start(wr[:, :, lo:hi], t[w][0].rearrange("(k p) n -> p k n", p=P)).then_inc(const_in, 16)
                    sp.dma_start(rb[:, lo:hi], t[b][0].partition_broadcast(P)).then_inc(const_in, 16)
                sp.dma_start(t["a_s"][:, PAST - DEC_S:PAST, :],
                             t["a_kv"][SEQ:N_TOK, :].rearrange("(b s) n -> b s n", b=DEC_B)).then_inc(rows_out, 16)
                sp.dma_start(t["w_s"][:, CWIN - DEC_S:CWIN, :],
                             t["c_win"][SEQ:N_TOK, :].rearrange("(b s) n -> b s n", b=DEC_B)).then_inc(rows_out, 16)

                def tile(i, T, T_next):
                    waits(sp, seen, (pe_s.sem, pe_s.at(i, 1)), (dve_s.sem, dve_s.at(i, 7)))
                    if T_next:
                        load(bass.ds((i + 1) * P, T_next), T_next)
                    waits(sp, seen, (dve_s.sem, dve_s.at(i, 9)))
                    if T_next:
                        sp.dma_start(x[0:T_next, :], t["x"][bass.ds((i + 1) * P, T_next), :]).then_inc(x_in.sem, 16)
                    waits(sp, seen, (dve_s.sem, dve_s.at(i, 11)))
                    sp.dma_start(t["h2"][bass.ds(i * P, T), :], h2[0:T, :]).then_inc(h2_out.sem, 16)

                with sp.Fori(0, PT - 1) as i:
                    tile(i, P, P)
                tile(PT - 1, P, N_DEC)
                tile(PT, N_DEC, 0)
                h2_out.wait(sp, TILES)
                sp.wait_ge(cleared, 3)
                sp.dma_start(t["tok_at"].rearrange("(p s) o -> p (s o)", s=SW), zi[:, :]).then_inc(tab0, 16)
                sp.wait_ge(rt_dve, SX_DONE)
                sp.dma_start(t["slot_expert"][:, :], sxi[0:1, :]).then_inc(sx_out, 16)
                sp.wait_ge(scat, 16 * 2 * TILES)
                sp.dma_start(tok[:, :], t["tok_at"].rearrange("(p s) o -> p (s o)", s=SW)).then_inc(tok_in, 16)
                sp.wait_ge(sx_out, 16)

                def load_slot(n, s, what):
                    e = sp.value_load(t["slot_expert"][0:1, bass.ds(n, 1)], min_val=0, max_val=NE - 1)
                    if what == "w13":
                        for k, w in enumerate(("moe_w1", "moe_w3")):
                            sp.dma_start(w13[s][:, :, k * DE:(k + 1) * DE],
                                         t[w][0, bass.ds(e, 1), :, :].rearrange("o (k p) f -> p (o k) f", p=P)
                                         ).then_inc(w13_in[s].sem, 16)
                    else:
                        sp.dma_start(w2[s][:, :, :],
                                     t["moe_w2"][0, bass.ds(e, 1), :, :].rearrange("o (k p) n -> p (o k) n", p=P)
                                     ).then_inc(w2_in[s].sem, 16)

                for s in range(2):
                    load_slot(s, s, "w13")
                    load_slot(s, s, "w2")
                with sp.Fori(0, NS) as i:
                    for s in range(2):
                        waits(sp, seen, (e_pe.sem, e_pe.at(i, 4 * s + 2)))
                        load_slot(i * 2 + (2 + s), s, "w13")
                        waits(sp, seen, (e_pe.sem, e_pe.at(i, 4 * s + 4)))
                        load_slot(i * 2 + (2 + s), s, "w2")
                        waits(sp, seen, (e_act.sem, e_act.at(i, 4 * s + 4)), (e_dve.sem, e_dve.at(i, 6 * s + 6)))
                        sp.dma_start(t["ys"][bass.ds((i * 2 + s) * P, P), :], yo[s][:, :]).then_inc(ys_out[s].sem, 16)
                for s in range(2):
                    w13_in[s].wait(sp, NS, 32)
                    w2_in[s].wait(sp, NS, 16)
                    ys_out[s].wait(sp, NS)
                sp.sem_inc(y_end, 1)
                for n in range(TILES):
                    T = P if n < PT else N_DEC
                    y_dve.after(sp, n, "b")
                    sp.dma_start(t["y"][n * P:n * P + T, :], yt[0:T, :]).then_inc(yt_out.sem, 16)
                yt_out.wait(sp, TILES)
                sp.wait_ge(rows_out, 32)

            @block.tensor
            def _(pe):
                for c in (pe_s, pe_r, e_pe):
                    c.open(pe)
                pe.wait_ge(const_in, 16 * 14)

                def project_out(i, T):
                    cat_in.wait(pe, i, 48)
                    dve_s.after(pe, i, "s2")
                    dve_r.after(pe, i - 1, "h2T")
                    act_r.after(pe, i - 1, "h2T")
                    if T < P:
                        pe.sem_inc(settled, 1)
                    for k in range(KD):
                        last = pe.transpose(tp[:, k, 0:T], cat[0:T, k * P:(k + 1) * P], ident[0:T, 0:T])
                    pe_s.did(last, "catT")
                    act_s.after(pe, i, "catT")
                    dve_s.after(pe, i, "catT")
                    if T < P:
                        pe.sem_inc(settled, 1)
                    for lo in (0, 512):
                        for k in range(KD):
                            last = pe.matmul(acc[0:T, lo:lo + 512], catT[:, k, 0:T], wo[:, k, lo:lo + 512],
                                             start=k == 0, stop=k == KD - 1)
                    pe_s.did(last, "wo")

                def router(i, T):
                    dve_s.after(pe, i, "h2")
                    for k in range(KD):
                        last = pe.transpose(tp[:, k, 0:T], h2[0:T, k * P:(k + 1) * P], ident[0:T, 0:T])
                    pe_r.did(last, "h2T")
                    act_r.after(pe, i, "h2T")
                    dve_r.after(pe, i, "h2T")
                    for k in range(KD):
                        last = pe.matmul(hTp[0:T, 0:20], h2T[:, k, 0:T], wr[:, k, :], start=k == 0, stop=k == KD - 1)
                    pe_r.did(last, "rout")

                with pe.Fori(0, PT) as i:
                    project_out(i, P)
                    router(i, P)
                project_out(PT, N_DEC)
                router(PT, N_DEC)
                pe.wait_ge(rt_dve, A_DONE)
                pe.matmul(hid[0][:, 0:N * NE], tri[:, :], A[:, :, :].rearrange("p n e -> p (n e)"),
                          start=True, stop=True)
                pe.matmul(hid[0][:, 256:256 + N * NE], ones[:, :], A[:, :, :].rearrange("p n e -> p (n e)"),
                          start=True, stop=True).then_inc(rt_pe, 1)
                pe.wait_ge(rt_dve, SX_DONE)

                def slot(i, s):
                    prev = (i, 0) if s else (i - 1, 1)
                    xg_in[s].wait(pe, i)
                    e_act.after(pe, prev[0], f"xT.{prev[1]}")
                    e_dve.after(pe, prev[0], f"xT.{prev[1]}")
                    for k in range(KD):
                        last = pe.transpose(tp[:, k, :], xg[s][:, k * P:(k + 1) * P], ident[:, :])
                    e_pe.did(last, f"xT.{s}")
                    e_act.after(pe, i, f"xT.{s}")
                    e_dve.after(pe, i, f"xT.{s}")
                    w13_in[s].wait(pe, i, 32)
                    e_dve.after(pe, i - 1, f"hh.{s}")
                    for k in range(KD):
                        last = pe.matmul(hid[s][:, :], xT[:, k, :], w13[s][:, k, :], start=k == 0, stop=k == KD - 1)
                    e_pe.did(last, f"hid.{s}")
                    e_dve.after(pe, i, f"hh.{s}")
                    for k in range(DE // P):
                        last = pe.transpose(hTp[:, k * P:(k + 1) * P], hh[:, k * P:(k + 1) * P], ident[:, :])
                    e_pe.did(last, f"hT.{s}")
                    e_act.after(pe, i, f"hT.{s}")
                    w2_in[s].wait(pe, i, 16)
                    e_act.after(pe, prev[0], f"out.{prev[1]}")
                    e_dve.after(pe, prev[0], f"out.{prev[1]}")
                    for lo in (0, 512):
                        for k in range(DE // P):
                            last = pe.matmul(acc[:, lo:lo + 512], hT[:, k, :], w2[s][:, k, lo:lo + 512],
                                             start=k == 0, stop=k == DE // P - 1)
                    e_pe.did(last, f"out.{s}")

                with pe.Fori(0, NS) as i:
                    slot(i, 0)
                    slot(i, 1)

            @block.scalar
            def _(act):
                for c in (act_s, act_r, e_act):
                    c.open(act)

                def tile(i, T):
                    cat_in.wait(act, i, 48)
                    dve_s.after(act, i - 1, "g2")
                    act_s.did(act.activation(eg[0:T, :], zg[0:T, :], ACT.Exp, scale=-1.0), "gate")
                    pe_s.after(act, i, "catT")
                    act_s.did(act.activation(catT[:, 0:4, 0:T], tp[:, 0:4, 0:T], ACT.Copy), "catT")
                    dve_s.after(act, i, "x1")
                    act_s.did(act.activation(sq[0:T, :], x1[0:T, bass.ds(i, 1), :].rearrange("p o n -> p (o n)"),
                                             ACT.Square, accum_out=st[0:T, 0:1]), "sq")
                    pe_r.after(act, i, "h2T")
                    act_r.did(act.activation(h2T[:, 0:4, 0:T], tp[:, 0:4, 0:T], ACT.Copy), "h2T")

                with act.Fori(0, PT) as i:
                    tile(i, P)
                tile(PT, N_DEC)
                act.wait_ge(rt_dve, G4_DONE)
                act.activation(g4[:, :, :], g4[:, :, :], ACT.Exp).then_inc(rt_act, 1)
                act.wait_ge(rt_dve, PD_DONE)
                act.activation(ee[:, :], pd[:, :], ACT.Exp).then_inc(rt_act, 1)

                def slot(i, s):
                    prev = (i, 0) if s else (i - 1, 1)
                    e_pe.after(act, i, f"xT.{s}")
                    e_act.did(act.activation(xT[:, 0:4, :], tp[:, 0:4, :], ACT.Copy), f"xT.{s}")
                    e_pe.after(act, i, f"hid.{s}")
                    e_act.did(act.activation(hs[:, :], hid[s][:, 0:DE], ACT.Exp, scale=-1.0), f"exp.{s}")
                    e_pe.after(act, i, f"hT.{s}")
                    e_act.did(act.activation(hT[:, :, :], hTp[:, 0:DE].rearrange("p (k t) -> p k t", t=P),
                                             ACT.Copy), f"hT.{s}")
                    e_pe.after(act, i, f"out.{s}")
                    ys_out[s].wait(act, i)
                    e_act.did(act.activation(yo[s][:, 0:512], acc[:, 0:512], ACT.Copy), f"out.{s}")

                with act.Fori(0, NS) as i:
                    slot(i, 0)
                    slot(i, 1)

            @block.gpsimd
            def _(pool):
                for c in (pool_s, e_pool, y_pool):
                    c.open(pool)
                pool.memset(nhalf[:, :], -0.5).then_inc(cleared, 1)
                pool.memset(zi[:, :], 0).then_inc(cleared, 1)
                pool.memset(L[:, :, :], 0.0).then_inc(cleared, 1)
                pool.wait_ge(cleared, 3)

                def tile(i, T):
                    dve_s.after(pool, i, "ms")
                    pool_s.did(pool.tensor_tensor(st[0:T, 2:3], st[0:T, 1:2], nhalf[0:T, :], ALU.pow), "rs")

                with pool.Fori(0, PT) as i:
                    tile(i, P)
                tile(PT, N_DEC)
                pool.wait_ge(rt_dve, AT_DONE)
                pool.wait_ge(tab0, 16)
                for n in range(2 * TILES):
                    T = P if n % TILES < PT else N_DEC
                    pool.indirect_dma_start(t["tok_at"][:, :], bass.IndirectOffsetOnAxis(at[0:T, n:n + 1], 0),
                                            tid[0:T, n % TILES:n % TILES + 1], None).then_inc(scat, 16)
                pool.wait_ge(tok_in, 16)
                h2_out.wait(pool, TILES)

                def gather(n, i, s, prev):
                    if prev:
                        xg_in[s].wait(pool, i)
                        e_pe.after(pool, i, f"xT.{s}")
                    e_pool.did(pool.tensor_copy(ix[s][:, :], tok[:, n]), f"ix.{s}")
                    e_pool.after(pool, i + 1 if prev else 0, f"ix.{s}")
                    pool.sem_inc(settled, 1)
                    pool.indirect_dma_start(xg[s][:, :], None, t["h2"][:, :],
                                            bass.IndirectOffsetOnAxis(ix[s][:, :], 0)).then_inc(xg_in[s].sem, 16)

                for s in range(2):
                    gather(slice(s, s + 1), 0, s, False)
                with pool.Fori(0, NS) as i:
                    for s in range(2):
                        gather(bass.ds(i * 2 + (2 + s), 1), i, s, True)
                for s in range(2):
                    xg_in[s].wait(pool, NS)
                pool.wait_ge(y_end, 1)

                def tile_y(i, T):
                    y_dve.after(pool, i - 1, "b")
                    pool.tensor_copy(iy[0][0:T, :], pos[0:T, bass.ds(i, 1)])
                    y_pool.did(pool.tensor_copy(iy[1][0:T, :], pos[0:T, bass.ds(i + N, 1)]), "ix")
                    y_pool.after(pool, i, "ix")
                    pool.sem_inc(settled, 1)
                    for k in range(2):
                        pool.indirect_dma_start(gy[k][0:T, :], None, t["ys"][:, :],
                                                bass.IndirectOffsetOnAxis(iy[k][0:T, :], 0)).then_inc(gy_in.sem, 16)

                with pool.Fori(0, PT) as i:
                    tile_y(i, P)
                tile_y(PT, N_DEC)

            @block.vector
            def _(dve):
                for c in (dve_s, dve_r, e_dve, y_dve):
                    c.open(dve)
                dve.wait_ge(const_in, 16 * 14)
                dve.wait_ge(cleared, 3)

                def tile(i, T):
                    tr = slice(0, T)
                    step = lambda name, ins: (dve_s.did(ins, name), dve_s.after(dve, i, name))
                    act_s.after(dve, i, "gate")
                    step("g1", dve.tensor_scalar(eg[tr, :], eg[tr, :], 1.0, None, ALU.add))
                    step("g2", dve.reciprocal(zg[tr, :], eg[tr, :]))
                    for b in range(3):
                        v = oc[tr, b, :].rearrange("p (h d) -> p h d", d=HD)
                        g = zg[tr, :].rearrange("p (h b) -> p h b", b=3)[:, :, b:b + 1].to_broadcast([T, HC, HD])
                        dve_s.did(dve.tensor_tensor(v, v, g, ALU.mult), f"b{b}")
                    dve_s.after(dve, i, "b2")
                    step("s1", dve.tensor_tensor(oc[tr, 0, :], oc[tr, 0, :], oc[tr, 1, :], ALU.add))
                    step("s2", dve.tensor_tensor(cat[tr, 640:1024], oc[tr, 0, :], oc[tr, 2, :], ALU.add))
                    pe_s.after(dve, i, "catT")
                    dve_s.did(dve.tensor_copy(catT[:, 4:8, tr], tp[:, 4:8, tr]), "catT")
                    pe_s.after(dve, i, "wo")
                    x_in.wait(dve, i, 16)
                    xi = x1[tr, bass.ds(i, 1), :].rearrange("p o n -> p (o n)")
                    step("x1", dve.tensor_tensor(xi, acc[tr, :], x[tr, :], ALU.add))
                    act_s.after(dve, i, "sq")
                    step("ms", dve.tensor_scalar(st[tr, 1:2], st[tr, 0:1], 1.0 / D, EPS, ALU.mult, ALU.add))
                    pool_s.after(dve, i, "rs")
                    h2_out.wait(dve, i)
                    step("h2", dve.scalar_tensor_tensor(out=h2[tr, :], in0=xi, scalar=st[tr, 2:3], in1=gain[tr, :],
                                                        op0=ALU.mult, op1=ALU.mult))
                    pe_r.after(dve, i, "h2T")
                    dve_r.did(dve.tensor_copy(h2T[:, 4:8, tr], tp[:, 4:8, tr]), "h2T")
                    pe_r.after(dve, i, "rout")
                    dve_r.did(dve.tensor_tensor(L[tr, bass.ds(i, 1), :].rearrange("p o n -> p (o n)"),
                                                hTp[tr, 0:20], rb[tr, :], ALU.add), "rout")

                with dve.Fori(0, PT) as i:
                    tile(i, P)
                tile(PT, N_DEC)
                dve_r.after(dve, PT, "rout")

                done = 0

                def step(ins):
                    nonlocal done
                    done += 1
                    ins.then_inc(rt_dve, 1)
                    dve.wait_ge(rt_dve, done)

                B4 = [P, N, 4]
                wide = lambda a, shape=B4: a.unsqueeze(2).to_broadcast(shape)

                def first_max(out, v, m):
                    step(dve.tensor_reduce(m[:, :], v, AX.X, ALU.max))
                    step(dve.tensor_tensor(tq4[:, :, :], v, wide(m[:, :]), ALU.is_equal))
                    step(dve.tensor_tensor(tq4[:, :, :], tq4[:, :, :], pri[:, :].unsqueeze(1).to_broadcast(B4),
                                           ALU.mult))
                    step(dve.tensor_reduce(mm[:, :], tq4[:, :, :], AX.X, ALU.max))
                    step(dve.tensor_tensor(out[:, :, :], tq4[:, :, :], wide(mm[:, :]), ALU.is_equal))

                first_max(og, L[:, :, 0:4], gm)
                step(dve.tensor_tensor(g4[:, :, :], L[:, :, 0:4], wide(gm[:, :]), ALU.subtract))
                assert done == G4_DONE
                le = L[:, :, 4:20].rearrange("p n (g e) -> p n g e", g=4)
                B44 = [P, N, 4, 4]
                v44 = lambda a: a.rearrange("p n (g e) -> p n g e", g=4)
                step(dve.tensor_tensor(v44(t16[:, :, :]), le, og[:, :, :].unsqueeze(3).to_broadcast(B44), ALU.mult))
                step(dve.tensor_reduce(es[:, :, :], t16[:, :, :].rearrange("p n (g e) -> p n e g", g=4),
                                       AX.X, ALU.add))
                first_max(o1, es[:, :, :], m1)
                step(dve.scalar_tensor_tensor(out=es[:, :, :], in0=o1[:, :, :], scalar=NEG, in1=es[:, :, :],
                                              op0=ALU.mult, op1=ALU.add))
                first_max(o2, es[:, :, :], m2)
                step(dve.tensor_tensor(pd[:, :], m2[:, :], m1[:, :], ALU.subtract))
                assert done == PD_DONE
                for k, o in enumerate((o1, o2)):
                    step(dve.tensor_tensor(v44(O[:, k, :, :]), og[:, :, :].unsqueeze(3).to_broadcast(B44),
                                           o[:, :, :].unsqueeze(2).to_broadcast(B44), ALU.mult))
                step(dve.tensor_tensor(A[:, :, :], O[:, 0, :, :], O[:, 1, :, :], ALU.add))
                step(dve.memset(A[N_DEC:P, PT:TILES, :], 0.0))
                assert done == A_DONE
                dve.wait_ge(rt_act, 2)
                step(dve.tensor_reduce(gs[:, :], g4[:, :, :], AX.X, ALU.add))
                step(dve.tensor_scalar(pd[:, :], ee[:, :], 1.0, None, ALU.add))
                step(dve.tensor_tensor(gs[:, :], gs[:, :], pd[:, :], ALU.mult))
                step(dve.reciprocal(wt[:, 0, :], gs[:, :]))
                step(dve.tensor_tensor(wt[:, 1, :], wt[:, 0, :], ee[:, :], ALU.mult))
                dve.wait_ge(rt_pe, 1)
                step(dve.tensor_copy(tot[:, :, :], hid[0][:, 256:256 + N * NE].rearrange("p (n e) -> p n e", e=NE)))
                step(dve.memset(base[:, 0, :], 0.0))
                for n in range(N):
                    step(dve.tensor_tensor(base[:, n + 1, :], base[:, n, :], tot[:, n, :], ALU.add))
                step(dve.tensor_tensor(rank[:, :, :], hid[0][:, 0:N * NE].rearrange("p (n e) -> p n e", e=NE),
                                       base[:, 0:N, :], ALU.add))
                B9 = [P, NE, N]
                step(dve.tensor_tensor(c9[:, :, :], base[:, N, :].unsqueeze(2).to_broadcast(B9),
                                       thr[:, :].unsqueeze(1).to_broadcast(B9), ALU.is_gt))
                step(dve.tensor_reduce(nsl[:, :], c9[:, :, :], AX.X, ALU.add))
                step(dve.tensor_tensor(c16[:, :, :], before[:, :, :],
                                       nsl[:, :].unsqueeze(1).to_broadcast([P, NE, NE]), ALU.mult))
                step(dve.tensor_reduce(first[:, :], c16[:, :, :], AX.X, ALU.add))
                step(dve.tensor_tensor(nsl[:, :], nsl[:, :], first[:, :], ALU.add))
                BS = [P, SW, NE]
                step(dve.tensor_tensor(c32[:, :, :], sno[:, :].unsqueeze(2).to_broadcast(BS),
                                       nsl[:, :].unsqueeze(1).to_broadcast(BS), ALU.is_ge))
                step(dve.tensor_reduce(sx[:, :], c32[:, :, :], AX.X, ALU.add))
                step(dve.tensor_scalar(sxi[:, :], sx[:, :], NE - 1.0, None, ALU.min))
                assert done == SX_DONE, done
                for k in range(2):
                    step(dve.tensor_tensor(t16[:, :, :], O[:, k, :, :], rank[:, :, :], ALU.mult))
                    step(dve.tensor_reduce(K[:, k, :], t16[:, :, :], AX.X, ALU.add))
                    step(dve.tensor_tensor(t16[:, :, :], O[:, k, :, :],
                                           first[:, :].unsqueeze(1).to_broadcast([P, N, NE]), ALU.mult))
                    step(dve.tensor_reduce(S[:, k, :], t16[:, :, :], AX.X, ALU.add))
                f2 = lambda a: a[:, :, :].rearrange("p k n -> p (k n)")
                B8 = [P, 2 * N, N - 1]
                step(dve.tensor_tensor(c8[:, :, :], f2(K).unsqueeze(2).to_broadcast(B8),
                                       thr[:, 1:N].unsqueeze(1).to_broadcast(B8), ALU.is_ge))
                step(dve.tensor_reduce(f2(fl), c8[:, :, :], AX.X, ALU.add))
                step(dve.scalar_tensor_tensor(out=f2(r), in0=f2(fl), scalar=-float(P), in1=f2(K),
                                              op0=ALU.mult, op1=ALU.add))
                step(dve.tensor_tensor(f2(S), f2(S), f2(fl), ALU.add))
                step(dve.scalar_tensor_tensor(out=at[:, :], in0=f2(r), scalar=float(SW), in1=f2(S),
                                              op0=ALU.mult, op1=ALU.add))
                step(dve.scalar_tensor_tensor(out=pos[:, :], in0=f2(S), scalar=float(P), in1=f2(r),
                                              op0=ALU.mult, op1=ALU.add))
                assert done == AT_DONE, done

                def slot(i, s):
                    prev = (i, 0) if s else (i - 1, 1)
                    step = lambda name, ins: (e_dve.did(ins, f"{name}.{s}"), e_dve.after(dve, i, f"{name}.{s}"))
                    e_pe.after(dve, i, f"xT.{s}")
                    e_dve.did(dve.tensor_copy(xT[:, 4:8, :], tp[:, 4:8, :]), f"xT.{s}")
                    e_act.after(dve, i, f"exp.{s}")
                    step("one", dve.tensor_scalar(hs[:, :], hs[:, :], 1.0, None, ALU.add))
                    step("rec", dve.reciprocal(hs[:, :], hs[:, :]))
                    step("sil", dve.tensor_tensor(hs[:, :], hs[:, :], hid[s][:, 0:DE], ALU.mult))
                    step("hh", dve.tensor_tensor(hh[:, :], hs[:, :], hid[s][:, DE:2 * DE], ALU.mult))
                    e_pe.after(dve, i, f"out.{s}")
                    ys_out[s].wait(dve, i)
                    e_dve.did(dve.tensor_copy(yo[s][:, 512:1024], acc[:, 512:1024]), f"out.{s}")

                with dve.Fori(0, NS) as i:
                    slot(i, 0)
                    slot(i, 1)

                def tile_y(i, T):
                    tr = slice(0, T)
                    step = lambda name, ins: (y_dve.did(ins, name), y_dve.after(dve, i, name))
                    step("wy", dve.tensor_copy(wy[tr, :], wt[tr, :, bass.ds(i, 1)].rearrange("p k o -> p (k o)")))
                    gy_in.wait(dve, i)
                    yt_out.wait(dve, i)
                    xi = x1[tr, bass.ds(i, 1), :].rearrange("p o n -> p (o n)")
                    step("a", dve.scalar_tensor_tensor(out=yt[tr, :], in0=gy[0][tr, :], scalar=wy[tr, 0:1],
                                                       in1=xi, op0=ALU.mult, op1=ALU.add))
                    step("b", dve.scalar_tensor_tensor(out=yt[tr, :], in0=gy[1][tr, :], scalar=wy[tr, 1:2],
                                                       in1=yt[tr, :], op0=ALU.mult, op1=ALU.add))

                with dve.Fori(0, PT) as i:
                    tile_y(i, P)
                tile_y(PT, N_DEC)


G4_DONE = 6
PD_DONE = G4_DONE + 14
A_DONE = PD_DONE + 4
SX_DONE = A_DONE + 5 + 2 + TILES + 1 + 8
AT_DONE = SX_DONE + 8 + 6


def routing_constants():
    f = lambda a: np.ascontiguousarray(a, np.float32)
    rep = lambda a: f(np.tile(a[None], (P,) + (1,) * a.ndim))
    e = np.arange(NE)
    return {"m_tri": f(np.arange(P)[:, None] < np.arange(P)[None, :]), "m_ones": f(np.ones((P, P))),
            "m_pri": rep(np.array([4, 3, 2, 1])), "m_thr": rep(np.arange(TILES) * P),
            "m_before": rep((e[None, :] < e[:, None]) * 1), "m_sno": rep(np.arange(SW)),
            "m_tid": (np.arange(P)[:, None] + P * np.arange(TILES)[None, :]).astype(np.uint32)}


def multiplicity(dist):
    n = np.zeros(dist.shape, np.float32)
    for window, dil in ((128, 1), (512, 4), (2048, 16)):
        n += (dist >= 0) & (dist <= window) & (dist % dil == 0)
    return n


def additive(n):
    return np.where(n > 0, np.log(np.maximum(n, 1)) / SCALE, NEG).astype(np.float32)


def constants():
    q, x = np.arange(P)[:, None], np.arange(PT * P + 3 * P * 3 + P * 2)[None, :]
    dist = q + (PT + 1) * P - np.arange((2 * PT + 1) * P)[None, :]
    c = np.arange((PT + 1) * 8 + 64)[None, :]
    block = c - 8 * (PT + 1)
    cmp_ok = 16 * block + 31 <= q
    return {
        "ident": np.eye(P, dtype=np.float32),
        "mask_a": additive(multiplicity(dist)),
        "mask_causal": additive(dist >= 0),
        "mask_win": additive((dist >= 0) & (dist <= CWIN)),
        "mask_cmp": additive(cmp_ok),
    }


def sample_constants():
    q, k = np.arange(DEC_S)[:, None], np.arange(PAST + DEC_S)[None, :]
    return {"mask_sa": np.tile(additive(multiplicity(PAST + q - k)), (HA, 1))}


def chunk_tables(T, block):
    u, c = np.arange(T)[:, None], np.arange(T)[None, :]
    same = u // block == c // block
    sums, pairs, m = [], [], block // 2
    while m:
        r = c // (2 * m) * 2 * m + m - 1
        second = c > r
        sums.append(np.where(second, (u > r) & (u <= c), (u > c) & (u <= r)))
        pairs.append((u // (2 * m) == c // (2 * m)) & (u // m % 2 == 0) & (c // m % 2 == 1))
        m //= 2
    sums.append(same & (u <= c))
    pairs.append(u == c)
    return (np.concatenate(sums, 1).astype(np.float32), (same & (u > c)).astype(np.float32),
            np.concatenate(pairs, 1).astype(np.float32))


def recurrence_constants():
    a, b = chunk_tables(P, P), chunk_tables(N_DEC, DEC_S)
    rows = (np.arange(N_DEC)[:, None] // DEC_S == np.arange(DEC_B)[None, :]).astype(np.float32)
    return {"b_sums": a[0], "b_suf": a[1], "b_pair": a[2], "bs_sums": b[0], "bs_suf": b[1],
            "bs_pair": b[2], "bs_rows": rows, "bs_cols": np.tile(rows.T[None], (P, 1, 1))}


def nsa_constants():
    cs, ss = np.arange(NCMP)[:, None] * 16, np.arange(17)[None, :] * 64
    share = np.maximum(np.minimum(cs + 31, ss + 63) - np.maximum(cs, ss) + 1, 0) / 32
    row = np.arange(64)
    g, q = row // 32, row % 8
    rsum = (g[:, None] == g[None, :]) & (q[:, None] == q[None, :]) & (row[:, None] % 32 < 24)
    ones2 = np.kron(np.eye(2), np.ones((HD, HD)))
    f = lambda a: np.ascontiguousarray(a, np.float32)
    return {"share": f(share), "rsum": f(rsum), "ones2": f(ones2), "blk": f(np.tile(np.arange(16), (64, 1))),
            "mask_new": additive(np.arange(8)[None, :] <= q[:, None]),
            "mask_sw": additive(np.arange(CWIN)[None, :] >= q[:, None])}


def tables():
    return {**constants(), **sample_constants(), **recurrence_constants(), **nsa_constants(),
            **routing_constants()}


def build(nc, t):
    rows = lambda n: bass.ds(n * P, P)
    mask = lambda name: lambda n: t[name][:, bass.ds(n * -P + (PT + 1) * P, SEQ)]
    cq = lambda n: t["zr"][rows(n), Z_CQ:Z_CQ + 384]
    branch = lambda b: lambda n: t["oc"][rows(n), b, :, :].rearrange("p h d -> p (h d)")
    units_a = [(h // 2, h % 2, h // 2, h, h) for h in range(HA)]
    units_c = [(r, g, 0, g, g * RC + r) for g in range(GC) for r in range(RC)]
    project(nc, t)
    prompt_attention(nc, t, "a_", lambda n: t["zr"][rows(n), Z_AQ:Z_AQ + 384], t["a_kv"][0:SEQ, 0:384],
                     t["a_kv"][0:SEQ, 384:768], mask("mask_a"), lambda n: t["cat"][rows(n), 0:384],
                     units_a, [P] * PT)
    sample_a(nc, t)
    hgrn(nc, t)
    sample_c(nc, t)
    prompt_attention(nc, t, "cc_", cq, t["pc"][0:NCMP, 0:P], t["pc"][0:NCMP, P:2 * P],
                     lambda n: t["mask_cmp"][:, bass.ds(n * -8 + (PT + 1) * 8, NCMP)], branch(0), units_c, [NCMP])
    prompt_attention(nc, t, "cs_", cq, t["c_kv"][0:SEQ, 256:384], t["c_kv"][0:SEQ, 384:512],
                     mask("mask_causal"), branch(1), units_c, [P] * PT)
    prompt_attention(nc, t, "cw_", cq, t["c_win"][0:SEQ, 0:P], t["c_win"][0:SEQ, P:2 * P],
                     mask("mask_win"), branch(2), units_c, [P] * PT)
    mix_and_experts(nc, t)


def kernel(x_prompt, x_sample, cache_a_kv, state_b, cache_c_kv, cache_c_win, page_table, **weights):
    import concourse.bacc as bacc
    from concourse.bass_utils import run_bass_kernel_spmd as run

    f = lambda a: np.ascontiguousarray(a)
    x = np.zeros(((TILES + 1) * P, D), np.float32)
    x[:SEQ] = x_prompt[0]
    x[SEQ:N_TOK] = np.reshape(x_sample, (N_DEC, D))
    ins = {"x": x, "cache_a": f(cache_a_kv[0]).reshape(DEC_B, PAST, 768),
           "cache_w": f(cache_c_win[0]).reshape(DEC_B, CWIN, 256),
           "cache_c": f(cache_c_kv[0]).reshape(-1, P, 512),
           "page_table": f(page_table), "state_b": f(state_b[0]), **tables()}
    ins.update({k: f(v) for k, v in weights.items()})
    outs = {"y": (N_TOK, D), "a_kv": (TILES * P, 768), "c_kv": (TILES * P, 512),
            "c_win": (TILES * P, 256), "a_s": (DEC_B, PAST, 768), "w_s": (DEC_B, CWIN, 256),
            "s_p": (HB, HD, HD), "s_s": (DEC_B, HB, HD, HD)}
    scratch = {"zr": ((PT + 2) * P, Z_W), "cat": (N_TOK, D), "oc": (N_TOK, 3, HC, HD), "pc": (HD, 2 * P),
               "h2": (N_TOK, D), "ys": (SLOTS * P, D)}
    tables_of_int = {"tok_at": ((P * SW, 1), U32), "slot_expert": ((1, SW), I32)}
    nc = bacc.Bacc("TRN2", target_bir_lowering=False, num_devices=1)
    t = {}
    for name, a in ins.items():
        t[name] = nc.dram_tensor("in_" + name, a.shape, mybir.dt.from_np(a.dtype), kind="ExternalInput").ap()
    for name, shape in outs.items():
        t[name] = nc.dram_tensor("out_" + name, shape, F32, kind="ExternalOutput").ap()
    for name, shape in scratch.items():
        t[name] = nc.dram_tensor("tmp_" + name, shape, F32, kind="Internal").ap()
    for name, (shape, dt) in tables_of_int.items():
        t[name] = nc.dram_tensor("tmp_" + name, shape, dt, kind="Internal").ap()
    build(nc, t)
    r = run(nc, [{"in_" + k: a for k, a in ins.items()}], core_ids=[0]).results[0]
    o = {k: r["out_" + k] for k in outs}
    kv = lambda a, *s: a.reshape(1, *s)
    return (o["y"][:SEQ].reshape(1, SEQ, D), o["y"][SEQ:N_TOK].reshape(DEC_B, DEC_S, D),
            kv(o["a_kv"][:SEQ], 1, SEQ, 2, HA, HD), kv(o["a_s"], DEC_B, PAST, 2, HA, HD),
            kv(o["s_p"], 1, HB, HD, HD), kv(o["s_s"], DEC_B, HB, HD, HD),
            kv(o["c_kv"][:SEQ], 1, SEQ, 4, GC, HD), kv(o["c_kv"][SEQ:N_TOK], DEC_B, DEC_S, 4, GC, HD),
            kv(o["c_win"][SEQ - CWIN:SEQ], 1, CWIN, 2, GC, HD), kv(o["w_s"], DEC_B, CWIN, 2, GC, HD))
```

```python
from contextlib import ExitStack, contextmanager

import numpy as np
import concourse.bass as bass
from concourse import mybir

F32 = mybir.dt.float32
I32 = mybir.dt.int32
U32 = mybir.dt.uint32
ALU = mybir.AluOpType
ACT = mybir.ActivationFunctionType
AX = mybir.AxisListType

P = 128
D = 1024
KD = D // P
SEQ = 1024
DEC_B, DEC_S = 8, 8
N_DEC = DEC_B * DEC_S
N_TOK = SEQ + N_DEC
PT = SEQ // P
TILES = PT + 1
HD = 64
HA, HB, HC, GC, RC = 6, 4, 6, 2, 3
PAST = 1024
CWIN = 512
NCMP = 63
EPS = 1e-6
NEG = -1e30
TINY = 1e-30
SCALE = HD ** -0.5
NE, DE = 16, 256

AQ, AK, AV, BQ, BF, BV, BG, CQ, CKC, CVC, CKS, CVS, CKW, CVW, CG, D_IN = (
    0, 384, 768, 1152, 1408, 1664, 1920, 2176, 2560, 2688, 2816, 2944, 3072, 3200, 3328, 3346)
Z_AQ, Z_B, Z_CQ, Z_G, Z_W = 0, 384, 1408, 1792, 1810


@contextmanager
def semaphores(nc, stage):
    held = []

    def new(name):
        held.append(nc.alloc_semaphore(stage + name))
        return held[-1]

    yield new
    nc.clear_and_free_semaphores(held)
    nc.all_engine_barrier()


class Count:

    def __init__(self, sem, per=1):
        self.sem, self.per = sem, per

    def open(self, eng):
        eng.sem_inc(self.sem, self.per)

    def at(self, i, n=0):
        return (i + 1) * self.per + n

    def wait(self, eng, i, n=0):
        eng.wait_ge(self.sem, self.at(i, n))


def waits(eng, seen, *pairs):
    for sem, v in pairs:
        eng.wait_ge(sem, v)
        eng.sem_inc(seen, 1)


CHUNKS = [
    (AQ, 384, [(0, 6, 0)]), (AK, 384, [(0, 6, 1)]), (AV, 384, []), (BQ, 512, []), (BV, 512, []),
    (CQ, 384, [(0, 6, 2)]), (CKC, 512, [(256, 2, 3)]), (CKW, 274, [(0, 2, 4)]),
]


def project(nc, t):
    NCH = len(CHUNKS)
    NORMED = [c for c, (_, _, n) in enumerate(CHUNKS) if n]
    with ExitStack() as ctx:
        sb = lambda name, shape, dt=F32: ctx.enter_context(nc.sbuf_tensor("p_" + name, shape, dt))
        ps = lambda name, shape: ctx.enter_context(nc.psum_tensor("p_" + name, shape, F32))
        sem = ctx.enter_context(semaphores(nc, "p_"))
        w = sb("w", [P, KD, D_IN])
        gx = sb("gx", [P, KD])
        gains = sb("gains", [P, 5, HD])
        ident = sb("ident", [P, P])
        x = sb("x", [P, D])
        xn = sb("xn", [P, D])
        sqx = sb("sqx", [P, D])
        hT = sb("hT", [P, KD, P])
        z = sb("z", [P, D_IN])
        sq = sb("sq", [P, 384])
        ssx = sb("ssx", [P, 3])
        ss = sb("ss", [P, 3, 6])
        tp = ps("tp", [P, KD, P])
        acc = [ps(f"acc{n}", [P, 512]) for n in range(4)]
        const_in, seen = sem("const_in"), sem("seen")
        w_in = [sem(f"w_in{c}") for c in range(NCH)]
        x_in, x_sq, x_ms, x_rt, x_rs, xn_ready, xn_read = map(sem, (
            "x_in", "x_sq", "x_ms", "x_rt", "x_rs", "xn_ready", "xn_read"))
        ht_ready, z_ps, z_sq, z_ms, z_rt, z_rs, z_nrm, z_cp, z_dve = map(sem, (
            "ht_ready", "z_ps", "z_sq", "z_ms", "z_rt", "z_rs", "z_nrm", "z_cp", "z_dve"))
        z_out = [sem(f"z_out{c}") for c in range(NCH)]
        shifted = sem("shifted")
        copies = []
        for c0, cw, norms in CHUNKS:
            lo, pieces = 0, []
            for o, h, _ in norms:
                if o > lo:
                    pieces.append((lo, o))
                lo = o + h * HD
            if lo < cw:
                pieces.append((lo, cw))
            copies.append(pieces)
        n_cp = [sum(len(p) for p in copies[:c + 1]) for c in range(NCH)]
        n_nm = [sum(c2 <= c for c2 in NORMED) for c in range(NCH)]
        NCP, NNM = n_cp[-1], n_nm[-1]
        xin, xnr, xnd = Count(x_in, 16), Count(xn_ready), Count(xn_read)
        xsq, xms, xrt, xrs = Count(x_sq), Count(x_ms), Count(x_rt), Count(x_rs)
        htr, zps, cp, nm = Count(ht_ready, 2), Count(z_ps, NCH), Count(z_cp, NCP), Count(z_nrm, NNM)
        zsq, zms, zrt, zdv = Count(z_sq, NNM), Count(z_ms, NNM), Count(z_rt, NNM), Count(z_dve, 3 * NNM)
        out = [Count(z_out[c], 32 if c == NCH - 1 else 16) for c in range(NCH)]
        with nc.Block() as block:

            @block.sync
            def _(sp):
                for c in (xin, *out):
                    c.open(sp)
                sp.dma_start(ident[:, :], t["ident"][:, :]).then_inc(const_in, 16)
                sp.dma_start(gx[:, :], t["attn_norm"][0, :].rearrange("(k p) -> p k", p=P),
                             allow_slow_non_contiguous=True).then_inc(const_in, 16)
                for n, g in enumerate((t["a_qnorm"][0], t["a_knorm"][0], t["c_qnorm"][0],
                                       t["c_knorm"][0, 1], t["c_knorm"][0, 2])):
                    sp.dma_start(gains[:, n, :], g.partition_broadcast(P)).then_inc(const_in, 16)
                sp.dma_start(x[:, :], t["x"][0:P, :]).then_inc(x_in, 16)
                for c, (c0, cw, _) in enumerate(CHUNKS):
                    sp.dma_start(w[:, :, c0:c0 + cw],
                                 t["w_in"][0, :, c0:c0 + cw].rearrange("(k p) n -> p k n", p=P)
                                 ).then_inc(w_in[c], 16)
                with sp.Fori(0, TILES) as i:
                    waits(sp, seen, (xn_ready, xnr.at(i, 1)))
                    sp.dma_start(x[:, :], t["x"][bass.ds((i + 1) * P, P), :]).then_inc(x_in, 16)
                    rows = bass.ds(i * P, P)
                    for c, (c0, cw, norms) in enumerate(CHUNKS):
                        waits(sp, seen, *([(z_cp, cp.at(i, n_cp[c]))] if copies[c] else []),
                              *([(z_nrm, nm.at(i, n_nm[c]))] if norms else []))
                        src = z[:, c0:c0 + cw]
                        if c in (0,):
                            dst = t["zr"][rows, Z_AQ:Z_AQ + 384]
                        elif c in (1, 2):
                            dst = t["a_kv"][rows, c0 - AK:c0 - AK + cw]
                        elif c in (3, 4):
                            dst = t["zr"][rows, Z_B + c0 - BQ:Z_B + c0 - BQ + cw]
                        elif c == 5:
                            dst = t["zr"][rows, Z_CQ:Z_CQ + 384]
                        elif c == 6:
                            dst = t["c_kv"][rows, :]
                        else:
                            sp.dma_start(t["c_win"][rows, :], z[:, CKW:CG]).then_inc(z_out[c], 16)
                            src, dst = z[:, CG:D_IN], t["zr"][rows, Z_G:Z_W]
                        sp.dma_start(dst, src).then_inc(z_out[c], 16)
                xin.wait(sp, TILES + 1)
                for c in out:
                    c.wait(sp, TILES)

            @block.gpsimd
            def _(pool):
                for b in range(DEC_B):
                    pool.dma_start(t["a_s"][b, 0:PAST - DEC_S, :],
                                   t["cache_a"][b, DEC_S:PAST, :]).then_inc(shifted, 16)
                    pool.dma_start(t["w_s"][b, 0:CWIN - DEC_S, :],
                                   t["cache_w"][b, DEC_S:CWIN, :]).then_inc(shifted, 16)
                pool.wait_ge(shifted, 32 * DEC_B)

            @block.tensor
            def _(pe):
                zps.open(pe)
                xnd.open(pe)
                pe.wait_ge(const_in, 16 * 7)
                with pe.Fori(0, TILES) as i:
                    xnr.wait(pe, i, 1)
                    for k in range(KD):
                        last = pe.transpose(tp[:, k, :], xn[:, k * P:(k + 1) * P], ident[:, :])
                    last.then_inc(xn_read, 1)
                    htr.wait(pe, i, 2)
                    for c, (c0, cw, norms) in enumerate(CHUNKS):
                        if c == 0:
                            cp.wait(pe, i)
                            nm.wait(pe, i)
                        if c >= 4:
                            if copies[c - 4]:
                                cp.wait(pe, i, n_cp[c - 4])
                            if CHUNKS[c - 4][2]:
                                nm.wait(pe, i, n_nm[c - 4])
                        pe.wait_ge(w_in[c], 16)
                        for k in range(KD):
                            last = pe.matmul(acc[c % 4][:, 0:cw], hT[:, k, :], w[:, k, c0:c0 + cw],
                                             start=k == 0, stop=k == KD - 1)
                        last.then_inc(z_ps, 1)

            @block.scalar
            def _(act):
                for c in (xsq, xrt, cp, zsq, zrt):
                    c.open(act)

                def norm_x(n):
                    xin.wait(act, n, 16)
                    act.activation(sqx[:, :], x[:, :], ACT.Square, accum_out=ssx[:, 0:1]).then_inc(x_sq, 1)
                    xms.wait(act, n, 1)
                    act.activation(ssx[:, 2:3], ssx[:, 1:2], ACT.Sqrt).then_inc(x_rt, 1)

                norm_x(0)
                with act.Fori(0, TILES) as i:
                    for c, (c0, cw, norms) in enumerate(CHUNKS):
                        zps.wait(act, i, c + 1)
                        out[c].wait(act, i)
                        if norms:
                            (o, h, _), = norms
                            zms.wait(act, i, n_nm[c] - 1)
                            act.activation(sq[:, 0:h * HD], acc[c % 4][:, o:o + h * HD],
                                           ACT.Square).then_inc(z_sq, 1)
                        for lo, hi in copies[c]:
                            act.activation(z[:, c0 + lo:c0 + hi], acc[c % 4][:, lo:hi],
                                           ACT.Copy).then_inc(z_cp, 1)
                        if norms:
                            zms.wait(act, i, n_nm[c])
                            act.activation(ss[:, 2, 0:h], ss[:, 1, 0:h], ACT.Sqrt).then_inc(z_rt, 1)
                        if c == 3:
                            norm_x(i + 1)

            @block.vector
            def _(dve):
                for c in (xms, xrs, xnr, htr, zms, nm, zdv):
                    c.open(dve)

                def norm_x(n):
                    xsq.wait(dve, n, 1)
                    dve.tensor_scalar(ssx[:, 1:2], ssx[:, 0:1], 1.0 / D, EPS, ALU.mult, ALU.add
                                      ).then_inc(x_ms, 1)
                    xrt.wait(dve, n, 1)
                    dve.reciprocal(ssx[:, 2:3], ssx[:, 2:3]).then_inc(x_rs, 1)
                    xrs.wait(dve, n, 1)
                    xnd.wait(dve, n)
                    dve.tensor_scalar(xn[:, :], x[:, :], ssx[:, 2:3], None, ALU.mult
                                      ).then_inc(xn_ready, 1)

                dve.wait_ge(const_in, 16 * 7)
                norm_x(0)
                with dve.Fori(0, TILES) as i:
                    xnd.wait(dve, i, 1)
                    zps.wait(dve, i)
                    for b in range(2):
                        ks = slice(4 * b, 4 * b + 4)
                        dve.tensor_tensor(hT[:, ks, :], tp[:, ks, :],
                                          gx[:, ks].unsqueeze(2).to_broadcast([P, 4, P]),
                                          ALU.mult).then_inc(ht_ready, 1)
                    for c, (c0, cw, norms) in enumerate(CHUNKS):
                        if norms:
                            (o, h, g), = norms
                            m = n_nm[c]
                            zsq.wait(dve, i, m)
                            dve.tensor_reduce(ss[:, 0, 0:h],
                                              sq[:, 0:h * HD].rearrange("p (h d) -> p h d", d=HD),
                                              AX.X, ALU.add).then_inc(z_dve, 1)
                            zdv.wait(dve, i, 3 * m - 2)
                            zrt.wait(dve, i, m - 1)
                            dve.tensor_scalar(ss[:, 1, 0:h], ss[:, 0, 0:h], 1.0 / HD, EPS,
                                              ALU.mult, ALU.add).then_inc(z_ms, 1)
                            zrt.wait(dve, i, m)
                            dve.reciprocal(ss[:, 0, 0:h], ss[:, 2, 0:h]).then_inc(z_dve, 1)
                            zdv.wait(dve, i, 3 * m - 1)
                            out[c].wait(dve, i)
                            src = acc[c % 4][:, o:o + h * HD]
                            dst = z[:, c0 + o:c0 + o + h * HD]
                            if c0 == CQ:
                                src = src.rearrange("p (g r d) -> p g r d", g=GC, r=RC)
                                dst = dst.rearrange("p (r g d) -> p g r d", g=GC, r=RC)
                                rs = ss[:, 0, 0:h].rearrange("p (g r) -> p g r", g=GC).unsqueeze(3
                                    ).to_broadcast([P, GC, RC, HD])
                            else:
                                src = src.rearrange("p (h d) -> p h d", d=HD)
                                dst = dst.rearrange("p (h d) -> p h d", d=HD)
                                rs = ss[:, 0, 0:h].unsqueeze(2).to_broadcast([P, h, HD])
                            dve.tensor_tensor(dst, src, rs, ALU.mult).then_inc(z_dve, 1)
                            zdv.wait(dve, i, 3 * m)
                            dst = z[:, c0 + o:c0 + o + h * HD].rearrange("p (h d) -> p h d", d=HD)
                            gain = gains[:, g, :].unsqueeze(1).to_broadcast([P, h, HD])
                            dve.tensor_tensor(dst, dst, gain, ALU.mult).then_inc(z_nrm, 1)
                        if c == 3:
                            norm_x(i + 1)


class Steps(Count):

    def __init__(self, sem, names):
        self.names = names.split()
        super().__init__(sem, len(self.names))
        self.next = 0

    def did(self, ins, name):
        assert self.names[self.next % self.per] == name, (name, self.names[self.next % self.per])
        self.next += 1
        ins.then_inc(self.sem, 1)

    def after(self, eng, i, name):
        eng.wait_ge(self.sem, self.at(i, self.names.index(name) + 1))


LN_TINY = float(np.log(np.float32(TINY)))


def hgrn(nc, t):
    LV = 7
    with ExitStack() as ctx:
        sb = lambda name, shape, dt=F32: ctx.enter_context(nc.sbuf_tensor("b_" + name, shape, dt))
        ps = lambda name, shape: ctx.enter_context(nc.psum_tensor("b_" + name, shape, F32))
        sem = ctx.enter_context(semaphores(nc, "b_"))
        ident = sb("ident", [P, P])
        sums_m = sb("sums_m", [P, (LV + 1) * P])
        suf_m = sb("suf_m", [P, P])
        pair_m = sb("pair_m", [P, (LV + 1) * P])
        sums_s = sb("sums_s", [N_DEC, 4 * N_DEC])
        suf_s = sb("suf_s", [N_DEC, N_DEC])
        pair_s = sb("pair_s", [N_DEC, 4 * N_DEC])
        rows_s = sb("rows_s", [N_DEC, DEC_B])
        cols_s = sb("cols_s", [P, DEC_B, N_DEC])
        gain = sb("gain", [P, HD])
        zb = sb("zb", [P, 1024])
        z_q, z_f, z_v, z_g = (zb[:, n * 256:(n + 1) * 256] for n in range(4))
        az, tt, ln1, r1, km, kk, lf = (sb(n, [P, 256]) for n in ("az", "tt", "ln1", "r1", "km", "kk", "lf"))
        qkT = sb("qkT", [P, 4, P])
        e = [sb(f"e{p}", [P, (LV + 1) * P]) for p in range(2)]
        x = [sb(f"x{p}", [P, (LV + 1) * P]) for p in range(2)]
        esuf, kdec = sb("esuf", [P, 256]), sb("kdec", [P, 256])
        w = sb("w", [P, (LV + 1) * P])
        at = sb("at", [P, HB, P])
        state = sb("state", [P, HB, HD])
        eg, g1, sil = sb("eg", [P, 256]), sb("g1", [P, 256]), sb("sil", [P, 256])
        oc, sq, ob = sb("oc", [P, 256]), sb("sq", [P, 256]), sb("ob", [P, 256])
        st = sb("st", [P, 4, HB])
        half = sb("half", [P, HB])
        s0 = sb("s0", [P, HB, DEC_B, HD])
        s1 = sb("s1", [P, 2, DEC_B, HD])
        qm = sb("qm", [P, 2, DEC_B, N_DEC])
        vm = sb("vm", [N_DEC, HB, DEC_B, HD])
        tq, sfo = ps("tq", [P, 512]), ps("sfo", [P, 512])
        sm = ps("sm", [P, 1024])
        sc = [ps(f"sc{n}", [P, 1024]) for n in range(2)]
        const_in, seen, zeroed, s_stored = map(sem, ("const_in", "seen", "zeroed", "s_stored"))
        z_in, ob_out = Count(sem("z_in"), 16), Count(sem("ob_out"), 16)
        by_act = Steps(sem("by_act"), "abs exp ln qkT suf sums0 sums1 gate")
        by_pe = Steps(sem("by_pe"), "qT kT suf sums0 sums1 sc0 sc1 sc2 sc3 out state")
        by_dve = Steps(sem("by_dve"), "one rec pick k min lf kdec x0 x1 w0 at0 w1 at1 w2 at2 w3 at3 "
                       "g1 g2 g3 g4 state oc sq ss ms on ob")
        by_pool = Steps(sem("by_pool"), "rsqrt")
        ALL = (z_in, ob_out, by_act, by_pe, by_dve, by_pool)
        fin = {n: sem("fin_" + n) for n in ("qm", "vm", "dec", "s1")}

        with nc.Block() as block:

            @block.sync
            def _(sp):
                z_in.open(sp)
                ob_out.open(sp)
                for a, b in ((ident, "ident"), (sums_m, "b_sums"), (suf_m, "b_suf"), (pair_m, "b_pair"),
                             (sums_s, "bs_sums"), (suf_s, "bs_suf"), (pair_s, "bs_pair"), (rows_s, "bs_rows")):
                    sp.dma_start(a[:, :], t[b][:, :]).then_inc(const_in, 16)
                sp.dma_start(cols_s[:, :, :], t["bs_cols"][:, :, :]).then_inc(const_in, 16)
                sp.dma_start(gain[:, :], t["b_onorm"][0].partition_broadcast(P)).then_inc(const_in, 16)
                sp.wait_ge(zeroed, 3)
                for h in range(HB):
                    r = slice(HD * (h % 2), HD * (h % 2) + HD)
                    sp.dma_start(s0[r, h, :, :], t["state_b"][:, h, :, :].rearrange("b c v -> c b v")
                                 ).then_inc(const_in, 16)
                sp.dma_start(zb[:, :], t["zr"][0:P, Z_B:Z_B + 1024]).then_inc(z_in.sem, 16)
                with sp.Fori(0, PT) as i:
                    waits(sp, seen, (by_dve.sem, by_dve.at(i, by_dve.per)))
                    sp.dma_start(t["cat"][bass.ds(i * P, P), 384:640], ob[:, :]).then_inc(ob_out.sem, 16)
                    waits(sp, seen, (by_pe.sem, by_pe.at(i, by_pe.per)))
                    sp.dma_start(zb[:, :], t["zr"][bass.ds(i * P + P, P), Z_B:Z_B + 1024]
                                 ).then_inc(z_in.sem, 16)
                for h in range(HB):
                    sp.dma_start(t["s_p"][h, :, :], state[HD * (h % 2):HD * (h % 2) + HD, h, :]
                                 ).then_inc(s_stored, 16)
                by_dve.after(sp, PT, "ob")
                sp.dma_start(t["cat"][SEQ:N_TOK, 384:640], ob[0:N_DEC, :]).then_inc(ob_out.sem, 16)
                sp.wait_ge(fin["s1"], 6)
                for p in range(2):
                    sp.dma_start(t["s_s"][:, 2 * p:2 * p + 2, :, :].rearrange("b j c v -> (j c) b v"),
                                 s1[:, p, :, :]).then_inc(s_stored, 16)
                sp.wait_ge(s_stored, 16 * 6)
                ob_out.wait(sp, PT + 1)

            def rows(sample):
                return (N_DEC, 3) if sample else (P, LV)

            @block.tensor
            def _(pe):
                by_pe.open(pe)
                pe.wait_ge(const_in, 16 * 14)

                def tile(i, sample=False):
                    T, L = rows(sample)
                    TP = T * (L + 1)
                    z_in.wait(pe, i, 16)
                    by_act.after(pe, i - 1, "qkT")
                    for p in range(2):
                        last = pe.transpose(tq[:, p * T:(p + 1) * T], z_q[0:T, p * P:(p + 1) * P], ident[0:T, 0:T])
                    by_pe.did(last, "qT")
                    by_dve.after(pe, i, "k")
                    for p in range(2):
                        last = pe.transpose(tq[:, (2 + p) * T:(3 + p) * T], kk[0:T, p * P:(p + 1) * P],
                                            ident[0:T, 0:T])
                    by_pe.did(last, "kT")
                    by_dve.after(pe, i, "lf")
                    by_dve.after(pe, i - 1, "oc")
                    by_pe.did(pe.matmul(sfo[0:T, 0:256], (suf_s if sample else suf_m)[:, :], lf[0:T, :],
                                        start=True, stop=True), "suf")
                    for p in range(2):
                        by_act.after(pe, i if p else i - 1, "sums0" if p else "sums1")
                        for lo in range(0, TP, 512):
                            hi = min(lo + 512, TP)
                            last = pe.matmul(sm[:, lo:hi], lf[0:T, p * P:(p + 1) * P],
                                             (sums_s if sample else sums_m)[:, lo:hi], start=True, stop=True)
                        by_pe.did(last, f"sums{p}")
                    by_act.after(pe, i, "qkT")
                    for h in range(HB):
                        p, r = h // 2, slice(HD * (h % 2), HD * (h % 2) + HD)
                        by_dve.after(pe, i, f"x{p}")
                        by_dve.after(pe, i if h >= 2 else i - 1, f"w{(h - 2) % 4}")
                        for n in range(L):
                            c = slice(n * T, n * T + T)
                            pe.matmul(sc[h % 2][0:T, c], x[p][r, c], x[p][r, c], start=True, stop=True)
                        by_pe.did(pe.matmul(sc[h % 2][0:T, L * T:TP], qkT[r, 2 + p, 0:T], qkT[r, p, 0:T],
                                            start=True, stop=True), f"sc{h}")
                    by_act.after(pe, i, "suf")
                    if sample:
                        pe.wait_ge(fin["qm"], 2)
                    else:
                        by_dve.after(pe, i - 1, "state")
                        pe.wait_ge(zeroed, 3)
                    for h in range(HB):
                        p, r = h // 2, slice(HD * (h % 2), HD * (h % 2) + HD)
                        by_dve.after(pe, i, f"at{h}")
                        dst = sfo[0:T, h * HD:(h + 1) * HD]
                        last = pe.matmul(dst, at[0:T, h, 0:T], z_v[0:T, h * HD:(h + 1) * HD], start=True, stop=False)
                        if sample:
                            for b in range(DEC_B):
                                last = pe.matmul(dst, qm[:, p, b, :], s0[:, h, b, :], start=False,
                                                 stop=b == DEC_B - 1)
                        else:
                            last = pe.matmul(dst, x[p][:, L * T:TP], state[:, h, :], start=False, stop=True)
                    by_pe.did(last, "out")
                    by_dve.after(pe, i, "kdec")
                    if sample:
                        pe.wait_ge(fin["vm"], 4)
                        for h in range(HB):
                            p, r = h // 2, slice(HD * (h % 2), HD * (h % 2) + HD)
                            last = pe.matmul(sm[r, p * 512:(p + 1) * 512], kdec[0:T, h * HD:(h + 1) * HD],
                                             vm[:, h, :, :].rearrange("s b v -> s (b v)"), start=True, stop=True)
                    else:
                        for h in range(HB):
                            p, r = h // 2, slice(HD * (h % 2), HD * (h % 2) + HD)
                            last = pe.matmul(tq[r, p * HD:(p + 1) * HD], kdec[:, h * HD:(h + 1) * HD],
                                             z_v[:, h * HD:(h + 1) * HD], start=True, stop=True)
                    by_pe.did(last, "state")

                with pe.Fori(0, PT) as i:
                    tile(i)
                tile(PT, sample=True)

            @block.scalar
            def _(act):
                by_act.open(act)

                def tile(i, sample=False):
                    T, L = rows(sample)
                    z_in.wait(act, i, 16)
                    by_act.did(act.activation(az[0:T, :], z_f[0:T, :], ACT.Abs), "abs")
                    by_act.after(act, i, "abs")
                    by_act.did(act.activation(tt[0:T, :], az[0:T, :], ACT.Exp, scale=-1.0), "exp")
                    by_act.after(act, i, "exp")
                    by_act.did(act.activation(ln1[0:T, :], tt[0:T, :], ACT.Ln, bias=1.0), "ln")
                    by_pe.after(act, i, "kT")
                    by_pe.after(act, i - 1, "sc3")
                    by_act.did(act.activation(qkT[:, :, 0:T], tq[:, 0:4 * T].rearrange("p (n t) -> p n t", t=T),
                                              ACT.Copy), "qkT")
                    by_pe.after(act, i, "suf")
                    by_act.did(act.activation(esuf[0:T, :], sfo[0:T, 0:256], ACT.Exp), "suf")
                    for p in range(2):
                        by_pe.after(act, i, f"sums{p}")
                        by_act.did(act.activation(e[p][:, 0:T * (L + 1)], sm[:, 0:T * (L + 1)], ACT.Exp), f"sums{p}")
                    by_act.did(act.activation(eg[0:T, :], z_g[0:T, :], ACT.Exp, scale=-1.0), "gate")

                with act.Fori(0, PT) as i:
                    tile(i)
                tile(PT, sample=True)

            @block.gpsimd
            def _(pool):
                by_pool.open(pool)
                pool.memset(state[:, :, :], 0.0).then_inc(zeroed, 1)
                pool.memset(half[:, :], -0.5).then_inc(zeroed, 1)
                pool.memset(s0[:, :, :, :], 0.0).then_inc(zeroed, 1)
                pool.wait_ge(zeroed, 3)

                def tile(i, T):
                    by_dve.after(pool, i, "ms")
                    by_pool.did(pool.tensor_tensor(st[0:T, 2, :], st[0:T, 1, :], half[0:T, :], ALU.pow), "rsqrt")

                with pool.Fori(0, PT) as i:
                    tile(i, P)
                tile(PT, N_DEC)

            @block.vector
            def _(dve):
                by_dve.open(dve)
                dve.wait_ge(const_in, 16 * 14)
                dve.wait_ge(zeroed, 3)

                def tile(i, sample=False):
                    T, L = rows(sample)
                    TP = T * (L + 1)
                    tr = slice(0, T)
                    step = lambda name, ins: (by_dve.did(ins, name), by_dve.after(dve, i, name))
                    by_act.after(dve, i, "exp")
                    step("one", dve.tensor_scalar(r1[tr, :], tt[tr, :], 1.0, None, ALU.add))
                    step("rec", dve.reciprocal(r1[tr, :], r1[tr, :]))
                    step("pick", dve.scalar_tensor_tensor(out=km[tr, :], in0=z_f[tr, :], scalar=0.0,
                                                          in1=tt[tr, :], op0=ALU.is_lt, op1=ALU.max))
                    step("k", dve.tensor_tensor(kk[tr, :], km[tr, :], r1[tr, :], ALU.mult))
                    by_act.after(dve, i, "ln")
                    step("min", dve.scalar_tensor_tensor(out=lf[tr, :], in0=z_f[tr, :], scalar=0.0,
                                                         in1=ln1[tr, :], op0=ALU.min, op1=ALU.subtract))
                    step("lf", dve.tensor_scalar(lf[tr, :], lf[tr, :], LN_TINY, None, ALU.max))
                    by_act.after(dve, i, "suf")
                    by_pe.after(dve, i - 1, "state")
                    step("kdec", dve.tensor_tensor(kdec[tr, :], kk[tr, :], esuf[tr, :], ALU.mult))
                    by_act.after(dve, i, "qkT")
                    for p in range(2):
                        by_act.after(dve, i, f"sums{p}")
                        for n in range(L):
                            m = 1 << (L - 1 - n)
                            v = lambda a: a.rearrange("p (b s m) -> p b s m", s=2, m=m)
                            xv, ev = v(x[p][:, n * T:n * T + T]), v(e[p][:, n * T:n * T + T])
                            for s, src in ((0, qkT[:, 2 + p, tr]), (1, qkT[:, p, tr])):
                                dve.tensor_tensor(xv[:, :, s, :], ev[:, :, s, :], v(src)[:, :, s, :], ALU.mult)
                        last = dve.tensor_tensor(x[p][:, L * T:TP], e[p][:, L * T:TP], qkT[:, p, tr], ALU.mult)
                        step(f"x{p}", last)
                        if sample:
                            dve.tensor_tensor(qm[:, p, :, :], x[p][:, L * T:TP].unsqueeze(1).to_broadcast(
                                [P, DEC_B, N_DEC]), cols_s[:, :, :], ALU.mult).then_inc(fin["qm"], 1)
                    if sample:
                        for h in range(HB):
                            dve.tensor_tensor(vm[:, h, :, :],
                                              z_v[tr, h * HD:(h + 1) * HD].unsqueeze(1).to_broadcast([T, DEC_B, HD]),
                                              rows_s[:, :].unsqueeze(2).to_broadcast([T, DEC_B, HD]),
                                              ALU.mult).then_inc(fin["vm"], 1)
                    for h in range(HB):
                        by_pe.after(dve, i, f"sc{h}")
                        step(f"w{h}", dve.tensor_tensor(w[tr, 0:TP], sc[h % 2][tr, 0:TP],
                                                        (pair_s if sample else pair_m)[:, 0:TP], ALU.mult))
                        step(f"at{h}", dve.tensor_reduce(at[tr, h, 0:T], w[tr, 0:TP].rearrange(
                            "p (n t) -> p t n", t=T), AX.X, ALU.add))
                    by_act.after(dve, i, "gate")
                    step("g1", dve.tensor_scalar(g1[tr, :], eg[tr, :], 1.0, None, ALU.add))
                    step("g2", dve.reciprocal(g1[tr, :], g1[tr, :]))
                    step("g3", dve.tensor_tensor(sil[tr, :], z_g[tr, :], g1[tr, :], ALU.mult))
                    hv = lambda a: a[tr, :].rearrange("p (h d) -> p h d", d=HD)
                    step("g4", dve.tensor_tensor(hv(sil), hv(sil), gain[tr, :].unsqueeze(1).to_broadcast(
                        [T, HB, HD]), ALU.mult))
                    by_pe.after(dve, i, "state")
                    if sample:
                        for h in range(HB):
                            p, r = h // 2, slice(HD * (h % 2), HD * (h % 2) + HD)
                            last_e = e[p][r, L * T:TP].rearrange("p (b q) -> p b q", q=DEC_S)[:, :, DEC_S - 1:DEC_S]
                            dve.tensor_tensor(s1[r, p, :, :], s0[r, h, :, :],
                                              last_e.to_broadcast([HD, DEC_B, HD]), ALU.mult).then_inc(fin["s1"], 1)
                        dve.wait_ge(fin["s1"], 4)
                        for p in range(2):
                            last = dve.tensor_tensor(s1[:, p, :, :], s1[:, p, :, :],
                                                     sm[:, p * 512:(p + 1) * 512].rearrange(
                                                         "p (b v) -> p b v", v=HD), ALU.add)
                            last.then_inc(fin["s1"], 1)
                    else:
                        for h in range(HB):
                            p, r = h // 2, slice(HD * (h % 2), HD * (h % 2) + HD)
                            last = dve.scalar_tensor_tensor(
                                out=state[r, h, :], in0=state[r, h, :], scalar=e[p][r, TP - 1:TP],
                                in1=tq[r, p * HD:(p + 1) * HD], op0=ALU.mult, op1=ALU.add)
                        step("state", last)
                    if sample:
                        by_dve.did(dve.memset(st[tr, 3, :], 0.0), "state")
                    step("oc", dve.tensor_copy(oc[tr, :], sfo[tr, 0:256]))
                    step("sq", dve.tensor_tensor(sq[tr, :], oc[tr, :], oc[tr, :], ALU.mult))
                    step("ss", dve.tensor_reduce(st[tr, 0, :], hv(sq), AX.X, ALU.add))
                    step("ms", dve.tensor_scalar(st[tr, 1, :], st[tr, 0, :], 1.0 / HD, EPS, ALU.mult, ALU.add))
                    by_pool.after(dve, i, "rsqrt")
                    step("on", dve.tensor_tensor(hv(oc), hv(oc), st[tr, 2, :].unsqueeze(2).to_broadcast(
                        [T, HB, HD]), ALU.mult))
                    ob_out.wait(dve, i)
                    step("ob", dve.tensor_tensor(ob[tr, :], oc[tr, :], sil[tr, :], ALU.mult))

                with dve.Fori(0, PT) as i:
                    tile(i)
                tile(PT, sample=True)


def chunk_plan(back):
    first = [max(0, n - back) for n in range(PT)]
    return [(f, max(2, n + 1 - f)) for n, f in enumerate(first)]


def prompt_attention(nc, t, pre, q_src, k_src, v_src, mask_src, dst, units, C, plan):
    LAG, AHEAD = 2, 2
    looped = isinstance(plan, tuple)
    plan = [plan] * PT if looped else plan
    NU, NC = len(units), max(n for _, n in plan)
    KC = k_src.shape[0] // C
    W = NC * C
    KP, VW = k_src.shape[1] // P, v_src.shape[1]
    G = min(2, NC)
    U = 2 * NU
    FILLS = 2 + U * G
    assert FILLS % 2 == 0 and PT % 2 == 0

    def group(n, g):
        first = -(-n // G)
        return (0, first) if g == 0 else (first, n)

    def run(eng, step):
        def chain(its):
            us = [(i, u) + plan[(0 if looped else 2 * i) + u // NU] for i in its for u in range(U)]
            get = lambda x: us[x] if 0 <= x < len(us) else None
            for x in range(len(us) + LAG + 1):
                step(get(x), get(x - LAG), get(x - LAG - 1))

        if looped:
            with eng.Fori(0, PT // 2) as i:
                chain([i])
        else:
            chain(range(PT // 2))

    with ExitStack() as ctx:
        sb = lambda name, shape, dt=F32: ctx.enter_context(nc.sbuf_tensor(pre + name, shape, dt))
        ps = lambda name, shape: ctx.enter_context(nc.psum_tensor(pre + name, shape, F32))
        sem = ctx.enter_context(semaphores(nc, pre))
        ident = sb("ident", [P, P])
        k = sb("k", [P, KC, KP * P])
        v = sb("v", [P, KC, VW])
        kT = sb("kT", [P, KP, KC * C])
        q = [sb(f"q{s}", [P, 384]) for s in range(2)]
        qT = [sb(f"qT{s}", [P, 2, 3, P]) for s in range(2)]
        mask = [sb(f"mask{s}", [P, W]) for s in range(2)]
        p = [sb(f"p{s}", [P, W]) for s in range(3)]
        pT = [sb(f"pT{s}", [P, NC, P]) for s in range(2)]
        mx = sb("mx", [P, U])
        nb = sb("nb", [P, U])
        l = sb("l", [P, U])
        rl = sb("rl", [P, 3, U])
        o = [sb(f"o{s}", [P, NU, HD]) for s in range(2)]
        sc = [ps(f"sc{s}", [P, 1024]) for s in range(2)]
        tp = [ps(f"tp{s}", [P, 4, P]) for s in range(2)]
        op = [ps(f"op{s}", [P, 512]) for s in range(2)]
        kv_in, seen, settled, k_tp, k_ev = map(sem, ("kv_in", "seen", "settled", "k_tp", "k_ev"))
        zeroed = sem("zeroed")
        q_in = [Count(sem(f"q_in{s}"), 16) for s in range(2)]
        mask_in = [Count(sem(f"mask_in{s}"), 16) for s in range(2)]
        o_out = [Count(sem(f"o_out{s}"), 16) for s in range(2)]
        scored = Count(sem("scored"), U)
        masked = Count(sem("masked"), U)
        bias = Count(sem("bias"), U)
        exped = Count(sem("exped"), U)
        filled = Count(sem("filled"), FILLS)
        ev_a = Count(sem("ev_a"), 2 + U)
        ev_d = Count(sem("ev_d"), U * (G - 1) or 1)
        summed = Count(sem("summed"), U)
        rec = Count(sem("rec"), 6)
        done = Count(sem("done"), 2)

        Q1, Q2 = NU - AHEAD - LAG, U - AHEAD - LAG

        def before(u):
            return (u >= Q1) + (u >= Q2)

        def fill_at(u, g=0):
            return u * G + before(u) + g

        fill_q = (Q1 * G, Q2 * G + 1)
        a_no = lambda u: u + 1 + before(u)
        a_q = (Q1 + 1, Q2 + 2)
        takers = {}
        for s in range(2):
            takers[fill_q[s]] = (ev_a, a_q[s])
        for u in range(U):
            takers[fill_at(u)] = (ev_a, a_no(u))
            if G > 1:
                takers[fill_at(u, 1)] = (ev_d, u + 1)

        def taken(eng, i, f):
            f -= 2
            if f < 0:
                i, f = i - 1, f + FILLS
            who, n = takers[f]
            who.wait(eng, i, n)

        with nc.Block() as block:

            @block.sync
            def _(sp):
                for c in (*q_in, *mask_in, *o_out):
                    c.open(sp)
                sp.dma_start(ident[:, :], t["ident"][:, :]).then_inc(kv_in, 16)
                if C == P:
                    kv = [(x, y.rearrange("(c p) n -> p c n", p=P)) for x, y in ((k, k_src), (v, v_src))]
                else:
                    kv = [(x[0:C, 0], y) for x, y in ((k, k_src), (v, v_src))]
                for x, y in kv:
                    sp.dma_start(x[:, :, :] if C == P else x, y).then_inc(kv_in, 16)
                def load(n, s, known):
                    first, number = plan[known]
                    sp.dma_start(q[s][:, :], q_src(n)).then_inc(q_in[s].sem, 16)
                    sp.dma_start(mask[s][:, 0:number * C], mask_src(n, first, number)).then_inc(mask_in[s].sem, 16)

                for s in range(2):
                    load(s, s, s)

                def pair(i):
                    for s in range(2):
                        waits(sp, seen, (done.sem, done.at(i, s + 1)))
                        sp.dma_start(dst(2 * i + s), o[s][:, :, :].rearrange("p h d -> p (h d)")
                                     ).then_inc(o_out[s].sem, 16)
                        n = (2 * i + (s + 2)) % PT
                        load(n, s, 0 if looped else n)

                if looped:
                    with sp.Fori(0, PT // 2) as i:
                        pair(i)
                else:
                    for i in range(PT // 2):
                        pair(i)
                for s in range(2):
                    q_in[s].wait(sp, PT // 2, 16)
                    mask_in[s].wait(sp, PT // 2, 16)
                    o_out[s].wait(sp, PT // 2)

            @block.gpsimd
            def _(pool):
                for s in range(2):
                    for j in range(2):
                        pool.memset(qT[s][HD * (1 - j):HD * (1 - j) + HD, j, :, :], 0.0).then_inc(zeroed, 1)

            @block.tensor
            def _(pe):
                for c in (scored, filled, summed):
                    c.open(pe)
                pe.wait_ge(kv_in, 48)
                n = 0
                for kp in range(KP):
                    for c in range(KC):
                        if n >= 2:
                            pe.wait_ge(k_ev, n - 1)
                        pe.transpose(tp[n % 2][:, 0, 0:C], k[0:C, c, kp * P:(kp + 1) * P],
                                     ident[0:C, 0:C]).then_inc(k_tp, 1)
                        n += 1
                pe.wait_ge(k_ev, KP * KC)

                def transpose_queries(bank, s):
                    for pr in range(3):
                        last = pe.transpose(bank[:, pr, :], q[s][:, pr * P:(pr + 1) * P], ident[:, :])
                    return last

                q_in[0].wait(pe, 0, 16)
                transpose_queries(tp[0], 0).then_inc(k_tp, 1)
                pe.wait_ge(k_ev, KP * KC + 1)
                pe.wait_ge(zeroed, 4)

                def queries(i, s):
                    q_in[s].wait(pe, i, 16) if s else q_in[s].wait(pe, i + 1, 16)
                    f = fill_q[1 - s]
                    taken(pe, i, f)
                    transpose_queries(tp[f % 2], s).then_inc(filled.sem, 1)

                def scores(i, u, k0, n):
                    s = u // NU
                    pr, j, kp, _, _ = units[u % NU]
                    if u % NU == 0:
                        ev_a.wait(pe, i, a_q[0]) if s else ev_a.wait(pe, i - 1, a_q[1])
                    masked.wait(pe, i, u - 1) if u else masked.wait(pe, i - 1, U - 1)
                    for lo in range(0, n * C, 512):
                        hi = min(lo + 512, n * C)
                        last = pe.matmul(sc[u % 2][:, lo:hi], qT[s][:, j, pr, :], kT[:, kp, k0 * C + lo:k0 * C + hi],
                                         start=True, stop=True)
                    last.then_inc(scored.sem, 1)

                def transposes(i, u, k0, n):
                    exped.wait(pe, i, u + 1)
                    for g in range(G):
                        f = fill_at(u, g)
                        taken(pe, i, f)
                        if C < P:
                            pe.sem_inc(settled, 1)
                        lo, hi = group(n, g)
                        for c in range(lo, hi):
                            last = pe.transpose(tp[f % 2][0:C, c - lo, :], p[u % 3][:, c * C:(c + 1) * C],
                                                ident[:, :])
                        last.then_inc(filled.sem, 1)

                def values(i, u, k0, n):
                    _, _, _, vc, h = units[u % NU]
                    if u % NU == 0:
                        done.wait(pe, i - 1, u // NU + 1)
                    ev_a.wait(pe, i, a_no(u))
                    if G > 1:
                        ev_d.wait(pe, i, (u + 1) * (G - 1))
                    for c in range(n):
                        last = pe.matmul(op[u // NU][:, h * HD:h * HD + HD], pT[u % 2][0:C, c, :],
                                         v[0:C, k0 + c, vc * HD:vc * HD + HD], start=c == 0, stop=c == n - 1)
                    last.then_inc(summed.sem, 1)

                def step(now, lagged, last):
                    if now:
                        if now[1] in (NU - AHEAD, U - AHEAD):
                            queries(now[0], 1 if now[1] < NU else 0)
                        scores(*now)
                    if lagged:
                        transposes(*lagged)
                    if last:
                        values(*last)

                run(pe, step)

            @block.scalar
            def _(act):
                for c in (exped, ev_a):
                    c.open(act)
                n = 0
                for kp in range(KP):
                    for c in range(KC):
                        act.wait_ge(k_tp, n + 1)
                        act.activation(kT[:, kp, c * C:(c + 1) * C], tp[n % 2][:, 0, 0:C],
                                       ACT.Copy).then_inc(k_ev, 1)
                        n += 1

                act.wait_ge(k_tp, n + 1)

                def copy_queries(s, bank):
                    for j in range(2):
                        r = slice(HD * j, HD * j + HD)
                        last = act.activation(qT[s][r, j, :, :], bank[r, 0:3, :], ACT.Copy)
                    return last

                act.wait_ge(zeroed, 4)
                copy_queries(0, tp[0]).then_inc(k_ev, 1)

                def queries(i, s):
                    f = fill_q[1 - s]
                    filled.wait(act, i, f + 1)
                    scored.wait(act, i) if s else scored.wait(act, i, NU)
                    copy_queries(s, tp[f % 2]).then_inc(ev_a.sem, 1)

                def transposed(i, u, k0, n):
                    f = fill_at(u)
                    filled.wait(act, i, f + 1)
                    summed.wait(act, i, u - 1) if u else summed.wait(act, i - 1, U - 1)
                    _, hi = group(n, 0)
                    act.activation(pT[u % 2][0:C, 0:hi, :], tp[f % 2][0:C, 0:hi, :], ACT.Copy).then_inc(ev_a.sem, 1)

                def exponentials(i, u, k0, n):
                    bias.wait(act, i, u + 1)
                    pu = p[u % 3][:, 0:n * C]
                    act.activation(pu, pu, ACT.Exp, bias=nb[:, u:u + 1], scale=SCALE,
                                   accum_out=l[:, u:u + 1]).then_inc(exped.sem, 1)

                def step(now, lagged, last):
                    if now and now[1] in (NU - AHEAD, U - AHEAD):
                        queries(now[0], 1 if now[1] < NU else 0)
                    if lagged:
                        transposed(*lagged)
                    if now:
                        exponentials(*now)

                run(act, step)

            @block.vector
            def _(dve):
                for c in (masked, bias, ev_d, rec, done):
                    c.open(dve)

                def tile_out(i, s):
                    us = slice(NU * s, NU * s + NU)
                    summed.wait(dve, i, NU * s + NU)
                    dve.tensor_scalar(rl[:, 0, us], l[:, us], TINY, None, ALU.max).then_inc(rec.sem, 1)
                    rec.wait(dve, i, 3 * s + 1)
                    dve.reciprocal(rl[:, 1, us], rl[:, 0, us]).then_inc(rec.sem, 1)
                    rec.wait(dve, i, 3 * s + 2)
                    dve.scalar_tensor_tensor(out=rl[:, 2, us], in0=nb[:, us], scalar=-0.5 * NEG * SCALE,
                                             in1=rl[:, 1, us], op0=ALU.is_lt, op1=ALU.mult
                                             ).then_inc(rec.sem, 1)
                    rec.wait(dve, i, 3 * s + 3)
                    o_out[s].wait(dve, i)
                    hs = [u[4] for u in units]
                    for n in range(NU):
                        ins = dve.tensor_scalar(o[s][:, hs[n], :], op[s][:, hs[n] * HD:hs[n] * HD + HD],
                                                rl[:, 2, NU * s + n:NU * s + n + 1], None, ALU.mult)
                    ins.then_inc(done.sem, 1)

                def mask_scores(i, u, k0, n):
                    s, w = u // NU, n * C
                    if u % NU == 0:
                        mask_in[s].wait(dve, i, 16)
                    scored.wait(dve, i, u + 1)
                    if u >= 3:
                        filled.wait(dve, i, fill_at(u - 3, G - 1) + 1)
                    else:
                        filled.wait(dve, i - 1, fill_at(U + u - 3, G - 1) + 1)
                    if u % NU == 0:
                        done.wait(dve, i - 1, s + 1)
                    dve.sem_inc(settled, 1)
                    dve.tensor_tensor_reduce(p[u % 3][:, 0:w], sc[u % 2][:, 0:w], mask[s][:, 0:w], 1.0,
                                             -3e38, ALU.add, ALU.max, mx[:, u:u + 1]).then_inc(masked.sem, 1)
                    masked.wait(dve, i, u + 1)
                    dve.tensor_scalar(nb[:, u:u + 1], mx[:, u:u + 1], -SCALE, None, ALU.mult).then_inc(bias.sem, 1)

                def transposed(i, u, k0, n):
                    f = fill_at(u, 1)
                    summed.wait(dve, i, u - 1) if u else summed.wait(dve, i - 1, U - 1)
                    filled.wait(dve, i, f + 1)
                    lo, hi = group(n, 1)
                    dve.tensor_copy(pT[u % 2][:, lo:hi, :], tp[f % 2][:, 0:hi - lo, :]).then_inc(ev_d.sem, 1)

                def step(now, lagged, last):
                    if now:
                        mask_scores(*now)
                    if lagged and G > 1:
                        transposed(*lagged)
                    if last and (last[1] + 1) % NU == 0:
                        tile_out(last[0], last[1] // NU)

                run(dve, step)


def sample_a(nc, t):
    NR, NC, NK, B2 = HA * DEC_S, PAST // P, PAST + DEC_S, 2
    FILLS = 16
    with ExitStack() as ctx:
        sb = lambda name, shape, dt=F32: ctx.enter_context(nc.sbuf_tensor("sa_" + name, shape, dt))
        ps = lambda name, shape: ctx.enter_context(nc.psum_tensor("sa_" + name, shape, F32))
        sem = ctx.enter_context(semaphores(nc, "sa_"))
        ident = sb("ident", [P, P])
        mask = sb("mask", [NR, NK])
        q = sb("q", [N_DEC, 384])
        qz = sb("qz", [P, DEC_B, 3, NR])
        kv = [sb(f"kv{s}", [P, NC, 768]) for s in range(B2)]
        new = [sb(f"new{s}", [DEC_S, 768]) for s in range(B2)]
        qs = [sb(f"qs{s}", [P, 3, NR]) for s in range(B2)]
        kT = sb("kT", [P, 3, NK])
        p = [sb(f"p{s}", [NR, NK]) for s in range(B2)]
        pT = [sb(f"pT{s}", [P, NC + 1, NR]) for s in range(B2)]
        st = sb("st", [NR, B2, 4])
        o = [sb(f"o{s}", [DEC_S, 384]) for s in range(B2)]
        sc = ps("sc", [P, 3 * 512])
        tp = [ps(f"tp{s}", [P, 512]) for s in range(2)]
        op = [ps(f"op{s}", [P, 512]) for s in range(2)]
        const_in, seen, settled, q_tp, q_zero, q_ev = map(sem, ("const_in", "seen", "settled", "q_tp", "q_zero", "q_ev"))
        kv_in = [Count(sem(f"kv_in{s}"), 32) for s in range(B2)]
        o_out = [Count(sem(f"o_out{s}"), 16) for s in range(B2)]
        filled = Count(sem("filled"), FILLS)
        ev_a, ev_d = Count(sem("ev_a"), 8), Count(sem("ev_d"), 8)
        q_here = Count(sem("q_here"), B2)
        scored, masked, biased = (Count(sem(n), B2) for n in ("scored", "masked", "biased"))
        exped, recip, normed = (Count(sem(n), B2) for n in ("exped", "recip", "normed"))
        summed, done = Count(sem("summed"), B2), Count(sem("done"), B2)

        def take_keys(i, s, parity, eng, copy, ev):
            for n in range(7):
                f = 7 * s + n
                if f % 2 != parity:
                    continue
                filled.wait(eng, i, f + 1)
                if n < 6:
                    ins = copy(kT[:, n // 2, 512 * (n % 2):512 * (n % 2) + 512], tp[f % 2][:, :])
                else:
                    ins = copy(kT[:, :, PAST:NK],
                               tp[f % 2][:, 0:3 * DEC_S].rearrange("p (c k) -> p c k", c=3))
                ins.then_inc(ev.sem, 1)

        def take_exps(i, s, eng, copy, ev):
            f = 14 + s
            filled.wait(eng, i, f + 1)
            summed.wait(eng, i - 1, s + 1)
            copy(pT[s][:, 0:NC, :], tp[f % 2][:, 0:NC * NR].rearrange("p (c r) -> p c r", r=NR))
            copy(pT[s][0:DEC_S, NC, :], tp[f % 2][0:DEC_S, NC * NR:(NC + 1) * NR]).then_inc(ev.sem, 1)

        with nc.Block() as block:

            @block.sync
            def _(sp):
                for c in (*kv_in, *o_out):
                    c.open(sp)
                sp.dma_start(ident[:, :], t["ident"][:, :]).then_inc(const_in, 16)
                sp.dma_start(mask[:, :], t["mask_sa"][:, :]).then_inc(const_in, 16)
                sp.dma_start(q[:, :], t["zr"][SEQ:N_TOK, Z_AQ:Z_AQ + 384]).then_inc(const_in, 16)

                def load(s, b):
                    sp.dma_start(kv[s][:, :, :], t["cache_a"][bass.ds(b, 1), :, :].rearrange(
                        "o (c p) n -> p (o c) n", p=P)).then_inc(kv_in[s].sem, 16)
                    sp.dma_start(new[s][:, :], t["a_kv"][bass.ds(b * DEC_S + SEQ, DEC_S), :]
                                 ).then_inc(kv_in[s].sem, 16)

                for s in range(B2):
                    load(s, s)
                with sp.Fori(0, DEC_B // B2) as i:
                    for s in range(B2):
                        waits(sp, seen, (done.sem, done.at(i, s + 1)))
                        sp.dma_start(t["cat"][bass.ds((i * B2 + s) * DEC_S + SEQ, DEC_S), 0:384],
                                     o[s][:, :]).then_inc(o_out[s].sem, 16)
                        waits(sp, seen, (summed.sem, summed.at(i, s + 1)))
                        load(s, (i * B2 + (B2 + s)) % DEC_B)
                for s in range(B2):
                    kv_in[s].wait(sp, DEC_B // B2, 32)
                    o_out[s].wait(sp, DEC_B // B2)

            @block.gpsimd
            def _(pool):
                pool.memset(qz[:, :, :, :], 0.0).then_inc(q_zero, 1)

            @block.tensor
            def _(pe):
                for c in (filled, scored, summed):
                    c.open(pe)
                pe.wait_ge(const_in, 48)
                for pr in range(3):
                    last = pe.transpose(tp[0][:, pr * N_DEC:(pr + 1) * N_DEC], q[:, pr * P:(pr + 1) * P],
                                        ident[0:N_DEC, 0:N_DEC])
                last.then_inc(q_tp, 1)
                pe.wait_ge(q_ev, 6)

                def taken(i, f):
                    f -= 2
                    if f < 0:
                        i, f = i - 1, f + FILLS
                    (ev_d if f % 2 else ev_a).wait(pe, i, f // 2 + 1)

                def keys(i, s):
                    kv_in[s].wait(pe, i, 32)
                    for n in range(6):
                        f = 7 * s + n
                        taken(i, f)
                        for c in range(4):
                            last = pe.transpose(tp[f % 2][:, c * P:(c + 1) * P],
                                                kv[s][:, 4 * (n % 2) + c, (n // 2) * P:(n // 2 + 1) * P], ident[:, :])
                        last.then_inc(filled.sem, 1)
                    f = 7 * s + 6
                    taken(i, f)
                    pe.sem_inc(settled, 1)
                    for pr in range(3):
                        last = pe.transpose(tp[f % 2][:, pr * DEC_S:(pr + 1) * DEC_S],
                                            new[s][:, pr * P:(pr + 1) * P], ident[0:DEC_S, 0:DEC_S])
                    last.then_inc(filled.sem, 1)

                def scores(i, s):
                    q_here.wait(pe, i, s + 1)
                    ev_a.wait(pe, i, 4 + 3 * s)
                    ev_d.wait(pe, i, 3 + 4 * s)
                    masked.wait(pe, i, s)
                    for lo, hi in ((0, 512), (512, 1024), (1024, NK)):
                        for pr in range(3):
                            last = pe.matmul(sc[0:NR, lo:hi], qs[s][:, pr, :], kT[:, pr, lo:hi],
                                             start=pr == 0, stop=pr == 2)
                    last.then_inc(scored.sem, 1)

                def values(i, s):
                    normed.wait(pe, i, s + 1)
                    f = 14 + s
                    taken(i, f)
                    pe.sem_inc(settled, 1)
                    for c in range(NC + 1):
                        kn = P if c < NC else DEC_S
                        last = pe.transpose(tp[f % 2][0:kn, c * NR:(c + 1) * NR],
                                            p[s][:, c * P:c * P + kn], ident[0:NR, 0:NR])
                    last.then_inc(filled.sem, 1)
                    (ev_d if s else ev_a).wait(pe, i, 8)
                    done.wait(pe, i - 1, s + 1)
                    for h in range(HA):
                        vs = slice(384 + h * HD, 384 + h * HD + HD)
                        for c in range(NC + 1):
                            kn = P if c < NC else DEC_S
                            last = pe.matmul(op[s][0:DEC_S, h * HD:(h + 1) * HD],
                                             pT[s][0:kn, c, h * DEC_S:(h + 1) * DEC_S],
                                             kv[s][:, c, vs] if c < NC else new[s][:, vs],
                                             start=c == 0, stop=c == NC)
                    last.then_inc(summed.sem, 1)

                with pe.Fori(0, DEC_B // B2) as i:
                    keys(i, 0)
                    scores(i, 0)
                    keys(i, 1)
                    scores(i, 1)
                    values(i, 0)
                    values(i, 1)

            @block.scalar
            def _(act):
                for c in (ev_a, q_here, exped):
                    c.open(act)
                act.wait_ge(q_zero, 1)
                act.wait_ge(q_tp, 1)
                for h in range(HA):
                    r = slice(HD * (h % 2), HD * (h % 2) + HD)
                    act.activation(qz[r, :, h // 2, h * DEC_S:(h + 1) * DEC_S],
                                   tp[0][r, (h // 2) * N_DEC:(h // 2 + 1) * N_DEC].rearrange(
                                       "p (b q) -> p b q", b=DEC_B), ACT.Copy).then_inc(q_ev, 1)
                act.wait_ge(q_ev, 6)

                copy = lambda out, in_: act.activation(out, in_, ACT.Copy)

                def keys(i, s):
                    scored.wait(act, i, s)
                    act.activation(qs[s][:, :, :], qz[:, bass.ds(i * B2 + s, 1), :, :].rearrange(
                        "p o c r -> p (o c) r"), ACT.Copy).then_inc(q_here.sem, 1)
                    take_keys(i, s, 0, act, copy, ev_a)

                def exps(i, s):
                    biased.wait(act, i, s + 1)
                    act.activation(p[s][:, :], p[s][:, :], ACT.Exp, bias=st[:, s, 1:2], scale=SCALE,
                                   accum_out=st[:, s, 2:3]).then_inc(exped.sem, 1)

                with act.Fori(0, DEC_B // B2) as i:
                    keys(i, 0)
                    exps(i, 0)
                    keys(i, 1)
                    take_exps(i, 0, act, copy, ev_a)
                    exps(i, 1)

            @block.vector
            def _(dve):
                for c in (ev_d, masked, biased, recip, normed, done):
                    c.open(dve)
                dve.wait_ge(const_in, 48)

                def keys(i, s):
                    scored.wait(dve, i, s)
                    take_keys(i, s, 1, dve, dve.tensor_copy, ev_d)

                def softmax(i, s):
                    scored.wait(dve, i, s + 1)
                    filled.wait(dve, i - 1, 15 + s)
                    dve.sem_inc(settled, 1)
                    dve.tensor_tensor_reduce(p[s][:, :], sc[0:NR, 0:NK], mask[:, :], 1.0, -3e38,
                                             ALU.add, ALU.max, st[:, s, 0:1]).then_inc(masked.sem, 1)
                    masked.wait(dve, i, s + 1)
                    dve.tensor_scalar(st[:, s, 1:2], st[:, s, 0:1], -SCALE, None, ALU.mult
                                      ).then_inc(biased.sem, 1)

                def norm(i, s):
                    exped.wait(dve, i, s + 1)
                    dve.reciprocal(st[:, s, 3:4], st[:, s, 2:3]).then_inc(recip.sem, 1)
                    recip.wait(dve, i, s + 1)
                    dve.tensor_scalar(p[s][:, :], p[s][:, :], st[:, s, 3:4], None, ALU.mult
                                      ).then_inc(normed.sem, 1)

                def out(i, s):
                    summed.wait(dve, i, s + 1)
                    o_out[s].wait(dve, i)
                    dve.tensor_copy(o[s][:, :], op[s][0:DEC_S, 0:384]).then_inc(done.sem, 1)

                with dve.Fori(0, DEC_B // B2) as i:
                    keys(i, 0)
                    softmax(i, 0)
                    norm(i, 0)
                    keys(i, 1)
                    softmax(i, 1)
                    norm(i, 1)
                    take_exps(i, 1, dve, dve.tensor_copy, ev_d)
                    out(i, 0)
                    out(i, 1)


def sample_c(nc, t):
    NR, NKS, NKW = 64, PAST + DEC_S, CWIN + DEC_S
    NB = PAST // HD
    with ExitStack() as ctx:
        sb = lambda name, shape, dt=F32: ctx.enter_context(nc.sbuf_tensor("sc_" + name, shape, dt))
        ps = lambda name, shape: ctx.enter_context(nc.psum_tensor("sc_" + name, shape, F32))
        sem = ctx.enter_context(semaphores(nc, "sc_"))
        ident = sb("ident", [P, P])
        wc = sb("wc", [P, 2, 32, P])
        peT = sb("peT", [P, 2, 32])
        peb = sb("peb", [P, 2])
        gain = sb("gain", [P, 1])
        ones = sb("ones", [P, P])
        share = sb("share", [NCMP, NB + 1])
        rsum = sb("rsum", [NR, NR])
        idx = sb("idx", [NR, NB])
        mnew = sb("mnew", [NR, DEC_S])
        mwin = sb("mwin", [NR, CWIN])
        nhalf = sb("nhalf", [P, NCMP])
        q = sb("q", [N_DEC, 384])
        qz = sb("qz", [P, DEC_B, NR])
        x = [sb(f"x{s}", [P, 4, 1024]) for s in range(2)]
        win = [sb(f"win{s}", [P, 4, 256]) for s in range(2)]
        nkv = [sb(f"nkv{s}", [DEC_S, 512]) for s in range(2)]
        nwin = [sb(f"nwin{s}", [DEC_S, 256]) for s in range(2)]
        qs = sb("qs", [P, NR])
        xT = sb("xT", [P, 4, 512])
        ksT, kwT, knT = sb("ksT", [P, 2, 512]), sb("kwT", [P, CWIN]), sb("knT", [P, 2 * DEC_S])
        kcf, vcf, sqk, msk, rsk, kcT = (sb(n, [P, NCMP]) for n in ("kcf", "vcf", "sqk", "msk", "rsk", "kcT"))
        vc = sb("vc", [NCMP, P])
        kcr = sb("kcr", [NCMP, 2 * P])
        pc, pcT = sb("pc", [NR, NCMP]), sb("pcT", [NCMP, NR])
        imp = sb("imp", [NR, NB + 1])
        sel = sb("sel", [NR, 64])
        drop = sb("drop", [NR, NB])
        pS, pW = sb("pS", [NR, NKS]), sb("pW", [NR, NKW])
        pTs, pTw = sb("pTs", [P, 8, NR]), sb("pTw", [P, 6, NR])
        st = sb("st", [NR, 3, 4])
        o = [sb(f"o{s}", [NR, 3, HD]) for s in range(2)]
        tp = [ps(f"tp{n}", [P, 512]) for n in range(2)]
        cps, ms = ps("cps", [P, 512]), ps("ms", [P, 512])
        sS, sW, sM = ps("sS", [P, 1024]), ps("sW", [P, 512]), ps("sM", [P, 512])
        const_in, seen, settled, zero, qtp, q_ev, pes, peb_in, pr_out = map(sem, (
            "const_in", "seen", "settled", "zero", "qtp", "q_ev", "pes", "peb_in", "pr_out"))
        x_in = [Count(sem(f"x_in{s}"), 16 * 11) for s in range(2)]
        o_out = [Count(sem(f"o_out{s}"), 16 * 6) for s in range(2)]
        two = lambda names: " ".join(f"{n}.{s}" for s in range(2) for n in names.split())
        by_pe = Steps(sem("by_pe"), two("tc0 tc1 tc2 tc3 tk0 tk1 tw tn comp nrm tv scS scC tpc imp1 imp2 tps tpw sum"))
        by_act = Steps(sem("by_act"), two("q tc0 tc1 tc2 tc3 ec es ew tps"))
        by_dve = Steps(sem("by_dve"), two(
            "tk0 tk1 tw tn kcf vcf sqk msk kcT vc mc bc rc pc pcT i1 i2 mn eq mi drop s0 s1 sn mS bS w0 wn mW bW "
            "rS pS rW pW tpw out"))
        by_pool = Steps(sem("by_pool"), two("rsk"))

        with nc.Block() as block:

            @block.sync
            def _(sp):
                for c in (*x_in, *o_out):
                    c.open(sp)
                for a, b in ((ident, "ident"), (ones, "ones2"), (share, "share"), (rsum, "rsum"), (idx, "blk"),
                             (mnew, "mask_new"), (mwin, "mask_sw")):
                    sp.dma_start(a[:, :], t[b][:, :]).then_inc(const_in, 16)
                sp.wait_ge(zero, 3)
                for g in range(2):
                    r = slice(HD * g, HD * g + HD)
                    sp.dma_start(wc[r, :, :, r], t["c_cmp_w"][0].rearrange("k (l r) e -> r k l e", r=HD)
                                 ).then_inc(const_in, 16)
                    sp.dma_start(peT[r, :, :], t["c_cmp_pe"][0].rearrange("k l d -> d k l"),
                                 allow_slow_non_contiguous=True).then_inc(const_in, 16)
                for g in range(2):
                    sp.dma_start(gain[HD * g:HD * g + HD, :], t["c_knorm"][0, 0, :].unsqueeze(1)
                                 ).then_inc(const_in, 16)
                sp.dma_start(q[:, :], t["zr"][SEQ:N_TOK, Z_CQ:Z_CQ + 384]).then_inc(const_in, 16)

                def load(s, b):
                    inc = lambda ins: ins.then_inc(x_in[s].sem, 16)
                    for n in range(8):
                        page = sp.value_load(t["page_table"][bass.ds(b, 1), n:n + 1], min_val=0,
                                             max_val=t["cache_c"].shape[0] - 1)
                        inc(sp.dma_start(x[s][64 * (n % 2):64 * (n % 2) + 64, n // 2, :],
                                         t["cache_c"][bass.ds(page, 1), :, :].rearrange(
                                             "o (a r) n -> (o a) (r n)", r=2)))
                    inc(sp.dma_start(win[s][:, :, :], t["cache_w"][bass.ds(b, 1), :, :].rearrange(
                        "o (c p) n -> p (o c) n", p=P)))
                    inc(sp.dma_start(nkv[s][:, :], t["c_kv"][bass.ds(b * DEC_S + SEQ, DEC_S), :]))
                    inc(sp.dma_start(nwin[s][:, :], t["c_win"][bass.ds(b * DEC_S + SEQ, DEC_S), :]))

                for s in range(2):
                    load(s, s)
                with sp.Fori(0, DEC_B // 2) as i:
                    for s in range(2):
                        waits(sp, seen, (by_dve.sem, by_dve.at(i, by_dve.names.index(f"out.{s}") + 1)))
                        for g in range(2):
                            for r in range(RC):
                                sp.dma_start(t["oc"][bass.ds((i * 2 + s) * DEC_S + SEQ, DEC_S), :, g * RC + r, :],
                                             o[s][32 * g + 8 * r:32 * g + 8 * r + 8, :, :]
                                             ).then_inc(o_out[s].sem, 16)
                        waits(sp, seen, (by_pe.sem, by_pe.at(i, by_pe.names.index(f"sum.{s}") + 1)))
                        load(s, (i * 2 + (2 + s)) % DEC_B)
                for s in range(2):
                    x_in[s].wait(sp, DEC_B // 2, 16 * 11)
                sp.dma_start(x[0][:, :, :], t["c_kv"][0:SEQ, :].rearrange("(c a r) n -> a c (r n)", a=P, r=2)
                             ).then_inc(x_in[0].sem, 16)
                sp.wait_ge(q_ev, 10)
                sp.dma_start(t["pc"][0:NCMP, :], kcr[:, :]).then_inc(pr_out, 16)
                sp.wait_ge(pr_out, 16)
                for s in range(2):
                    o_out[s].wait(sp, DEC_B // 2)

            @block.gpsimd
            def _(pool):
                by_pool.open(pool)
                pool.memset(qz[:, :, :], 0.0).then_inc(zero, 1)
                pool.memset(nhalf[:, :], -0.5).then_inc(zero, 1)
                pool.memset(wc[:, :, :, :], 0.0).then_inc(zero, 1)
                pool.wait_ge(zero, 3)

                def tile(i, s):
                    by_dve.after(pool, i, f"msk.{s}")
                    by_pool.did(pool.tensor_tensor(rsk[:, :], msk[:, :], nhalf[:, :], ALU.pow), f"rsk.{s}")

                with pool.Fori(0, DEC_B // 2) as i:
                    tile(i, 0)
                    tile(i, 1)
                tile(DEC_B // 2, 0)

            @block.tensor
            def _(pe):
                by_pe.open(pe)
                pe.wait_ge(const_in, 16 * 14)
                for r in range(RC):
                    last = pe.transpose(ms[:, r * N_DEC:(r + 1) * N_DEC], q[:, r * P:(r + 1) * P],
                                        ident[0:N_DEC, 0:N_DEC])
                last.then_inc(qtp, 1)
                for k in range(2):
                    for n in range(32):
                        last = pe.matmul(cps[:, k:k + 1], wc[:, k, n, :], peT[:, k, n:n + 1],
                                         start=n == 0, stop=n == 31)
                last.then_inc(pes, 1)
                pe.wait_ge(q_ev, 6)
                pe.wait_ge(peb_in, 1)

                def row_of(s):
                    return lambda c, r, kind: x[s][:, c, 512 * r + P * kind:512 * r + P * kind + P]

                def compress(i, s):
                    prev, row = (i, 0) if s else (i - 1, 1), row_of(s)
                    by_act.after(pe, prev[0], f"tps.{prev[1]}")
                    by_dve.after(pe, prev[0], f"tpw.{prev[1]}")
                    for n in range(4):
                        if n >= 2:
                            by_act.after(pe, i, f"tc{n - 2}.{s}")
                        pe.sem_inc(settled, 1)
                        for c in range(4):
                            last = pe.transpose(tp[n % 2][:, c * P:(c + 1) * P],
                                                row(c, n % 2, n // 2), ident[:, :])
                        by_pe.did(last, f"tc{n}.{s}")

                def products(i, s):
                    prev = (i, 0) if s else (i - 1, 1)
                    by_dve.after(pe, prev[0], f"out.{prev[1]}")
                    by_act.after(pe, i, f"tc3.{s}")
                    for k in range(2):
                        for n in range(32):
                            last = pe.matmul(cps[:, k * 64:k * 64 + NCMP], wc[:, k, n, :],
                                             xT[:, 2 * k + n % 2, n // 2:n // 2 + 8 * (NCMP - 1) + 1:8],
                                             start=n == 0, stop=n == 31)
                    by_pe.did(last, f"comp.{s}")
                    by_dve.after(pe, i, f"sqk.{s}")
                    by_pe.did(pe.matmul(ms[:, 0:NCMP], ones[:, :], sqk[:, :], start=True, stop=True), f"nrm.{s}")
                    by_dve.after(pe, i, f"msk.{s}")
                    by_dve.after(pe, i, f"vcf.{s}")
                    pe.sem_inc(settled, 1)
                    by_pe.did(pe.transpose(ms[0:NCMP, 64:64 + P], vcf[:, :], ident[:, :]), f"tv.{s}")

                def front(i, s):
                    row = row_of(s)
                    compress(i, s)
                    for r in range(2):
                        by_act.after(pe, i, f"tc{2 + r}.{s}")
                        for c in range(4):
                            last = pe.transpose(tp[r][:, c * P:(c + 1) * P], row(c, r, 2), ident[:, :])
                        by_pe.did(last, f"tk{r}.{s}")
                    by_dve.after(pe, i, f"tk0.{s}")
                    for c in range(4):
                        last = pe.transpose(tp[0][:, c * P:(c + 1) * P], win[s][:, c, 0:P], ident[:, :])
                    by_pe.did(last, f"tw.{s}")
                    by_dve.after(pe, i, f"tk1.{s}")
                    pe.sem_inc(settled, 1)
                    pe.transpose(tp[1][:, 0:DEC_S], nkv[s][:, 256:384], ident[0:DEC_S, 0:DEC_S])
                    by_pe.did(pe.transpose(tp[1][:, DEC_S:2 * DEC_S], nwin[s][:, 0:P], ident[0:DEC_S, 0:DEC_S]),
                              f"tn.{s}")
                    products(i, s)

                def tile(i, s):
                    row = row_of(s)
                    x_in[s].wait(pe, i, 16 * 11)
                    front(i, s)
                    by_act.after(pe, i, f"q.{s}")
                    by_dve.after(pe, i, f"tn.{s}")
                    for r in range(2):
                        pe.matmul(sS[0:NR, 512 * r:512 * r + 512], qs[:, :], ksT[:, r, :], start=True, stop=True)
                    pe.matmul(sW[0:NR, :], qs[:, :], kwT[:, :], start=True, stop=True)
                    by_pe.did(pe.matmul(sM[0:NR, 64:64 + 2 * DEC_S], qs[:, :], knT[:, :], start=True, stop=True),
                              f"scS.{s}")
                    by_dve.after(pe, i, f"kcT.{s}")
                    by_pe.did(pe.matmul(sM[0:NR, 0:NCMP], qs[:, :], kcT[:, :], start=True, stop=True), f"scC.{s}")
                    by_dve.after(pe, i, f"pc.{s}")
                    by_dve.after(pe, i, f"vc.{s}")
                    pe.sem_inc(settled, 1)
                    by_pe.did(pe.transpose(ms[0:NCMP, 192:192 + NR], pc[:, :], ident[0:NR, 0:NR]), f"tpc.{s}")
                    by_dve.after(pe, i, f"pcT.{s}")
                    pe.sem_inc(settled, 1)
                    by_pe.did(pe.matmul(ms[0:NR, 256:256 + NB + 1], pcT[:, :], share[:, :], start=True, stop=True),
                              f"imp1.{s}")
                    by_dve.after(pe, i, f"i1.{s}")
                    pe.sem_inc(settled, 1)
                    by_pe.did(pe.matmul(ms[0:NR, 288:288 + NB + 1], rsum[:, :], imp[:, :], start=True, stop=True),
                              f"imp2.{s}")
                    by_dve.after(pe, i, f"pS.{s}")
                    pe.sem_inc(settled, 1)
                    for c in range(8):
                        last = pe.transpose(tp[0][:, c * NR:(c + 1) * NR], pS[:, c * P:(c + 1) * P], ident[0:NR, 0:NR])
                    by_pe.did(last, f"tps.{s}")
                    by_dve.after(pe, i, f"pW.{s}")
                    pe.sem_inc(settled, 1)
                    for c in range(4):
                        pe.transpose(tp[1][:, c * NR:(c + 1) * NR], pW[:, c * P:(c + 1) * P], ident[0:NR, 0:NR])
                    pe.transpose(tp[1][0:DEC_S, 256:256 + NR], pW[:, CWIN:NKW], ident[0:NR, 0:NR])
                    by_pe.did(pe.transpose(tp[1][0:DEC_S, 320:320 + NR], pS[:, PAST:NKS], ident[0:NR, 0:NR]),
                              f"tpw.{s}")
                    by_act.after(pe, i, f"tps.{s}")
                    by_dve.after(pe, i, f"tpw.{s}")
                    pe.sem_inc(settled, 1)
                    out = lambda n: cps[0:NR, P + n * P:2 * P + n * P]
                    pe.matmul(out(0), pcT[:, :], vc[:, :], start=True, stop=True)
                    for c in range(8):
                        pe.matmul(out(1), pTs[:, c, :], row(c % 4, c // 4, 3), start=c == 0, stop=False)
                    pe.matmul(out(1), pTw[0:DEC_S, 5, :], nkv[s][:, 384:512], start=False, stop=True)
                    for c in range(4):
                        pe.matmul(out(2), pTw[:, c, :], win[s][:, c, P:2 * P], start=c == 0, stop=False)
                    by_pe.did(pe.matmul(out(2), pTw[0:DEC_S, 4, :], nwin[s][:, P:2 * P], start=False, stop=True),
                              f"sum.{s}")

                with pe.Fori(0, DEC_B // 2) as i:
                    tile(i, 0)
                    tile(i, 1)
                n = DEC_B // 2
                x_in[0].wait(pe, n + 1, 16)
                front(n, 0)
                by_dve.after(pe, n, "vc.0")
                pe.transpose(ms[0:NCMP, 192:192 + P], kcT[:, :], ident[:, :]).then_inc(qtp, 1)

            @block.scalar
            def _(act):
                by_act.open(act)
                act.wait_ge(zero, 3)
                act.wait_ge(qtp, 1)
                for g in range(2):
                    for r in range(RC):
                        rs = slice(HD * g, HD * g + HD)
                        act.activation(qz[rs, :, 32 * g + 8 * r:32 * g + 8 * r + 8],
                                       ms[rs, r * N_DEC:(r + 1) * N_DEC].rearrange("p (b q) -> p b q", b=DEC_B),
                                       ACT.Copy).then_inc(q_ev, 1)
                act.wait_ge(q_ev, 6)

                def take(i, s):
                    for n in range(4):
                        by_pe.after(act, i, f"tc{n}.{s}")
                        by_act.did(act.activation(xT[:, n, :], tp[n % 2][:, :], ACT.Copy), f"tc{n}.{s}")

                def queries(i, s, b):
                    by_pe.after(act, *((i, "scC.0") if s else (i - 1, "scC.1")))
                    by_act.did(act.activation(qs[:, :], qz[:, bass.ds(b, 1), :].rearrange(
                        "p o r -> p (o r)"), ACT.Copy), f"q.{s}")

                def tile(i, s):
                    queries(i, s, i * 2 + s)
                    take(i, s)
                    for k, buf, n in (("c", pc, 0), ("s", pS, 1), ("w", pW, 2)):
                        by_dve.after(act, i, {"c": f"bc.{s}", "s": f"bS.{s}", "w": f"bW.{s}"}[k])
                        by_act.did(act.activation(buf[:, :], sM[0:NR, 0:NCMP] if n == 0 else buf[:, :], ACT.Exp,
                                                  bias=st[:, n, 1:2], scale=SCALE, accum_out=st[:, n, 2:3]),
                                   f"e{k}.{s}")
                    by_pe.after(act, i, f"tps.{s}")
                    by_act.did(act.activation(pTs[:, :, :], tp[0][:, :].rearrange("p (c r) -> p c r", r=NR),
                                              ACT.Copy), f"tps.{s}")

                with act.Fori(0, DEC_B // 2) as i:
                    tile(i, 0)
                    tile(i, 1)
                queries(DEC_B // 2, 0, 0)
                take(DEC_B // 2, 0)

            @block.vector
            def _(dve):
                by_dve.open(dve)
                dve.wait_ge(const_in, 16 * 14)
                dve.wait_ge(pes, 1)
                dve.tensor_copy(peb[:, :], cps[:, 0:2]).then_inc(peb_in, 1)
                dve.wait_ge(peb_in, 1)

                def compress(i, s):
                    step = lambda name, ins: (by_dve.did(ins, f"{name}.{s}"), by_dve.after(dve, i, f"{name}.{s}"))
                    by_pe.after(dve, i, f"comp.{s}")
                    step("kcf", dve.tensor_scalar(kcf[:, :], cps[:, 0:NCMP], peb[:, 0:1], None, ALU.add))
                    by_pe.after(dve, *((i, "tv.0") if s else (i - 1, "tv.1")))
                    step("vcf", dve.tensor_scalar(vcf[:, :], cps[:, 64:64 + NCMP], peb[:, 1:2], None, ALU.add))
                    step("sqk", dve.tensor_tensor(sqk[:, :], kcf[:, :], kcf[:, :], ALU.mult))
                    by_pe.after(dve, i, f"nrm.{s}")
                    step("msk", dve.tensor_scalar(msk[:, :], ms[:, 0:NCMP], 1.0 / HD, EPS, ALU.mult, ALU.add))
                    by_pool.after(dve, i, f"rsk.{s}")
                    by_pe.after(dve, *((i, "scC.0") if s else (i - 1, "scC.1")))
                    step("kcT", dve.scalar_tensor_tensor(out=kcT[:, :], in0=kcf[:, :], scalar=gain[:, :],
                                                         in1=rsk[:, :], op0=ALU.mult, op1=ALU.mult))
                    by_pe.after(dve, i, f"tv.{s}")
                    by_pe.after(dve, *((i, "sum.0") if s else (i - 1, "sum.1")))
                    step("vc", dve.tensor_copy(vc[:, :], ms[0:NCMP, 64:64 + P]))

                def front(i, s):
                    step = lambda name, ins: (by_dve.did(ins, f"{name}.{s}"), by_dve.after(dve, i, f"{name}.{s}"))
                    prev = (i, 0) if s else (i - 1, 1)
                    by_pe.after(dve, prev[0], f"scS.{prev[1]}")
                    for r in range(2):
                        by_pe.after(dve, i, f"tk{r}.{s}")
                        step(f"tk{r}", dve.tensor_copy(ksT[:, r, :], tp[r][:, :]))
                    by_pe.after(dve, i, f"tw.{s}")
                    step("tw", dve.tensor_copy(kwT[:, :], tp[0][:, :]))
                    by_pe.after(dve, i, f"tn.{s}")
                    step("tn", dve.tensor_copy(knT[:, :], tp[1][:, 0:2 * DEC_S]))
                    compress(i, s)

                def tile(i, s):
                    step = lambda name, ins: (by_dve.did(ins, f"{name}.{s}"), by_dve.after(dve, i, f"{name}.{s}"))
                    prev = (i, 0) if s else (i - 1, 1)
                    front(i, s)
                    by_pe.after(dve, i, f"scC.{s}")
                    step("mc", dve.tensor_reduce(st[:, 0, 0:1], sM[0:NR, 0:NCMP], AX.X, ALU.max))
                    step("bc", dve.tensor_scalar(st[:, 0, 1:2], st[:, 0, 0:1], -SCALE, None, ALU.mult))
                    by_act.after(dve, i, f"ec.{s}")
                    step("rc", dve.reciprocal(st[:, 0, 3:4], st[:, 0, 2:3]))
                    step("pc", dve.tensor_scalar(pc[:, :], pc[:, :], st[:, 0, 3:4], None, ALU.mult))
                    by_pe.after(dve, i, f"tpc.{s}")
                    step("pcT", dve.tensor_copy(pcT[:, :], ms[0:NCMP, 192:192 + NR]))
                    by_pe.after(dve, i, f"imp1.{s}")
                    step("i1", dve.tensor_copy(imp[:, :], ms[0:NR, 256:256 + NB + 1]))
                    by_pe.after(dve, i, f"imp2.{s}")
                    step("i2", dve.tensor_copy(sel[:, 0:NB + 1], ms[0:NR, 288:288 + NB + 1]))
                    step("mn", dve.tensor_reduce(sel[:, 40:41], sel[:, 1:NB - 1], AX.X, ALU.min))
                    step("eq", dve.scalar_tensor_tensor(out=sel[:, 20:20 + NB - 2], in0=sel[:, 1:NB - 1],
                                                        scalar=sel[:, 40:41], in1=idx[:, 1:NB - 1],
                                                        op0=ALU.is_equal, op1=ALU.mult))
                    step("mi", dve.tensor_reduce(sel[:, 41:42], sel[:, 20:20 + NB - 2], AX.X, ALU.max))
                    step("drop", dve.tensor_scalar(drop[:, :], idx[:, :], sel[:, 41:42], NEG, ALU.is_equal, ALU.mult))
                    by_pe.after(dve, prev[0], f"tpw.{prev[1]}")
                    for r in range(2):
                        step(f"s{r}", dve.tensor_tensor(
                            pS[:, 512 * r:512 * r + 512].rearrange("p (b k) -> p b k", b=NB),
                            sS[0:NR, 512 * r:512 * r + 512].rearrange("p (b k) -> p b k", b=NB),
                            drop[:, :].unsqueeze(2).to_broadcast([NR, NB, 32]), ALU.add))
                    step("sn", dve.tensor_tensor(pS[:, PAST:NKS], sM[0:NR, 64:64 + DEC_S], mnew[:, :], ALU.add))
                    step("mS", dve.tensor_reduce(st[:, 1, 0:1], pS[:, :], AX.X, ALU.max))
                    step("bS", dve.tensor_scalar(st[:, 1, 1:2], st[:, 1, 0:1], -SCALE, None, ALU.mult))
                    step("w0", dve.tensor_tensor(pW[:, 0:CWIN], sW[0:NR, :], mwin[:, :], ALU.add))
                    step("wn", dve.tensor_tensor(pW[:, CWIN:NKW], sM[0:NR, 64 + DEC_S:64 + 2 * DEC_S], mnew[:, :],
                                                 ALU.add))
                    step("mW", dve.tensor_reduce(st[:, 2, 0:1], pW[:, :], AX.X, ALU.max))
                    step("bW", dve.tensor_scalar(st[:, 2, 1:2], st[:, 2, 0:1], -SCALE, None, ALU.mult))
                    for n, k, e, buf in ((1, "S", "es", pS), (2, "W", "ew", pW)):
                        by_act.after(dve, i, f"{e}.{s}")
                        step(f"r{k}", dve.reciprocal(st[:, n, 3:4], st[:, n, 2:3]))
                        step(f"p{k}", dve.tensor_scalar(buf[:, :], buf[:, :], st[:, n, 3:4], None, ALU.mult))
                    by_pe.after(dve, i, f"tpw.{s}")
                    dve.tensor_copy(pTw[:, 0:4, :], tp[1][:, 0:256].rearrange("p (c r) -> p c r", r=NR))
                    step("tpw", dve.tensor_copy(pTw[0:DEC_S, 4:6, :], tp[1][0:DEC_S, 256:384].rearrange(
                        "p (c r) -> p c r", r=NR)))
                    by_pe.after(dve, i, f"sum.{s}")
                    o_out[s].wait(dve, i)
                    for g in range(2):
                        rs = slice(32 * g, 32 * g + 32)
                        last = dve.tensor_copy(o[s][rs, :, :], cps[rs, P:4 * P].rearrange(
                            "p (n c) -> p n c", n=3)[:, :, HD * g:HD * g + HD])
                    step("out", last)

                with dve.Fori(0, DEC_B // 2) as i:
                    tile(i, 0)
                    tile(i, 1)
                n = DEC_B // 2
                front(n, 0)
                dve.tensor_copy(kcr[:, P:2 * P], vc[:, :]).then_inc(q_ev, 2)
                dve.wait_ge(qtp, 2)
                dve.tensor_copy(kcr[:, 0:P], ms[0:NCMP, 192:192 + P]).then_inc(q_ev, 2)


SLOTS = (2 * N_TOK + NE * (P - 1)) // P
WB = 3
SW = SLOTS + 2


def mix_and_experts(nc, t):
    with ExitStack() as ctx:
        sb = lambda name, shape, dt=F32: ctx.enter_context(nc.sbuf_tensor("m_" + name, shape, dt))
        ps = lambda name, shape: ctx.enter_context(nc.psum_tensor("m_" + name, shape, F32))
        sem = ctx.enter_context(semaphores(nc, "m_"))
        ident, tri, ones = sb("ident", [P, P]), sb("tri", [P, P]), sb("ones", [P, P])
        wo = sb("wo", [P, KD, D])
        wr = sb("wr", [P, KD, 20])
        rb = sb("rb", [P, 20])
        gain = sb("gain", [P, D])
        pri = sb("pri", [P, 4])
        thr = sb("thr", [P, TILES])
        before = sb("before", [P, NE, NE])
        sno = sb("sno", [P, SW])
        tid = sb("tid", [P, TILES], U32)
        cat = sb("cat", [P, D])
        oc = sb("oc", [P, 3, 384])
        zg = sb("zg", [P, 18])
        eg = sb("eg", [P, 18])
        x = sb("x", [P, D])
        catT = sb("catT", [P, KD, P])
        x1 = sb("x1", [P, TILES, D])
        sq = sb("sq", [P, D])
        st = sb("st", [P, 3])
        nhalf = sb("nhalf", [P, 1])
        h2 = sb("h2", [P, D])
        h2T = sb("h2T", [P, KD, P])
        tp, acc = ps("tp", [P, KD, P]), ps("acc", [P, D])
        hid = [ps(f"hid{s}", [P, 512]) for s in range(2)]
        hTp = ps("hTp", [P, 512])
        N = TILES
        L = sb("L", [P, N, 20])
        gm, gs, m1, m2, mm, pd, ee = (sb(n, [P, N]) for n in ("gm", "gs", "m1", "m2", "mm", "pd", "ee"))
        g4, og, es, o1, o2, tq4 = (sb(n, [P, N, 4]) for n in ("g4", "og", "es", "o1", "o2", "tq4"))
        t16, A, rank = (sb(n, [P, N, NE]) for n in ("t16", "A", "rank"))
        O = sb("O", [P, 2, N, NE])
        wt = sb("wt", [P, 2, N])
        base = sb("base", [P, N + 1, NE])
        tot = sb("tot", [P, N, NE])
        c9, nsl, first, c16 = sb("c9", [P, NE, N]), sb("nsl", [P, NE]), sb("first", [P, NE]), sb("c16", [P, NE, NE])
        K, S, fl, r = (sb(n, [P, 2, N]) for n in ("K", "S", "fl", "r"))
        c8 = sb("c8", [P, 2 * N, N - 1])
        at, pos = sb("at", [P, 2 * N], U32), sb("pos", [P, 2 * N], U32)
        c32, sx = sb("c32", [P, SW, NE]), sb("sx", [P, SW])
        sxi = sb("sxi", [P, SW + NE], I32)
        zi = sb("zi", [P, SW], U32)
        tok = sb("tok", [P, SW], U32)
        w13 = sb("w13", [P, WB * KD, 2 * DE])
        w2 = sb("w2", [P, WB * DE // P, D])
        xg = [sb(f"xg{s}", [P, D]) for s in range(2)]
        ix = [sb(f"ix{s}", [P, 1], U32) for s in range(2)]
        xT = sb("xT", [P, KD, P])
        hs, hh = (sb(n, [P, DE]) for n in ("hs", "hh"))
        hT = sb("hT", [P, DE // P, P])
        yo = [cat, x]
        gy = [[w13[:, 4 * s + 2 * k:4 * s + 2 * k + 2, :].rearrange("p a b -> p (a b)") for k in range(2)]
              for s in range(2)]
        iy = [[sb(f"iy{s}{k}", [P, 1], U32) for k in range(2)] for s in range(2)]
        wy = sb("wy", [P, 2])
        yt = yo
        const_in, seen, settled, cleared, rows_out, tab0, scat, sx_out, tok_in, y_end = map(sem, (
            "const_in", "seen", "settled", "cleared", "rows_out", "tab0", "scat", "sx_out", "tok_in", "y_end"))
        cat_in, x_in = Count(sem("cat_in"), 16 * 3), Count(sem("x_in"), 16)
        h2_out = Count(sem("h2_out"), 16)
        act_g, dve_g = Steps(sem("act_g"), "gate"), Steps(sem("dve_g"), "g1 g2 b0 b1 b2 s1 s2")
        pe_s = Steps(sem("pe_s"), "catT wo")
        pe_r = Steps(sem("pe_r"), "h2T rout")
        act_c, act_s = Steps(sem("act_c"), "catT"), Steps(sem("act_s"), "sq")
        act_r = Steps(sem("act_r"), "h2T")
        dve_c, dve_s = Steps(sem("dve_c"), "catT"), Steps(sem("dve_s"), "x1 ms h2")
        dve_r = Steps(sem("dve_r"), "h2T rout")
        pool_s = Steps(sem("pool_s"), "rs")
        rt_dve, rt_act, rt_pe, rt_pool = map(sem, ("rt_dve", "rt_act", "rt_pe", "rt_pool"))
        w_in, hidden = Count(sem("w_in"), 48), Steps(sem("hidden"), "one rec sil hh")
        ps_xT, ps_hid, ps_hT, ps_out = (Count(sem("ps_" + n)) for n in ("xT", "hid", "hT", "out"))
        a_xT, a_exp, a_hT, a_out = (Count(sem("a_" + n)) for n in ("xT", "exp", "hT", "out"))
        d_xT, d_out = (Count(sem("d_" + n)) for n in ("xT", "out"))
        xg_in = [Count(sem(f"xg_in{s}"), 16) for s in range(2)]
        ys_out = [Count(sem(f"ys_out{s}"), 16) for s in range(2)]
        e_pool = Steps(sem("e_pool"), "ix.0 ix.1")
        y_pool = Steps(sem("y_pool"), "ix")
        y_dve = Steps(sem("y_dve"), "wy a b")
        gy_in = [Count(sem(f"gy_in{s}"), 32) for s in range(2)]
        yt_out = [Count(sem(f"yt_out{s}"), 16) for s in range(2)]
        NS = SLOTS // 2
        assert SLOTS % 2 == 0

        with nc.Block() as block:

            @block.sync
            def _(sp):
                for c in (cat_in, x_in, h2_out, w_in, *yt_out):
                    c.open(sp)
                for a, b in ((ident, "ident"), (tri, "m_tri"), (ones, "m_ones"), (pri, "m_pri"), (thr, "m_thr"),
                             (before, "m_before"), (sno, "m_sno"), (tid, "m_tid")):
                    sp.dma_start(a[:], t[b][:]).then_inc(const_in, 16)
                sp.dma_start(gain[:, :], t["ffn_norm"][0].partition_broadcast(P)).then_inc(const_in, 16)

                def load(rows, T):
                    sp.dma_start(cat[0:T, 0:640], t["cat"][rows, 0:640]).then_inc(cat_in.sem, 16)
                    sp.dma_start(oc[0:T, :, :], t["oc"][rows, :, :, :].rearrange("p b h d -> p b (h d)")
                                 ).then_inc(cat_in.sem, 16)
                    sp.dma_start(zg[0:T, :], t["zr"][rows, Z_G:Z_W]).then_inc(cat_in.sem, 16)

                load(slice(0, P), P)
                sp.dma_start(x[:, :], t["x"][0:P, :]).then_inc(x_in.sem, 16)
                sp.dma_start(wo[:, :, :], t["w_o"][0].rearrange("(k p) n -> p k n", p=P)).then_inc(const_in, 16)
                for lo, hi, w, b in ((0, 4, "moe_wg", "moe_bg"), (4, 20, "moe_we", "moe_be")):
                    sp.dma_start(wr[:, :, lo:hi], t[w][0].rearrange("(k p) n -> p k n", p=P)).then_inc(const_in, 16)
                    sp.dma_start(rb[:, lo:hi], t[b][0].partition_broadcast(P)).then_inc(const_in, 16)
                def load_expert(e, free=None):
                    if free is not None:
                        waits(sp, seen, (ps_out.sem, free + 1))
                    for k, w in enumerate(("moe_w1", "moe_w3")):
                        sp.dma_start(w13[:, bass.ds(e % WB * KD, KD), k * DE:(k + 1) * DE],
                                     t[w][0, bass.ds(e, 1), :, :].rearrange("o (k p) f -> p (o k) f", p=P)
                                     ).then_inc(w_in.sem, 16)
                    sp.dma_start(w2[:, bass.ds(e % WB * (DE // P), DE // P), :],
                                 t["moe_w2"][0, bass.ds(e, 1), :, :].rearrange("o (k p) n -> p (o k) n", p=P)
                                 ).then_inc(w_in.sem, 16)
                    if free is not None:
                        waits(sp, seen, (w_in.sem, w_in.at(e, 48)))

                sp.dma_start(t["a_s"][:, PAST - DEC_S:PAST, :],
                             t["a_kv"][SEQ:N_TOK, :].rearrange("(b s) n -> b s n", b=DEC_B)).then_inc(rows_out, 16)
                sp.dma_start(t["w_s"][:, CWIN - DEC_S:CWIN, :],
                             t["c_win"][SEQ:N_TOK, :].rearrange("(b s) n -> b s n", b=DEC_B)).then_inc(rows_out, 16)

                def tile(i, T, T_next):
                    waits(sp, seen, (pe_s.sem, pe_s.at(i, 1)), (dve_g.sem, dve_g.at(i, 7)))
                    if T_next:
                        load(bass.ds((i + 1) * P, T_next), T_next)
                    waits(sp, seen, (dve_s.sem, dve_s.at(i, 1)))
                    if T_next:
                        sp.dma_start(x[0:T_next, :], t["x"][bass.ds((i + 1) * P, T_next), :]).then_inc(x_in.sem, 16)
                    waits(sp, seen, (dve_s.sem, dve_s.at(i, 3)))
                    sp.dma_start(t["h2"][bass.ds(i * P, T), :], h2[0:T, :]).then_inc(h2_out.sem, 16)

                with sp.Fori(0, PT - 1) as i:
                    tile(i, P, P)
                tile(PT - 1, P, N_DEC)
                for e in range(WB):
                    load_expert(e)
                tile(PT, N_DEC, 0)
                h2_out.wait(sp, TILES)
                sp.wait_ge(cleared, 3)
                sp.dma_start(t["tok_at"].rearrange("(p s) o -> p (s o)", s=SW), zi[:, :]).then_inc(tab0, 16)
                sp.wait_ge(rt_dve, SX_DONE)
                sp.dma_start(t["slot_expert"][:, :], sxi[0:1, :]).then_inc(sx_out, 16)
                sp.wait_ge(scat, 16 * 2 * TILES)
                sp.dma_start(tok[:, :], t["tok_at"].rearrange("(p s) o -> p (s o)", s=SW)).then_inc(tok_in, 16)
                sp.wait_ge(sx_out, 16)
                w_in.wait(sp, WB)
                with sp.Fori(WB, NE) as e:
                    load_expert(e, sp.value_load(t["slot_expert"][0:1, bass.ds(e + (SW - WB), 1)],
                                                 min_val=0, max_val=SLOTS))
                for k in range(2):
                    ys_out[k].wait(sp, NS)
                sp.sem_inc(y_end, 1)
                def store_y(n, s, T):
                    waits(sp, seen, (y_dve.sem, y_dve.at(n, 3)))
                    sp.dma_start(t["y"][bass.ds(n * P, T), :], yt[s][0:T, :]).then_inc(yt_out[s].sem, 16)

                with sp.Fori(0, PT // 2) as i:
                    store_y(i * 2, 0, P)
                    store_y(i * 2 + 1, 1, P)
                store_y(PT, 0, N_DEC)
                yt_out[0].wait(sp, PT // 2 + 1)
                yt_out[1].wait(sp, PT // 2)
                sp.wait_ge(rows_out, 32)

            @block.tensor
            def _(pe):
                for c in (pe_s, pe_r, ps_xT, ps_hid, ps_hT, ps_out):
                    c.open(pe)
                pe.wait_ge(const_in, 16 * 14)

                def transpose_cat(i, T, first=False):
                    cat_in.wait(pe, i, 48)
                    dve_g.after(pe, i, "s2")
                    if not first:
                        dve_r.after(pe, i - 2, "h2T")
                        act_r.after(pe, i - 2, "h2T")
                    if T < P:
                        pe.sem_inc(settled, 1)
                    for k in range(KD):
                        last = pe.transpose(tp[:, k, 0:T], cat[0:T, k * P:(k + 1) * P], ident[0:T, 0:T])
                    pe_s.did(last, "catT")
                    act_c.after(pe, i, "catT")
                    dve_c.after(pe, i, "catT")
                    dve_s.after(pe, i - 1, "x1")
                    if T < P:
                        pe.sem_inc(settled, 1)

                def project_out(T, lo):
                    for k in range(KD):
                        last = pe.matmul(acc[0:T, lo:lo + 512], catT[:, k, 0:T], wo[:, k, lo:lo + 512],
                                         start=k == 0, stop=k == KD - 1)
                    if lo:
                        pe_s.did(last, "wo")

                def transpose_h2(i, T):
                    dve_s.after(pe, i, "h2")
                    for k in range(KD):
                        last = pe.transpose(tp[:, k, 0:T], h2[0:T, k * P:(k + 1) * P], ident[0:T, 0:T])
                    pe_r.did(last, "h2T")

                def router(i, T):
                    act_r.after(pe, i, "h2T")
                    dve_r.after(pe, i, "h2T")
                    dve_r.after(pe, i - 1, "rout")
                    for k in range(KD):
                        last = pe.matmul(hTp[0:T, 0:20], h2T[:, k, 0:T], wr[:, k, :], start=k == 0, stop=k == KD - 1)
                    pe_r.did(last, "rout")

                def tile(i, T):
                    transpose_cat(i, T)
                    project_out(T, 0)
                    transpose_h2(i - 1, P)
                    project_out(T, 512)
                    router(i - 1, P)

                transpose_cat(0, P, first=True)
                project_out(P, 0)
                project_out(P, 512)
                with pe.Fori(1, PT) as i:
                    tile(i, P)
                tile(PT, N_DEC)
                transpose_h2(PT, N_DEC)
                router(PT, N_DEC)
                pe.wait_ge(rt_dve, A_DONE)
                pe.matmul(hid[0][:, 0:N * NE], tri[:, :], A[:, :, :].rearrange("p n e -> p (n e)"),
                          start=True, stop=True)
                pe.matmul(hid[0][:, 256:256 + N * NE], ones[:, :], A[:, :, :].rearrange("p n e -> p (n e)"),
                          start=True, stop=True).then_inc(rt_pe, 1)
                pe.wait_ge(rt_dve, SX_DONE)

                def transpose_rows(j, s, fill):
                    xg_in[s].wait(pe, fill)
                    a_xT.wait(pe, j)
                    d_xT.wait(pe, j)
                    for k in range(KD):
                        last = pe.transpose(tp[:, k, :], xg[s][:, k * P:(k + 1) * P], ident[:, :])
                    last.then_inc(ps_xT.sem, 1)

                def hidden_rows(j, s, e):
                    a_xT.wait(pe, j, 1)
                    d_xT.wait(pe, j, 1)
                    w_in.wait(pe, e, 48)
                    for k in range(KD):
                        last = pe.matmul(hid[s][:, :], xT[:, k, :], w13[:, bass.ds(e % WB * KD + k, 1), :].rearrange(
                            "p o n -> p (o n)"), start=k == 0, stop=k == KD - 1)
                    last.then_inc(ps_hid.sem, 1)

                def transpose_hidden(j):
                    hidden.after(pe, j, "hh")
                    a_hT.wait(pe, j)
                    for k in range(DE // P):
                        last = pe.transpose(hTp[:, k * P:(k + 1) * P], hh[:, k * P:(k + 1) * P], ident[:, :])
                    last.then_inc(ps_hT.sem, 1)

                def output_rows(j, e):
                    a_hT.wait(pe, j, 1)
                    a_out.wait(pe, j)
                    d_out.wait(pe, j)
                    for lo in (0, 512):
                        for k in range(DE // P):
                            last = pe.matmul(acc[:, lo:lo + 512], hT[:, k, :],
                                             w2[:, bass.ds(e % WB * (DE // P) + k, 1), lo:lo + 512].rearrange(
                                                 "p o n -> p (o n)"), start=k == 0, stop=k == DE // P - 1)
                    last.then_inc(ps_out.sem, 1)

                expert = lambda j: pe.value_load(sxi[0:1, bass.ds(j, 1)], min_val=0, max_val=NE - 1)

                def slot(j, s, fill_next):
                    hidden_rows(j, s, expert(j))
                    transpose_rows(j + 1, 1 - s, fill_next)
                    output_rows(j - 1, expert(j - 1))
                    transpose_hidden(j)

                w_in.wait(pe, WB)
                transpose_rows(0, 0, 0)
                hidden_rows(0, 0, expert(0))
                transpose_rows(1, 1, 0)
                transpose_hidden(0)
                with pe.Fori(0, NS - 1) as i:
                    slot(i * 2 + 1, 1, i + 1)
                    slot(i * 2 + 2, 0, i + 1)
                hidden_rows(SLOTS - 1, 1, expert(SLOTS - 1))
                output_rows(SLOTS - 2, expert(SLOTS - 2))
                transpose_hidden(SLOTS - 1)
                output_rows(SLOTS - 1, expert(SLOTS - 1))

            @block.scalar
            def _(act):
                for c in (act_g, act_c, act_s, act_r, a_xT, a_exp, a_hT, a_out):
                    c.open(act)

                def gates(i, T):
                    cat_in.wait(act, i, 48)
                    dve_g.after(act, i - 1, "g2")
                    act_g.did(act.activation(eg[0:T, :], zg[0:T, :], ACT.Exp, scale=-1.0), "gate")

                def transposed(i, T):
                    pe_s.after(act, i, "catT")
                    act_c.did(act.activation(catT[:, 0:4, 0:T], tp[:, 0:4, 0:T], ACT.Copy), "catT")

                def squares(i, T):
                    dve_s.after(act, i, "x1")
                    act_s.did(act.activation(sq[0:T, :], x1[0:T, bass.ds(i, 1), :].rearrange("p o n -> p (o n)"),
                                             ACT.Square, accum_out=st[0:T, 0:1]), "sq")

                def router(i, T):
                    pe_r.after(act, i, "h2T")
                    pe_r.after(act, i - 1, "rout")
                    act_r.did(act.activation(h2T[:, 0:4, 0:T], tp[:, 0:4, 0:T], ACT.Copy), "h2T")

                def tile(i, T, T_next):
                    squares(i - 1, P)
                    transposed(i, T)
                    if T_next:
                        gates(i + 1, T_next)
                    router(i - 1, P)

                gates(0, P)
                transposed(0, P)
                gates(1, P)
                with act.Fori(1, PT - 1) as i:
                    tile(i, P, P)
                tile(PT - 1, P, N_DEC)
                tile(PT, N_DEC, 0)
                squares(PT, N_DEC)
                router(PT, N_DEC)
                act.wait_ge(rt_dve, G4_DONE)
                act.activation(g4[:, :, :], g4[:, :, :], ACT.Exp).then_inc(rt_act, 1)
                act.wait_ge(rt_dve, PD_DONE)
                act.activation(ee[:, :], pd[:, :], ACT.Exp).then_inc(rt_act, 1)

                def transposed(j):
                    ps_xT.wait(act, j, 1)
                    ps_hid.wait(act, j)
                    act.activation(xT[:, 0:4, :], tp[:, 0:4, :], ACT.Copy).then_inc(a_xT.sem, 1)

                def exponential(j, s):
                    ps_hid.wait(act, j, 1)
                    act.activation(hs[:, :], hid[s][:, 0:DE], ACT.Exp, scale=-1.0).then_inc(a_exp.sem, 1)

                def hidden_transposed(j):
                    ps_hT.wait(act, j, 1)
                    ps_out.wait(act, j)
                    act.activation(hT[:, :, :], hTp[:, 0:DE].rearrange("p (k t) -> p k t", t=P),
                                   ACT.Copy).then_inc(a_hT.sem, 1)

                def output(j, s, fill):
                    ps_out.wait(act, j, 1)
                    ys_out[s].wait(act, fill)
                    act.activation(yo[s][:, 0:512], acc[:, 0:512], ACT.Copy).then_inc(a_out.sem, 1)
                    waits(act, seen, (a_out.sem, a_out.at(j, 1)), (d_out.sem, d_out.at(j, 1)))
                    act.dma_start(t["ys"][bass.ds(j * P, P), :], yo[s][:, :]).then_inc(ys_out[s].sem, 16)

                def slot(j, s, fill):
                    exponential(j, s)
                    transposed(j + 1)
                    output(j - 1, 1 - s, fill)
                    hidden_transposed(j)

                for k in range(2):
                    ys_out[k].open(act)
                transposed(0)
                exponential(0, 0)
                transposed(1)
                hidden_transposed(0)
                with act.Fori(0, NS - 1) as i:
                    slot(i * 2 + 1, 1, i)
                    slot(i * 2 + 2, 0, i)
                exponential(SLOTS - 1, 1)
                output(SLOTS - 2, 0, NS - 1)
                hidden_transposed(SLOTS - 1)
                output(SLOTS - 1, 1, NS - 1)

            @block.gpsimd
            def _(pool):
                for c in (pool_s, e_pool, y_pool):
                    c.open(pool)
                pool.memset(nhalf[:, :], -0.5).then_inc(cleared, 1)
                pool.memset(zi[:, :], 0).then_inc(cleared, 1)
                pool.memset(L[:, :, :], 0.0).then_inc(cleared, 1)
                pool.wait_ge(cleared, 3)

                def tile(i, T):
                    dve_s.after(pool, i, "ms")
                    pool_s.did(pool.tensor_tensor(st[0:T, 2:3], st[0:T, 1:2], nhalf[0:T, :], ALU.pow), "rs")

                with pool.Fori(0, PT) as i:
                    tile(i, P)
                tile(PT, N_DEC)
                pool.wait_ge(rt_dve, AT_DONE)
                pool.wait_ge(tab0, 16)
                for n in range(2 * TILES):
                    T = P if n % TILES < PT else N_DEC
                    pool.indirect_dma_start(t["tok_at"][:, :], bass.IndirectOffsetOnAxis(at[0:T, n:n + 1], 0),
                                            tid[0:T, n % TILES:n % TILES + 1], None).then_inc(scat, 16)
                pool.wait_ge(tok_in, 16)
                h2_out.wait(pool, TILES)

                def gather(n, i, s, prev):
                    if prev:
                        xg_in[s].wait(pool, i)
                        ps_xT.wait(pool, i * 2 + s, 1)
                    e_pool.did(pool.tensor_copy(ix[s][:, :], tok[:, n]), f"ix.{s}")
                    e_pool.after(pool, i + 1 if prev else 0, f"ix.{s}")
                    pool.sem_inc(settled, 1)
                    pool.indirect_dma_start(xg[s][:, :], None, t["h2"][:, :],
                                            bass.IndirectOffsetOnAxis(ix[s][:, :], 0)).then_inc(xg_in[s].sem, 16)

                for s in range(2):
                    gather(slice(s, s + 1), 0, s, False)
                with pool.Fori(0, NS) as i:
                    for s in range(2):
                        gather(bass.ds(i * 2 + (2 + s), 1), i, s, True)
                for s in range(2):
                    xg_in[s].wait(pool, NS)
                pool.wait_ge(y_end, 1)

                def gather_y(n, s, T, first=False):
                    if not first:
                        y_dve.after(pool, n - 2, "b")
                    pool.tensor_copy(iy[s][0][0:T, :], pos[0:T, bass.ds(n, 1)])
                    y_pool.did(pool.tensor_copy(iy[s][1][0:T, :], pos[0:T, bass.ds(n + N, 1)]), "ix")
                    y_pool.after(pool, n, "ix")
                    pool.sem_inc(settled, 1)
                    for k in range(2):
                        pool.indirect_dma_start(gy[s][k][0:T, :], None, t["ys"][:, :],
                                                bass.IndirectOffsetOnAxis(iy[s][k][0:T, :], 0)
                                                ).then_inc(gy_in[s].sem, 16)

                gather_y(0, 0, P, first=True)
                gather_y(1, 1, P, first=True)
                with pool.Fori(1, PT // 2) as i:
                    gather_y(i * 2, 0, P)
                    gather_y(i * 2 + 1, 1, P)
                gather_y(PT, 0, N_DEC)

            @block.vector
            def _(dve):
                for c in (dve_g, dve_c, dve_s, dve_r, hidden, d_xT, d_out, y_dve):
                    c.open(dve)
                dve.wait_ge(const_in, 16 * 14)
                dve.wait_ge(cleared, 3)

                def gates(i, T):
                    tr = slice(0, T)
                    step = lambda name, ins: (dve_g.did(ins, name), dve_g.after(dve, i, name))
                    act_g.after(dve, i, "gate")
                    step("g1", dve.tensor_scalar(eg[tr, :], eg[tr, :], 1.0, None, ALU.add))
                    step("g2", dve.reciprocal(zg[tr, :], eg[tr, :]))
                    for b in range(3):
                        v = oc[tr, b, :].rearrange("p (h d) -> p h d", d=HD)
                        g = zg[tr, :].rearrange("p (h b) -> p h b", b=3)[:, :, b:b + 1].to_broadcast([T, HC, HD])
                        dve_g.did(dve.tensor_tensor(v, v, g, ALU.mult), f"b{b}")
                    dve_g.after(dve, i, "b2")
                    step("s1", dve.tensor_tensor(oc[tr, 0, :], oc[tr, 0, :], oc[tr, 1, :], ALU.add))
                    step("s2", dve.tensor_tensor(cat[tr, 640:1024], oc[tr, 0, :], oc[tr, 2, :], ALU.add))

                rows = lambda i, T: x1[0:T, bass.ds(i, 1), :].rearrange("p o n -> p (o n)")

                def transposed(i, T):
                    pe_s.after(dve, i, "catT")
                    dve_c.did(dve.tensor_copy(catT[:, 4:8, 0:T], tp[:, 4:8, 0:T]), "catT")

                def residual(i, T):
                    pe_s.after(dve, i, "wo")
                    x_in.wait(dve, i, 16)
                    dve_s.did(dve.tensor_tensor(rows(i, T), acc[0:T, :], x[0:T, :], ALU.add), "x1")

                def norm(i, T):
                    tr = slice(0, T)
                    act_s.after(dve, i, "sq")
                    dve_s.did(dve.tensor_scalar(st[tr, 1:2], st[tr, 0:1], 1.0 / D, EPS, ALU.mult, ALU.add), "ms")
                    pool_s.after(dve, i, "rs")
                    h2_out.wait(dve, i)
                    pe_r.after(dve, i - 1, "h2T")
                    dve_s.did(dve.scalar_tensor_tensor(out=h2[tr, :], in0=rows(i, T), scalar=st[tr, 2:3],
                                                       in1=gain[tr, :], op0=ALU.mult, op1=ALU.mult), "h2")

                def router(i, T):
                    tr = slice(0, T)
                    pe_r.after(dve, i, "h2T")
                    pe_r.after(dve, i - 1, "rout")
                    dve_r.did(dve.tensor_copy(h2T[:, 4:8, tr], tp[:, 4:8, tr]), "h2T")
                    pe_r.after(dve, i, "rout")
                    dve_r.did(dve.tensor_tensor(L[tr, bass.ds(i, 1), :].rearrange("p o n -> p (o n)"),
                                                hTp[tr, 0:20], rb[tr, :], ALU.add), "rout")

                def tile(i, T, T_next):
                    residual(i - 1, P)
                    transposed(i, T)
                    norm(i - 1, P)
                    if T_next:
                        gates(i + 1, T_next)
                    router(i - 1, P)

                gates(0, P)
                transposed(0, P)
                gates(1, P)
                with dve.Fori(1, PT - 1) as i:
                    tile(i, P, P)
                tile(PT - 1, P, N_DEC)
                tile(PT, N_DEC, 0)
                residual(PT, N_DEC)
                norm(PT, N_DEC)
                router(PT, N_DEC)
                dve_r.after(dve, PT, "rout")

                done = 0

                def step(ins):
                    nonlocal done
                    done += 1
                    ins.then_inc(rt_dve, 1)
                    dve.wait_ge(rt_dve, done)

                B4 = [P, N, 4]
                wide = lambda a, shape=B4: a.unsqueeze(2).to_broadcast(shape)

                def first_max(out, v, m):
                    step(dve.tensor_reduce(m[:, :], v, AX.X, ALU.max))
                    step(dve.tensor_tensor(tq4[:, :, :], v, wide(m[:, :]), ALU.is_equal))
                    step(dve.tensor_tensor(tq4[:, :, :], tq4[:, :, :], pri[:, :].unsqueeze(1).to_broadcast(B4),
                                           ALU.mult))
                    step(dve.tensor_reduce(mm[:, :], tq4[:, :, :], AX.X, ALU.max))
                    step(dve.tensor_tensor(out[:, :, :], tq4[:, :, :], wide(mm[:, :]), ALU.is_equal))

                first_max(og, L[:, :, 0:4], gm)
                step(dve.tensor_tensor(g4[:, :, :], L[:, :, 0:4], wide(gm[:, :]), ALU.subtract))
                assert done == G4_DONE
                le = L[:, :, 4:20].rearrange("p n (g e) -> p n g e", g=4)
                B44 = [P, N, 4, 4]
                v44 = lambda a: a.rearrange("p n (g e) -> p n g e", g=4)
                step(dve.tensor_tensor(v44(t16[:, :, :]), le, og[:, :, :].unsqueeze(3).to_broadcast(B44), ALU.mult))
                step(dve.tensor_reduce(es[:, :, :], t16[:, :, :].rearrange("p n (g e) -> p n e g", g=4),
                                       AX.X, ALU.add))
                first_max(o1, es[:, :, :], m1)
                step(dve.scalar_tensor_tensor(out=es[:, :, :], in0=o1[:, :, :], scalar=NEG, in1=es[:, :, :],
                                              op0=ALU.mult, op1=ALU.add))
                first_max(o2, es[:, :, :], m2)
                step(dve.tensor_tensor(pd[:, :], m2[:, :], m1[:, :], ALU.subtract))
                assert done == PD_DONE
                for k, o in enumerate((o1, o2)):
                    step(dve.tensor_tensor(v44(O[:, k, :, :]), og[:, :, :].unsqueeze(3).to_broadcast(B44),
                                           o[:, :, :].unsqueeze(2).to_broadcast(B44), ALU.mult))
                step(dve.tensor_tensor(A[:, :, :], O[:, 0, :, :], O[:, 1, :, :], ALU.add))
                step(dve.memset(A[N_DEC:P, PT:TILES, :], 0.0))
                assert done == A_DONE
                dve.wait_ge(rt_act, 2)
                step(dve.tensor_reduce(gs[:, :], g4[:, :, :], AX.X, ALU.add))
                step(dve.tensor_scalar(pd[:, :], ee[:, :], 1.0, None, ALU.add))
                step(dve.tensor_tensor(gs[:, :], gs[:, :], pd[:, :], ALU.mult))
                step(dve.reciprocal(wt[:, 0, :], gs[:, :]))
                step(dve.tensor_tensor(wt[:, 1, :], wt[:, 0, :], ee[:, :], ALU.mult))
                dve.wait_ge(rt_pe, 1)
                step(dve.tensor_copy(tot[:, :, :], hid[0][:, 256:256 + N * NE].rearrange("p (n e) -> p n e", e=NE)))
                step(dve.memset(base[:, 0, :], 0.0))
                for n in range(N):
                    step(dve.tensor_tensor(base[:, n + 1, :], base[:, n, :], tot[:, n, :], ALU.add))
                step(dve.tensor_tensor(rank[:, :, :], hid[0][:, 0:N * NE].rearrange("p (n e) -> p n e", e=NE),
                                       base[:, 0:N, :], ALU.add))
                B9 = [P, NE, N]
                step(dve.tensor_tensor(c9[:, :, :], base[:, N, :].unsqueeze(2).to_broadcast(B9),
                                       thr[:, :].unsqueeze(1).to_broadcast(B9), ALU.is_gt))
                step(dve.tensor_reduce(nsl[:, :], c9[:, :, :], AX.X, ALU.add))
                step(dve.tensor_tensor(c16[:, :, :], before[:, :, :],
                                       nsl[:, :].unsqueeze(1).to_broadcast([P, NE, NE]), ALU.mult))
                step(dve.tensor_reduce(first[:, :], c16[:, :, :], AX.X, ALU.add))
                step(dve.tensor_tensor(nsl[:, :], nsl[:, :], first[:, :], ALU.add))
                BS = [P, SW, NE]
                step(dve.tensor_tensor(c32[:, :, :], sno[:, :].unsqueeze(2).to_broadcast(BS),
                                       nsl[:, :].unsqueeze(1).to_broadcast(BS), ALU.is_ge))
                step(dve.tensor_reduce(sx[:, :], c32[:, :, :], AX.X, ALU.add))
                step(dve.tensor_copy(sxi[:, SW:SW + NE], nsl[:, :]))
                step(dve.tensor_scalar(sxi[:, 0:SW], sx[:, :], NE - 1.0, None, ALU.min))
                assert done == SX_DONE, done
                for k in range(2):
                    step(dve.tensor_tensor(t16[:, :, :], O[:, k, :, :], rank[:, :, :], ALU.mult))
                    step(dve.tensor_reduce(K[:, k, :], t16[:, :, :], AX.X, ALU.add))
                    step(dve.tensor_tensor(t16[:, :, :], O[:, k, :, :],
                                           first[:, :].unsqueeze(1).to_broadcast([P, N, NE]), ALU.mult))
                    step(dve.tensor_reduce(S[:, k, :], t16[:, :, :], AX.X, ALU.add))
                f2 = lambda a: a[:, :, :].rearrange("p k n -> p (k n)")
                B8 = [P, 2 * N, N - 1]
                step(dve.tensor_tensor(c8[:, :, :], f2(K).unsqueeze(2).to_broadcast(B8),
                                       thr[:, 1:N].unsqueeze(1).to_broadcast(B8), ALU.is_ge))
                step(dve.tensor_reduce(f2(fl), c8[:, :, :], AX.X, ALU.add))
                step(dve.scalar_tensor_tensor(out=f2(r), in0=f2(fl), scalar=-float(P), in1=f2(K),
                                              op0=ALU.mult, op1=ALU.add))
                step(dve.tensor_tensor(f2(S), f2(S), f2(fl), ALU.add))
                step(dve.scalar_tensor_tensor(out=at[:, :], in0=f2(r), scalar=float(SW), in1=f2(S),
                                              op0=ALU.mult, op1=ALU.add))
                step(dve.scalar_tensor_tensor(out=pos[:, :], in0=f2(S), scalar=float(P), in1=f2(r),
                                              op0=ALU.mult, op1=ALU.add))
                assert done == AT_DONE, done

                def transposed(j):
                    ps_xT.wait(dve, j, 1)
                    ps_hid.wait(dve, j)
                    dve.tensor_copy(xT[:, 4:8, :], tp[:, 4:8, :]).then_inc(d_xT.sem, 1)

                def silu(j, s):
                    step = lambda name, ins: (hidden.did(ins, name), hidden.after(dve, j, name))
                    a_exp.wait(dve, j, 1)
                    step("one", dve.tensor_scalar(hs[:, :], hs[:, :], 1.0, None, ALU.add))
                    step("rec", dve.reciprocal(hs[:, :], hs[:, :]))
                    step("sil", dve.tensor_tensor(hs[:, :], hs[:, :], hid[s][:, 0:DE], ALU.mult))
                    ps_hT.wait(dve, j)
                    step("hh", dve.tensor_tensor(hh[:, :], hs[:, :], hid[s][:, DE:2 * DE], ALU.mult))

                def output(j, s, fill):
                    ps_out.wait(dve, j, 1)
                    ys_out[s].wait(dve, fill)
                    dve.tensor_copy(yo[s][:, 512:1024], acc[:, 512:1024]).then_inc(d_out.sem, 1)

                def slot(j, s, fill):
                    transposed(j + 1)
                    silu(j, s)
                    output(j - 1, 1 - s, fill)

                transposed(0)
                transposed(1)
                silu(0, 0)
                with dve.Fori(0, NS - 1) as i:
                    slot(i * 2 + 1, 1, i)
                    slot(i * 2 + 2, 0, i)
                silu(SLOTS - 1, 1)
                output(SLOTS - 2, 0, NS - 1)
                output(SLOTS - 1, 1, NS - 1)

                def weigh(n, s, i, T):
                    tr = slice(0, T)
                    step = lambda name, ins: (y_dve.did(ins, name), y_dve.after(dve, n, name))
                    step("wy", dve.tensor_copy(wy[tr, :], wt[tr, :, bass.ds(n, 1)].rearrange("p k o -> p (k o)")))
                    gy_in[s].wait(dve, i)
                    yt_out[s].wait(dve, i)
                    step("a", dve.scalar_tensor_tensor(out=yt[s][tr, :], in0=gy[s][0][tr, :], scalar=wy[tr, 0:1],
                                                       in1=rows(n, T), op0=ALU.mult, op1=ALU.add))
                    step("b", dve.scalar_tensor_tensor(out=yt[s][tr, :], in0=gy[s][1][tr, :], scalar=wy[tr, 1:2],
                                                       in1=yt[s][tr, :], op0=ALU.mult, op1=ALU.add))

                with dve.Fori(0, PT // 2) as i:
                    weigh(i * 2, 0, i, P)
                    weigh(i * 2 + 1, 1, i, P)
                weigh(PT, 0, PT // 2, N_DEC)


G4_DONE = 6
PD_DONE = G4_DONE + 14
A_DONE = PD_DONE + 4
SX_DONE = A_DONE + 5 + 2 + TILES + 1 + 9
AT_DONE = SX_DONE + 8 + 6


def routing_constants():
    f = lambda a: np.ascontiguousarray(a, np.float32)
    rep = lambda a: f(np.tile(a[None], (P,) + (1,) * a.ndim))
    e = np.arange(NE)
    return {"m_tri": f(np.arange(P)[:, None] < np.arange(P)[None, :]), "m_ones": f(np.ones((P, P))),
            "m_pri": rep(np.array([4, 3, 2, 1])), "m_thr": rep(np.arange(TILES) * P),
            "m_before": rep((e[None, :] < e[:, None]) * 1), "m_sno": rep(np.arange(SW)),
            "m_tid": (np.arange(P)[:, None] + P * np.arange(TILES)[None, :]).astype(np.uint32)}


def multiplicity(dist):
    n = np.zeros(dist.shape, np.float32)
    for window, dil in ((128, 1), (512, 4), (2048, 16)):
        n += (dist >= 0) & (dist <= window) & (dist % dil == 0)
    return n


def additive(n):
    return np.where(n > 0, np.log(np.maximum(n, 1)) / SCALE, NEG).astype(np.float32)


def constants():
    q, x = np.arange(P)[:, None], np.arange(PT * P + 3 * P * 3 + P * 2)[None, :]
    dist = q + (PT + 1) * P - np.arange((2 * PT + 1) * P)[None, :]
    c = np.arange((PT + 1) * 8 + 64)[None, :]
    block = c - 8 * (PT + 1)
    cmp_ok = 16 * block + 31 <= q
    return {
        "ident": np.eye(P, dtype=np.float32),
        "mask_a": additive(multiplicity(dist)),
        "mask_causal": additive(dist >= 0),
        "mask_win": additive((dist >= 0) & (dist <= CWIN)),
        "mask_cmp": additive(cmp_ok),
    }


def sample_constants():
    q, k = np.arange(DEC_S)[:, None], np.arange(PAST + DEC_S)[None, :]
    return {"mask_sa": np.tile(additive(multiplicity(PAST + q - k)), (HA, 1))}


def chunk_tables(T, block):
    u, c = np.arange(T)[:, None], np.arange(T)[None, :]
    same = u // block == c // block
    sums, pairs, m = [], [], block // 2
    while m:
        r = c // (2 * m) * 2 * m + m - 1
        second = c > r
        sums.append(np.where(second, (u > r) & (u <= c), (u > c) & (u <= r)))
        pairs.append((u // (2 * m) == c // (2 * m)) & (u // m % 2 == 0) & (c // m % 2 == 1))
        m //= 2
    sums.append(same & (u <= c))
    pairs.append(u == c)
    return (np.concatenate(sums, 1).astype(np.float32), (same & (u > c)).astype(np.float32),
            np.concatenate(pairs, 1).astype(np.float32))


def recurrence_constants():
    a, b = chunk_tables(P, P), chunk_tables(N_DEC, DEC_S)
    rows = (np.arange(N_DEC)[:, None] // DEC_S == np.arange(DEC_B)[None, :]).astype(np.float32)
    return {"b_sums": a[0], "b_suf": a[1], "b_pair": a[2], "bs_sums": b[0], "bs_suf": b[1],
            "bs_pair": b[2], "bs_rows": rows, "bs_cols": np.tile(rows.T[None], (P, 1, 1))}


def nsa_constants():
    cs, ss = np.arange(NCMP)[:, None] * 16, np.arange(17)[None, :] * 64
    share = np.maximum(np.minimum(cs + 31, ss + 63) - np.maximum(cs, ss) + 1, 0) / 32
    row = np.arange(64)
    g, q = row // 32, row % 8
    rsum = (g[:, None] == g[None, :]) & (q[:, None] == q[None, :]) & (row[:, None] % 32 < 24)
    ones2 = np.kron(np.eye(2), np.ones((HD, HD)))
    f = lambda a: np.ascontiguousarray(a, np.float32)
    return {"share": f(share), "rsum": f(rsum), "ones2": f(ones2), "blk": f(np.tile(np.arange(16), (64, 1))),
            "mask_new": additive(np.arange(8)[None, :] <= q[:, None]),
            "mask_sw": additive(np.arange(CWIN)[None, :] >= q[:, None])}


def tables():
    return {**constants(), **sample_constants(), **recurrence_constants(), **nsa_constants(),
            **routing_constants()}


def build(nc, t):
    rows = lambda n: bass.ds(n * P, P)
    mask = lambda name: lambda n, first, number: t[name][:, bass.ds(n * -P + (PT + 1 + first) * P, number * P)]
    cq = lambda n: t["zr"][rows(n), Z_CQ:Z_CQ + 384]
    branch = lambda b: lambda n: t["oc"][rows(n), b, :, :].rearrange("p h d -> p (h d)")
    units_a = [(h // 2, h % 2, h // 2, h, h) for h in range(HA)]
    units_c = [(r, g, 0, g, g * RC + r) for g in range(GC) for r in range(RC)]
    project(nc, t)
    prompt_attention(nc, t, "a_", lambda n: t["zr"][rows(n), Z_AQ:Z_AQ + 384], t["a_kv"][0:SEQ, 0:384],
                     t["a_kv"][0:SEQ, 384:768], mask("mask_a"), lambda n: t["cat"][rows(n), 0:384],
                     units_a, P, chunk_plan(PT))
    sample_a(nc, t)
    hgrn(nc, t)
    sample_c(nc, t)
    prompt_attention(nc, t, "cc_", cq, t["pc"][0:NCMP, 0:P], t["pc"][0:NCMP, P:2 * P],
                     lambda n, first, number: t["mask_cmp"][:, bass.ds(n * -8 + (PT + 1) * 8, NCMP)],
                     branch(0), units_c, NCMP, (0, 1))
    prompt_attention(nc, t, "cs_", cq, t["c_kv"][0:SEQ, 256:384], t["c_kv"][0:SEQ, 384:512],
                     mask("mask_causal"), branch(1), units_c, P, chunk_plan(PT))
    prompt_attention(nc, t, "cw_", cq, t["c_win"][0:SEQ, 0:P], t["c_win"][0:SEQ, P:2 * P],
                     mask("mask_win"), branch(2), units_c, P, chunk_plan(CWIN // P))
    mix_and_experts(nc, t)


def kernel(x_prompt, x_sample, cache_a_kv, state_b, cache_c_kv, cache_c_win, page_table, **weights):
    import concourse.bacc as bacc
    from concourse.bass_utils import run_bass_kernel_spmd as run

    f = lambda a: np.ascontiguousarray(a)
    x = np.zeros(((TILES + 1) * P, D), np.float32)
    x[:SEQ] = x_prompt[0]
    x[SEQ:N_TOK] = np.reshape(x_sample, (N_DEC, D))
    ins = {"x": x, "cache_a": f(cache_a_kv[0]).reshape(DEC_B, PAST, 768),
           "cache_w": f(cache_c_win[0]).reshape(DEC_B, CWIN, 256),
           "cache_c": f(cache_c_kv[0]).reshape(-1, P, 512),
           "page_table": f(page_table), "state_b": f(state_b[0]), **tables()}
    ins.update({k: f(v) for k, v in weights.items()})
    outs = {"y": (N_TOK, D), "a_kv": (TILES * P, 768), "c_kv": (TILES * P, 512),
            "c_win": (TILES * P, 256), "a_s": (DEC_B, PAST, 768), "w_s": (DEC_B, CWIN, 256),
            "s_p": (HB, HD, HD), "s_s": (DEC_B, HB, HD, HD)}
    scratch = {"zr": ((PT + 2) * P, Z_W), "cat": (N_TOK, D), "oc": (N_TOK, 3, HC, HD), "pc": (HD, 2 * P),
               "h2": (N_TOK, D), "ys": (SLOTS * P, D)}
    tables_of_int = {"tok_at": ((P * SW, 1), U32), "slot_expert": ((1, SW + NE), I32)}
    nc = bacc.Bacc("TRN2", target_bir_lowering=False, num_devices=1)
    t = {}
    for name, a in ins.items():
        t[name] = nc.dram_tensor("in_" + name, a.shape, mybir.dt.from_np(a.dtype), kind="ExternalInput").ap()
    for name, shape in outs.items():
        t[name] = nc.dram_tensor("out_" + name, shape, F32, kind="ExternalOutput").ap()
    for name, shape in scratch.items():
        t[name] = nc.dram_tensor("tmp_" + name, shape, F32, kind="Internal").ap()
    for name, (shape, dt) in tables_of_int.items():
        t[name] = nc.dram_tensor("tmp_" + name, shape, dt, kind="Internal").ap()
    build(nc, t)
    r = run(nc, [{"in_" + k: a for k, a in ins.items()}], core_ids=[0]).results[0]
    o = {k: r["out_" + k] for k in outs}
    kv = lambda a, *s: a.reshape(1, *s)
    return (o["y"][:SEQ].reshape(1, SEQ, D), o["y"][SEQ:N_TOK].reshape(DEC_B, DEC_S, D),
            kv(o["a_kv"][:SEQ], 1, SEQ, 2, HA, HD), kv(o["a_s"], DEC_B, PAST, 2, HA, HD),
            kv(o["s_p"], 1, HB, HD, HD), kv(o["s_s"], DEC_B, HB, HD, HD),
            kv(o["c_kv"][:SEQ], 1, SEQ, 4, GC, HD), kv(o["c_kv"][SEQ:N_TOK], DEC_B, DEC_S, 4, GC, HD),
            kv(o["c_win"][SEQ - CWIN:SEQ], 1, CWIN, 2, GC, HD), kv(o["w_s"], DEC_B, CWIN, 2, GC, HD))
```

```python
from contextlib import ExitStack, contextmanager

import numpy as np
import concourse.bass as bass
from concourse import mybir

F32 = mybir.dt.float32
I32 = mybir.dt.int32
U32 = mybir.dt.uint32
ALU = mybir.AluOpType
ACT = mybir.ActivationFunctionType
AX = mybir.AxisListType

P = 128
D = 1024
KD = D // P
SEQ = 1024
DEC_B, DEC_S = 8, 8
N_DEC = DEC_B * DEC_S
N_TOK = SEQ + N_DEC
PT = SEQ // P
TILES = PT + 1
HD = 64
HA, HB, HC, GC, RC = 6, 4, 6, 2, 3
PAST = 1024
CWIN = 512
NCMP = 63
EPS = 1e-6
NEG = -1e30
TINY = 1e-30
SCALE = HD ** -0.5
NE, DE = 16, 256

AQ, AK, AV, BQ, BF, BV, BG, CQ, CKC, CVC, CKS, CVS, CKW, CVW, CG, D_IN = (
    0, 384, 768, 1152, 1408, 1664, 1920, 2176, 2560, 2688, 2816, 2944, 3072, 3200, 3328, 3346)
Z_AQ, Z_B, Z_CQ, Z_G, Z_W = 0, 384, 1408, 1792, 1810


@contextmanager
def semaphores(nc, stage):
    held = []

    def new(name):
        held.append(nc.alloc_semaphore(stage + name))
        return held[-1]

    yield new
    nc.clear_and_free_semaphores(held)
    nc.all_engine_barrier()


class Count:

    def __init__(self, sem, per=1):
        self.sem, self.per = sem, per

    def open(self, eng):
        eng.sem_inc(self.sem, self.per)

    def at(self, i, n=0):
        return (i + 1) * self.per + n

    def wait(self, eng, i, n=0):
        eng.wait_ge(self.sem, self.at(i, n))


def waits(eng, seen, *pairs):
    for sem, v in pairs:
        eng.wait_ge(sem, v)
        eng.sem_inc(seen, 1)


CHUNKS = [
    (AQ, 384, [(0, 6, 0)]), (AK, 384, [(0, 6, 1)]), (AV, 384, []), (BQ, 512, []), (BV, 512, []),
    (CQ, 384, [(0, 6, 2)]), (CKC, 512, [(256, 2, 3)]), (CKW, 274, [(0, 2, 4)]),
]


def project(nc, t):
    NCH = len(CHUNKS)
    NORMED = [c for c, (_, _, n) in enumerate(CHUNKS) if n]
    with ExitStack() as ctx:
        sb = lambda name, shape, dt=F32: ctx.enter_context(nc.sbuf_tensor("p_" + name, shape, dt))
        ps = lambda name, shape: ctx.enter_context(nc.psum_tensor("p_" + name, shape, F32))
        sem = ctx.enter_context(semaphores(nc, "p_"))
        w = sb("w", [P, KD, D_IN])
        gx = sb("gx", [P, KD])
        gains = sb("gains", [P, 5, HD])
        ident = sb("ident", [P, P])
        x = sb("x", [P, D])
        xn = sb("xn", [P, D])
        sqx = sb("sqx", [P, D])
        hT = sb("hT", [P, KD, P])
        z = sb("z", [P, D_IN])
        sq = sb("sq", [P, 384])
        ssx = sb("ssx", [P, 3])
        ss = sb("ss", [P, 3, 6])
        tp = ps("tp", [P, KD, P])
        acc = [ps(f"acc{n}", [P, 512]) for n in range(4)]
        const_in, seen = sem("const_in"), sem("seen")
        w_in = [sem(f"w_in{c}") for c in range(NCH)]
        x_in, x_sq, x_ms, x_rt, x_rs, xn_ready, xn_read = map(sem, (
            "x_in", "x_sq", "x_ms", "x_rt", "x_rs", "xn_ready", "xn_read"))
        ht_ready, z_ps, z_sq, z_ms, z_rt, z_rs, z_nrm, z_cp, z_dve = map(sem, (
            "ht_ready", "z_ps", "z_sq", "z_ms", "z_rt", "z_rs", "z_nrm", "z_cp", "z_dve"))
        z_out = [sem(f"z_out{c}") for c in range(NCH)]
        copies = []
        for c0, cw, norms in CHUNKS:
            lo, pieces = 0, []
            for o, h, _ in norms:
                if o > lo:
                    pieces.append((lo, o))
                lo = o + h * HD
            if lo < cw:
                pieces.append((lo, cw))
            copies.append(pieces)
        n_cp = [sum(len(p) for p in copies[:c + 1]) for c in range(NCH)]
        n_nm = [sum(c2 <= c for c2 in NORMED) for c in range(NCH)]
        NCP, NNM = n_cp[-1], n_nm[-1]
        xin, xnr, xnd = Count(x_in, 16), Count(xn_ready), Count(xn_read)
        xsq, xms, xrt, xrs = Count(x_sq), Count(x_ms), Count(x_rt), Count(x_rs)
        htr, zps, cp, nm = Count(ht_ready, 2), Count(z_ps, NCH), Count(z_cp, NCP), Count(z_nrm, NNM)
        zsq, zms, zrt, zdv = Count(z_sq, NNM), Count(z_ms, NNM), Count(z_rt, NNM), Count(z_dve, 3 * NNM)
        out = [Count(z_out[c], 32 if c == NCH - 1 else 16) for c in range(NCH)]
        with nc.Block() as block:

            @block.sync
            def _(sp):
                for c in (xin, *out):
                    c.open(sp)
                sp.dma_start(ident[:, :], t["ident"][:, :]).then_inc(const_in, 16)
                sp.dma_start(gx[:, :], t["attn_norm"][0, :].rearrange("(k p) -> p k", p=P),
                             allow_slow_non_contiguous=True).then_inc(const_in, 16)
                for n, g in enumerate((t["a_qnorm"][0], t["a_knorm"][0], t["c_qnorm"][0],
                                       t["c_knorm"][0, 1], t["c_knorm"][0, 2])):
                    sp.dma_start(gains[:, n, :], g.partition_broadcast(P)).then_inc(const_in, 16)
                sp.dma_start(x[:, :], t["x"][0:P, :]).then_inc(x_in, 16)
                for c, (c0, cw, _) in enumerate(CHUNKS):
                    sp.dma_start(w[:, :, c0:c0 + cw],
                                 t["w_in"][0, :, c0:c0 + cw].rearrange("(k p) n -> p k n", p=P)
                                 ).then_inc(w_in[c], 16)
                with sp.Fori(0, TILES) as i:
                    waits(sp, seen, (xn_ready, xnr.at(i, 1)))
                    sp.dma_start(x[:, :], t["x"][bass.ds((i + 1) * P, P), :]).then_inc(x_in, 16)
                    rows = bass.ds(i * P, P)
                    for c, (c0, cw, norms) in enumerate(CHUNKS):
                        waits(sp, seen, *([(z_cp, cp.at(i, n_cp[c]))] if copies[c] else []),
                              *([(z_nrm, nm.at(i, n_nm[c]))] if norms else []))
                        src = z[:, c0:c0 + cw]
                        if c in (0,):
                            dst = t["zr"][rows, Z_AQ:Z_AQ + 384]
                        elif c in (1, 2):
                            dst = t["a_kv"][rows, c0 - AK:c0 - AK + cw]
                        elif c in (3, 4):
                            dst = t["zr"][rows, Z_B + c0 - BQ:Z_B + c0 - BQ + cw]
                        elif c == 5:
                            dst = t["zr"][rows, Z_CQ:Z_CQ + 384]
                        elif c == 6:
                            dst = t["c_kv"][rows, :]
                        else:
                            sp.dma_start(t["c_win"][rows, :], z[:, CKW:CG]).then_inc(z_out[c], 16)
                            src, dst = z[:, CG:D_IN], t["zr"][rows, Z_G:Z_W]
                        sp.dma_start(dst, src).then_inc(z_out[c], 16)
                xin.wait(sp, TILES + 1)
                for c in out:
                    c.wait(sp, TILES)

            @block.tensor
            def _(pe):
                zps.open(pe)
                xnd.open(pe)
                pe.wait_ge(const_in, 16 * 7)
                with pe.Fori(0, TILES) as i:
                    xnr.wait(pe, i, 1)
                    for k in range(KD):
                        last = pe.transpose(tp[:, k, :], xn[:, k * P:(k + 1) * P], ident[:, :])
                    last.then_inc(xn_read, 1)
                    htr.wait(pe, i, 2)
                    for c, (c0, cw, norms) in enumerate(CHUNKS):
                        if c == 0:
                            cp.wait(pe, i)
                            nm.wait(pe, i)
                        if c >= 4:
                            if copies[c - 4]:
                                cp.wait(pe, i, n_cp[c - 4])
                            if CHUNKS[c - 4][2]:
                                nm.wait(pe, i, n_nm[c - 4])
                        pe.wait_ge(w_in[c], 16)
                        for k in range(KD):
                            last = pe.matmul(acc[c % 4][:, 0:cw], hT[:, k, :], w[:, k, c0:c0 + cw],
                                             start=k == 0, stop=k == KD - 1)
                        last.then_inc(z_ps, 1)

            @block.scalar
            def _(act):
                for c in (xsq, xrt, cp, zsq, zrt):
                    c.open(act)

                def norm_x(n):
                    xin.wait(act, n, 16)
                    act.activation(sqx[:, :], x[:, :], ACT.Square, accum_out=ssx[:, 0:1]).then_inc(x_sq, 1)
                    xms.wait(act, n, 1)
                    act.activation(ssx[:, 2:3], ssx[:, 1:2], ACT.Sqrt).then_inc(x_rt, 1)

                norm_x(0)
                with act.Fori(0, TILES) as i:
                    for c, (c0, cw, norms) in enumerate(CHUNKS):
                        zps.wait(act, i, c + 1)
                        out[c].wait(act, i)
                        if norms:
                            (o, h, _), = norms
                            zms.wait(act, i, n_nm[c] - 1)
                            act.activation(sq[:, 0:h * HD], acc[c % 4][:, o:o + h * HD],
                                           ACT.Square).then_inc(z_sq, 1)
                        for lo, hi in copies[c]:
                            act.activation(z[:, c0 + lo:c0 + hi], acc[c % 4][:, lo:hi],
                                           ACT.Copy).then_inc(z_cp, 1)
                        if norms:
                            zms.wait(act, i, n_nm[c])
                            act.activation(ss[:, 2, 0:h], ss[:, 1, 0:h], ACT.Sqrt).then_inc(z_rt, 1)
                        if c == 3:
                            norm_x(i + 1)

            @block.vector
            def _(dve):
                for c in (xms, xrs, xnr, htr, zms, nm, zdv):
                    c.open(dve)

                def norm_x(n):
                    xsq.wait(dve, n, 1)
                    dve.tensor_scalar(ssx[:, 1:2], ssx[:, 0:1], 1.0 / D, EPS, ALU.mult, ALU.add
                                      ).then_inc(x_ms, 1)
                    xrt.wait(dve, n, 1)
                    dve.reciprocal(ssx[:, 2:3], ssx[:, 2:3]).then_inc(x_rs, 1)
                    xrs.wait(dve, n, 1)
                    xnd.wait(dve, n)
                    dve.tensor_scalar(xn[:, :], x[:, :], ssx[:, 2:3], None, ALU.mult
                                      ).then_inc(xn_ready, 1)

                dve.wait_ge(const_in, 16 * 7)
                norm_x(0)
                with dve.Fori(0, TILES) as i:
                    xnd.wait(dve, i, 1)
                    zps.wait(dve, i)
                    for b in range(2):
                        ks = slice(4 * b, 4 * b + 4)
                        dve.tensor_tensor(hT[:, ks, :], tp[:, ks, :],
                                          gx[:, ks].unsqueeze(2).to_broadcast([P, 4, P]),
                                          ALU.mult).then_inc(ht_ready, 1)
                    for c, (c0, cw, norms) in enumerate(CHUNKS):
                        if norms:
                            (o, h, g), = norms
                            m = n_nm[c]
                            zsq.wait(dve, i, m)
                            dve.tensor_reduce(ss[:, 0, 0:h],
                                              sq[:, 0:h * HD].rearrange("p (h d) -> p h d", d=HD),
                                              AX.X, ALU.add).then_inc(z_dve, 1)
                            zdv.wait(dve, i, 3 * m - 2)
                            zrt.wait(dve, i, m - 1)
                            dve.tensor_scalar(ss[:, 1, 0:h], ss[:, 0, 0:h], 1.0 / HD, EPS,
                                              ALU.mult, ALU.add).then_inc(z_ms, 1)
                            zrt.wait(dve, i, m)
                            dve.reciprocal(ss[:, 0, 0:h], ss[:, 2, 0:h]).then_inc(z_dve, 1)
                            zdv.wait(dve, i, 3 * m - 1)
                            out[c].wait(dve, i)
                            src = acc[c % 4][:, o:o + h * HD]
                            dst = z[:, c0 + o:c0 + o + h * HD]
                            if c0 == CQ:
                                src = src.rearrange("p (g r d) -> p g r d", g=GC, r=RC)
                                dst = dst.rearrange("p (r g d) -> p g r d", g=GC, r=RC)
                                rs = ss[:, 0, 0:h].rearrange("p (g r) -> p g r", g=GC).unsqueeze(3
                                    ).to_broadcast([P, GC, RC, HD])
                            else:
                                src = src.rearrange("p (h d) -> p h d", d=HD)
                                dst = dst.rearrange("p (h d) -> p h d", d=HD)
                                rs = ss[:, 0, 0:h].unsqueeze(2).to_broadcast([P, h, HD])
                            dve.tensor_tensor(dst, src, rs, ALU.mult).then_inc(z_dve, 1)
                            zdv.wait(dve, i, 3 * m)
                            dst = z[:, c0 + o:c0 + o + h * HD].rearrange("p (h d) -> p h d", d=HD)
                            gain = gains[:, g, :].unsqueeze(1).to_broadcast([P, h, HD])
                            dve.tensor_tensor(dst, dst, gain, ALU.mult).then_inc(z_nrm, 1)
                        if c == 3:
                            norm_x(i + 1)


class Steps(Count):

    def __init__(self, sem, names):
        self.names = names.split()
        super().__init__(sem, len(self.names))
        self.next = 0

    def did(self, ins, name):
        assert self.names[self.next % self.per] == name, (name, self.names[self.next % self.per])
        self.next += 1
        ins.then_inc(self.sem, 1)

    def after(self, eng, i, name):
        eng.wait_ge(self.sem, self.at(i, self.names.index(name) + 1))


LN_TINY = float(np.log(np.float32(TINY)))


def hgrn(nc, t):
    LV = 7
    with ExitStack() as ctx:
        sb = lambda name, shape, dt=F32: ctx.enter_context(nc.sbuf_tensor("b_" + name, shape, dt))
        ps = lambda name, shape: ctx.enter_context(nc.psum_tensor("b_" + name, shape, F32))
        sem = ctx.enter_context(semaphores(nc, "b_"))
        ident = sb("ident", [P, P])
        sums_m = sb("sums_m", [P, (LV + 1) * P])
        suf_m = sb("suf_m", [P, P])
        pair_m = sb("pair_m", [P, (LV + 1) * P])
        sums_s = sb("sums_s", [N_DEC, 4 * N_DEC])
        suf_s = sb("suf_s", [N_DEC, N_DEC])
        pair_s = sb("pair_s", [N_DEC, 4 * N_DEC])
        rows_s = sb("rows_s", [N_DEC, DEC_B])
        cols_s = sb("cols_s", [P, DEC_B, N_DEC])
        gain = sb("gain", [P, HD])
        zb = [sb(f"zb{s}", [P, 1024]) for s in range(2)]
        z_q, z_f, z_v, z_g = ([z[:, n * 256:(n + 1) * 256] for z in zb] for n in range(4))
        az, tt, ln1, r1, km, kk, lf = (sb(n, [P, 256]) for n in ("az", "tt", "ln1", "r1", "km", "kk", "lf"))
        qkT = [sb(f"qkT{s}", [P, 4, P]) for s in range(2)]
        e = [[sb(f"e{s}{p}", [P, (LV + 1) * P]) for p in range(2)] for s in range(2)]
        x = [[sb(f"x{s}{p}", [P, (LV + 1) * P]) for p in range(2)] for s in range(2)]
        esuf, kdec = sb("esuf", [P, 256]), [sb(f"kdec{s}", [P, 256]) for s in range(2)]
        w = sb("w", [P, (LV + 1) * P])
        at = sb("at", [P, HB, P])
        state = sb("state", [P, HB, HD])
        eg, g1, sil = sb("eg", [P, 256]), sb("g1", [P, 256]), sb("sil", [P, 256])
        oc, sq, ob = sb("oc", [P, 256]), sb("sq", [P, 256]), sb("ob", [P, 256])
        st = sb("st", [P, 4, HB])
        half = sb("half", [P, HB])
        s0 = sb("s0", [P, HB, DEC_B, HD])
        s1 = sb("s1", [P, 2, DEC_B, HD])
        qm = sb("qm", [P, 2, DEC_B, N_DEC])
        vm = sb("vm", [N_DEC, HB, DEC_B, HD])
        tq, sfx = ps("tq", [P, 512]), ps("sfx", [P, 512])
        op, stp = ps("op", [P, 512]), ps("stp", [P, 512])
        sm, sc = ps("sm", [P, 1024]), ps("sc", [P, 1024])
        const_in, seen, zeroed, s_stored = map(sem, ("const_in", "seen", "zeroed", "s_stored"))
        z_in, ob_out = [Count(sem(f"z_in{s}"), 16) for s in range(2)], Count(sem("ob_out"), 16)
        act_a, act_b = Steps(sem("act_a"), "abs exp ln qkT suf sums0 sums1"), Steps(sem("act_b"), "gate")
        pe_a, pe_b = Steps(sem("pe_a"), "qT kT suf sums0 sums1"), Steps(sem("pe_b"), "sc0 sc1 sc2 sc3 out state")
        dve_a = Steps(sem("dve_a"), "one rec pick k min lf kdec x0 x1")
        dve_b = Steps(sem("dve_b"), "w0 at0 w1 at1 w2 at2 w3 at3 g1 g2 g3 g4 state oc sq ss ms on ob")
        by_pool = Steps(sem("by_pool"), "rsqrt")
        fin = {n: sem("fin_" + n) for n in ("qm", "vm", "dec", "s1")}

        with nc.Block() as block:

            @block.sync
            def _(sp):
                z_in[0].open(sp)
                z_in[1].open(sp)
                ob_out.open(sp)
                for a, b in ((ident, "ident"), (sums_m, "b_sums"), (suf_m, "b_suf"), (pair_m, "b_pair"),
                             (sums_s, "bs_sums"), (suf_s, "bs_suf"), (pair_s, "bs_pair"), (rows_s, "bs_rows")):
                    sp.dma_start(a[:, :], t[b][:, :]).then_inc(const_in, 16)
                sp.dma_start(cols_s[:, :, :], t["bs_cols"][:, :, :]).then_inc(const_in, 16)
                sp.dma_start(gain[:, :], t["b_onorm"][0].partition_broadcast(P)).then_inc(const_in, 16)
                sp.wait_ge(zeroed, 3)
                for h in range(HB):
                    r = slice(HD * (h % 2), HD * (h % 2) + HD)
                    sp.dma_start(s0[r, h, :, :], t["state_b"][:, h, :, :].rearrange("b c v -> c b v")
                                 ).then_inc(const_in, 16)

                def load(j, s):
                    sp.dma_start(zb[s][:, :], t["zr"][bass.ds(j * P, P), Z_B:Z_B + 1024]).then_inc(z_in[s].sem, 16)

                def tile(j, s, more=True):
                    waits(sp, seen, (dve_b.sem, dve_b.at(j, dve_b.names.index("state") + 1)))
                    if more:
                        load(j + 2, s)
                    waits(sp, seen, (dve_b.sem, dve_b.at(j, dve_b.per)))
                    sp.dma_start(t["cat"][bass.ds(j * P, P), 384:640], ob[:, :]).then_inc(ob_out.sem, 16)

                load(0, 0)
                load(1, 1)
                with sp.Fori(0, PT // 2 - 1) as i:
                    for s in range(2):
                        tile(i * 2 + s, s)
                tile(PT - 2, 0)
                tile(PT - 1, 1, more=False)
                for h in range(HB):
                    sp.dma_start(t["s_p"][h, :, :], state[HD * (h % 2):HD * (h % 2) + HD, h, :]
                                 ).then_inc(s_stored, 16)
                dve_b.after(sp, PT, "ob")
                sp.dma_start(t["cat"][SEQ:N_TOK, 384:640], ob[0:N_DEC, :]).then_inc(ob_out.sem, 16)
                sp.wait_ge(fin["s1"], 6)
                for p in range(2):
                    sp.dma_start(t["s_s"][:, 2 * p:2 * p + 2, :, :].rearrange("b j c v -> (j c) b v"),
                                 s1[:, p, :, :]).then_inc(s_stored, 16)
                sp.wait_ge(s_stored, 16 * 6)
                ob_out.wait(sp, PT + 1)

            def rows(sample):
                return (N_DEC, 3) if sample else (P, LV)

            def tiles(eng, first, both, last):
                first()
                with eng.Fori(0, PT // 2 - 1) as i:
                    both(i * 2, 0, i, False)
                    both(i * 2 + 1, 1, i + 1, False)
                both(PT - 2, 0, PT // 2 - 1, False)
                both(PT - 1, 1, PT // 2, True)
                last()

            @block.tensor
            def _(pe):
                pe_a.open(pe)
                pe_b.open(pe)
                pe.wait_ge(const_in, 16 * 14)

                def queries(j, s, f, sample):
                    T, _ = rows(sample)
                    z_in[s].wait(pe, f, 16)
                    act_a.after(pe, j - 1, "qkT")
                    for p in range(2):
                        last = pe.transpose(tq[:, p * T:(p + 1) * T], z_q[s][0:T, p * P:(p + 1) * P], ident[0:T, 0:T])
                    pe_a.did(last, "qT")

                def keys(j, s, sample):
                    T, _ = rows(sample)
                    dve_a.after(pe, j, "k")
                    for p in range(2):
                        last = pe.transpose(tq[:, (2 + p) * T:(3 + p) * T], kk[0:T, p * P:(p + 1) * P],
                                            ident[0:T, 0:T])
                    pe_a.did(last, "kT")

                def suffix(j, s, sample):
                    T, _ = rows(sample)
                    dve_a.after(pe, j, "lf")
                    act_a.after(pe, j - 1, "suf")
                    pe_a.did(pe.matmul(sfx[0:T, 0:256], (suf_s if sample else suf_m)[:, :], lf[0:T, :],
                                       start=True, stop=True), "suf")

                def sums(j, p, sample):
                    T, L = rows(sample)
                    act_a.after(pe, j if p else j - 1, "sums0" if p else "sums1")
                    for lo in range(0, T * (L + 1), 512):
                        hi = min(lo + 512, T * (L + 1))
                        last = pe.matmul(sm[:, lo:hi], lf[0:T, p * P:(p + 1) * P],
                                         (sums_s if sample else sums_m)[:, lo:hi], start=True, stop=True)
                    pe_a.did(last, f"sums{p}")

                def scores(j, s, h, sample=False):
                    T, L = rows(sample)
                    p, r = h // 2, slice(HD * (h % 2), HD * (h % 2) + HD)
                    dve_a.after(pe, j, f"x{p}")
                    act_a.after(pe, j, "qkT")
                    dve_b.after(pe, j if h else j - 1, f"w{(h - 1) % 4}")
                    for n in range(L):
                        c = slice(n * T, n * T + T)
                        pe.matmul(sc[0:T, c], x[s][p][r, c], x[s][p][r, c], start=True, stop=True)
                    pe_b.did(pe.matmul(sc[0:T, L * T:T * (L + 1)], qkT[s][r, 2 + p, 0:T], qkT[s][r, p, 0:T],
                                       start=True, stop=True), f"sc{h}")

                def results(j, s, sample=False):
                    T, L = rows(sample)
                    TP = T * (L + 1)
                    dve_b.after(pe, j - 1, "oc")
                    if sample:
                        pe.wait_ge(fin["qm"], 2)
                    else:
                        dve_b.after(pe, j - 1, "state")
                        pe.wait_ge(zeroed, 3)
                    for h in range(HB):
                        p, r = h // 2, slice(HD * (h % 2), HD * (h % 2) + HD)
                        dve_b.after(pe, j, f"at{h}")
                        dst = op[0:T, h * HD:(h + 1) * HD]
                        last = pe.matmul(dst, at[0:T, h, 0:T], z_v[s][0:T, h * HD:(h + 1) * HD],
                                         start=True, stop=False)
                        if sample:
                            for b in range(DEC_B):
                                last = pe.matmul(dst, qm[:, p, b, :], s0[:, h, b, :], start=False,
                                                 stop=b == DEC_B - 1)
                        else:
                            last = pe.matmul(dst, x[s][p][:, L * T:TP], state[:, h, :], start=False, stop=True)
                    pe_b.did(last, "out")
                    dve_a.after(pe, j, "kdec")
                    if sample:
                        pe.wait_ge(fin["vm"], 4)
                        act_a.after(pe, j, "sums1")
                        for h in range(HB):
                            p, r = h // 2, slice(HD * (h % 2), HD * (h % 2) + HD)
                            last = pe.matmul(sm[r, p * 512:(p + 1) * 512], kdec[s][0:T, h * HD:(h + 1) * HD],
                                             vm[:, h, :, :].rearrange("s b v -> s (b v)"), start=True, stop=True)
                    else:
                        dve_b.after(pe, j - 1, "state")
                        for h in range(HB):
                            p, r = h // 2, slice(HD * (h % 2), HD * (h % 2) + HD)
                            last = pe.matmul(stp[r, p * HD:(p + 1) * HD], kdec[s][:, h * HD:(h + 1) * HD],
                                             z_v[s][:, h * HD:(h + 1) * HD], start=True, stop=True)
                    pe_b.did(last, "state")

                def first():
                    queries(0, 0, 0, False)
                    keys(0, 0, False)
                    suffix(0, 0, False)
                    sums(0, 0, False)
                    sums(0, 1, False)

                def both(j, s, f, sample):
                    scores(j, s, 0)
                    queries(j + 1, 1 - s, f, sample)
                    scores(j, s, 1)
                    keys(j + 1, 1 - s, sample)
                    suffix(j + 1, 1 - s, sample)
                    sums(j + 1, 0, sample)
                    scores(j, s, 2)
                    sums(j + 1, 1, sample)
                    scores(j, s, 3)
                    results(j, s)

                def last():
                    for h in range(HB):
                        scores(PT, 0, h, True)
                    results(PT, 0, True)

                tiles(pe, first, both, last)

            @block.scalar
            def _(act):
                act_a.open(act)
                act_b.open(act)

                def part_a(j, s, f, sample=False, gate=None):
                    T, L = rows(sample)
                    old = not isinstance(j, int) or j >= 2
                    z_in[s].wait(act, f, 16)
                    act_a.did(act.activation(az[0:T, :], z_f[s][0:T, :], ACT.Abs), "abs")
                    act_a.after(act, j, "abs")
                    dve_a.after(act, j - 1, "lf")
                    act_a.did(act.activation(tt[0:T, :], az[0:T, :], ACT.Exp, scale=-1.0), "exp")
                    if gate:
                        gate()
                    act_a.after(act, j, "exp")
                    act_a.did(act.activation(ln1[0:T, :], tt[0:T, :], ACT.Ln, bias=1.0), "ln")
                    pe_a.after(act, j, "kT")
                    if old:
                        pe_b.after(act, j - 2, "sc3")
                    act_a.did(act.activation(qkT[s][:, :, 0:T], tq[:, 0:4 * T].rearrange("p (n t) -> p n t", t=T),
                                             ACT.Copy), "qkT")
                    pe_a.after(act, j, "suf")
                    dve_a.after(act, j - 1, "kdec")
                    act_a.did(act.activation(esuf[0:T, :], sfx[0:T, 0:256], ACT.Exp), "suf")
                    for p in range(2):
                        pe_a.after(act, j, f"sums{p}")
                        if old:
                            dve_b.after(act, j - 2, "state")
                        act_a.did(act.activation(e[s][p][:, 0:T * (L + 1)], sm[:, 0:T * (L + 1)], ACT.Exp), f"sums{p}")

                def gate(j, s, sample=False):
                    T, _ = rows(sample)
                    dve_b.after(act, j - 1, "g1")
                    act_b.did(act.activation(eg[0:T, :], z_g[s][0:T, :], ACT.Exp, scale=-1.0), "gate")

                tiles(act, lambda: part_a(0, 0, 0),
                      lambda j, s, f, sample: part_a(j + 1, 1 - s, f, sample, lambda: gate(j, s)),
                      lambda: gate(PT, 0, True))

            @block.gpsimd
            def _(pool):
                by_pool.open(pool)
                pool.memset(state[:, :, :], 0.0).then_inc(zeroed, 1)
                pool.memset(half[:, :], -0.5).then_inc(zeroed, 1)
                pool.memset(s0[:, :, :, :], 0.0).then_inc(zeroed, 1)
                pool.wait_ge(zeroed, 3)

                def tile(i, T):
                    dve_b.after(pool, i, "ms")
                    by_pool.did(pool.tensor_tensor(st[0:T, 2, :], st[0:T, 1, :], half[0:T, :], ALU.pow), "rsqrt")

                with pool.Fori(0, PT) as i:
                    tile(i, P)
                tile(PT, N_DEC)

            @block.vector
            def _(dve):
                dve_a.open(dve)
                dve_b.open(dve)
                dve.wait_ge(const_in, 16 * 14)
                dve.wait_ge(zeroed, 3)

                def step_a(j, name, ins):
                    dve_a.did(ins, name)
                    dve_a.after(dve, j, name)

                def step_b(j, name, ins):
                    dve_b.did(ins, name)
                    dve_b.after(dve, j, name)

                def gates(j, s, sample):
                    tr = slice(0, rows(sample)[0])
                    step = lambda name, ins: step_a(j, name, ins)
                    act_a.after(dve, j, "exp")
                    step("one", dve.tensor_scalar(r1[tr, :], tt[tr, :], 1.0, None, ALU.add))
                    step("rec", dve.reciprocal(r1[tr, :], r1[tr, :]))
                    step("pick", dve.scalar_tensor_tensor(out=km[tr, :], in0=z_f[s][tr, :], scalar=0.0,
                                                          in1=tt[tr, :], op0=ALU.is_lt, op1=ALU.max))
                    pe_a.after(dve, j - 1, "sums1")
                    step("k", dve.tensor_tensor(kk[tr, :], km[tr, :], r1[tr, :], ALU.mult))
                    act_a.after(dve, j, "ln")
                    step("min", dve.scalar_tensor_tensor(out=lf[tr, :], in0=z_f[s][tr, :], scalar=0.0,
                                                         in1=ln1[tr, :], op0=ALU.min, op1=ALU.subtract))
                    step("lf", dve.tensor_scalar(lf[tr, :], lf[tr, :], LN_TINY, None, ALU.max))

                def decay(j, s, sample):
                    tr = slice(0, rows(sample)[0])
                    act_a.after(dve, j, "suf")
                    if not isinstance(j, int) or j >= 2:
                        pe_b.after(dve, j - 2, "state")
                    step_a(j, "kdec", dve.tensor_tensor(kdec[s][tr, :], kk[tr, :], esuf[tr, :], ALU.mult))
                    act_a.after(dve, j, "qkT")

                def scale(j, s, p, sample):
                    T, L = rows(sample)
                    tr, TP = slice(0, T), T * (L + 1)
                    act_a.after(dve, j, f"sums{p}")
                    for n in range(L):
                        m = 1 << (L - 1 - n)
                        v = lambda a: a.rearrange("p (b s m) -> p b s m", s=2, m=m)
                        xv, ev = v(x[s][p][:, n * T:n * T + T]), v(e[s][p][:, n * T:n * T + T])
                        for half_, src in ((0, qkT[s][:, 2 + p, tr]), (1, qkT[s][:, p, tr])):
                            dve.tensor_tensor(xv[:, :, half_, :], ev[:, :, half_, :], v(src)[:, :, half_, :], ALU.mult)
                    step_a(j, f"x{p}", dve.tensor_tensor(x[s][p][:, L * T:TP], e[s][p][:, L * T:TP], qkT[s][:, p, tr],
                                                         ALU.mult))
                    if sample:
                        dve.tensor_tensor(qm[:, p, :, :], x[s][p][:, L * T:TP].unsqueeze(1).to_broadcast(
                            [P, DEC_B, N_DEC]), cols_s[:, :, :], ALU.mult).then_inc(fin["qm"], 1)

                def attend(j, h, sample=False):
                    T, L = rows(sample)
                    tr, TP = slice(0, T), T * (L + 1)
                    pe_b.after(dve, j, f"sc{h}")
                    if h == 0:
                        pe_b.after(dve, j - 1, "out")
                    step_b(j, f"w{h}", dve.tensor_tensor(w[tr, 0:TP], sc[tr, 0:TP],
                                                         (pair_s if sample else pair_m)[:, 0:TP], ALU.mult))
                    step_b(j, f"at{h}", dve.tensor_reduce(at[tr, h, 0:T], w[tr, 0:TP].rearrange(
                        "p (n t) -> p t n", t=T), AX.X, ALU.add))

                def finish(j, s, sample=False):
                    T, L = rows(sample)
                    tr, TP = slice(0, T), T * (L + 1)
                    step = lambda name, ins: step_b(j, name, ins)
                    if sample:
                        for h in range(HB):
                            dve.tensor_tensor(vm[:, h, :, :],
                                              z_v[s][tr, h * HD:(h + 1) * HD].unsqueeze(1).to_broadcast([T, DEC_B, HD]),
                                              rows_s[:, :].unsqueeze(2).to_broadcast([T, DEC_B, HD]),
                                              ALU.mult).then_inc(fin["vm"], 1)
                    act_b.after(dve, j, "gate")
                    step("g1", dve.tensor_scalar(g1[tr, :], eg[tr, :], 1.0, None, ALU.add))
                    step("g2", dve.reciprocal(g1[tr, :], g1[tr, :]))
                    step("g3", dve.tensor_tensor(sil[tr, :], z_g[s][tr, :], g1[tr, :], ALU.mult))
                    hv = lambda a: a[tr, :].rearrange("p (h d) -> p h d", d=HD)
                    step("g4", dve.tensor_tensor(hv(sil), hv(sil), gain[tr, :].unsqueeze(1).to_broadcast(
                        [T, HB, HD]), ALU.mult))
                    pe_b.after(dve, j, "state")
                    if sample:
                        for h in range(HB):
                            p, r = h // 2, slice(HD * (h % 2), HD * (h % 2) + HD)
                            last_e = e[s][p][r, L * T:TP].rearrange("p (b q) -> p b q", q=DEC_S)[:, :, DEC_S - 1:DEC_S]
                            dve.tensor_tensor(s1[r, p, :, :], s0[r, h, :, :],
                                              last_e.to_broadcast([HD, DEC_B, HD]), ALU.mult).then_inc(fin["s1"], 1)
                        dve.wait_ge(fin["s1"], 4)
                        for p in range(2):
                            dve.tensor_tensor(s1[:, p, :, :], s1[:, p, :, :],
                                              sm[:, p * 512:(p + 1) * 512].rearrange("p (b v) -> p b v", v=HD),
                                              ALU.add).then_inc(fin["s1"], 1)
                        dve_b.did(dve.memset(st[tr, 3, :], 0.0), "state")
                    else:
                        for h in range(HB):
                            p, r = h // 2, slice(HD * (h % 2), HD * (h % 2) + HD)
                            last = dve.scalar_tensor_tensor(
                                out=state[r, h, :], in0=state[r, h, :], scalar=e[s][p][r, TP - 1:TP],
                                in1=stp[r, p * HD:(p + 1) * HD], op0=ALU.mult, op1=ALU.add)
                        step("state", last)
                    step("oc", dve.tensor_copy(oc[tr, :], op[tr, 0:256]))
                    step("sq", dve.tensor_tensor(sq[tr, :], oc[tr, :], oc[tr, :], ALU.mult))
                    step("ss", dve.tensor_reduce(st[tr, 0, :], hv(sq), AX.X, ALU.add))
                    step("ms", dve.tensor_scalar(st[tr, 1, :], st[tr, 0, :], 1.0 / HD, EPS, ALU.mult, ALU.add))

                def norm(j, sample=False):
                    T, L = rows(sample)
                    tr = slice(0, T)
                    step = lambda name, ins: step_b(j, name, ins)
                    hv = lambda a: a[tr, :].rearrange("p (h d) -> p h d", d=HD)
                    by_pool.after(dve, j, "rsqrt")
                    step("on", dve.tensor_tensor(hv(oc), hv(oc), st[tr, 2, :].unsqueeze(2).to_broadcast(
                        [T, HB, HD]), ALU.mult))
                    ob_out.wait(dve, j)
                    step("ob", dve.tensor_tensor(ob[tr, :], oc[tr, :], sil[tr, :], ALU.mult))

                def first():
                    gates(0, 0, False)
                    decay(0, 0, False)
                    scale(0, 0, 0, False)
                    scale(0, 0, 1, False)

                def both(j, s, f, sample):
                    attend(j, 0)
                    gates(j + 1, 1 - s, sample)
                    attend(j, 1)
                    attend(j, 2)
                    decay(j + 1, 1 - s, sample)
                    scale(j + 1, 1 - s, 0, sample)
                    attend(j, 3)
                    finish(j, s)
                    scale(j + 1, 1 - s, 1, sample)
                    norm(j)

                def last():
                    for h in range(HB):
                        attend(PT, h, True)
                    finish(PT, 0, True)
                    norm(PT, True)

                tiles(dve, first, both, last)


def chunk_plan(back):
    first = [max(0, n - back) for n in range(PT)]
    return [(f, max(2, n + 1 - f)) for n, f in enumerate(first)]


def prompt_attention(nc, t, sets, jobs):
    LAG, AHEAD = 2, 2
    NU = len(jobs[0][4])
    passes = [(job, n) for n in range(PT) for job in jobs]
    IT = len(passes) // 2
    W = P * max(c for job in jobs for _, c in job[5])
    G = 2
    U = 2 * NU
    FILLS = 2 + U * G
    assert FILLS % 2 == 0 and len(passes) % 2 == 0

    def group(n, g):
        first = -(-n // G)
        return (0, first) if g == 0 else (first, n)

    def shape(i, s):
        job, n = passes[2 * i + s]
        first, number = job[5][n]
        return job[0], first, number, sets[job[0]][2]

    def run(step):
        us = [(i, u) for i in range(IT) for u in range(U)]
        get = lambda x: us[x] if 0 <= x < len(us) else None
        for x in range(len(us) + LAG + 2):
            step(get(x), get(x - LAG), get(x - LAG - 1), get(x - LAG - 2))

    with ExitStack() as ctx:
        sb = lambda name, shape, dt=F32: ctx.enter_context(nc.sbuf_tensor("pa_" + name, shape, dt))
        ps = lambda name, shape: ctx.enter_context(nc.psum_tensor("pa_" + name, shape, F32))
        sem = ctx.enter_context(semaphores(nc, "pa_"))
        ident = sb("ident", [P, P])
        k = [sb(f"k{x}", [P, ks.shape[0] // C, ks.shape[1]]) for x, (ks, _, C) in enumerate(sets)]
        v = [sb(f"v{x}", [P, vs.shape[0] // C, vs.shape[1]]) for x, (_, vs, C) in enumerate(sets)]
        kT = [sb(f"kT{x}", [P, ks.shape[1] // P, ks.shape[0]]) for x, (ks, _, C) in enumerate(sets)]
        kfill = [(x, kp, c, min(c + 4, ks.shape[0] // C)) for x, (ks, _, C) in enumerate(sets)
                 for kp in range(ks.shape[1] // P) for c in range(0, ks.shape[0] // C, 4)]
        q = [sb(f"q{s}", [P, 384]) for s in range(2)]
        qT = [sb(f"qT{s}", [P, 2, 3, P]) for s in range(2)]
        mask = [sb(f"mask{s}", [P, W]) for s in range(2)]
        p = [sb(f"p{s}", [P, W]) for s in range(3)]
        pT = [sb(f"pT{s}", [P, W // P, P]) for s in range(2)]
        mx = sb("mx", [P, U])
        nb = sb("nb", [P, U])
        l = sb("l", [P, U])
        rl = sb("rl", [P, 3, U])
        o = [sb(f"o{s}", [P, NU, HD]) for s in range(2)]
        sc = [ps(f"sc{s}", [P, 1024]) for s in range(2)]
        tp = [ps(f"tp{s}", [P, 4, P]) for s in range(2)]
        op = [ps(f"op{s}", [P, 512]) for s in range(2)]
        const_in, k_tp, k_ev_a, k_ev_d, shifted = map(sem, ("const_in", "k_tp", "k_ev_a", "k_ev_d", "shifted"))
        seen, settled = sem("seen"), sem("settled")
        kv_in = [sem(f"kv_in{x}") for x in range(len(sets))]
        zeroed = sem("zeroed")
        q_in = [Count(sem(f"q_in{s}"), 16) for s in range(2)]
        mask_in = [Count(sem(f"mask_in{s}"), 16) for s in range(2)]
        o_out = [Count(sem(f"o_out{s}"), 16) for s in range(2)]
        scored = Count(sem("scored"), U)
        masked = Count(sem("masked"), U)
        bias = Count(sem("bias"), U)
        exped = Count(sem("exped"), U)
        filled = Count(sem("filled"), FILLS)
        ev_a = Count(sem("ev_a"), 2 + U)
        ev_d = Count(sem("ev_d"), U)
        summed = Count(sem("summed"), U)
        rec = Count(sem("rec"), 6)
        done = Count(sem("done"), 2)

        Q1, Q2 = NU - AHEAD - LAG, U - AHEAD - LAG

        def before(u):
            return (u >= Q1) + (u >= Q2)

        def fill_at(u, g=0):
            return u * G + before(u) + g

        fill_q = (Q1 * G, Q2 * G + 1)
        a_no = lambda u: u + 1 + before(u)
        a_q = (Q1 + 1, Q2 + 2)
        takers = {}
        for s in range(2):
            takers[fill_q[s]] = (ev_a, a_q[s])
        for u in range(U):
            takers[fill_at(u)] = (ev_a, a_no(u))
            takers[fill_at(u, 1)] = (ev_d, u + 1)

        def taken(eng, i, f):
            f -= 2
            if f < 0:
                i, f = i - 1, f + FILLS
            who, n = takers[f]
            who.wait(eng, i, n)

        def key_bank(n):
            x, kp, lo, hi = kfill[n]
            C = sets[x][2]
            return (kT[x][:, kp, lo * C:hi * C].rearrange("p (c k) -> p c k", k=C), tp[n % 2][:, 0:hi - lo, 0:C])

        with nc.Block() as block:

            @block.sync
            def _(sp):
                for c in (*q_in, *mask_in, *o_out):
                    c.open(sp)
                sp.dma_start(ident[:, :], t["ident"][:, :]).then_inc(const_in, 16)
                for x, (ks, vs, C) in enumerate(sets):
                    for dst, src in ((k[x], ks), (v[x], vs)):
                        sp.dma_start(dst[0:C, :, :], src.rearrange("(c p) n -> p c n", p=C)).then_inc(kv_in[x], 16)

                def load_queries(x):
                    if x < len(passes):
                        job, n = passes[x]
                        sp.dma_start(q[x % 2][:, :], job[1](n)).then_inc(q_in[x % 2].sem, 16)

                def load_mask(x):
                    if x < len(passes):
                        job, n = passes[x]
                        w = job[5][n][1] * sets[job[0]][2]
                        sp.dma_start(mask[x % 2][:, 0:w], job[2](n, *job[5][n])).then_inc(mask_in[x % 2].sem, 16)

                def store(x):
                    job, n = passes[x]
                    sp.dma_start(job[3](n), o[x % 2][:, :, :].rearrange("p h d -> p (h d)")
                                 ).then_inc(o_out[x % 2].sem, 16)

                for x in range(2):
                    load_queries(x)
                    load_mask(x)
                sp.wait_ge(k_ev_a, -(-len(kfill) // 2) + 1)
                load_queries(2)
                for i in range(IT):
                    if i > 0:
                        waits(sp, seen, (masked.sem, masked.at(i - 1, U)))
                        load_mask(2 * i + 1)
                    waits(sp, seen, (ev_a.sem, ev_a.at(i, a_q[0])))
                    load_queries(2 * i + 3)
                    if i > 0:
                        waits(sp, seen, (done.sem, done.at(i - 1, 2)))
                        store(2 * i - 1)
                    waits(sp, seen, (masked.sem, masked.at(i, NU)))
                    load_mask(2 * i + 2)
                    waits(sp, seen, (ev_a.sem, ev_a.at(i, a_q[1])))
                    load_queries(2 * i + 4)
                    waits(sp, seen, (done.sem, done.at(i, 1)))
                    store(2 * i)
                waits(sp, seen, (done.sem, done.at(IT - 1, 2)))
                store(2 * IT - 1)
                for s in range(2):
                    o_out[s].wait(sp, IT)

            @block.gpsimd
            def _(pool):
                for s in range(2):
                    for j in range(2):
                        pool.memset(qT[s][HD * (1 - j):HD * (1 - j) + HD, j, :, :], 0.0).then_inc(zeroed, 1)
                for b in range(DEC_B):
                    done.wait(pool, b * IT // DEC_B, 1)
                    pool.dma_start(t["a_s"][b, 0:PAST - DEC_S, :], t["cache_a"][b, DEC_S:PAST, :]).then_inc(shifted, 16)
                    pool.dma_start(t["w_s"][b, 0:CWIN - DEC_S, :], t["cache_w"][b, DEC_S:CWIN, :]).then_inc(shifted, 16)
                pool.wait_ge(shifted, 32 * DEC_B)

            @block.tensor
            def _(pe):
                for c in (scored, filled, summed):
                    c.open(pe)
                pe.wait_ge(const_in, 16)

                def key_bank_read(n):
                    pe.wait_ge(k_ev_d if n % 2 else k_ev_a, n // 2 + 1)

                for n, (x, kp, lo, hi) in enumerate(kfill):
                    C = sets[x][2]
                    if n >= 2:
                        key_bank_read(n - 2)
                    pe.wait_ge(kv_in[x], 32)
                    for c in range(lo, hi):
                        last = pe.transpose(tp[n % 2][:, c - lo, 0:C], k[x][0:C, c, kp * P:(kp + 1) * P],
                                            ident[0:C, 0:C])
                    last.then_inc(k_tp, 1)
                for n in (len(kfill) - 2, len(kfill) - 1):
                    key_bank_read(n)

                def transpose_queries(bank, s):
                    for pr in range(3):
                        last = pe.transpose(bank[:, pr, :], q[s][:, pr * P:(pr + 1) * P], ident[:, :])
                    return last

                q_in[0].wait(pe, 0, 16)
                transpose_queries(tp[0], 0).then_inc(k_tp, 1)
                pe.wait_ge(k_ev_a, -(-len(kfill) // 2) + 1)
                pe.wait_ge(zeroed, 4)

                def queries(i, s):
                    if s or i < IT - 1:
                        q_in[s].wait(pe, i, 16) if s else q_in[s].wait(pe, i + 1, 16)
                    f = fill_q[1 - s]
                    taken(pe, i, f)
                    transpose_queries(tp[f % 2], s).then_inc(filled.sem, 1)

                def scores(i, u):
                    s = u // NU
                    x, k0, n, C = shape(i, s)
                    pr, j, kp, _ = passes[2 * i + s][0][4][u % NU]
                    if u % NU == 0:
                        ev_a.wait(pe, i, a_q[0]) if s else ev_a.wait(pe, i - 1, a_q[1])
                    masked.wait(pe, i, u - 1) if u else masked.wait(pe, i - 1, U - 1)
                    for lo in range(0, n * C, 512):
                        hi = min(lo + 512, n * C)
                        last = pe.matmul(sc[u % 2][:, lo:hi], qT[s][:, j, pr, :], kT[x][:, kp, k0 * C + lo:k0 * C + hi],
                                         start=True, stop=True)
                    last.then_inc(scored.sem, 1)

                def transposes(i, u):
                    _, _, n, C = shape(i, u // NU)
                    exped.wait(pe, i, u + 1)
                    for g in range(G):
                        f = fill_at(u, g)
                        taken(pe, i, f)
                        lo, hi = group(n, g)
                        for c in range(lo, hi):
                            last = pe.transpose(tp[f % 2][0:C, c - lo, :], p[u % 3][:, c * C:(c + 1) * C],
                                                ident[:, :])
                        last.then_inc(filled.sem, 1)

                def values(i, u):
                    x, k0, n, C = shape(i, u // NU)
                    h = u % NU
                    vc = passes[2 * i + u // NU][0][4][h][3]
                    if u % NU == 0:
                        done.wait(pe, i - 1, u // NU + 1)
                    ev_a.wait(pe, i, a_no(u))
                    ev_d.wait(pe, i, u + 1)
                    for c in range(n):
                        last = pe.matmul(op[u // NU][:, h * HD:h * HD + HD], pT[u % 2][0:C, c, :],
                                         v[x][0:C, k0 + c, vc * HD:vc * HD + HD], start=c == 0, stop=c == n - 1)
                    last.then_inc(summed.sem, 1)

                def step(now, lagged, last, past):
                    if now:
                        if now[1] == NU - AHEAD:
                            queries(now[0], 1)
                        if now[1] == U - AHEAD:
                            queries(now[0], 0)
                        scores(*now)
                    if lagged:
                        transposes(*lagged)
                    if last:
                        values(*last)

                run(step)

            @block.scalar
            def _(act):
                for c in (exped, ev_a):
                    c.open(act)
                for n in range(0, len(kfill), 2):
                    act.wait_ge(k_tp, n + 1)
                    act.activation(*key_bank(n), ACT.Copy).then_inc(k_ev_a, 1)
                act.wait_ge(k_tp, len(kfill) + 1)

                def copy_queries(s, bank):
                    for j in range(2):
                        r = slice(HD * j, HD * j + HD)
                        last = act.activation(qT[s][r, j, :, :], bank[r, 0:3, :], ACT.Copy)
                    return last

                act.wait_ge(zeroed, 4)
                copy_queries(0, tp[0]).then_inc(k_ev_a, 1)

                def queries(i, s):
                    f = fill_q[1 - s]
                    filled.wait(act, i, f + 1)
                    scored.wait(act, i) if s else scored.wait(act, i, NU)
                    copy_queries(s, tp[f % 2]).then_inc(ev_a.sem, 1)

                def transposed(i, u):
                    _, _, n, C = shape(i, u // NU)
                    f = fill_at(u)
                    filled.wait(act, i, f + 1)
                    summed.wait(act, i, u - 1) if u else summed.wait(act, i - 1, U - 1)
                    _, hi = group(n, 0)
                    act.activation(pT[u % 2][0:C, 0:hi, :], tp[f % 2][0:C, 0:hi, :], ACT.Copy).then_inc(ev_a.sem, 1)

                def exponentials(i, u):
                    _, _, n, C = shape(i, u // NU)
                    bias.wait(act, i, u + 1)
                    pu = p[u % 3][:, 0:n * C]
                    act.activation(pu, pu, ACT.Exp, bias=nb[:, u:u + 1], scale=SCALE,
                                   accum_out=l[:, u:u + 1]).then_inc(exped.sem, 1)

                def step(now, lagged, last, past):
                    if now and now[1] == NU - AHEAD:
                        queries(now[0], 1)
                    if now and now[1] == U - AHEAD:
                        queries(now[0], 0)
                    if lagged:
                        transposed(*lagged)
                    if now:
                        exponentials(*now)

                run(step)

            @block.vector
            def _(dve):
                for c in (masked, bias, ev_d, rec, done):
                    c.open(dve)

                def tile_out(i, s):
                    us = slice(NU * s, NU * s + NU)
                    summed.wait(dve, i, NU * s + NU)
                    dve.tensor_scalar(rl[:, 0, us], l[:, us], TINY, None, ALU.max).then_inc(rec.sem, 1)
                    rec.wait(dve, i, 3 * s + 1)
                    dve.reciprocal(rl[:, 1, us], rl[:, 0, us]).then_inc(rec.sem, 1)
                    rec.wait(dve, i, 3 * s + 2)
                    dve.scalar_tensor_tensor(out=rl[:, 2, us], in0=nb[:, us], scalar=-0.5 * NEG * SCALE,
                                             in1=rl[:, 1, us], op0=ALU.is_lt, op1=ALU.mult
                                             ).then_inc(rec.sem, 1)
                    rec.wait(dve, i, 3 * s + 3)
                    o_out[s].wait(dve, i)
                    dve.tensor_tensor(o[s][:, :, :], op[s][:, 0:NU * HD].rearrange("p (h d) -> p h d", d=HD),
                                      rl[:, 2, us].unsqueeze(2).to_broadcast([P, NU, HD]), ALU.mult
                                      ).then_inc(done.sem, 1)

                for n in range(1, len(kfill), 2):
                    dve.wait_ge(k_tp, n + 1)
                    dve.tensor_copy(*key_bank(n)).then_inc(k_ev_d, 1)

                def mask_scores(i, u):
                    s = u // NU
                    _, _, n, C = shape(i, s)
                    w = n * C
                    if u % NU == 0:
                        mask_in[s].wait(dve, i, 16)
                    scored.wait(dve, i, u + 1)
                    if u >= 3:
                        filled.wait(dve, i, fill_at(u - 3, G - 1) + 1)
                    else:
                        filled.wait(dve, i - 1, fill_at(U + u - 3, G - 1) + 1)
                    if u % NU == 0:
                        done.wait(dve, i - 1, s + 1)
                    dve.sem_inc(settled, 1)
                    dve.tensor_tensor_reduce(p[u % 3][:, 0:w], sc[u % 2][:, 0:w], mask[s][:, 0:w], 1.0,
                                             -3e38, ALU.add, ALU.max, mx[:, u:u + 1]).then_inc(masked.sem, 1)
                    masked.wait(dve, i, u + 1)
                    dve.tensor_scalar(nb[:, u:u + 1], mx[:, u:u + 1], -SCALE, None, ALU.mult).then_inc(bias.sem, 1)

                def transposed(i, u):
                    _, _, n, C = shape(i, u // NU)
                    f = fill_at(u, 1)
                    summed.wait(dve, i, u - 1) if u else summed.wait(dve, i - 1, U - 1)
                    filled.wait(dve, i, f + 1)
                    lo, hi = group(n, 1)
                    dve.tensor_copy(pT[u % 2][0:C, lo:hi, :], tp[f % 2][0:C, 0:hi - lo, :]).then_inc(ev_d.sem, 1)

                def step(now, lagged, last, past):
                    if now:
                        mask_scores(*now)
                    if lagged:
                        transposed(*lagged)
                    if past and (past[1] + 1) % NU == 0:
                        tile_out(past[0], past[1] // NU)

                run(step)


def sample_a(nc, t):
    NR, NC, NK, B2 = HA * DEC_S, PAST // P, PAST + DEC_S, 2
    FILLS = 16
    with ExitStack() as ctx:
        sb = lambda name, shape, dt=F32: ctx.enter_context(nc.sbuf_tensor("sa_" + name, shape, dt))
        ps = lambda name, shape: ctx.enter_context(nc.psum_tensor("sa_" + name, shape, F32))
        sem = ctx.enter_context(semaphores(nc, "sa_"))
        ident = sb("ident", [P, P])
        mask = sb("mask", [NR, NK])
        q = sb("q", [N_DEC, 384])
        qz = sb("qz", [P, DEC_B, 3, NR])
        kv = [sb(f"kv{s}", [P, NC, 768]) for s in range(B2)]
        new = [sb(f"new{s}", [DEC_S, 768]) for s in range(B2)]
        qs = [sb(f"qs{s}", [P, 3, NR]) for s in range(B2)]
        kT = sb("kT", [P, 3, NK])
        p = [sb(f"p{s}", [NR, NK]) for s in range(B2)]
        pT = [sb(f"pT{s}", [P, NC + 1, NR]) for s in range(B2)]
        st = sb("st", [NR, B2, 4])
        o = [sb(f"o{s}", [DEC_S, 384]) for s in range(B2)]
        sc = ps("sc", [P, 3 * 512])
        tp = [ps(f"tp{s}", [P, 512]) for s in range(2)]
        op = [ps(f"op{s}", [P, 512]) for s in range(2)]
        const_in, seen, settled, q_tp, q_zero, q_ev = map(sem, ("const_in", "seen", "settled", "q_tp", "q_zero", "q_ev"))
        k_in, v_in = ([Count(sem(f"{n}_in{s}"), 32) for s in range(B2)] for n in "kv")
        o_out = [Count(sem(f"o_out{s}"), 16) for s in range(B2)]
        filled = Count(sem("filled"), FILLS)
        ev_a, ev_d = Count(sem("ev_a"), 8), Count(sem("ev_d"), 8)
        q_here = Count(sem("q_here"), B2)
        scored, masked, biased = (Count(sem(n), B2) for n in ("scored", "masked", "biased"))
        exped, recip, normed = (Count(sem(n), B2) for n in ("exped", "recip", "normed"))
        summed, done = Count(sem("summed"), B2), Count(sem("done"), B2)

        def take_keys(i, s, parity, eng, copy, ev):
            for n in range(7):
                f = 7 * s + n
                if f % 2 != parity:
                    continue
                filled.wait(eng, i, f + 1)
                if n < 6:
                    ins = copy(kT[:, n // 2, 512 * (n % 2):512 * (n % 2) + 512], tp[f % 2][:, :])
                else:
                    ins = copy(kT[:, :, PAST:NK],
                               tp[f % 2][:, 0:3 * DEC_S].rearrange("p (c k) -> p c k", c=3))
                ins.then_inc(ev.sem, 1)

        def take_exps(i, s, eng, copy, ev):
            f = 14 + s
            filled.wait(eng, i, f + 1)
            summed.wait(eng, i - 1, s + 1)
            copy(pT[s][:, 0:NC, :], tp[f % 2][:, 0:NC * NR].rearrange("p (c r) -> p c r", r=NR))
            copy(pT[s][0:DEC_S, NC, :], tp[f % 2][0:DEC_S, NC * NR:(NC + 1) * NR]).then_inc(ev.sem, 1)

        with nc.Block() as block:

            @block.sync
            def _(sp):
                for c in (*k_in, *v_in, *o_out):
                    c.open(sp)
                sp.dma_start(ident[:, :], t["ident"][:, :]).then_inc(const_in, 16)
                sp.dma_start(mask[:, :], t["mask_sa"][:, :]).then_inc(const_in, 16)
                sp.dma_start(q[:, :], t["zr"][SEQ:N_TOK, Z_AQ:Z_AQ + 384]).then_inc(const_in, 16)

                def load(s, b, half, count):
                    c = slice(384 * half, 384 * half + 384)
                    sp.dma_start(kv[s][:, :, c], t["cache_a"][bass.ds(b, 1), :, c].rearrange(
                        "o (c p) n -> p (o c) n", p=P)).then_inc(count[s].sem, 16)
                    sp.dma_start(new[s][:, c], t["a_kv"][bass.ds(b * DEC_S + SEQ, DEC_S), c]
                                 ).then_inc(count[s].sem, 16)

                for half, count in enumerate((k_in, v_in)):
                    for s in range(B2):
                        load(s, s, half, count)
                with sp.Fori(0, DEC_B // B2) as i:
                    for s in range(B2):
                        waits(sp, seen, (filled.sem, filled.at(i, 7 * s + 7)))
                        load(s, (i * B2 + (B2 + s)) % DEC_B, 0, k_in)
                    for s in range(B2):
                        waits(sp, seen, (summed.sem, summed.at(i, s + 1)))
                        load(s, (i * B2 + (B2 + s)) % DEC_B, 1, v_in)
                        waits(sp, seen, (done.sem, done.at(i, s + 1)))
                        sp.dma_start(t["cat"][bass.ds((i * B2 + s) * DEC_S + SEQ, DEC_S), 0:384],
                                     o[s][:, :]).then_inc(o_out[s].sem, 16)
                for s in range(B2):
                    k_in[s].wait(sp, DEC_B // B2, 32)
                    v_in[s].wait(sp, DEC_B // B2, 32)
                    o_out[s].wait(sp, DEC_B // B2)

            @block.gpsimd
            def _(pool):
                pool.memset(qz[:, :, :, :], 0.0).then_inc(q_zero, 1)

            @block.tensor
            def _(pe):
                for c in (filled, scored, summed):
                    c.open(pe)
                pe.wait_ge(const_in, 48)
                for pr in range(3):
                    last = pe.transpose(tp[0][:, pr * N_DEC:(pr + 1) * N_DEC], q[:, pr * P:(pr + 1) * P],
                                        ident[0:N_DEC, 0:N_DEC])
                last.then_inc(q_tp, 1)
                pe.wait_ge(q_ev, 6)

                def taken(i, f):
                    f -= 2
                    if f < 0:
                        i, f = i - 1, f + FILLS
                    (ev_d if f % 2 else ev_a).wait(pe, i, f // 2 + 1)

                def keys(i, s):
                    k_in[s].wait(pe, i, 32)
                    for n in range(6):
                        f = 7 * s + n
                        taken(i, f)
                        for c in range(4):
                            last = pe.transpose(tp[f % 2][:, c * P:(c + 1) * P],
                                                kv[s][:, 4 * (n % 2) + c, (n // 2) * P:(n // 2 + 1) * P], ident[:, :])
                        last.then_inc(filled.sem, 1)
                    f = 7 * s + 6
                    taken(i, f)
                    pe.sem_inc(settled, 1)
                    for pr in range(3):
                        last = pe.transpose(tp[f % 2][:, pr * DEC_S:(pr + 1) * DEC_S],
                                            new[s][:, pr * P:(pr + 1) * P], ident[0:DEC_S, 0:DEC_S])
                    last.then_inc(filled.sem, 1)

                def scores(i, s):
                    q_here.wait(pe, i, s + 1)
                    ev_a.wait(pe, i, 4 + 3 * s)
                    ev_d.wait(pe, i, 3 + 4 * s)
                    masked.wait(pe, i, s)
                    for lo, hi in ((0, 512), (512, 1024), (1024, NK)):
                        for pr in range(3):
                            last = pe.matmul(sc[0:NR, lo:hi], qs[s][:, pr, :], kT[:, pr, lo:hi],
                                             start=pr == 0, stop=pr == 2)
                    last.then_inc(scored.sem, 1)

                def values(i, s):
                    normed.wait(pe, i, s + 1)
                    f = 14 + s
                    taken(i, f)
                    pe.sem_inc(settled, 1)
                    for c in range(NC + 1):
                        kn = P if c < NC else DEC_S
                        last = pe.transpose(tp[f % 2][0:kn, c * NR:(c + 1) * NR],
                                            p[s][:, c * P:c * P + kn], ident[0:NR, 0:NR])
                    last.then_inc(filled.sem, 1)
                    (ev_d if s else ev_a).wait(pe, i, 8)
                    done.wait(pe, i - 1, s + 1)
                    v_in[s].wait(pe, i, 32)
                    for h in range(HA):
                        vs = slice(384 + h * HD, 384 + h * HD + HD)
                        for c in range(NC + 1):
                            kn = P if c < NC else DEC_S
                            last = pe.matmul(op[s][0:DEC_S, h * HD:(h + 1) * HD],
                                             pT[s][0:kn, c, h * DEC_S:(h + 1) * DEC_S],
                                             kv[s][:, c, vs] if c < NC else new[s][:, vs],
                                             start=c == 0, stop=c == NC)
                    last.then_inc(summed.sem, 1)

                with pe.Fori(0, DEC_B // B2) as i:
                    keys(i, 0)
                    scores(i, 0)
                    keys(i, 1)
                    scores(i, 1)
                    values(i, 0)
                    values(i, 1)

            @block.scalar
            def _(act):
                for c in (ev_a, q_here, exped):
                    c.open(act)
                act.wait_ge(q_zero, 1)
                act.wait_ge(q_tp, 1)
                for h in range(HA):
                    r = slice(HD * (h % 2), HD * (h % 2) + HD)
                    act.activation(qz[r, :, h // 2, h * DEC_S:(h + 1) * DEC_S],
                                   tp[0][r, (h // 2) * N_DEC:(h // 2 + 1) * N_DEC].rearrange(
                                       "p (b q) -> p b q", b=DEC_B), ACT.Copy).then_inc(q_ev, 1)
                act.wait_ge(q_ev, 6)

                copy = lambda out, in_: act.activation(out, in_, ACT.Copy)

                def keys(i, s):
                    scored.wait(act, i, s)
                    act.activation(qs[s][:, :, :], qz[:, bass.ds(i * B2 + s, 1), :, :].rearrange(
                        "p o c r -> p (o c) r"), ACT.Copy).then_inc(q_here.sem, 1)
                    take_keys(i, s, 0, act, copy, ev_a)

                def exps(i, s):
                    biased.wait(act, i, s + 1)
                    act.activation(p[s][:, :], p[s][:, :], ACT.Exp, bias=st[:, s, 1:2], scale=SCALE,
                                   accum_out=st[:, s, 2:3]).then_inc(exped.sem, 1)

                with act.Fori(0, DEC_B // B2) as i:
                    keys(i, 0)
                    exps(i, 0)
                    keys(i, 1)
                    take_exps(i, 0, act, copy, ev_a)
                    exps(i, 1)

            @block.vector
            def _(dve):
                for c in (ev_d, masked, biased, recip, normed, done):
                    c.open(dve)
                dve.wait_ge(const_in, 48)

                def keys(i, s):
                    scored.wait(dve, i, s)
                    take_keys(i, s, 1, dve, dve.tensor_copy, ev_d)

                def softmax(i, s):
                    scored.wait(dve, i, s + 1)
                    filled.wait(dve, i - 1, 15 + s)
                    dve.sem_inc(settled, 1)
                    dve.tensor_tensor_reduce(p[s][:, :], sc[0:NR, 0:NK], mask[:, :], 1.0, -3e38,
                                             ALU.add, ALU.max, st[:, s, 0:1]).then_inc(masked.sem, 1)
                    masked.wait(dve, i, s + 1)
                    dve.tensor_scalar(st[:, s, 1:2], st[:, s, 0:1], -SCALE, None, ALU.mult
                                      ).then_inc(biased.sem, 1)

                def norm(i, s):
                    exped.wait(dve, i, s + 1)
                    dve.reciprocal(st[:, s, 3:4], st[:, s, 2:3]).then_inc(recip.sem, 1)
                    recip.wait(dve, i, s + 1)
                    dve.tensor_scalar(p[s][:, :], p[s][:, :], st[:, s, 3:4], None, ALU.mult
                                      ).then_inc(normed.sem, 1)

                def out(i, s):
                    summed.wait(dve, i, s + 1)
                    o_out[s].wait(dve, i)
                    dve.tensor_copy(o[s][:, :], op[s][0:DEC_S, 0:384]).then_inc(done.sem, 1)

                with dve.Fori(0, DEC_B // B2) as i:
                    keys(i, 0)
                    softmax(i, 0)
                    norm(i, 0)
                    keys(i, 1)
                    softmax(i, 1)
                    norm(i, 1)
                    take_exps(i, 1, dve, dve.tensor_copy, ev_d)
                    out(i, 0)
                    out(i, 1)


def sample_c(nc, t):
    NR, NKS, NKW = 64, PAST + DEC_S, CWIN + DEC_S
    NB = PAST // HD
    with ExitStack() as ctx:
        sb = lambda name, shape, dt=F32: ctx.enter_context(nc.sbuf_tensor("sc_" + name, shape, dt))
        ps = lambda name, shape: ctx.enter_context(nc.psum_tensor("sc_" + name, shape, F32))
        sem = ctx.enter_context(semaphores(nc, "sc_"))
        ident = sb("ident", [P, P])
        wc = sb("wc", [P, 2, 32, P])
        peT = sb("peT", [P, 2, 32])
        peb = sb("peb", [P, 2])
        gain = sb("gain", [P, 1])
        ones = sb("ones", [P, P])
        share = sb("share", [NCMP, NB + 1])
        rsum = sb("rsum", [NR, NR])
        idx = sb("idx", [NR, NB])
        mnew = sb("mnew", [NR, DEC_S])
        mwin = sb("mwin", [NR, CWIN])
        q = sb("q", [N_DEC, 384])
        qz = sb("qz", [P, DEC_B, NR])
        x = [sb(f"x{s}", [P, 4, 1024]) for s in range(2)]
        win = [sb(f"win{s}", [P, 4, 256]) for s in range(2)]
        nkv = [sb(f"nkv{s}", [DEC_S, 512]) for s in range(2)]
        nwin = [sb(f"nwin{s}", [DEC_S, 256]) for s in range(2)]
        qs = sb("qs", [P, NR])
        xT = sb("xT", [P, 4, 512])
        ksT, kwT, knT = sb("ksT", [P, 2, 512]), sb("kwT", [P, CWIN]), sb("knT", [P, 2 * DEC_S])
        kcf, vcf, sqk, msk, rsk, kcT = (sb(n, [P, NCMP]) for n in ("kcf", "vcf", "sqk", "msk", "rsk", "kcT"))
        vc = sb("vc", [NCMP, P])
        kcr = sb("kcr", [HD, 2 * P])
        pc, pcT = sb("pc", [NR, NCMP]), sb("pcT", [NCMP, NR])
        imp = sb("imp", [NR, NB + 1])
        sel = sb("sel", [NR, 64])
        drop = sb("drop", [NR, NB])
        pS, pW = sb("pS", [NR, NKS]), sb("pW", [NR, NKW])
        pTs, pTw = sb("pTs", [P, 8, NR]), sb("pTw", [P, 6, NR])
        st = sb("st", [NR, 3, 4])
        o = [sb(f"o{s}", [NR, 3, HD]) for s in range(2)]
        tp = [ps(f"tp{n}", [P, 512]) for n in range(2)]
        cps, ms = ps("cps", [P, 512]), ps("ms", [P, 512])
        sS, sW, sM = ps("sS", [P, 1024]), ps("sW", [P, 512]), ps("sM", [P, 512])
        const_in, seen, settled, zero, qtp, q_ev, pes, peb_in, pr_out = map(sem, (
            "const_in", "seen", "settled", "zero", "qtp", "q_ev", "pes", "peb_in", "pr_out"))
        x_in = [Count(sem(f"x_in{s}"), 16 * 11) for s in range(2)]
        o_out = [Count(sem(f"o_out{s}"), 16 * 6) for s in range(2)]
        two = lambda names: " ".join(f"{n}.{s}" for s in range(2) for n in names.split())
        by_pe = Steps(sem("by_pe"), two("tc0 tc1 tc2 tc3 tk0 tk1 tw tn comp nrm tv scS scC tpc imp1 imp2 tps tpw sum"))
        by_act = Steps(sem("by_act"), two("q tc0 tc1 tc2 tc3 rt ec es ew tps"))
        by_dve = Steps(sem("by_dve"), two(
            "tk0 tk1 tw tn kcf vcf sqk msk rsk kcT vc mc bc rc pc pcT i1 i2 mn eq mi drop s0 s1 sn mS bS w0 wn mW bW "
            "rS pS rW pW tpw out"))

        with nc.Block() as block:

            @block.sync
            def _(sp):
                for c in (*x_in, *o_out):
                    c.open(sp)
                for a, b in ((ident, "ident"), (ones, "ones2"), (share, "share"), (rsum, "rsum"), (idx, "blk"),
                             (mnew, "mask_new"), (mwin, "mask_sw")):
                    sp.dma_start(a[:, :], t[b][:, :]).then_inc(const_in, 16)
                sp.wait_ge(zero, 3)
                for g in range(2):
                    r = slice(HD * g, HD * g + HD)
                    sp.dma_start(wc[r, :, :, r], t["c_cmp_w"][0].rearrange("k (l r) e -> r k l e", r=HD)
                                 ).then_inc(const_in, 16)
                    sp.dma_start(peT[r, :, :], t["c_cmp_pe"][0].rearrange("k l d -> d k l"),
                                 allow_slow_non_contiguous=True).then_inc(const_in, 16)
                for g in range(2):
                    sp.dma_start(gain[HD * g:HD * g + HD, :], t["c_knorm"][0, 0, :].unsqueeze(1)
                                 ).then_inc(const_in, 16)
                sp.dma_start(q[:, :], t["zr"][SEQ:N_TOK, Z_CQ:Z_CQ + 384]).then_inc(const_in, 16)

                def load(s, b):
                    inc = lambda ins: ins.then_inc(x_in[s].sem, 16)
                    for n in range(8):
                        page = sp.value_load(t["page_table"][bass.ds(b, 1), n:n + 1], min_val=0,
                                             max_val=t["cache_c"].shape[0] - 1)
                        inc(sp.dma_start(x[s][64 * (n % 2):64 * (n % 2) + 64, n // 2, :],
                                         t["cache_c"][bass.ds(page, 1), :, :].rearrange(
                                             "o (a r) n -> (o a) (r n)", r=2)))
                    inc(sp.dma_start(win[s][:, :, :], t["cache_w"][bass.ds(b, 1), :, :].rearrange(
                        "o (c p) n -> p (o c) n", p=P)))
                    inc(sp.dma_start(nkv[s][:, :], t["c_kv"][bass.ds(b * DEC_S + SEQ, DEC_S), :]))
                    inc(sp.dma_start(nwin[s][:, :], t["c_win"][bass.ds(b * DEC_S + SEQ, DEC_S), :]))

                for s in range(2):
                    load(s, s)
                with sp.Fori(0, DEC_B // 2) as i:
                    for s in range(2):
                        waits(sp, seen, (by_dve.sem, by_dve.at(i, by_dve.names.index(f"out.{s}") + 1)))
                        for g in range(2):
                            for r in range(RC):
                                sp.dma_start(t["oc"][bass.ds((i * 2 + s) * DEC_S + SEQ, DEC_S), :, g * RC + r, :],
                                             o[s][32 * g + 8 * r:32 * g + 8 * r + 8, :, :]
                                             ).then_inc(o_out[s].sem, 16)
                        waits(sp, seen, (by_pe.sem, by_pe.at(i, by_pe.names.index(f"sum.{s}") + 1)))
                        load(s, (i * 2 + (2 + s)) % DEC_B)
                for s in range(2):
                    x_in[s].wait(sp, DEC_B // 2, 16 * 11)
                sp.dma_start(x[0][:, :, :], t["c_kv"][0:SEQ, :].rearrange("(c a r) n -> a c (r n)", a=P, r=2)
                             ).then_inc(x_in[0].sem, 16)
                sp.wait_ge(q_ev, 10)
                sp.dma_start(t["pc"][:, :], kcr[:, :]).then_inc(pr_out, 16)
                sp.wait_ge(pr_out, 16)
                for s in range(2):
                    o_out[s].wait(sp, DEC_B // 2)

            @block.gpsimd
            def _(pool):
                pool.memset(qz[:, :, :], 0.0).then_inc(zero, 1)
                pool.memset(kcr[:, :], 0.0).then_inc(zero, 1)
                pool.memset(wc[:, :, :, :], 0.0).then_inc(zero, 1)

            @block.tensor
            def _(pe):
                by_pe.open(pe)
                pe.wait_ge(const_in, 16 * 14)
                for r in range(RC):
                    last = pe.transpose(ms[:, r * N_DEC:(r + 1) * N_DEC], q[:, r * P:(r + 1) * P],
                                        ident[0:N_DEC, 0:N_DEC])
                last.then_inc(qtp, 1)
                for k in range(2):
                    for n in range(32):
                        last = pe.matmul(cps[:, k:k + 1], wc[:, k, n, :], peT[:, k, n:n + 1],
                                         start=n == 0, stop=n == 31)
                last.then_inc(pes, 1)
                pe.wait_ge(q_ev, 6)
                pe.wait_ge(peb_in, 1)

                def row_of(s):
                    return lambda c, r, kind: x[s][:, c, 512 * r + P * kind:512 * r + P * kind + P]

                def compress(i, s):
                    prev, row = (i, 0) if s else (i - 1, 1), row_of(s)
                    by_act.after(pe, prev[0], f"tps.{prev[1]}")
                    by_dve.after(pe, prev[0], f"tpw.{prev[1]}")
                    for n in range(4):
                        if n >= 2:
                            by_act.after(pe, i, f"tc{n - 2}.{s}")
                        pe.sem_inc(settled, 1)
                        for c in range(4):
                            last = pe.transpose(tp[n % 2][:, c * P:(c + 1) * P],
                                                row(c, n % 2, n // 2), ident[:, :])
                        by_pe.did(last, f"tc{n}.{s}")

                def products(i, s):
                    prev = (i, 0) if s else (i - 1, 1)
                    by_dve.after(pe, prev[0], f"out.{prev[1]}")
                    by_act.after(pe, i, f"tc3.{s}")
                    for k in range(2):
                        for n in range(32):
                            last = pe.matmul(cps[:, k * 64:k * 64 + NCMP], wc[:, k, n, :],
                                             xT[:, 2 * k + n % 2, n // 2:n // 2 + 8 * (NCMP - 1) + 1:8],
                                             start=n == 0, stop=n == 31)
                    by_pe.did(last, f"comp.{s}")
                    by_dve.after(pe, i, f"sqk.{s}")
                    by_pe.did(pe.matmul(ms[:, 0:NCMP], ones[:, :], sqk[:, :], start=True, stop=True), f"nrm.{s}")
                    by_dve.after(pe, i, f"msk.{s}")
                    by_dve.after(pe, i, f"vcf.{s}")
                    pe.sem_inc(settled, 1)
                    by_pe.did(pe.transpose(ms[0:NCMP, 64:64 + P], vcf[:, :], ident[:, :]), f"tv.{s}")

                def front(i, s):
                    row = row_of(s)
                    compress(i, s)
                    for r in range(2):
                        by_act.after(pe, i, f"tc{2 + r}.{s}")
                        for c in range(4):
                            last = pe.transpose(tp[r][:, c * P:(c + 1) * P], row(c, r, 2), ident[:, :])
                        by_pe.did(last, f"tk{r}.{s}")
                    by_dve.after(pe, i, f"tk0.{s}")
                    for c in range(4):
                        last = pe.transpose(tp[0][:, c * P:(c + 1) * P], win[s][:, c, 0:P], ident[:, :])
                    by_pe.did(last, f"tw.{s}")
                    by_dve.after(pe, i, f"tk1.{s}")
                    pe.sem_inc(settled, 1)
                    pe.transpose(tp[1][:, 0:DEC_S], nkv[s][:, 256:384], ident[0:DEC_S, 0:DEC_S])
                    by_pe.did(pe.transpose(tp[1][:, DEC_S:2 * DEC_S], nwin[s][:, 0:P], ident[0:DEC_S, 0:DEC_S]),
                              f"tn.{s}")
                    products(i, s)

                def tile(i, s):
                    row = row_of(s)
                    x_in[s].wait(pe, i, 16 * 11)
                    front(i, s)
                    by_act.after(pe, i, f"q.{s}")
                    by_dve.after(pe, i, f"tn.{s}")
                    for r in range(2):
                        pe.matmul(sS[0:NR, 512 * r:512 * r + 512], qs[:, :], ksT[:, r, :], start=True, stop=True)
                    pe.matmul(sW[0:NR, :], qs[:, :], kwT[:, :], start=True, stop=True)
                    by_pe.did(pe.matmul(sM[0:NR, 64:64 + 2 * DEC_S], qs[:, :], knT[:, :], start=True, stop=True),
                              f"scS.{s}")
                    by_dve.after(pe, i, f"kcT.{s}")
                    by_pe.did(pe.matmul(sM[0:NR, 0:NCMP], qs[:, :], kcT[:, :], start=True, stop=True), f"scC.{s}")
                    by_dve.after(pe, i, f"pc.{s}")
                    by_dve.after(pe, i, f"vc.{s}")
                    pe.sem_inc(settled, 1)
                    by_pe.did(pe.transpose(ms[0:NCMP, 192:192 + NR], pc[:, :], ident[0:NR, 0:NR]), f"tpc.{s}")
                    by_dve.after(pe, i, f"pcT.{s}")
                    pe.sem_inc(settled, 1)
                    by_pe.did(pe.matmul(ms[0:NR, 256:256 + NB + 1], pcT[:, :], share[:, :], start=True, stop=True),
                              f"imp1.{s}")
                    by_dve.after(pe, i, f"i1.{s}")
                    pe.sem_inc(settled, 1)
                    by_pe.did(pe.matmul(ms[0:NR, 288:288 + NB + 1], rsum[:, :], imp[:, :], start=True, stop=True),
                              f"imp2.{s}")
                    by_dve.after(pe, i, f"pS.{s}")
                    pe.sem_inc(settled, 1)
                    for c in range(8):
                        last = pe.transpose(tp[0][:, c * NR:(c + 1) * NR], pS[:, c * P:(c + 1) * P], ident[0:NR, 0:NR])
                    by_pe.did(last, f"tps.{s}")
                    by_dve.after(pe, i, f"pW.{s}")
                    pe.sem_inc(settled, 1)
                    for c in range(4):
                        pe.transpose(tp[1][:, c * NR:(c + 1) * NR], pW[:, c * P:(c + 1) * P], ident[0:NR, 0:NR])
                    pe.transpose(tp[1][0:DEC_S, 256:256 + NR], pW[:, CWIN:NKW], ident[0:NR, 0:NR])
                    by_pe.did(pe.transpose(tp[1][0:DEC_S, 320:320 + NR], pS[:, PAST:NKS], ident[0:NR, 0:NR]),
                              f"tpw.{s}")
                    by_act.after(pe, i, f"tps.{s}")
                    by_dve.after(pe, i, f"tpw.{s}")
                    pe.sem_inc(settled, 1)
                    out = lambda n: cps[0:NR, P + n * P:2 * P + n * P]
                    pe.matmul(out(0), pcT[:, :], vc[:, :], start=True, stop=True)
                    for c in range(8):
                        pe.matmul(out(1), pTs[:, c, :], row(c % 4, c // 4, 3), start=c == 0, stop=False)
                    pe.matmul(out(1), pTw[0:DEC_S, 5, :], nkv[s][:, 384:512], start=False, stop=True)
                    for c in range(4):
                        pe.matmul(out(2), pTw[:, c, :], win[s][:, c, P:2 * P], start=c == 0, stop=False)
                    by_pe.did(pe.matmul(out(2), pTw[0:DEC_S, 4, :], nwin[s][:, P:2 * P], start=False, stop=True),
                              f"sum.{s}")

                with pe.Fori(0, DEC_B // 2) as i:
                    tile(i, 0)
                    tile(i, 1)
                n = DEC_B // 2
                x_in[0].wait(pe, n + 1, 16)
                front(n, 0)
                by_dve.after(pe, n, "vc.0")
                pe.transpose(ms[0:NCMP, 192:192 + P], kcT[:, :], ident[:, :]).then_inc(qtp, 1)

            @block.scalar
            def _(act):
                by_act.open(act)
                act.wait_ge(zero, 3)
                act.wait_ge(qtp, 1)
                for g in range(2):
                    for r in range(RC):
                        rs = slice(HD * g, HD * g + HD)
                        act.activation(qz[rs, :, 32 * g + 8 * r:32 * g + 8 * r + 8],
                                       ms[rs, r * N_DEC:(r + 1) * N_DEC].rearrange("p (b q) -> p b q", b=DEC_B),
                                       ACT.Copy).then_inc(q_ev, 1)
                act.wait_ge(q_ev, 6)

                def take(i, s):
                    for n in range(4):
                        by_pe.after(act, i, f"tc{n}.{s}")
                        by_act.did(act.activation(xT[:, n, :], tp[n % 2][:, :], ACT.Copy), f"tc{n}.{s}")
                    by_dve.after(act, i, f"msk.{s}")
                    by_act.did(act.activation(rsk[:, :], msk[:, :], ACT.Sqrt), f"rt.{s}")

                def queries(i, s, b):
                    by_pe.after(act, *((i, "scC.0") if s else (i - 1, "scC.1")))
                    by_act.did(act.activation(qs[:, :], qz[:, bass.ds(b, 1), :].rearrange(
                        "p o r -> p (o r)"), ACT.Copy), f"q.{s}")

                def tile(i, s):
                    queries(i, s, i * 2 + s)
                    take(i, s)
                    for k, buf, n in (("c", pc, 0), ("s", pS, 1), ("w", pW, 2)):
                        by_dve.after(act, i, {"c": f"bc.{s}", "s": f"bS.{s}", "w": f"bW.{s}"}[k])
                        by_act.did(act.activation(buf[:, :], sM[0:NR, 0:NCMP] if n == 0 else buf[:, :], ACT.Exp,
                                                  bias=st[:, n, 1:2], scale=SCALE, accum_out=st[:, n, 2:3]),
                                   f"e{k}.{s}")
                    by_pe.after(act, i, f"tps.{s}")
                    by_act.did(act.activation(pTs[:, :, :], tp[0][:, :].rearrange("p (c r) -> p c r", r=NR),
                                              ACT.Copy), f"tps.{s}")

                with act.Fori(0, DEC_B // 2) as i:
                    tile(i, 0)
                    tile(i, 1)
                queries(DEC_B // 2, 0, 0)
                take(DEC_B // 2, 0)

            @block.vector
            def _(dve):
                by_dve.open(dve)
                dve.wait_ge(const_in, 16 * 14)
                dve.wait_ge(pes, 1)
                dve.tensor_copy(peb[:, :], cps[:, 0:2]).then_inc(peb_in, 1)
                dve.wait_ge(peb_in, 1)

                def compress(i, s):
                    step = lambda name, ins: (by_dve.did(ins, f"{name}.{s}"), by_dve.after(dve, i, f"{name}.{s}"))
                    by_pe.after(dve, i, f"comp.{s}")
                    step("kcf", dve.tensor_scalar(kcf[:, :], cps[:, 0:NCMP], peb[:, 0:1], None, ALU.add))
                    by_pe.after(dve, *((i, "tv.0") if s else (i - 1, "tv.1")))
                    step("vcf", dve.tensor_scalar(vcf[:, :], cps[:, 64:64 + NCMP], peb[:, 1:2], None, ALU.add))
                    step("sqk", dve.tensor_tensor(sqk[:, :], kcf[:, :], kcf[:, :], ALU.mult))
                    by_pe.after(dve, i, f"nrm.{s}")
                    step("msk", dve.tensor_scalar(msk[:, :], ms[:, 0:NCMP], 1.0 / HD, EPS, ALU.mult, ALU.add))
                    by_act.after(dve, i, f"rt.{s}")
                    step("rsk", dve.reciprocal(rsk[:, :], rsk[:, :]))
                    by_pe.after(dve, *((i, "scC.0") if s else (i - 1, "scC.1")))
                    step("kcT", dve.scalar_tensor_tensor(out=kcT[:, :], in0=kcf[:, :], scalar=gain[:, :],
                                                         in1=rsk[:, :], op0=ALU.mult, op1=ALU.mult))
                    by_pe.after(dve, i, f"tv.{s}")
                    by_pe.after(dve, *((i, "sum.0") if s else (i - 1, "sum.1")))
                    step("vc", dve.tensor_copy(vc[:, :], ms[0:NCMP, 64:64 + P]))

                def front(i, s):
                    step = lambda name, ins: (by_dve.did(ins, f"{name}.{s}"), by_dve.after(dve, i, f"{name}.{s}"))
                    prev = (i, 0) if s else (i - 1, 1)
                    by_pe.after(dve, prev[0], f"scS.{prev[1]}")
                    for r in range(2):
                        by_pe.after(dve, i, f"tk{r}.{s}")
                        step(f"tk{r}", dve.tensor_copy(ksT[:, r, :], tp[r][:, :]))
                    by_pe.after(dve, i, f"tw.{s}")
                    step("tw", dve.tensor_copy(kwT[:, :], tp[0][:, :]))
                    by_pe.after(dve, i, f"tn.{s}")
                    step("tn", dve.tensor_copy(knT[:, :], tp[1][:, 0:2 * DEC_S]))
                    compress(i, s)

                def tile(i, s):
                    step = lambda name, ins: (by_dve.did(ins, f"{name}.{s}"), by_dve.after(dve, i, f"{name}.{s}"))
                    prev = (i, 0) if s else (i - 1, 1)
                    front(i, s)
                    by_pe.after(dve, i, f"scC.{s}")
                    step("mc", dve.tensor_reduce(st[:, 0, 0:1], sM[0:NR, 0:NCMP], AX.X, ALU.max))
                    step("bc", dve.tensor_scalar(st[:, 0, 1:2], st[:, 0, 0:1], -SCALE, None, ALU.mult))
                    by_act.after(dve, i, f"ec.{s}")
                    step("rc", dve.reciprocal(st[:, 0, 3:4], st[:, 0, 2:3]))
                    step("pc", dve.tensor_scalar(pc[:, :], pc[:, :], st[:, 0, 3:4], None, ALU.mult))
                    by_pe.after(dve, i, f"tpc.{s}")
                    step("pcT", dve.tensor_copy(pcT[:, :], ms[0:NCMP, 192:192 + NR]))
                    by_pe.after(dve, i, f"imp1.{s}")
                    step("i1", dve.tensor_copy(imp[:, :], ms[0:NR, 256:256 + NB + 1]))
                    by_pe.after(dve, i, f"imp2.{s}")
                    step("i2", dve.tensor_copy(sel[:, 0:NB + 1], ms[0:NR, 288:288 + NB + 1]))
                    step("mn", dve.tensor_reduce(sel[:, 40:41], sel[:, 1:NB - 1], AX.X, ALU.min))
                    step("eq", dve.scalar_tensor_tensor(out=sel[:, 20:20 + NB - 2], in0=sel[:, 1:NB - 1],
                                                        scalar=sel[:, 40:41], in1=idx[:, 1:NB - 1],
                                                        op0=ALU.is_equal, op1=ALU.mult))
                    step("mi", dve.tensor_reduce(sel[:, 41:42], sel[:, 20:20 + NB - 2], AX.X, ALU.max))
                    step("drop", dve.tensor_scalar(drop[:, :], idx[:, :], sel[:, 41:42], NEG, ALU.is_equal, ALU.mult))
                    by_pe.after(dve, prev[0], f"tpw.{prev[1]}")
                    for r in range(2):
                        step(f"s{r}", dve.tensor_tensor(
                            pS[:, 512 * r:512 * r + 512].rearrange("p (b k) -> p b k", b=NB),
                            sS[0:NR, 512 * r:512 * r + 512].rearrange("p (b k) -> p b k", b=NB),
                            drop[:, :].unsqueeze(2).to_broadcast([NR, NB, 32]), ALU.add))
                    step("sn", dve.tensor_tensor(pS[:, PAST:NKS], sM[0:NR, 64:64 + DEC_S], mnew[:, :], ALU.add))
                    step("mS", dve.tensor_reduce(st[:, 1, 0:1], pS[:, :], AX.X, ALU.max))
                    step("bS", dve.tensor_scalar(st[:, 1, 1:2], st[:, 1, 0:1], -SCALE, None, ALU.mult))
                    step("w0", dve.tensor_tensor(pW[:, 0:CWIN], sW[0:NR, :], mwin[:, :], ALU.add))
                    step("wn", dve.tensor_tensor(pW[:, CWIN:NKW], sM[0:NR, 64 + DEC_S:64 + 2 * DEC_S], mnew[:, :],
                                                 ALU.add))
                    step("mW", dve.tensor_reduce(st[:, 2, 0:1], pW[:, :], AX.X, ALU.max))
                    step("bW", dve.tensor_scalar(st[:, 2, 1:2], st[:, 2, 0:1], -SCALE, None, ALU.mult))
                    for n, k, e, buf in ((1, "S", "es", pS), (2, "W", "ew", pW)):
                        by_act.after(dve, i, f"{e}.{s}")
                        step(f"r{k}", dve.reciprocal(st[:, n, 3:4], st[:, n, 2:3]))
                        step(f"p{k}", dve.tensor_scalar(buf[:, :], buf[:, :], st[:, n, 3:4], None, ALU.mult))
                    by_pe.after(dve, i, f"tpw.{s}")
                    dve.tensor_copy(pTw[:, 0:4, :], tp[1][:, 0:256].rearrange("p (c r) -> p c r", r=NR))
                    step("tpw", dve.tensor_copy(pTw[0:DEC_S, 4:6, :], tp[1][0:DEC_S, 256:384].rearrange(
                        "p (c r) -> p c r", r=NR)))
                    by_pe.after(dve, i, f"sum.{s}")
                    o_out[s].wait(dve, i)
                    for g in range(2):
                        rs = slice(32 * g, 32 * g + 32)
                        last = dve.tensor_copy(o[s][rs, :, :], cps[rs, P:4 * P].rearrange(
                            "p (n c) -> p n c", n=3)[:, :, HD * g:HD * g + HD])
                    step("out", last)

                with dve.Fori(0, DEC_B // 2) as i:
                    tile(i, 0)
                    tile(i, 1)
                n = DEC_B // 2
                front(n, 0)
                dve.wait_ge(zero, 3)
                dve.tensor_copy(kcr[0:NCMP, P:2 * P], vc[:, :]).then_inc(q_ev, 2)
                dve.wait_ge(qtp, 2)
                dve.tensor_copy(kcr[0:NCMP, 0:P], ms[0:NCMP, 192:192 + P]).then_inc(q_ev, 2)


SLOTS = (2 * N_TOK + NE * (P - 1)) // P
WB = 3
SW = SLOTS + 2


def mix_and_experts(nc, t):
    with ExitStack() as ctx:
        sb = lambda name, shape, dt=F32: ctx.enter_context(nc.sbuf_tensor("m_" + name, shape, dt))
        ps = lambda name, shape: ctx.enter_context(nc.psum_tensor("m_" + name, shape, F32))
        sem = ctx.enter_context(semaphores(nc, "m_"))
        ident, tri, ones = sb("ident", [P, P]), sb("tri", [P, P]), sb("ones", [P, P])
        wo = sb("wo", [P, KD, D])
        wr = sb("wr", [P, KD, 20])
        rb = sb("rb", [P, 20])
        gain = sb("gain", [P, D])
        pri = sb("pri", [P, 4])
        thr = sb("thr", [P, TILES])
        before = sb("before", [P, NE, NE])
        sno = sb("sno", [P, SW])
        tid = sb("tid", [P, TILES], U32)
        cat = sb("cat", [P, D])
        oc = sb("oc", [P, 3, 384])
        zg = sb("zg", [P, 18])
        eg = sb("eg", [P, 18])
        x = sb("x", [P, D])
        catT = sb("catT", [P, KD, P])
        x1 = sb("x1", [P, TILES, D])
        sq = sb("sq", [P, D])
        st = sb("st", [P, 3])
        nhalf = sb("nhalf", [P, 1])
        h2 = sb("h2", [P, D])
        h2T = sb("h2T", [P, KD, P])
        tp, acc = ps("tp", [P, KD, P]), ps("acc", [P, D])
        hid = [ps(f"hid{s}", [P, 512]) for s in range(2)]
        hTp = ps("hTp", [P, 512])
        N = TILES
        L = sb("L", [P, N, 20])
        gm, gs, m1, m2, mm, pd, ee = (sb(n, [P, N]) for n in ("gm", "gs", "m1", "m2", "mm", "pd", "ee"))
        g4, og, es, o1, o2, tq4 = (sb(n, [P, N, 4]) for n in ("g4", "og", "es", "o1", "o2", "tq4"))
        t16, A, rank = (sb(n, [P, N, NE]) for n in ("t16", "A", "rank"))
        O = sb("O", [P, 2, N, NE])
        wt = sb("wt", [P, 2, N])
        base = sb("base", [P, N + 1, NE])
        tot = sb("tot", [P, N, NE])
        c9, nsl, first, c16 = sb("c9", [P, NE, N]), sb("nsl", [P, NE]), sb("first", [P, NE]), sb("c16", [P, NE, NE])
        K, S, fl, r = (sb(n, [P, 2, N]) for n in ("K", "S", "fl", "r"))
        c8 = sb("c8", [P, 2 * N, N - 1])
        at, pos = sb("at", [P, 2 * N], U32), sb("pos", [P, 2 * N], U32)
        c32, sx = sb("c32", [P, SW, NE]), sb("sx", [P, SW])
        sxi = sb("sxi", [P, SW + NE], I32)
        zi = sb("zi", [P, SW], U32)
        tok = sb("tok", [P, SW], U32)
        w13 = sb("w13", [P, WB * KD, 2 * DE])
        w2 = sb("w2", [P, WB * DE // P, D])
        xg = [sb(f"xg{s}", [P, D]) for s in range(2)]
        ix = [sb(f"ix{s}", [P, 1], U32) for s in range(2)]
        xT = sb("xT", [P, KD, P])
        hs, hh = (sb(n, [P, DE]) for n in ("hs", "hh"))
        hT = sb("hT", [P, DE // P, P])
        yo = [cat, x]
        gy = [[w13[:, 4 * s + 2 * k:4 * s + 2 * k + 2, :].rearrange("p a b -> p (a b)") for k in range(2)]
              for s in range(2)]
        iy = [[sb(f"iy{s}{k}", [P, 1], U32) for k in range(2)] for s in range(2)]
        wy = sb("wy", [P, 2])
        yt = yo
        const_in, seen, settled, cleared, rows_out, tab0, scat, sx_out, tok_in, y_end = map(sem, (
            "const_in", "seen", "settled", "cleared", "rows_out", "tab0", "scat", "sx_out", "tok_in", "y_end"))
        cat_in, x_in = Count(sem("cat_in"), 16 * 3), Count(sem("x_in"), 16)
        h2_out = Count(sem("h2_out"), 16)
        act_g, dve_g = Steps(sem("act_g"), "gate"), Steps(sem("dve_g"), "g1 g2 b0 b1 b2 s1 s2")
        pe_s = Steps(sem("pe_s"), "catT wo")
        pe_r = Steps(sem("pe_r"), "h2T rout")
        act_c, act_s = Steps(sem("act_c"), "catT"), Steps(sem("act_s"), "sq")
        act_r = Steps(sem("act_r"), "h2T")
        dve_c, dve_s = Steps(sem("dve_c"), "catT"), Steps(sem("dve_s"), "x1 ms h2")
        dve_r = Steps(sem("dve_r"), "h2T rout")
        pool_s = Steps(sem("pool_s"), "rs")
        rt_dve, rt_act, rt_pe, rt_pool = map(sem, ("rt_dve", "rt_act", "rt_pe", "rt_pool"))
        w_in, hidden = Count(sem("w_in"), 48), Steps(sem("hidden"), "one rec sil hh")
        ps_xT, ps_hid, ps_hT, ps_out = (Count(sem("ps_" + n)) for n in ("xT", "hid", "hT", "out"))
        a_xT, a_exp, a_hT, a_out = (Count(sem("a_" + n)) for n in ("xT", "exp", "hT", "out"))
        d_xT, d_out = (Count(sem("d_" + n)) for n in ("xT", "out"))
        xg_in = [Count(sem(f"xg_in{s}"), 16) for s in range(2)]
        ys_out = [Count(sem(f"ys_out{s}"), 16) for s in range(2)]
        e_pool = Steps(sem("e_pool"), "ix.0 ix.1")
        y_pool = Steps(sem("y_pool"), "ix")
        y_dve = Steps(sem("y_dve"), "wy a b")
        gy_in = [Count(sem(f"gy_in{s}"), 32) for s in range(2)]
        yt_out = [Count(sem(f"yt_out{s}"), 16) for s in range(2)]
        NS = SLOTS // 2
        assert SLOTS % 2 == 0

        with nc.Block() as block:

            @block.sync
            def _(sp):
                for c in (cat_in, x_in, h2_out, w_in, *yt_out):
                    c.open(sp)
                for a, b in ((ident, "ident"), (tri, "m_tri"), (ones, "m_ones"), (pri, "m_pri"), (thr, "m_thr"),
                             (before, "m_before"), (sno, "m_sno"), (tid, "m_tid")):
                    sp.dma_start(a[:], t[b][:]).then_inc(const_in, 16)
                sp.dma_start(gain[:, :], t["ffn_norm"][0].partition_broadcast(P)).then_inc(const_in, 16)

                def load(rows, T):
                    sp.dma_start(cat[0:T, 0:640], t["cat"][rows, 0:640]).then_inc(cat_in.sem, 16)
                    sp.dma_start(oc[0:T, :, :], t["oc"][rows, :, :, :].rearrange("p b h d -> p b (h d)")
                                 ).then_inc(cat_in.sem, 16)
                    sp.dma_start(zg[0:T, :], t["zr"][rows, Z_G:Z_W]).then_inc(cat_in.sem, 16)

                load(slice(0, P), P)
                sp.dma_start(x[:, :], t["x"][0:P, :]).then_inc(x_in.sem, 16)
                sp.dma_start(wo[:, :, :], t["w_o"][0].rearrange("(k p) n -> p k n", p=P)).then_inc(const_in, 16)
                for lo, hi, w, b in ((0, 4, "moe_wg", "moe_bg"), (4, 20, "moe_we", "moe_be")):
                    sp.dma_start(wr[:, :, lo:hi], t[w][0].rearrange("(k p) n -> p k n", p=P)).then_inc(const_in, 16)
                    sp.dma_start(rb[:, lo:hi], t[b][0].partition_broadcast(P)).then_inc(const_in, 16)
                def load_expert(e, free=None):
                    if free is not None:
                        waits(sp, seen, (ps_out.sem, free + 1))
                    for k, w in enumerate(("moe_w1", "moe_w3")):
                        sp.dma_start(w13[:, bass.ds(e % WB * KD, KD), k * DE:(k + 1) * DE],
                                     t[w][0, bass.ds(e, 1), :, :].rearrange("o (k p) f -> p (o k) f", p=P)
                                     ).then_inc(w_in.sem, 16)
                    sp.dma_start(w2[:, bass.ds(e % WB * (DE // P), DE // P), :],
                                 t["moe_w2"][0, bass.ds(e, 1), :, :].rearrange("o (k p) n -> p (o k) n", p=P)
                                 ).then_inc(w_in.sem, 16)
                    if free is not None:
                        waits(sp, seen, (w_in.sem, w_in.at(e, 48)))

                sp.dma_start(t["a_s"][:, PAST - DEC_S:PAST, :],
                             t["a_kv"][SEQ:N_TOK, :].rearrange("(b s) n -> b s n", b=DEC_B)).then_inc(rows_out, 16)
                sp.dma_start(t["w_s"][:, CWIN - DEC_S:CWIN, :],
                             t["c_win"][SEQ:N_TOK, :].rearrange("(b s) n -> b s n", b=DEC_B)).then_inc(rows_out, 16)

                def tile(i, T, T_next):
                    waits(sp, seen, (pe_s.sem, pe_s.at(i, 1)), (dve_g.sem, dve_g.at(i, 7)))
                    if T_next:
                        load(bass.ds((i + 1) * P, T_next), T_next)
                    waits(sp, seen, (dve_s.sem, dve_s.at(i, 1)))
                    if T_next:
                        sp.dma_start(x[0:T_next, :], t["x"][bass.ds((i + 1) * P, T_next), :]).then_inc(x_in.sem, 16)
                    waits(sp, seen, (dve_s.sem, dve_s.at(i, 3)))
                    sp.dma_start(t["h2"][bass.ds(i * P, T), :], h2[0:T, :]).then_inc(h2_out.sem, 16)

                with sp.Fori(0, PT - 1) as i:
                    tile(i, P, P)
                tile(PT - 1, P, N_DEC)
                for e in range(WB):
                    load_expert(e)
                tile(PT, N_DEC, 0)
                h2_out.wait(sp, TILES)
                sp.wait_ge(cleared, 3)
                sp.dma_start(t["tok_at"].rearrange("(p s) o -> p (s o)", s=SW), zi[:, :]).then_inc(tab0, 16)
                sp.wait_ge(rt_dve, SX_DONE)
                sp.dma_start(t["slot_expert"][:, :], sxi[0:1, :]).then_inc(sx_out, 16)
                sp.wait_ge(scat, 16 * 2 * TILES)
                sp.dma_start(tok[:, :], t["tok_at"].rearrange("(p s) o -> p (s o)", s=SW)).then_inc(tok_in, 16)
                sp.wait_ge(sx_out, 16)
                w_in.wait(sp, WB)
                with sp.Fori(WB, NE) as e:
                    load_expert(e, sp.value_load(t["slot_expert"][0:1, bass.ds(e + (SW - WB), 1)],
                                                 min_val=0, max_val=SLOTS))
                for k in range(2):
                    ys_out[k].wait(sp, NS)
                sp.sem_inc(y_end, 1)
                def store_y(n, s, T):
                    waits(sp, seen, (y_dve.sem, y_dve.at(n, 3)))
                    sp.dma_start(t["y"][bass.ds(n * P, T), :], yt[s][0:T, :]).then_inc(yt_out[s].sem, 16)

                with sp.Fori(0, PT // 2) as i:
                    store_y(i * 2, 0, P)
                    store_y(i * 2 + 1, 1, P)
                store_y(PT, 0, N_DEC)
                yt_out[0].wait(sp, PT // 2 + 1)
                yt_out[1].wait(sp, PT // 2)
                sp.wait_ge(rows_out, 32)

            @block.tensor
            def _(pe):
                for c in (pe_s, pe_r, ps_xT, ps_hid, ps_hT, ps_out):
                    c.open(pe)
                pe.wait_ge(const_in, 16 * 14)

                def transpose_cat(i, T, first=False):
                    cat_in.wait(pe, i, 48)
                    dve_g.after(pe, i, "s2")
                    if not first:
                        dve_r.after(pe, i - 2, "h2T")
                        act_r.after(pe, i - 2, "h2T")
                    if T < P:
                        pe.sem_inc(settled, 1)
                    for k in range(KD):
                        last = pe.transpose(tp[:, k, 0:T], cat[0:T, k * P:(k + 1) * P], ident[0:T, 0:T])
                    pe_s.did(last, "catT")
                    act_c.after(pe, i, "catT")
                    dve_c.after(pe, i, "catT")
                    dve_s.after(pe, i - 1, "x1")
                    if T < P:
                        pe.sem_inc(settled, 1)

                def project_out(T, lo):
                    for k in range(KD):
                        last = pe.matmul(acc[0:T, lo:lo + 512], catT[:, k, 0:T], wo[:, k, lo:lo + 512],
                                         start=k == 0, stop=k == KD - 1)
                    if lo:
                        pe_s.did(last, "wo")

                def transpose_h2(i, T):
                    dve_s.after(pe, i, "h2")
                    for k in range(KD):
                        last = pe.transpose(tp[:, k, 0:T], h2[0:T, k * P:(k + 1) * P], ident[0:T, 0:T])
                    pe_r.did(last, "h2T")

                def router(i, T):
                    act_r.after(pe, i, "h2T")
                    dve_r.after(pe, i, "h2T")
                    dve_r.after(pe, i - 1, "rout")
                    for k in range(KD):
                        last = pe.matmul(hTp[0:T, 0:20], h2T[:, k, 0:T], wr[:, k, :], start=k == 0, stop=k == KD - 1)
                    pe_r.did(last, "rout")

                def tile(i, T):
                    transpose_cat(i, T)
                    project_out(T, 0)
                    transpose_h2(i - 1, P)
                    project_out(T, 512)
                    router(i - 1, P)

                transpose_cat(0, P, first=True)
                project_out(P, 0)
                project_out(P, 512)
                with pe.Fori(1, PT) as i:
                    tile(i, P)
                tile(PT, N_DEC)
                transpose_h2(PT, N_DEC)
                router(PT, N_DEC)
                pe.wait_ge(rt_dve, A_DONE)
                pe.matmul(hid[0][:, 0:N * NE], tri[:, :], A[:, :, :].rearrange("p n e -> p (n e)"),
                          start=True, stop=True)
                pe.matmul(hid[0][:, 256:256 + N * NE], ones[:, :], A[:, :, :].rearrange("p n e -> p (n e)"),
                          start=True, stop=True).then_inc(rt_pe, 1)
                pe.wait_ge(rt_dve, SX_DONE)

                def transpose_rows(j, s, fill):
                    xg_in[s].wait(pe, fill)
                    a_xT.wait(pe, j)
                    d_xT.wait(pe, j)
                    for k in range(KD):
                        last = pe.transpose(tp[:, k, :], xg[s][:, k * P:(k + 1) * P], ident[:, :])
                    last.then_inc(ps_xT.sem, 1)

                def hidden_rows(j, s, e):
                    a_xT.wait(pe, j, 1)
                    d_xT.wait(pe, j, 1)
                    w_in.wait(pe, e, 48)
                    for k in range(KD):
                        last = pe.matmul(hid[s][:, :], xT[:, k, :], w13[:, bass.ds(e % WB * KD + k, 1), :].rearrange(
                            "p o n -> p (o n)"), start=k == 0, stop=k == KD - 1)
                    last.then_inc(ps_hid.sem, 1)

                def transpose_hidden(j):
                    hidden.after(pe, j, "hh")
                    a_hT.wait(pe, j)
                    for k in range(DE // P):
                        last = pe.transpose(hTp[:, k * P:(k + 1) * P], hh[:, k * P:(k + 1) * P], ident[:, :])
                    last.then_inc(ps_hT.sem, 1)

                def output_rows(j, e):
                    a_hT.wait(pe, j, 1)
                    a_out.wait(pe, j)
                    d_out.wait(pe, j)
                    for lo in (0, 512):
                        for k in range(DE // P):
                            last = pe.matmul(acc[:, lo:lo + 512], hT[:, k, :],
                                             w2[:, bass.ds(e % WB * (DE // P) + k, 1), lo:lo + 512].rearrange(
                                                 "p o n -> p (o n)"), start=k == 0, stop=k == DE // P - 1)
                    last.then_inc(ps_out.sem, 1)

                expert = lambda j: pe.value_load(sxi[0:1, bass.ds(j, 1)], min_val=0, max_val=NE - 1)

                def slot(j, s, fill_next):
                    hidden_rows(j, s, expert(j))
                    transpose_rows(j + 1, 1 - s, fill_next)
                    output_rows(j - 1, expert(j - 1))
                    transpose_hidden(j)

                w_in.wait(pe, WB)
                transpose_rows(0, 0, 0)
                hidden_rows(0, 0, expert(0))
                transpose_rows(1, 1, 0)
                transpose_hidden(0)
                with pe.Fori(0, NS - 1) as i:
                    slot(i * 2 + 1, 1, i + 1)
                    slot(i * 2 + 2, 0, i + 1)
                hidden_rows(SLOTS - 1, 1, expert(SLOTS - 1))
                output_rows(SLOTS - 2, expert(SLOTS - 2))
                transpose_hidden(SLOTS - 1)
                output_rows(SLOTS - 1, expert(SLOTS - 1))

            @block.scalar
            def _(act):
                for c in (act_g, act_c, act_s, act_r, a_xT, a_exp, a_hT, a_out):
                    c.open(act)

                def gates(i, T):
                    cat_in.wait(act, i, 48)
                    dve_g.after(act, i - 1, "g2")
                    act_g.did(act.activation(eg[0:T, :], zg[0:T, :], ACT.Exp, scale=-1.0), "gate")

                def transposed(i, T):
                    pe_s.after(act, i, "catT")
                    act_c.did(act.activation(catT[:, 0:4, 0:T], tp[:, 0:4, 0:T], ACT.Copy), "catT")

                def squares(i, T):
                    dve_s.after(act, i, "x1")
                    act_s.did(act.activation(sq[0:T, :], x1[0:T, bass.ds(i, 1), :].rearrange("p o n -> p (o n)"),
                                             ACT.Square, accum_out=st[0:T, 0:1]), "sq")

                def router(i, T):
                    pe_r.after(act, i, "h2T")
                    pe_r.after(act, i - 1, "rout")
                    act_r.did(act.activation(h2T[:, 0:4, 0:T], tp[:, 0:4, 0:T], ACT.Copy), "h2T")

                def tile(i, T, T_next):
                    squares(i - 1, P)
                    transposed(i, T)
                    if T_next:
                        gates(i + 1, T_next)
                    router(i - 1, P)

                gates(0, P)
                transposed(0, P)
                gates(1, P)
                with act.Fori(1, PT - 1) as i:
                    tile(i, P, P)
                tile(PT - 1, P, N_DEC)
                tile(PT, N_DEC, 0)
                squares(PT, N_DEC)
                router(PT, N_DEC)
                act.wait_ge(rt_dve, G4_DONE)
                act.activation(g4[:, :, :], g4[:, :, :], ACT.Exp).then_inc(rt_act, 1)
                act.wait_ge(rt_dve, PD_DONE)
                act.activation(ee[:, :], pd[:, :], ACT.Exp).then_inc(rt_act, 1)

                def transposed(j):
                    ps_xT.wait(act, j, 1)
                    ps_hid.wait(act, j)
                    act.activation(xT[:, 0:4, :], tp[:, 0:4, :], ACT.Copy).then_inc(a_xT.sem, 1)

                def exponential(j, s):
                    ps_hid.wait(act, j, 1)
                    act.activation(hs[:, :], hid[s][:, 0:DE], ACT.Exp, scale=-1.0).then_inc(a_exp.sem, 1)

                def hidden_transposed(j):
                    ps_hT.wait(act, j, 1)
                    ps_out.wait(act, j)
                    act.activation(hT[:, :, :], hTp[:, 0:DE].rearrange("p (k t) -> p k t", t=P),
                                   ACT.Copy).then_inc(a_hT.sem, 1)

                def output(j, s, fill):
                    ps_out.wait(act, j, 1)
                    ys_out[s].wait(act, fill)
                    act.activation(yo[s][:, 0:512], acc[:, 0:512], ACT.Copy).then_inc(a_out.sem, 1)
                    waits(act, seen, (a_out.sem, a_out.at(j, 1)), (d_out.sem, d_out.at(j, 1)))
                    act.dma_start(t["ys"][bass.ds(j * P, P), :], yo[s][:, :]).then_inc(ys_out[s].sem, 16)

                def slot(j, s, fill):
                    exponential(j, s)
                    transposed(j + 1)
                    output(j - 1, 1 - s, fill)
                    hidden_transposed(j)

                for k in range(2):
                    ys_out[k].open(act)
                transposed(0)
                exponential(0, 0)
                transposed(1)
                hidden_transposed(0)
                with act.Fori(0, NS - 1) as i:
                    slot(i * 2 + 1, 1, i)
                    slot(i * 2 + 2, 0, i)
                exponential(SLOTS - 1, 1)
                output(SLOTS - 2, 0, NS - 1)
                hidden_transposed(SLOTS - 1)
                output(SLOTS - 1, 1, NS - 1)

            @block.gpsimd
            def _(pool):
                for c in (pool_s, e_pool, y_pool):
                    c.open(pool)
                pool.memset(nhalf[:, :], -0.5).then_inc(cleared, 1)
                pool.memset(zi[:, :], 0).then_inc(cleared, 1)
                pool.memset(L[:, :, :], 0.0).then_inc(cleared, 1)
                pool.wait_ge(cleared, 3)

                def tile(i, T):
                    dve_s.after(pool, i, "ms")
                    pool_s.did(pool.tensor_tensor(st[0:T, 2:3], st[0:T, 1:2], nhalf[0:T, :], ALU.pow), "rs")

                with pool.Fori(0, PT) as i:
                    tile(i, P)
                tile(PT, N_DEC)
                pool.wait_ge(rt_dve, AT_DONE)
                pool.wait_ge(tab0, 16)
                for n in range(2 * TILES):
                    T = P if n % TILES < PT else N_DEC
                    pool.indirect_dma_start(t["tok_at"][:, :], bass.IndirectOffsetOnAxis(at[0:T, n:n + 1], 0),
                                            tid[0:T, n % TILES:n % TILES + 1], None).then_inc(scat, 16)
                pool.wait_ge(tok_in, 16)
                h2_out.wait(pool, TILES)

                def gather(n, i, s, prev):
                    if prev:
                        xg_in[s].wait(pool, i)
                        ps_xT.wait(pool, i * 2 + s, 1)
                    e_pool.did(pool.tensor_copy(ix[s][:, :], tok[:, n]), f"ix.{s}")
                    e_pool.after(pool, i + 1 if prev else 0, f"ix.{s}")
                    pool.sem_inc(settled, 1)
                    pool.indirect_dma_start(xg[s][:, :], None, t["h2"][:, :],
                                            bass.IndirectOffsetOnAxis(ix[s][:, :], 0)).then_inc(xg_in[s].sem, 16)

                for s in range(2):
                    gather(slice(s, s + 1), 0, s, False)
                with pool.Fori(0, NS) as i:
                    for s in range(2):
                        gather(bass.ds(i * 2 + (2 + s), 1), i, s, True)
                for s in range(2):
                    xg_in[s].wait(pool, NS)
                pool.wait_ge(y_end, 1)

                def gather_y(n, s, T, first=False):
                    if not first:
                        y_dve.after(pool, n - 2, "b")
                    pool.tensor_copy(iy[s][0][0:T, :], pos[0:T, bass.ds(n, 1)])
                    y_pool.did(pool.tensor_copy(iy[s][1][0:T, :], pos[0:T, bass.ds(n + N, 1)]), "ix")
                    y_pool.after(pool, n, "ix")
                    pool.sem_inc(settled, 1)
                    for k in range(2):
                        pool.indirect_dma_start(gy[s][k][0:T, :], None, t["ys"][:, :],
                                                bass.IndirectOffsetOnAxis(iy[s][k][0:T, :], 0)
                                                ).then_inc(gy_in[s].sem, 16)

                gather_y(0, 0, P, first=True)
                gather_y(1, 1, P, first=True)
                with pool.Fori(1, PT // 2) as i:
                    gather_y(i * 2, 0, P)
                    gather_y(i * 2 + 1, 1, P)
                gather_y(PT, 0, N_DEC)

            @block.vector
            def _(dve):
                for c in (dve_g, dve_c, dve_s, dve_r, hidden, d_xT, d_out, y_dve):
                    c.open(dve)
                dve.wait_ge(const_in, 16 * 14)
                dve.wait_ge(cleared, 3)

                def gates(i, T):
                    tr = slice(0, T)
                    step = lambda name, ins: (dve_g.did(ins, name), dve_g.after(dve, i, name))
                    act_g.after(dve, i, "gate")
                    step("g1", dve.tensor_scalar(eg[tr, :], eg[tr, :], 1.0, None, ALU.add))
                    step("g2", dve.reciprocal(zg[tr, :], eg[tr, :]))
                    for b in range(3):
                        v = oc[tr, b, :].rearrange("p (h d) -> p h d", d=HD)
                        g = zg[tr, :].rearrange("p (h b) -> p h b", b=3)[:, :, b:b + 1].to_broadcast([T, HC, HD])
                        dve_g.did(dve.tensor_tensor(v, v, g, ALU.mult), f"b{b}")
                    dve_g.after(dve, i, "b2")
                    step("s1", dve.tensor_tensor(oc[tr, 0, :], oc[tr, 0, :], oc[tr, 1, :], ALU.add))
                    step("s2", dve.tensor_tensor(cat[tr, 640:1024], oc[tr, 0, :], oc[tr, 2, :], ALU.add))

                rows = lambda i, T: x1[0:T, bass.ds(i, 1), :].rearrange("p o n -> p (o n)")

                def transposed(i, T):
                    pe_s.after(dve, i, "catT")
                    dve_c.did(dve.tensor_copy(catT[:, 4:8, 0:T], tp[:, 4:8, 0:T]), "catT")

                def residual(i, T):
                    pe_s.after(dve, i, "wo")
                    x_in.wait(dve, i, 16)
                    dve_s.did(dve.tensor_tensor(rows(i, T), acc[0:T, :], x[0:T, :], ALU.add), "x1")

                def norm(i, T):
                    tr = slice(0, T)
                    act_s.after(dve, i, "sq")
                    dve_s.did(dve.tensor_scalar(st[tr, 1:2], st[tr, 0:1], 1.0 / D, EPS, ALU.mult, ALU.add), "ms")
                    pool_s.after(dve, i, "rs")
                    h2_out.wait(dve, i)
                    pe_r.after(dve, i - 1, "h2T")
                    dve_s.did(dve.scalar_tensor_tensor(out=h2[tr, :], in0=rows(i, T), scalar=st[tr, 2:3],
                                                       in1=gain[tr, :], op0=ALU.mult, op1=ALU.mult), "h2")

                def router(i, T):
                    tr = slice(0, T)
                    pe_r.after(dve, i, "h2T")
                    pe_r.after(dve, i - 1, "rout")
                    dve_r.did(dve.tensor_copy(h2T[:, 4:8, tr], tp[:, 4:8, tr]), "h2T")
                    pe_r.after(dve, i, "rout")
                    dve_r.did(dve.tensor_tensor(L[tr, bass.ds(i, 1), :].rearrange("p o n -> p (o n)"),
                                                hTp[tr, 0:20], rb[tr, :], ALU.add), "rout")

                def tile(i, T, T_next):
                    residual(i - 1, P)
                    transposed(i, T)
                    norm(i - 1, P)
                    if T_next:
                        gates(i + 1, T_next)
                    router(i - 1, P)

                gates(0, P)
                transposed(0, P)
                gates(1, P)
                with dve.Fori(1, PT - 1) as i:
                    tile(i, P, P)
                tile(PT - 1, P, N_DEC)
                tile(PT, N_DEC, 0)
                residual(PT, N_DEC)
                norm(PT, N_DEC)
                router(PT, N_DEC)
                dve_r.after(dve, PT, "rout")

                done = 0

                def step(ins):
                    nonlocal done
                    done += 1
                    ins.then_inc(rt_dve, 1)
                    dve.wait_ge(rt_dve, done)

                B4 = [P, N, 4]
                wide = lambda a, shape=B4: a.unsqueeze(2).to_broadcast(shape)

                def first_max(out, v, m):
                    step(dve.tensor_reduce(m[:, :], v, AX.X, ALU.max))
                    step(dve.tensor_tensor(tq4[:, :, :], v, wide(m[:, :]), ALU.is_equal))
                    step(dve.tensor_tensor(tq4[:, :, :], tq4[:, :, :], pri[:, :].unsqueeze(1).to_broadcast(B4),
                                           ALU.mult))
                    step(dve.tensor_reduce(mm[:, :], tq4[:, :, :], AX.X, ALU.max))
                    step(dve.tensor_tensor(out[:, :, :], tq4[:, :, :], wide(mm[:, :]), ALU.is_equal))

                first_max(og, L[:, :, 0:4], gm)
                step(dve.tensor_tensor(g4[:, :, :], L[:, :, 0:4], wide(gm[:, :]), ALU.subtract))
                assert done == G4_DONE
                le = L[:, :, 4:20].rearrange("p n (g e) -> p n g e", g=4)
                B44 = [P, N, 4, 4]
                v44 = lambda a: a.rearrange("p n (g e) -> p n g e", g=4)
                step(dve.tensor_tensor(v44(t16[:, :, :]), le, og[:, :, :].unsqueeze(3).to_broadcast(B44), ALU.mult))
                step(dve.tensor_reduce(es[:, :, :], t16[:, :, :].rearrange("p n (g e) -> p n e g", g=4),
                                       AX.X, ALU.add))
                first_max(o1, es[:, :, :], m1)
                step(dve.scalar_tensor_tensor(out=es[:, :, :], in0=o1[:, :, :], scalar=NEG, in1=es[:, :, :],
                                              op0=ALU.mult, op1=ALU.add))
                first_max(o2, es[:, :, :], m2)
                step(dve.tensor_tensor(pd[:, :], m2[:, :], m1[:, :], ALU.subtract))
                assert done == PD_DONE
                for k, o in enumerate((o1, o2)):
                    step(dve.tensor_tensor(v44(O[:, k, :, :]), og[:, :, :].unsqueeze(3).to_broadcast(B44),
                                           o[:, :, :].unsqueeze(2).to_broadcast(B44), ALU.mult))
                step(dve.tensor_tensor(A[:, :, :], O[:, 0, :, :], O[:, 1, :, :], ALU.add))
                step(dve.memset(A[N_DEC:P, PT:TILES, :], 0.0))
                assert done == A_DONE
                dve.wait_ge(rt_act, 2)
                step(dve.tensor_reduce(gs[:, :], g4[:, :, :], AX.X, ALU.add))
                step(dve.tensor_scalar(pd[:, :], ee[:, :], 1.0, None, ALU.add))
                step(dve.tensor_tensor(gs[:, :], gs[:, :], pd[:, :], ALU.mult))
                step(dve.reciprocal(wt[:, 0, :], gs[:, :]))
                step(dve.tensor_tensor(wt[:, 1, :], wt[:, 0, :], ee[:, :], ALU.mult))
                dve.wait_ge(rt_pe, 1)
                step(dve.tensor_copy(tot[:, :, :], hid[0][:, 256:256 + N * NE].rearrange("p (n e) -> p n e", e=NE)))
                step(dve.memset(base[:, 0, :], 0.0))
                for n in range(N):
                    step(dve.tensor_tensor(base[:, n + 1, :], base[:, n, :], tot[:, n, :], ALU.add))
                step(dve.tensor_tensor(rank[:, :, :], hid[0][:, 0:N * NE].rearrange("p (n e) -> p n e", e=NE),
                                       base[:, 0:N, :], ALU.add))
                B9 = [P, NE, N]
                step(dve.tensor_tensor(c9[:, :, :], base[:, N, :].unsqueeze(2).to_broadcast(B9),
                                       thr[:, :].unsqueeze(1).to_broadcast(B9), ALU.is_gt))
                step(dve.tensor_reduce(nsl[:, :], c9[:, :, :], AX.X, ALU.add))
                step(dve.tensor_tensor(c16[:, :, :], before[:, :, :],
                                       nsl[:, :].unsqueeze(1).to_broadcast([P, NE, NE]), ALU.mult))
                step(dve.tensor_reduce(first[:, :], c16[:, :, :], AX.X, ALU.add))
                step(dve.tensor_tensor(nsl[:, :], nsl[:, :], first[:, :], ALU.add))
                BS = [P, SW, NE]
                step(dve.tensor_tensor(c32[:, :, :], sno[:, :].unsqueeze(2).to_broadcast(BS),
                                       nsl[:, :].unsqueeze(1).to_broadcast(BS), ALU.is_ge))
                step(dve.tensor_reduce(sx[:, :], c32[:, :, :], AX.X, ALU.add))
                step(dve.tensor_copy(sxi[:, SW:SW + NE], nsl[:, :]))
                step(dve.tensor_scalar(sxi[:, 0:SW], sx[:, :], NE - 1.0, None, ALU.min))
                assert done == SX_DONE, done
                for k in range(2):
                    step(dve.tensor_tensor(t16[:, :, :], O[:, k, :, :], rank[:, :, :], ALU.mult))
                    step(dve.tensor_reduce(K[:, k, :], t16[:, :, :], AX.X, ALU.add))
                    step(dve.tensor_tensor(t16[:, :, :], O[:, k, :, :],
                                           first[:, :].unsqueeze(1).to_broadcast([P, N, NE]), ALU.mult))
                    step(dve.tensor_reduce(S[:, k, :], t16[:, :, :], AX.X, ALU.add))
                f2 = lambda a: a[:, :, :].rearrange("p k n -> p (k n)")
                B8 = [P, 2 * N, N - 1]
                step(dve.tensor_tensor(c8[:, :, :], f2(K).unsqueeze(2).to_broadcast(B8),
                                       thr[:, 1:N].unsqueeze(1).to_broadcast(B8), ALU.is_ge))
                step(dve.tensor_reduce(f2(fl), c8[:, :, :], AX.X, ALU.add))
                step(dve.scalar_tensor_tensor(out=f2(r), in0=f2(fl), scalar=-float(P), in1=f2(K),
                                              op0=ALU.mult, op1=ALU.add))
                step(dve.tensor_tensor(f2(S), f2(S), f2(fl), ALU.add))
                step(dve.scalar_tensor_tensor(out=at[:, :], in0=f2(r), scalar=float(SW), in1=f2(S),
                                              op0=ALU.mult, op1=ALU.add))
                step(dve.scalar_tensor_tensor(out=pos[:, :], in0=f2(S), scalar=float(P), in1=f2(r),
                                              op0=ALU.mult, op1=ALU.add))
                assert done == AT_DONE, done

                def transposed(j):
                    ps_xT.wait(dve, j, 1)
                    ps_hid.wait(dve, j)
                    dve.tensor_copy(xT[:, 4:8, :], tp[:, 4:8, :]).then_inc(d_xT.sem, 1)

                def silu(j, s):
                    step = lambda name, ins: (hidden.did(ins, name), hidden.after(dve, j, name))
                    a_exp.wait(dve, j, 1)
                    step("one", dve.tensor_scalar(hs[:, :], hs[:, :], 1.0, None, ALU.add))
                    step("rec", dve.reciprocal(hs[:, :], hs[:, :]))
                    step("sil", dve.tensor_tensor(hs[:, :], hs[:, :], hid[s][:, 0:DE], ALU.mult))
                    ps_hT.wait(dve, j)
                    step("hh", dve.tensor_tensor(hh[:, :], hs[:, :], hid[s][:, DE:2 * DE], ALU.mult))

                def output(j, s, fill):
                    ps_out.wait(dve, j, 1)
                    ys_out[s].wait(dve, fill)
                    dve.tensor_copy(yo[s][:, 512:1024], acc[:, 512:1024]).then_inc(d_out.sem, 1)

                def slot(j, s, fill):
                    transposed(j + 1)
                    silu(j, s)
                    output(j - 1, 1 - s, fill)

                transposed(0)
                transposed(1)
                silu(0, 0)
                with dve.Fori(0, NS - 1) as i:
                    slot(i * 2 + 1, 1, i)
                    slot(i * 2 + 2, 0, i)
                silu(SLOTS - 1, 1)
                output(SLOTS - 2, 0, NS - 1)
                output(SLOTS - 1, 1, NS - 1)

                def weigh(n, s, i, T):
                    tr = slice(0, T)
                    step = lambda name, ins: (y_dve.did(ins, name), y_dve.after(dve, n, name))
                    step("wy", dve.tensor_copy(wy[tr, :], wt[tr, :, bass.ds(n, 1)].rearrange("p k o -> p (k o)")))
                    gy_in[s].wait(dve, i)
                    yt_out[s].wait(dve, i)
                    step("a", dve.scalar_tensor_tensor(out=yt[s][tr, :], in0=gy[s][0][tr, :], scalar=wy[tr, 0:1],
                                                       in1=rows(n, T), op0=ALU.mult, op1=ALU.add))
                    step("b", dve.scalar_tensor_tensor(out=yt[s][tr, :], in0=gy[s][1][tr, :], scalar=wy[tr, 1:2],
                                                       in1=yt[s][tr, :], op0=ALU.mult, op1=ALU.add))

                with dve.Fori(0, PT // 2) as i:
                    weigh(i * 2, 0, i, P)
                    weigh(i * 2 + 1, 1, i, P)
                weigh(PT, 0, PT // 2, N_DEC)


G4_DONE = 6
PD_DONE = G4_DONE + 14
A_DONE = PD_DONE + 4
SX_DONE = A_DONE + 5 + 2 + TILES + 1 + 9
AT_DONE = SX_DONE + 8 + 6


def routing_constants():
    f = lambda a: np.ascontiguousarray(a, np.float32)
    rep = lambda a: f(np.tile(a[None], (P,) + (1,) * a.ndim))
    e = np.arange(NE)
    return {"m_tri": f(np.arange(P)[:, None] < np.arange(P)[None, :]), "m_ones": f(np.ones((P, P))),
            "m_pri": rep(np.array([4, 3, 2, 1])), "m_thr": rep(np.arange(TILES) * P),
            "m_before": rep((e[None, :] < e[:, None]) * 1), "m_sno": rep(np.arange(SW)),
            "m_tid": (np.arange(P)[:, None] + P * np.arange(TILES)[None, :]).astype(np.uint32)}


def multiplicity(dist):
    n = np.zeros(dist.shape, np.float32)
    for window, dil in ((128, 1), (512, 4), (2048, 16)):
        n += (dist >= 0) & (dist <= window) & (dist % dil == 0)
    return n


def additive(n):
    return np.where(n > 0, np.log(np.maximum(n, 1)) / SCALE, NEG).astype(np.float32)


def constants():
    q, x = np.arange(P)[:, None], np.arange(PT * P + 3 * P * 3 + P * 2)[None, :]
    dist = q + (PT + 1) * P - np.arange((2 * PT + 1) * P)[None, :]
    c = np.arange((PT + 1) * 8 + 64)[None, :]
    block = c - 8 * (PT + 1)
    cmp_ok = 16 * block + 31 <= q
    return {
        "ident": np.eye(P, dtype=np.float32),
        "mask_a": additive(multiplicity(dist)),
        "mask_causal": additive(dist >= 0),
        "mask_win": additive((dist >= 0) & (dist <= CWIN)),
        "mask_cmp": additive(cmp_ok),
    }


def sample_constants():
    q, k = np.arange(DEC_S)[:, None], np.arange(PAST + DEC_S)[None, :]
    return {"mask_sa": np.tile(additive(multiplicity(PAST + q - k)), (HA, 1))}


def chunk_tables(T, block):
    u, c = np.arange(T)[:, None], np.arange(T)[None, :]
    same = u // block == c // block
    sums, pairs, m = [], [], block // 2
    while m:
        r = c // (2 * m) * 2 * m + m - 1
        second = c > r
        sums.append(np.where(second, (u > r) & (u <= c), (u > c) & (u <= r)))
        pairs.append((u // (2 * m) == c // (2 * m)) & (u // m % 2 == 0) & (c // m % 2 == 1))
        m //= 2
    sums.append(same & (u <= c))
    pairs.append(u == c)
    return (np.concatenate(sums, 1).astype(np.float32), (same & (u > c)).astype(np.float32),
            np.concatenate(pairs, 1).astype(np.float32))


def recurrence_constants():
    a, b = chunk_tables(P, P), chunk_tables(N_DEC, DEC_S)
    rows = (np.arange(N_DEC)[:, None] // DEC_S == np.arange(DEC_B)[None, :]).astype(np.float32)
    return {"b_sums": a[0], "b_suf": a[1], "b_pair": a[2], "bs_sums": b[0], "bs_suf": b[1],
            "bs_pair": b[2], "bs_rows": rows, "bs_cols": np.tile(rows.T[None], (P, 1, 1))}


def nsa_constants():
    cs, ss = np.arange(NCMP)[:, None] * 16, np.arange(17)[None, :] * 64
    share = np.maximum(np.minimum(cs + 31, ss + 63) - np.maximum(cs, ss) + 1, 0) / 32
    row = np.arange(64)
    g, q = row // 32, row % 8
    rsum = (g[:, None] == g[None, :]) & (q[:, None] == q[None, :]) & (row[:, None] % 32 < 24)
    ones2 = np.kron(np.eye(2), np.ones((HD, HD)))
    f = lambda a: np.ascontiguousarray(a, np.float32)
    return {"share": f(share), "rsum": f(rsum), "ones2": f(ones2), "blk": f(np.tile(np.arange(16), (64, 1))),
            "mask_new": additive(np.arange(8)[None, :] <= q[:, None]),
            "mask_sw": additive(np.arange(CWIN)[None, :] >= q[:, None])}


def tables():
    return {**constants(), **sample_constants(), **recurrence_constants(), **nsa_constants(),
            **routing_constants()}


def build(nc, t):
    rows = lambda n: slice(n * P, (n + 1) * P)
    mask = lambda name: lambda n, first, number: t[name][:, (PT + 1 + first - n) * P:(PT + 1 + first - n + number) * P]
    aq = lambda n: t["zr"][rows(n), Z_AQ:Z_AQ + 384]
    cq = lambda n: t["zr"][rows(n), Z_CQ:Z_CQ + 384]
    branch = lambda b: lambda n: t["oc"][rows(n), b, :, :].rearrange("p h d -> p (h d)")
    units_a = [(h // 2, h % 2, h // 2, h) for h in range(HA)]
    units_c = [(r, g, 0, g) for g in range(GC) for r in range(RC)]
    project(nc, t)
    sample_a(nc, t)
    hgrn(nc, t)
    sample_c(nc, t)
    sets = [(t["a_kv"][0:SEQ, 0:384], t["a_kv"][0:SEQ, 384:768], P),
            (t["pc"][:, 0:P], t["pc"][:, P:2 * P], HD // 2),
            (t["c_kv"][0:SEQ, 256:384], t["c_kv"][0:SEQ, 384:512], P),
            (t["c_win"][0:SEQ, 0:P], t["c_win"][0:SEQ, P:2 * P], P)]
    prompt_attention(nc, t, sets, [
        (0, aq, mask("mask_a"), lambda n: t["cat"][rows(n), 0:384], units_a, chunk_plan(PT)),
        (1, cq, lambda n, first, number: t["mask_cmp"][:, (PT + 1 - n) * 8:(PT + 1 - n) * 8 + HD], branch(0),
         units_c, [(0, 2)] * PT),
        (2, cq, mask("mask_causal"), branch(1), units_c, chunk_plan(PT)),
        (3, cq, mask("mask_win"), branch(2), units_c, chunk_plan(CWIN // P))])
    mix_and_experts(nc, t)


def kernel(x_prompt, x_sample, cache_a_kv, state_b, cache_c_kv, cache_c_win, page_table, **weights):
    import concourse.bacc as bacc
    from concourse.bass_utils import run_bass_kernel_spmd as run

    f = lambda a: np.ascontiguousarray(a)
    x = np.zeros(((TILES + 1) * P, D), np.float32)
    x[:SEQ] = x_prompt[0]
    x[SEQ:N_TOK] = np.reshape(x_sample, (N_DEC, D))
    ins = {"x": x, "cache_a": f(cache_a_kv[0]).reshape(DEC_B, PAST, 768),
           "cache_w": f(cache_c_win[0]).reshape(DEC_B, CWIN, 256),
           "cache_c": f(cache_c_kv[0]).reshape(-1, P, 512),
           "page_table": f(page_table), "state_b": f(state_b[0]), **tables()}
    ins.update({k: f(v) for k, v in weights.items()})
    outs = {"y": (N_TOK, D), "a_kv": (TILES * P, 768), "c_kv": (TILES * P, 512),
            "c_win": (TILES * P, 256), "a_s": (DEC_B, PAST, 768), "w_s": (DEC_B, CWIN, 256),
            "s_p": (HB, HD, HD), "s_s": (DEC_B, HB, HD, HD)}
    scratch = {"zr": ((PT + 2) * P, Z_W), "cat": (N_TOK, D), "oc": (N_TOK, 3, HC, HD), "pc": (HD, 2 * P),
               "h2": (N_TOK, D), "ys": (SLOTS * P, D)}
    tables_of_int = {"tok_at": ((P * SW, 1), U32), "slot_expert": ((1, SW + NE), I32)}
    nc = bacc.Bacc("TRN2", target_bir_lowering=False, num_devices=1)
    t = {}
    for name, a in ins.items():
        t[name] = nc.dram_tensor("in_" + name, a.shape, mybir.dt.from_np(a.dtype), kind="ExternalInput").ap()
    for name, shape in outs.items():
        t[name] = nc.dram_tensor("out_" + name, shape, F32, kind="ExternalOutput").ap()
    for name, shape in scratch.items():
        t[name] = nc.dram_tensor("tmp_" + name, shape, F32, kind="Internal").ap()
    for name, (shape, dt) in tables_of_int.items():
        t[name] = nc.dram_tensor("tmp_" + name, shape, dt, kind="Internal").ap()
    build(nc, t)
    r = run(nc, [{"in_" + k: a for k, a in ins.items()}], core_ids=[0]).results[0]
    o = {k: r["out_" + k] for k in outs}
    kv = lambda a, *s: a.reshape(1, *s)
    return (o["y"][:SEQ].reshape(1, SEQ, D), o["y"][SEQ:N_TOK].reshape(DEC_B, DEC_S, D),
            kv(o["a_kv"][:SEQ], 1, SEQ, 2, HA, HD), kv(o["a_s"], DEC_B, PAST, 2, HA, HD),
            kv(o["s_p"], 1, HB, HD, HD), kv(o["s_s"], DEC_B, HB, HD, HD),
            kv(o["c_kv"][:SEQ], 1, SEQ, 4, GC, HD), kv(o["c_kv"][SEQ:N_TOK], DEC_B, DEC_S, 4, GC, HD),
            kv(o["c_win"][SEQ - CWIN:SEQ], 1, CWIN, 2, GC, HD), kv(o["w_s"], DEC_B, CWIN, 2, GC, HD))
```
